# Optimizing a Trainium2 kernel written in Bass

```python
import math
import jax, jax.numpy as jnp
from jax import lax
import numpy as np

D_MODEL = 1024
BATCH = 1
SEQ = 256
DEPTH = 2

HEAD_DIM = 64
MIX_WIDTH = D_MODEL
DIFF_WIDTH = MIX_WIDTH // 2
MOBA_WIDTH = MIX_WIDTH - DIFF_WIDTH
DIFF_HEADS = DIFF_WIDTH // (2 * HEAD_DIM)
DIFF_V_DIM = 2 * HEAD_DIM
MOBA_HEADS = MOBA_WIDTH // HEAD_DIM
PROJ_WIDTH = 3 * DIFF_WIDTH + 3 * MOBA_WIDTH
N_BIAS_HEADS = DIFF_HEADS + MOBA_HEADS
D_FF = ((8 * D_MODEL // 3 + 127) // 128) * 128
CONV_WIDTH = 3
DIFF_Q_BLOCK = 128
MOBA_BLOCK = 256
MOBA_TOPK = 3
MOBA_Q_CHUNK = 64
REL_BUCKETS = 32
REL_MAX_EXACT = REL_BUCKETS // 2
REL_MAX_DISTANCE = 1024
NORM_EPS = 1e-6


def rms_norm(x, g):
    xf = x.astype(jnp.float32)
    y = xf * lax.rsqrt(jnp.mean(xf * xf, axis=-1, keepdims=True) + NORM_EPS)
    return (y * g).astype(x.dtype)

def rel_bucket(dist):
    n = jnp.maximum(dist, 0)
    nf = jnp.maximum(n, REL_MAX_EXACT).astype(jnp.float32)
    large = REL_MAX_EXACT + (jnp.log(nf / REL_MAX_EXACT) / math.log(REL_MAX_DISTANCE / REL_MAX_EXACT)
                             * (REL_BUCKETS - REL_MAX_EXACT)).astype(jnp.int32)
    large = jnp.minimum(large, REL_BUCKETS - 1)
    return jnp.where(n < REL_MAX_EXACT, n, large)

def diff_attention(q, k, v, lam, lam_init, sub_g, bias_tab):
    B, S, H = q.shape[:3]
    nqb = S // DIFF_Q_BLOCK
    qb = q.reshape(B, nqb, DIFF_Q_BLOCK, H, 2, HEAD_DIM).transpose(1, 0, 2, 3, 4, 5)
    kpos = jnp.arange(S)
    scale = HEAD_DIM ** -0.5

    def block(args):
        qblk, i = args
        qpos = i * DIFF_Q_BLOCK + jnp.arange(DIFF_Q_BLOCK)
        dist = qpos[:, None] - kpos[None, :]
        bias = jnp.moveaxis(bias_tab[rel_bucket(dist)], -1, 0)
        logits = jnp.einsum('bqhmd,bkhmd->bmhqk', qblk, k).astype(jnp.float32) * scale + bias
        logits = jnp.where(dist >= 0, logits, -jnp.inf)
        p = jax.nn.softmax(logits, axis=-1)
        a = p[:, 0] - lam * p[:, 1]
        return jnp.einsum('bhqk,bkhe->bqhe', a.astype(v.dtype), v)

    out = lax.map(block, (qb, jnp.arange(nqb)))
    out = out.transpose(1, 0, 2, 3, 4).reshape(B, S, H, DIFF_V_DIM)
    out = rms_norm(out, sub_g) * (1.0 - lam_init)
    return out.reshape(B, S, H * DIFF_V_DIM)

def moba_attention(q, k, v, bias_tab):
    B, S, H, D = q.shape
    nb = -(-S // MOBA_BLOCK)
    pad = nb * MOBA_BLOCK - S
    padw = ((0, 0), (0, pad), (0, 0), (0, 0))
    kb = jnp.pad(k, padw).reshape(B, nb, MOBA_BLOCK, H, D).transpose(0, 3, 1, 2, 4)
    vb = jnp.pad(v, padw).reshape(B, nb, MOBA_BLOCK, H, D).transpose(0, 3, 1, 2, 4)
    kmean = jnp.mean(kb.astype(jnp.float32), axis=3)
    gate = jnp.einsum('bshd,bhnd->bhsn', q.astype(jnp.float32), kmean)
    past = jnp.arange(nb)[None, :] < (jnp.arange(S) // MOBA_BLOCK)[:, None]
    gate = jnp.where(past, gate, -jnp.inf)
    topk = min(MOBA_TOPK, nb)
    sel_score, sel_idx = lax.top_k(gate, topk)
    sel_valid = jnp.isfinite(sel_score)

    nc = S // MOBA_Q_CHUNK
    qc = q.reshape(B, nc, MOBA_Q_CHUNK, H, D).transpose(1, 0, 3, 2, 4)
    idx_c = sel_idx.reshape(B, H, nc, MOBA_Q_CHUNK, topk).transpose(2, 0, 1, 3, 4)
    val_c = sel_valid.reshape(B, H, nc, MOBA_Q_CHUNK, topk).transpose(2, 0, 1, 3, 4)
    bi = jnp.arange(B)[:, None, None, None]
    hi = jnp.arange(H)[None, :, None, None]
    hi5 = jnp.arange(H)[None, :, None, None, None]
    tab_h = bias_tab.T
    j = jnp.arange(MOBA_BLOCK)
    scale = D ** -0.5
    n_sel = topk * MOBA_BLOCK

    def chunk(args):
        qch, idx, valid, c = args
        qpos = c * MOBA_Q_CHUNK + jnp.arange(MOBA_Q_CHUNK)
        gk = kb[bi, hi, idx]
        gv = vb[bi, hi, idx]
        dist_p = qpos[None, None, :, None, None] - (idx[..., None] * MOBA_BLOCK + j)
        bias_p = tab_h[hi5, rel_bucket(dist_p)]
        lp = jnp.einsum('bhqd,bhqnjd->bhqnj', qch, gk).astype(jnp.float32) * scale + bias_p
        lp = jnp.where(valid[..., None], lp, -jnp.inf).reshape(B, H, MOBA_Q_CHUNK, n_sel)
        ob = (c * MOBA_Q_CHUNK) // MOBA_BLOCK
        ko = lax.dynamic_index_in_dim(kb, ob, axis=2, keepdims=False)
        vo = lax.dynamic_index_in_dim(vb, ob, axis=2, keepdims=False)
        dist_o = qpos[:, None] - (ob * MOBA_BLOCK + j)[None, :]
        bias_o = tab_h[:, rel_bucket(dist_o)]
        lo = jnp.einsum('bhqd,bhjd->bhqj', qch, ko).astype(jnp.float32) * scale + bias_o
        lo = jnp.where(dist_o >= 0, lo, -jnp.inf)
        p = jax.nn.softmax(jnp.concatenate([lp, lo], axis=-1), axis=-1).astype(v.dtype)
        pp = p[..., :n_sel].reshape(B, H, MOBA_Q_CHUNK, topk, MOBA_BLOCK)
        po = p[..., n_sel:]
        return (jnp.einsum('bhqnj,bhqnje->bhqe', pp, gv)
                + jnp.einsum('bhqj,bhje->bhqe', po, vo))

    out = lax.map(chunk, (qc, idx_c, val_c, jnp.arange(nc)))
    return out.transpose(1, 0, 3, 2, 4).reshape(B, S, H * D)

def causal_dwconv(u, w, b):
    C = u.shape[-1]
    y = lax.conv_general_dilated(u, w[:, None, :], window_strides=(1,),
                                 padding=[(CONV_WIDTH - 1, 0)],
                                 dimension_numbers=('NWC', 'WIO', 'NWC'),
                                 feature_group_count=C)
    return y + b

def conv_ffn(h, w_up, conv_w, conv_b, w_down):
    u = causal_dwconv(h @ w_up, conv_w, conv_b)
    g, up = jnp.split(u, 2, axis=-1)
    return (jax.nn.silu(g) * up) @ w_down

def first_inputs(seed: int = 0) -> dict:
    key = jax.random.key(seed)
    ks = jax.random.split(key, 14)
    f32 = jnp.float32
    nrm = lambda k, s: jax.random.normal(k, s, f32)
    resid = (2 * DEPTH) ** -0.5
    return {
        'x': nrm(ks[0], (BATCH, SEQ, D_MODEL)),
        'ln_attn_g': 1.0 + 0.02 * nrm(ks[1], (DEPTH, D_MODEL)),
        'w_in': nrm(ks[2], (DEPTH, D_MODEL, PROJ_WIDTH)) * D_MODEL ** -0.5,
        'qk_norm_g': 1.0 + 0.02 * nrm(ks[3], (DEPTH, 4, HEAD_DIM)),
        'diff_lambda': 0.1 * nrm(ks[4], (DEPTH, 4, HEAD_DIM)),
        'diff_subln_g': 1.0 + 0.02 * nrm(ks[5], (DEPTH, DIFF_V_DIM)),
        'w_out': nrm(ks[6], (DEPTH, MIX_WIDTH, D_MODEL)) * MIX_WIDTH ** -0.5 * resid,
        'ln_ffn_g': 1.0 + 0.02 * nrm(ks[7], (DEPTH, D_MODEL)),
        'w_up': nrm(ks[8], (DEPTH, D_MODEL, 2 * D_FF)) * D_MODEL ** -0.5,
        'conv_w': nrm(ks[9], (DEPTH, CONV_WIDTH, 2 * D_FF)) * CONV_WIDTH ** -0.5,
        'conv_b': 0.02 * nrm(ks[10], (DEPTH, 2 * D_FF)),
        'w_down': nrm(ks[11], (DEPTH, D_FF, D_MODEL)) * D_FF ** -0.5 * resid,
        'rel_bias': 0.5 * nrm(ks[12], (REL_BUCKETS, N_BIAS_HEADS)),
    }

def first_block(x, ln_attn_g, w_in, qk_norm_g, diff_lambda, diff_subln_g, w_out,
              ln_ffn_g, w_up, conv_w, conv_b, w_down, rel_bias):
    B, S = x.shape[:2]
    cuts = [DIFF_WIDTH, 2 * DIFF_WIDTH, 3 * DIFF_WIDTH,
            3 * DIFF_WIDTH + MOBA_WIDTH, 3 * DIFF_WIDTH + 2 * MOBA_WIDTH]
    bias_diff = rel_bias[:, :DIFF_HEADS]
    bias_moba = rel_bias[:, DIFF_HEADS:]
    for i in range(DEPTH):
        lam_init = 0.8 - 0.6 * math.exp(-0.3 * i)
        h = rms_norm(x, ln_attn_g[i])
        dq, dk, dv, mq, mk, mv = jnp.split(h @ w_in[i], cuts, axis=-1)
        dq = rms_norm(dq.reshape(B, S, DIFF_HEADS, 2, HEAD_DIM), qk_norm_g[i, 0])
        dk = rms_norm(dk.reshape(B, S, DIFF_HEADS, 2, HEAD_DIM), qk_norm_g[i, 1])
        dv = dv.reshape(B, S, DIFF_HEADS, DIFF_V_DIM)
        lf = diff_lambda[i].astype(jnp.float32)
        lam = jnp.exp(jnp.sum(lf[0] * lf[1])) - jnp.exp(jnp.sum(lf[2] * lf[3])) + lam_init
        y_diff = diff_attention(dq, dk, dv, lam, lam_init, diff_subln_g[i], bias_diff)
        mq = rms_norm(mq.reshape(B, S, MOBA_HEADS, HEAD_DIM), qk_norm_g[i, 2])
        mk = rms_norm(mk.reshape(B, S, MOBA_HEADS, HEAD_DIM), qk_norm_g[i, 3])
        mv = mv.reshape(B, S, MOBA_HEADS, HEAD_DIM)
        y_moba = moba_attention(mq, mk, mv, bias_moba)
        x = x + jnp.concatenate([y_diff, y_moba], axis=-1) @ w_out[i]
        x = x + conv_ffn(rms_norm(x, ln_ffn_g[i]), w_up[i], conv_w[i], conv_b[i], w_down[i])
    return x


GRID_W = 64
CTX_LEN = 256
MIX_WIDTH_2 = D_MODEL
A_HEADS = MIX_WIDTH_2 // (2 * HEAD_DIM)
A_WIDTH = A_HEADS * HEAD_DIM
DECAY_LORA = 64
ICLR_LORA = 64
GATE_LORA = 128
B_HEADS = MIX_WIDTH_2 // (2 * HEAD_DIM)
B_KV_HEADS = 2
WINDOW = 128
BLOCK = 128
C_HEADS = MIX_WIDTH_2 // (2 * HEAD_DIM)
NA_KH = 8
NA_KW = 16
NA_QC = 16
NA_KC = 32
D_HEADS = MIX_WIDTH_2 // (2 * HEAD_DIM)
D_KV_HEADS = 2
D_FF_2 = 4 * D_MODEL
ROPE_BASE = 10000.0
GN_EPS = 64e-5
NEG_INF = -1e30
ATTN_SCALE = HEAD_DIM ** -0.5
N_EVEN = (DEPTH + 1) // 2
N_ODD = DEPTH // 2
A_IN = 3 * A_WIDTH + 2 * DECAY_LORA + 2 * ICLR_LORA + GATE_LORA
B_IN = (B_HEADS + 2 * B_KV_HEADS) * HEAD_DIM
C_IN = 3 * C_HEADS * HEAD_DIM
D_IN = (D_HEADS + 2 * D_KV_HEADS) * HEAD_DIM
EVEN_IN = A_IN + B_IN
ODD_IN = C_IN + D_IN
A_SPLITS = (A_WIDTH, 2 * A_WIDTH, 3 * A_WIDTH, 3 * A_WIDTH + 2 * DECAY_LORA,
            3 * A_WIDTH + 2 * DECAY_LORA + 2 * ICLR_LORA)


def rms_norm_2(x, g):
    xf = x.astype(jnp.float32)
    y = xf * lax.rsqrt(jnp.mean(xf * xf, axis=-1, keepdims=True) + NORM_EPS)
    return (y * g.astype(jnp.float32)).astype(x.dtype)

def modulate(h, gain, shift, scale):
    return rms_norm_2(h, gain) * (1 + scale) + shift

def sqrelu_mlp(u, w1, w2):
    return jnp.square(jax.nn.relu(u @ w1)) @ w2

def axial_angles(n_tok):
    t = jnp.arange(n_tok, dtype=jnp.int32)
    n_freq = HEAD_DIM // 4
    inv_freq = ROPE_BASE ** (-jnp.arange(n_freq, dtype=jnp.float32) / n_freq)
    row = (t // GRID_W).astype(jnp.float32)[:, None] * inv_freq
    col = (t % GRID_W).astype(jnp.float32)[:, None] * inv_freq
    return row, col

def _rotate(x, ang):
    f = ang.shape[-1]
    cos = jnp.cos(ang)[None, :, None, :]
    sin = jnp.sin(ang)[None, :, None, :]
    x1 = x[..., :f].astype(jnp.float32)
    x2 = x[..., f:].astype(jnp.float32)
    return jnp.concatenate([x1 * cos - x2 * sin, x1 * sin + x2 * cos], axis=-1).astype(x.dtype)

def axial_rope(x, ang):
    half = HEAD_DIM // 2
    return jnp.concatenate([_rotate(x[..., :half], ang[0]), _rotate(x[..., half:], ang[1])], axis=-1)

def split_qkv(p, hq, hkv):
    bn, s, _ = p.shape
    q, k, v = jnp.split(p, [hq * HEAD_DIM, (hq + hkv) * HEAD_DIM], axis=-1)
    return (q.reshape(bn, s, hq, HEAD_DIM), k.reshape(bn, s, hkv, HEAD_DIM), v.reshape(bn, s, hkv, HEAD_DIM))

def softmax_with_sink(s, sink):
    sk = jnp.broadcast_to(sink.astype(jnp.float32)[:, :, None, None], s.shape[:-1] + (1,))
    return jax.nn.softmax(jnp.concatenate([s, sk], axis=-1), axis=-1)[..., :-1]

def context_attention(q, k, v, sink=None):
    bn, l, h, d = q.shape
    hkv = k.shape[2]
    qg = q.reshape(bn, l, hkv, h // hkv, d)
    s = jnp.einsum('blkgd,bckd->bkglc', qg, k).astype(jnp.float32) * ATTN_SCALE
    p = jax.nn.softmax(s, axis=-1) if sink is None else softmax_with_sink(s, sink)
    o = jnp.einsum('bkglc,bckd->blkgd', p.astype(v.dtype), v)
    return o.reshape(bn, l, h * d)

def centred_shift(p, mu_prev, mu_next):
    prev = jnp.pad(p, ((0, 0), (1, 0), (0, 0)))[:, :-1]
    nxt = jnp.pad(p, ((0, 0), (0, 1), (0, 0)))[:, 1:]
    return p + mu_prev * (prev - p) + mu_next * (nxt - p)

def rwkv7_prepare(pa, prm):
    p = centred_shift(pa, prm['mu_prev'], prm['mu_next']).astype(jnp.float32)
    bn, s, _ = p.shape
    r, k, v, wl, al, gl = jnp.split(p, A_SPLITS, axis=-1)
    wl = wl.reshape(bn, s, 2, DECAY_LORA)
    al = al.reshape(bn, s, 2, ICLR_LORA)
    w_raw = prm['w0'] + jnp.einsum('bsdl,dlc->bsdc', jnp.tanh(wl), prm['w2'])
    decay = jnp.exp(-jnp.exp(-jax.nn.softplus(-w_raw) - 0.5))
    iclr = jax.nn.sigmoid(prm['a0'] + jnp.einsum('bsdl,dlc->bsdc', al, prm['a2']))
    g = jax.nn.sigmoid(gl) @ prm['g2']
    kk = (k * prm['k_k']).reshape(bn, s, A_HEADS, HEAD_DIM)
    kk = kk / jnp.maximum(jnp.sqrt(jnp.sum(kk * kk, axis=-1, keepdims=True)), 1e-12)
    k_dir = k[:, :, None, :] * (1 + (iclr - 1) * prm['k_a'])
    heads = lambda t: t.reshape(t.shape[:-1] + (A_HEADS, HEAD_DIM))
    return dict(r=heads(r), v=heads(v), g=g, kk=kk, k=heads(k_dir), w=heads(decay), a=heads(iclr))

def rwkv7_scan(f, d, s0, reverse):
    def step(state, inp):
        r_t, w_t, k_t, v_t, kk_t, a_t = inp
        sa = jnp.einsum('bhvk,bhk->bhv', state, -kk_t)
        state = (state * w_t[:, :, None, :] + sa[..., None] * (kk_t * a_t)[:, :, None, :]
                 + v_t[..., None] * k_t[:, :, None, :])
        return state, jnp.einsum('bhvk,bhk->bhv', state, r_t)
    seq = (f['r'], f['w'][:, :, d], f['k'][:, :, d], f['v'], f['kk'], f['a'][:, :, d])
    xs = tuple(jnp.moveaxis(t, 1, 0) for t in seq)
    s_last, ys = lax.scan(step, s0, xs, reverse=reverse)
    return s_last, jnp.moveaxis(ys, 0, 1)

def rwkv7_output(f, y, prm, dtype):
    bn, s = y.shape[:2]
    mu = jnp.mean(y, axis=-1, keepdims=True)
    var = jnp.mean(jnp.square(y - mu), axis=-1, keepdims=True)
    yn = ((y - mu) * lax.rsqrt(var + GN_EPS)).reshape(bn, s, A_WIDTH) * prm['gn_w'] + prm['gn_b']
    bonus = jnp.sum(f['r'][:, :, None] * f['k'] * prm['r_k'], axis=(2, 4))
    yn = yn + (bonus[..., None] * f['v']).reshape(bn, s, A_WIDTH)
    return (yn * f['g']).astype(dtype)

def rwkv7_mixer(pa_ctx, pa_lat, prm, need_ctx):
    fc = rwkv7_prepare(pa_ctx, prm)
    fl = rwkv7_prepare(pa_lat, prm)
    zero = jnp.zeros((pa_lat.shape[0], A_HEADS, HEAD_DIM, HEAD_DIM), jnp.float32)
    s_cf, yc_f = rwkv7_scan(fc, 0, zero, False)
    _, yl_f = rwkv7_scan(fl, 0, s_cf, False)
    s_cb, yc_b = rwkv7_scan(fc, 1, zero, True)
    _, yl_b = rwkv7_scan(fl, 1, s_cb, True)
    out_lat = rwkv7_output(fl, yl_f + yl_b, prm, pa_lat.dtype)
    out_ctx = rwkv7_output(fc, yc_f + yc_b, prm, pa_ctx.dtype) if need_ctx else None
    return out_lat, out_ctx

def banded_window_attention(q, k, v, k_ctx, v_ctx, sink):
    bn, s, h, d = q.shape
    hkv = k.shape[2]
    nb = s // BLOCK
    qb = q.reshape(bn, nb, BLOCK, hkv, h // hkv, d)

    def band(t):
        tp = jnp.pad(t, ((0, 0), (BLOCK, BLOCK), (0, 0), (0, 0)))
        return jnp.concatenate([tp[:, j * BLOCK: j * BLOCK + s].reshape(bn, nb, BLOCK, hkv, d)
                                for j in range(3)], axis=2)
    kb, vb = band(k), band(v)
    qi = np.arange(BLOCK)[:, None]
    kj = np.arange(3 * BLOCK)[None, :]
    kpos = (np.arange(nb) * BLOCK)[:, None, None] - BLOCK + kj[None]
    ok = (np.abs(kj - BLOCK - qi) <= WINDOW)[None] & (kpos >= 0) & (kpos < s)
    s_lat = jnp.einsum('bnqkgd,bnjkd->bnkgqj', qb, kb).astype(jnp.float32) * ATTN_SCALE
    s_lat = jnp.where(ok[None, :, None, None], s_lat, NEG_INF)
    s_ctx = jnp.einsum('bnqkgd,bckd->bnkgqc', qb, k_ctx).astype(jnp.float32) * ATTN_SCALE
    p = softmax_with_sink(jnp.concatenate([s_lat, s_ctx], axis=-1), sink)
    p_lat, p_ctx = p[..., :3 * BLOCK].astype(v.dtype), p[..., 3 * BLOCK:].astype(v.dtype)
    o = (jnp.einsum('bnkgqj,bnjkd->bnqkgd', p_lat, vb)
         + jnp.einsum('bnkgqc,bckd->bnqkgd', p_ctx, v_ctx))
    return o.reshape(bn, s, h * d)

def neighbourhood_tables(rows):
    kh = min(NA_KH, rows)
    r = np.arange(rows)
    row_idx = np.clip(r - kh // 2, 0, rows - kh)[:, None] + np.arange(kh)[None, :]
    dr = row_idx - r[:, None] + NA_KH - 1
    ncb = GRID_W // NA_QC
    q_col = np.arange(ncb)[:, None] * NA_QC + np.arange(NA_QC)[None, :]
    key_col = (np.clip(np.arange(ncb) * NA_QC - NA_KW // 2, 0, GRID_W - NA_KC)[:, None]
               + np.arange(NA_KC)[None, :])
    win_start = np.clip(q_col - NA_KW // 2, 0, GRID_W - NA_KW)[:, :, None]
    kc = key_col[:, None, :]
    col_ok = (kc >= win_start) & (kc < win_start + NA_KW)
    dc = np.clip(kc - q_col[:, :, None] + NA_KW - 1, 0, 2 * NA_KW - 2)
    return row_idx, dr, key_col, col_ok, dc

def neighbourhood_attention(q, k, v, k_ctx, v_ctx, rpb):
    bn, s, h, d = q.shape
    rows = s // GRID_W
    ncb = GRID_W // NA_QC
    row_idx, dr, key_col, col_ok, dc = neighbourhood_tables(rows)
    kh = row_idx.shape[1]

    def gather(t):
        return t.reshape(bn, rows, GRID_W, h, d)[:, row_idx][:, :, :, key_col]
    kg, vg = gather(k), gather(v)
    qg = q.reshape(bn, rows, ncb, NA_QC, h, d)
    s_lat = jnp.einsum('brmqhd,brtmjhd->brmhqtj', qg, kg).astype(jnp.float32) * ATTN_SCALE
    bias = rpb[:, dr[:, None, None, :, None], dc[None, :, :, None, :]]
    s_lat = s_lat + bias.transpose(1, 2, 0, 3, 4, 5).astype(jnp.float32)
    s_lat = jnp.where(col_ok[:, None, :, None, :], s_lat, NEG_INF)
    s_lat = s_lat.reshape(s_lat.shape[:-2] + (kh * NA_KC,))
    s_ctx = jnp.einsum('brmqhd,bchd->brmhqc', qg, k_ctx).astype(jnp.float32) * ATTN_SCALE
    p = jax.nn.softmax(jnp.concatenate([s_lat, s_ctx], axis=-1), axis=-1)
    p_lat = p[..., :kh * NA_KC].reshape(p.shape[:-1] + (kh, NA_KC)).astype(v.dtype)
    p_ctx = p[..., kh * NA_KC:].astype(v.dtype)
    o = (jnp.einsum('brmhqtj,brtmjhd->brmqhd', p_lat, vg)
         + jnp.einsum('brmhqc,bchd->brmqhd', p_ctx, v_ctx))
    return o.reshape(bn, s, h * d)

def global_block_attention(q, k, v, k_ctx, v_ctx):
    bn, s, h, d = q.shape
    hkv = k.shape[2]
    nb = s // BLOCK
    k_all = jnp.concatenate([k_ctx, k], axis=1)
    v_all = jnp.concatenate([v_ctx, v], axis=1)
    qb = q.reshape(bn, nb, BLOCK, hkv, h // hkv, d).transpose(1, 0, 2, 3, 4, 5)

    def one_block(qblk):
        sc = jnp.einsum('bqkgd,bskd->bkgqs', qblk, k_all).astype(jnp.float32) * ATTN_SCALE
        p = jax.nn.softmax(sc, axis=-1).astype(v_all.dtype)
        return jnp.einsum('bkgqs,bskd->bqkgd', p, v_all)
    o = lax.map(one_block, qb)
    return o.transpose(1, 0, 2, 3, 4, 5).reshape(bn, s, h * d)

def even_mixer(u_ctx, u_lat, w_in, w_out, a_prm, sink, rope_ang, need_ctx):
    p_ctx = u_ctx @ w_in
    p_lat = u_lat @ w_in
    a_lat, a_ctx = rwkv7_mixer(p_ctx[..., :A_IN], p_lat[..., :A_IN], a_prm, need_ctx)
    qc, kc, vc = split_qkv(p_ctx[..., A_IN:], B_HEADS, B_KV_HEADS)
    ql, kl, vl = split_qkv(p_lat[..., A_IN:], B_HEADS, B_KV_HEADS)
    ql, kl = axial_rope(ql, rope_ang), axial_rope(kl, rope_ang)
    sink_g = sink.reshape(B_KV_HEADS, B_HEADS // B_KV_HEADS)
    b_lat = banded_window_attention(ql, kl, vl, kc, vc, sink_g)
    out_lat = jnp.concatenate([a_lat, b_lat], axis=-1) @ w_out
    if not need_ctx:
        return out_lat, None
    b_ctx = context_attention(qc, kc, vc, sink_g)
    return out_lat, jnp.concatenate([a_ctx, b_ctx], axis=-1) @ w_out

def odd_mixer(u_ctx, u_lat, w_in, w_out, rpb, q_gain, k_gain, rope_ang, need_ctx):
    p_ctx = u_ctx @ w_in
    p_lat = u_lat @ w_in
    cq_c, ck_c, cv_c = split_qkv(p_ctx[..., :C_IN], C_HEADS, C_HEADS)
    cq_l, ck_l, cv_l = split_qkv(p_lat[..., :C_IN], C_HEADS, C_HEADS)
    c_lat = neighbourhood_attention(cq_l, ck_l, cv_l, ck_c, cv_c, rpb)
    dq_c, dk_c, dv_c = split_qkv(p_ctx[..., C_IN:], D_HEADS, D_KV_HEADS)
    dq_l, dk_l, dv_l = split_qkv(p_lat[..., C_IN:], D_HEADS, D_KV_HEADS)
    dq_c, dk_c = rms_norm_2(dq_c, q_gain), rms_norm_2(dk_c, k_gain)
    dq_l = axial_rope(rms_norm_2(dq_l, q_gain), rope_ang)
    dk_l = axial_rope(rms_norm_2(dk_l, k_gain), rope_ang)
    d_lat = global_block_attention(dq_l, dk_l, dv_l, dk_c, dv_c)
    out_lat = jnp.concatenate([c_lat, d_lat], axis=-1) @ w_out
    if not need_ctx:
        return out_lat, None
    c_ctx_o = context_attention(cq_c, ck_c, cv_c)
    d_ctx_o = context_attention(dq_c, dk_c, dv_c)
    return out_lat, jnp.concatenate([c_ctx_o, d_ctx_o], axis=-1) @ w_out

def second_inputs(seed: int = 0) -> dict:
    key = jax.random.key(seed)
    ks = iter(jax.random.split(key, 40))
    nrm = lambda shape, scale: scale * jax.random.normal(next(ks), shape, jnp.float32)
    unif = lambda shape, lo, hi: jax.random.uniform(next(ks), shape, jnp.float32, lo, hi)
    D = D_MODEL
    return {
        "x": nrm((BATCH, SEQ, D), 1.0),
        "c": nrm((BATCH, D), 1.0),
        "ctx": nrm((BATCH, CTX_LEN, D), 1.0),
        "c_ctx": nrm((D,), 1.0),
        "w_ada": nrm((DEPTH, D, 6 * D), 0.5 * D ** -0.5),
        "b_ada": nrm((DEPTH, 6 * D), 0.02),
        "g_pre_mix": 1.0 + nrm((DEPTH, D), 0.05),
        "g_post_mix": 1.0 + nrm((DEPTH, D), 0.05),
        "g_pre_ff": 1.0 + nrm((DEPTH, D), 0.05),
        "g_post_ff": 1.0 + nrm((DEPTH, D), 0.05),
        "w_in_even": nrm((N_EVEN, D, EVEN_IN), D ** -0.5),
        "w_in_odd": nrm((N_ODD, D, ODD_IN), D ** -0.5),
        "w_out": nrm((DEPTH, MIX_WIDTH_2, D), MIX_WIDTH_2 ** -0.5),
        "w_ff1": nrm((DEPTH, D, D_FF_2), D ** -0.5),
        "w_ff2": nrm((DEPTH, D_FF_2, D), D_FF_2 ** -0.5),
        "a_mu_prev": unif((N_EVEN, A_IN), 0.05, 0.45),
        "a_mu_next": unif((N_EVEN, A_IN), 0.05, 0.45),
        "a_w0": unif((N_EVEN, 2, A_WIDTH), -5.0, -0.5),
        "a_w2": nrm((N_EVEN, 2, DECAY_LORA, A_WIDTH), 0.1 * DECAY_LORA ** -0.5),
        "a_a0": nrm((N_EVEN, 2, A_WIDTH), 0.1),
        "a_a2": nrm((N_EVEN, 2, ICLR_LORA, A_WIDTH), 0.5 * ICLR_LORA ** -0.5),
        "a_g2": nrm((N_EVEN, GATE_LORA, A_WIDTH), GATE_LORA ** -0.5),
        "a_k_k": 0.85 + nrm((N_EVEN, A_WIDTH), 0.05),
        "a_k_a": 1.0 + nrm((N_EVEN, A_WIDTH), 0.05),
        "a_r_k": nrm((N_EVEN, A_HEADS, HEAD_DIM), 0.1),
        "a_gn_w": 1.0 + nrm((N_EVEN, A_WIDTH), 0.05),
        "a_gn_b": nrm((N_EVEN, A_WIDTH), 0.02),
        "b_sink": nrm((N_EVEN, B_HEADS), 0.5),
        "c_rpb": nrm((N_ODD, C_HEADS, 2 * NA_KH - 1, 2 * NA_KW - 1), 0.5),
        "d_q_gain": 1.0 + nrm((N_ODD, HEAD_DIM), 0.05),
        "d_k_gain": 1.0 + nrm((N_ODD, HEAD_DIM), 0.05),
    }

def second_block(x, c, ctx, c_ctx, w_ada, b_ada, g_pre_mix, g_post_mix, g_pre_ff, g_post_ff,
              w_in_even, w_in_odd, w_out, w_ff1, w_ff2,
              a_mu_prev, a_mu_next, a_w0, a_w2, a_a0, a_a2, a_g2, a_k_k, a_k_a, a_r_k, a_gn_w, a_gn_b,
              b_sink, c_rpb, d_q_gain, d_k_gain):
    rope_ang = axial_angles(x.shape[1])
    s_lat = jax.nn.silu(c)[:, None, :]
    s_ctx = jax.nn.silu(c_ctx)[None, None, :]
    h_lat, h_ctx = x, ctx
    for i in range(DEPTH):
        need_ctx = i < DEPTH - 1
        j = i // 2
        ml = jnp.split(s_lat @ w_ada[i] + b_ada[i], 6, axis=-1)
        mc = jnp.split(s_ctx @ w_ada[i] + b_ada[i], 6, axis=-1)
        u_lat = modulate(h_lat, g_pre_mix[i], ml[0], ml[1])
        u_ctx = modulate(h_ctx, g_pre_mix[i], mc[0], mc[1])
        if i % 2 == 0:
            a_prm = dict(mu_prev=a_mu_prev[j], mu_next=a_mu_next[j], w0=a_w0[j], w2=a_w2[j],
                         a0=a_a0[j], a2=a_a2[j], g2=a_g2[j], k_k=a_k_k[j], k_a=a_k_a[j],
                         r_k=a_r_k[j], gn_w=a_gn_w[j], gn_b=a_gn_b[j])
            o_lat, o_ctx = even_mixer(u_ctx, u_lat, w_in_even[j], w_out[i], a_prm, b_sink[j], rope_ang, need_ctx)
        else:
            o_lat, o_ctx = odd_mixer(u_ctx, u_lat, w_in_odd[j], w_out[i], c_rpb[j], d_q_gain[j], d_k_gain[j],
                                     rope_ang, need_ctx)
        h_lat = h_lat + ml[2] * rms_norm_2(o_lat, g_post_mix[i])
        f_lat = sqrelu_mlp(modulate(h_lat, g_pre_ff[i], ml[3], ml[4]), w_ff1[i], w_ff2[i])
        h_lat = h_lat + ml[5] * rms_norm_2(f_lat, g_post_ff[i])
        if need_ctx:
            h_ctx = h_ctx + mc[2] * rms_norm_2(o_ctx, g_post_mix[i])
            f_ctx = sqrelu_mlp(modulate(h_ctx, g_pre_ff[i], mc[3], mc[4]), w_ff1[i], w_ff2[i])
            h_ctx = h_ctx + mc[5] * rms_norm_2(f_ctx, g_post_ff[i])
    return h_lat


def setup_inputs(seed=0):
    out = dict(first_inputs(seed))
    for name, value in second_inputs(seed + 1).items():
        if name != "x":
            out[name + "_2"] = value
    return out


def reference(
    x, ln_attn_g, w_in, qk_norm_g, diff_lambda, diff_subln_g, w_out, ln_ffn_g, w_up, conv_w,
    conv_b, w_down, rel_bias, c_2, ctx_2, c_ctx_2, w_ada_2, b_ada_2, g_pre_mix_2, g_post_mix_2,
    g_pre_ff_2, g_post_ff_2, w_in_even_2, w_in_odd_2, w_out_2, w_ff1_2, w_ff2_2, a_mu_prev_2,
    a_mu_next_2, a_w0_2, a_w2_2, a_a0_2, a_a2_2, a_g2_2, a_k_k_2, a_k_a_2, a_r_k_2, a_gn_w_2,
    a_gn_b_2, b_sink_2, c_rpb_2, d_q_gain_2, d_k_gain_2,
):
    x = first_block(
        x, ln_attn_g, w_in, qk_norm_g, diff_lambda, diff_subln_g, w_out, ln_ffn_g, w_up, conv_w,
        conv_b, w_down, rel_bias,
    )
    return second_block(
        x, c_2, ctx_2, c_ctx_2, w_ada_2, b_ada_2, g_pre_mix_2, g_post_mix_2, g_pre_ff_2,
        g_post_ff_2, w_in_even_2, w_in_odd_2, w_out_2, w_ff1_2, w_ff2_2, a_mu_prev_2,
        a_mu_next_2, a_w0_2, a_w2_2, a_a0_2, a_a2_2, a_g2_2, a_k_k_2, a_k_a_2, a_r_k_2,
        a_gn_w_2, a_gn_b_2, b_sink_2, c_rpb_2, d_q_gain_2, d_k_gain_2,
    )


_drawn_inputs = setup_inputs


def setup_inputs(seed=0):
    import zlib

    import numpy as np

    out = dict(_drawn_inputs(seed))
    spreads = {}
    factors = {'ln_attn_g': 3.881,
     'qk_norm_g': 5.699,
     'diff_subln_g': 6.801,
     'ln_ffn_g': 4.736,
     'conv_b': 4.69,
     'g_post_mix_2': 13.652,
     'g_pre_ff_2': 11.17,
     'g_post_ff_2': 16.459,
     'a_w2_2': 22.273,
     'a_a0_2': 6.065,
     'a_gn_w_2': 24.531,
     'a_gn_b_2': 56.944,
     'b_sink_2': 45.798,
     'c_rpb_2': 10.391,
     'd_q_gain_2': 8.0,
     'd_k_gain_2': 8.0,
     'a_k_k_2': 2.757,
     'a_r_k_2': 4.145}
    for name, (base, spread) in spreads.items():
        noise = np.random.default_rng([zlib.crc32(name.encode()), seed]).standard_normal(out[name].shape)
        drawn = base * np.exp(spread * noise) if base else spread * noise
        out[name] = __import__('jax').numpy.asarray(drawn.astype(out[name].dtype))
    for name, factor in factors.items():
        out[name] = (out[name] * factor).astype(out[name].dtype)
    return out
```

```python
import math
from contextlib import ExitStack

import numpy as np

import concourse.bass as bass
from concourse import mybir

F32 = mybir.dt.float32
U8 = mybir.dt.uint8
ALU = mybir.AluOpType
ACT = mybir.ActivationFunctionType
AX_X = mybir.AxisListType.X

P = 128
D = 1024
KT = D // P
SEQ = 256
TT = SEQ // P
DEPTH = 2
HD = 64
REL_BUCKETS = 32
N_BIAS = 12
D_FF = 2816
FT = D_FF // P
D_FF2 = 4096
FT2 = D_FF2 // P
CONV = 3
A_IN = 1920
AT = A_IN // P
EPS = 1e-6
GN_EPS = 64e-5
NEG = -1e30
SCALE = HD ** -0.5
LAMBDA_INIT = [0.8 - 0.6 * math.exp(-0.3 * i) for i in range(DEPTH)]
CH = 64
NCH = 2 * SEQ // CH
DECAY = math.exp(-0.5)
RING = 5
SLOT = 4 * 512
GRID_W, NA_KH, NA_KW = 64, 8, 16


def rel_bucket(dist):
    n = np.maximum(dist, 0)
    nf = np.maximum(n, 16).astype(np.float32)
    large = 16 + (np.log(nf / np.float32(16)) / np.float32(math.log(64.0)) * np.float32(16)).astype(np.int32)
    return np.where(n < 16, n, np.minimum(large, 31))


def constants():
    f = np.float32
    keep, first, masks = {}, {}, {}
    eye = np.eye(P, dtype=f)
    keep["ident"] = eye
    keep["flip64"] = np.kron(np.eye(2, dtype=f), np.eye(64, dtype=f)[::-1])
    keep["ones"] = np.ones((P, P), f)
    head = np.arange(P) // 64
    same = (head[:, None] == head[None, :])
    keep["head_ones"] = same.astype(f)
    s, t = np.arange(P)[:, None] % 64, np.arange(P)[None, :] % 64
    for d, (strict, incl) in enumerate([((s < t) & same, (s <= t) & same), ((s > t) & same, (s >= t) & same)]):
        keep[f"tri{d}"] = np.concatenate([strict, incl, strict, incl], 1).astype(f)
    edge = np.ones(2 * SEQ + 2, f)
    edge[::CH] = 0
    keep["scan_edge"] = np.broadcast_to(edge, (P, edge.size))
    tok = np.arange(SEQ)
    inv = (np.float32(10000.0) ** (-np.arange(16, dtype=f) / f(16))).astype(f)
    row, colm = (tok // GRID_W).astype(f)[:, None] * inv, (tok % GRID_W).astype(f)[:, None] * inv
    cos = np.concatenate([np.cos(row), np.cos(row), np.cos(colm), np.cos(colm)], 1).astype(f)
    sin = np.concatenate([-np.sin(row), np.sin(row), -np.sin(colm), np.sin(colm)], 1).astype(f)
    tile = lambda a: a.reshape(TT, P, -1).transpose(1, 0, 2).reshape(P, -1)
    keep["cos"], keep["sin"] = tile(cos), tile(sin)
    q, k = np.arange(SEQ)[:, None], np.arange(SEQ)[None, :]
    keep["band"] = tile(np.where(np.abs(q - k) <= 128, 0, NEG).astype(f))
    qc, kc = q % GRID_W, k % GRID_W
    start = np.clip(qc - NA_KW // 2, 0, GRID_W - NA_KW)
    keep["near"] = tile(np.where((kc >= start) & (kc < start + NA_KW), 0, NEG).astype(f))

    first["flip"] = eye[::-1]
    first["causal"] = np.where(np.arange(SEQ)[None, :] <= P + np.arange(P)[:, None], 0, NEG).astype(f)
    hot = np.zeros((P, 384), f)
    hot[rel_bucket(255 - np.arange(384)), np.arange(384)] = 1
    first["bucket_hot"] = hot

    for lev in range(6):
        m = 1 << lev
        low = (np.arange(P)[:, None] // (2 * m) == np.arange(P)[None, :] // (2 * m)) & (
            (np.arange(P)[:, None] // m) % 2 == 1) & ((np.arange(P)[None, :] // m) % 2 == 0)
        masks[f"low{lev}"] = low.astype(f)
        masks[f"up{lev}"] = low.T.astype(f)
    return keep, first, masks


def packed(parts):
    at, where = 0, {}
    for name, a in parts.items():
        where[name] = (at, a.shape[1])
        at += a.shape[1]
    return np.ascontiguousarray(np.concatenate(list(parts.values()), 1)), where


KEEP, KEEP_AT = packed(constants()[0])
FIRST, FIRST_AT = packed(constants()[1])
MASKS, MASKS_AT = packed(constants()[2])

PARAM_GROUPS = [
    [("ln_attn_g", 16), ("ln_ffn_g", 16), ("diff_subln_g", 2), ("qk_norm_g", 8), ("g_pre_mix_2", 16),
     ("g_post_mix_2", 16), ("g_pre_ff_2", 16), ("g_post_ff_2", 16), ("d_q_gain_2", 1), ("d_k_gain_2", 1),
     ("c_2", 8), ("c_ctx_2", 8)],
    [("a_mu_prev_2", 15), ("a_mu_next_2", 15), ("a_w0_2", 8), ("a_a0_2", 8), ("a_k_k_2", 4), ("a_k_a_2", 4),
     ("a_r_k_2", 4), ("a_gn_w_2", 4), ("a_gn_b_2", 4)],
    [("b_ada_2", 96)],
    [("conv_b", 88)],
    [("conv_w", 128)], [("conv_w", 128)], [("conv_w", 8)],
]
HALF_ROWS = ("qk_norm_g", "d_q_gain_2", "d_k_gain_2")


def first_and_second_block(nc, I, consts, out):
    with ExitStack() as ctx:
        def sb(name, shape, dt=F32):
            return ctx.enter_context(nc.sbuf_tensor(name, shape, dt))

        made = {}

        def sem(name):
            if name not in made:
                made[name] = ctx.enter_context(nc.semaphore(name))
            return made[name]

        ring = sb("ring", [P, RING, SLOT])
        h_lat = sb("h_lat", [P, TT, D])
        h_ctx = sb("h_ctx", [P, TT, D])
        pcol = sb("pcol", [P, len(PARAM_GROUPS), P])
        keep = sb("keep", [P, KEEP.shape[1]])
        masks = sb("masks", [P, MASKS.shape[1]], U8)
        mod = sb("mod", [P, DEPTH, 6 * KT, 2])
        mod_gain = sb("mod_gain", [P, DEPTH, 2, KT, 2])
        mod_gate = sb("mod_gate", [P, DEPTH, 2, KT, 2])
        silu_c = sb("silu_c", [P, KT, 2])
        bcast = sb("bcast", [P, 10])
        neg_sink = sb("neg_sink", [P, 8])
        stat = sb("stat", [P, 1250])
        n_arena = 32520
        arena = sb("arena", [P, n_arena])
        half = sb("half", [P, 8])
        banks = [ctx.enter_context(nc.psum_tensor(f"acc{i}", [P, 512], F32)) for i in range(4)]
        trs = [ctx.enter_context(nc.psum_tensor(f"tr{i}", [P, 512], F32)) for i in range(2)]
        scs = [ctx.enter_context(nc.psum_tensor(f"sc{i}", [P, 512], F32)) for i in range(2)]
        t5_scratch = nc.dram_tensor("t5_scratch", [N_BIAS, 384], F32, kind="Internal").ap()

        def const(name):
            at, n = KEEP_AT[name]
            return keep[:, at:at + n]

        def mask(name):
            at, n = MASKS_AT[name]
            return masks[:, at:at + n]

        ident, head_ones, flip64, ones = const("ident"), const("head_ones"), const("flip64"), const("ones")

        stat_at = [0]

        def stats(n):
            at = stat_at[0]
            stat_at[0] += n
            assert stat_at[0] <= 1250
            return stat[:, at:at + n]

        class Region:

            def __init__(self, at=0):
                self.at = at

            def take(self, *shape):
                n = int(np.prod(shape))
                v = arena[:, self.at:self.at + n]
                self.at += n
                assert self.at <= n_arena, self.at
                if len(shape) == 2:
                    v = v.rearrange("p (a b) -> p a b", a=shape[0])
                elif len(shape) == 3:
                    v = v.rearrange("p (a b c) -> p a b c", a=shape[0], b=shape[1])
                elif len(shape) == 4:
                    v = v.rearrange("p (a b c d) -> p a b c d", a=shape[0], b=shape[1], c=shape[2])
                return v

        param_at = {}
        for g, group in enumerate(PARAM_GROUPS):
            r = 0
            for name, n in group:
                if name != "conv_w":
                    param_at[name] = (g, r)
                r += n

        def col(name, i=0, n=1):
            if name == "conv_w":
                return pcol[:, 4 + i // P, i % P:i % P + n]
            g, r = param_at[name]
            return pcol[:, g, r + i:r + i + n]

        acc_at, tr_at, sc_at = {}, {}, {}
        fills = [0, 0, 0]

        def stage(key, acc=0, tr=0, sc=0):
            acc_at[key], tr_at[key], sc_at[key] = fills
            fills[0] += acc
            fills[1] += tr
            fills[2] += sc

        acc_full, tr_full, sc_full = sem("acc_full"), sem("tr_full"), sem("sc_full")
        acc_drained = [sem(f"acc_drained{i}") for i in range(4)]
        tr_drained = [sem(f"tr_drained{i}") for i in range(2)]
        sc_drained = [sem(f"sc_drained{i}") for i in range(2)]
        POOLS = {"acc": (banks, acc_full, acc_drained), "tr": (trs, tr_full, tr_drained), "sc": (scs, sc_full, sc_drained)}

        def bank(pool, f):
            return POOLS[pool][0][f % len(POOLS[pool][0])]

        def claim(pe, pool, f):
            b, _, drained = POOLS[pool]
            if f >= len(b):
                pe.wait_ge(drained[f % len(b)], f // len(b))
            return b[f % len(b)]

        def filled(eng, pool, f):
            b, full, _ = POOLS[pool]
            eng.wait_ge(full, f + 1)
            return b[f % len(b)]

        def drain(pool, f):
            _, _, drained = POOLS[pool]
            return drained[f % len(drained)]

        def wait_drained(eng, pool, f):
            _, _, drained = POOLS[pool]
            eng.wait_ge(drained[f % len(drained)], f // len(drained) + 1)

        chunks = []
        release = []
        chunk_at = {}
        partial = [0]
        chunk_read = sem("chunk_read")

        def plan_tok(key, w, kts, f0, blocks):
            chunk_at[key] = len(chunks)
            n = w.shape[1]
            view = w.rearrange("(k p) n -> p k n", p=P)
            for c, tts in enumerate(blocks):
                f0 += len(tts)
                for k0 in range(0, kts, 4):
                    chunks.append(view[:, k0:min(k0 + 4, kts), 512 * c:min(512 * c + 512, n)])
                    if k0 + 4 >= kts:
                        release.append((acc_full, f0))
                    else:
                        partial[0] += 1
                        release.append((chunk_read, partial[0]))

        def plan_feat(key, w, cols, fills_of):
            chunk_at[key] = len(chunks)
            view = w.rearrange("(k p) n -> p k n", p=P)
            for (c0, c1), f in zip(cols, fills_of):
                chunks.append(view[:, :, c0:c1])
                release.append((acc_full, f))

        def slot(g):
            k, n = chunks[g].shape[1], chunks[g].shape[2]
            return ring[:, g % RING, 0:k * n].rearrange("p (k n) -> p k n", k=k)

        weights_landed = [sem(f"weights_landed{i}") for i in range(RING)]

        def landed(pe, g):
            pe.wait_ge(weights_landed[g % RING], 16 * (g // RING + 1))
            return slot(g)

        LAT = [0, 1]
        ALL = [0, 1, 2, 3]
        LATS = [2, 3]
        stage("params", tr=2)
        stage("bcast", acc=1)
        stage("t5", acc=1 + N_BIAS // 2)
        for l in range(DEPTH):
            stage(("ada", l), acc=12, tr=12)
            plan_tok(("ada", l), I["w_ada_2"][l], KT, acc_at[("ada", l)], [[0]] * 12)
        norm_n = {}

        def plan_norm(key):
            norm_n[key] = len(norm_n)
            stage(("norm", key), tr=4)

        def pairs(ncols):
            return [(c, min(c + 256, ncols)) for c in range(0, ncols, 256)]

        for l in range(DEPTH):
            plan_norm(("attn", l))
            stage(("qkv", l), acc=12, tr=8)
            plan_tok(("qkv", l), I["w_in"][l], KT, acc_at[("qkv", l)], [LAT] * 6)
            stage(("att1", l), acc=32, tr=16, sc=16)
            stage(("yT1", l), tr=4)
            stage(("out1", l), acc=4)
            plan_tok(("out1", l), I["w_out"][l], KT, acc_at[("out1", l)], [LAT] * 2)
            plan_norm(("ffn", l))
            stage(("up1", l), acc=FT)
            plan_feat(("up1", l), I["w_up"][l],
                      [(o + 256 * c, o + 256 * c + 256) for c in range(FT // 2) for o in (0, D_FF)],
                      [acc_at[("up1", l)] + 2 * c + 2 for c in range(FT // 2) for _ in range(2)])
            stage(("down1", l), acc=4)
            plan_tok(("down1", l), I["w_down"][l], FT, acc_at[("down1", l)], [LAT] * 2)

        def pair_fills(key, n):
            return [acc_at[key] + min(i + 2, n) for i in range(0, n, 2)]

        plan_norm(("mix", 0, 1))
        plan_norm(("mix", 0, 0))
        stage("projA", acc=AT)
        plan_feat("projA", I["w_in_even_2"][0][:, 0:A_IN], pairs(A_IN), pair_fills("projA", AT))
        stage("projB", acc=8, tr=8)
        plan_tok("projB", I["w_in_even_2"][0][:, A_IN:A_IN + 768], KT, acc_at["projB"], [ALL] * 2)
        stage("attBl", acc=16, tr=16, sc=8)
        stage("attBc", acc=16, tr=8, sc=8)
        stage("yTB", tr=4)
        stage("kk", acc=4)
        for d in range(2):
            stage(("prep", d), acc=8)
            for s in range(NCH):
                stage(("chunk", d, s), acc=28, tr=3)
        stage("rwkv_out", acc=8, tr=8)
        stage("post_mix0", acc=4 + 8)
        plan_tok("out2_0", I["w_out_2"][0], KT, acc_at["post_mix0"] + 4, [ALL] * 2)
        plan_norm(("ff", 0, 1))
        plan_norm(("ff", 0, 0))
        stage("ff1_0", acc=FT2)
        plan_feat("ff1_0", I["w_ff1_2"][0], pairs(D_FF2), pair_fills("ff1_0", FT2))
        stage("post_ff0", acc=4 + 8)
        plan_tok("ff2_0", I["w_ff2_2"][0], FT2, acc_at["post_ff0"] + 4, [ALL] * 2)
        plan_norm(("mix", 1, 1))
        plan_norm(("mix", 1, 0))
        stage("near", acc=8)
        stage("proj1", acc=4 + 4 + 4 + 2 + 4, tr=6)
        f = acc_at["proj1"]
        plan_feat("proj1", I["w_in_odd_2"][0][:, 0:1024], pairs(1024), [f + 2, f + 4, f + 6, f + 8])
        chunk_at["proj1_k"] = chunk_at["proj1"] + 2
        plan_tok("proj1_tok", I["w_in_odd_2"][0][:, 1024:2304], KT, f + 8, [ALL, LATS, ALL])
        stage("attC", acc=16, tr=16, sc=8)
        stage("attD", acc=16, tr=16, sc=8)
        stage("yT1_2", tr=4)
        stage("post_mix1", acc=2 + 4)
        plan_tok("out2_1", I["w_out_2"][1], KT, acc_at["post_mix1"] + 2, [LAT] * 2)
        plan_norm(("ff", 1, 0))
        stage("ff1_1", acc=FT2)
        plan_feat("ff1_1", I["w_ff1_2"][1], pairs(D_FF2), pair_fills("ff1_1", FT2))
        stage("post_ff1", acc=2 + 4)
        plan_tok("ff2_1", I["w_ff2_2"][1], FT2, acc_at["post_ff1"] + 2, [LAT] * 2)

        r1 = Region()
        t5_bias = r1.take(N_BIAS, SEQ)
        xn = r1.take(TT, D)
        at1 = r1.at
        hT = r1.take(KT, SEQ)
        qkT = r1.take(4, 4, SEQ)
        vv = r1.take(2, TT, 512)
        qn = r1.take(2, 512)
        sq = r1.take(2, 512)
        prob = r1.take(2, 2, 512)
        probT = r1.take(2, 1024)
        y1 = r1.take(TT, D)
        yT1 = r1.take(KT, SEQ)
        r1b = Region(at1 + KT * SEQ)
        gT = r1b.take(FT, SEQ)
        conv = r1b.take(2, 2, SEQ)
        act_g = r1b.take(2, SEQ)
        r0 = Region(at1)
        prow = r0.take(len(PARAM_GROUPS), P)
        first = r0.take(FIRST.shape[1])
        mask_rows = r0.take(MASKS.shape[1])
        lrow = r0.take(520)
        lprod = r0.take(2 * DEPTH * HD)
        lsum = r0.take(8)
        relb = r0.take(N_BIAS)
        t5_vec = r0.take(384)
        hankel = r0.take(N_BIAS, SEQ)
        mod_row = r0.take(2, 512)

        def first_const(name):
            at, n = FIRST_AT[name]
            return first[:, at:at + n]

        norm_ss = norm_ms = norm_rs = stats(2 * 16)
        norm_summed, norm_mean, norm_rstd, norm_xn = (
            sem("norm_summed"), sem("norm_mean"), sem("norm_rstd"), sem("norm_xn"))
        dve_chain = sem("dve_chain")
        chain = [0]

        def link(dve, ins):
            chain[0] += 1
            ins.then_inc(dve_chain, 1)
            dve.wait_ge(dve_chain, chain[0])

        def norm_act(act, key, src, ready):
            n = norm_n[key]
            ready(act)
            if n:
                act.wait_ge(tr_full, tr_at[("norm", [k for k in norm_n if norm_n[k] == n - 1][0])] + 4)
            for tt in range(TT):
                act.activation(xn[:, tt, :], src[:, tt, :], ACT.Square,
                               accum_out=norm_ss[:, 2 * n + tt:2 * n + tt + 1]).then_inc(norm_summed, 1)

        def norm_pool(pool, key):
            n = norm_n[key]
            pool.wait_ge(norm_mean, n + 1)
            pool.tensor_tensor(norm_rs[:, 2 * n:2 * n + 2], norm_ms[:, 2 * n:2 * n + 2], half[:, 0:2],
                               ALU.pow).then_inc(norm_rstd, 1)

        def norm_dve(dve, key, src, ready, gain, shift, dst):
            n = norm_n[key]
            dve.wait_ge(norm_summed, 2 * n + 2)
            dve.tensor_scalar(norm_ms[:, 2 * n:2 * n + 2], norm_ss[:, 2 * n:2 * n + 2], 1.0 / D, EPS,
                              ALU.mult, ALU.add).then_inc(norm_mean, 1)
            ready(dve)
            dve.wait_ge(norm_rstd, n + 1)
            for tt in range(TT):
                dve.tensor_scalar(xn[:, tt, :], src[:, tt, :], norm_rs[:, 2 * n + tt:2 * n + tt + 1], None,
                                  ALU.mult).then_inc(norm_xn, 1)
            for g in range(4):
                f = tr_at[("norm", key)] + g
                ps = filled(dve, "tr", f)
                for i in range(2):
                    kt = 2 * g + i
                    ins = dve.tensor_scalar(dst[:, kt, :], ps[:, i * SEQ:(i + 1) * SEQ], gain(kt),
                                            shift(kt) if shift else None, ALU.mult, *([ALU.add] if shift else []))
                ins.then_inc(drain("tr", f), 1)

        def norm_pe(pe, key):
            n = norm_n[key]
            for g in range(4):
                f = tr_at[("norm", key)] + g
                ps = claim(pe, "tr", f)
                for i in range(2):
                    for tt in range(TT):
                        if g == 0 and i == 0:
                            pe.wait_ge(norm_xn, 2 * n + tt + 1)
                        kt = 2 * g + i
                        ins = pe.transpose(ps[:, i * SEQ + tt * P:i * SEQ + (tt + 1) * P],
                                           xn[:, tt, kt * P:(kt + 1) * P], ident)
                ins.then_inc(tr_full, 1)

        def norm_wait(pe, key):
            for g in (2, 3):
                wait_drained(pe, "tr", tr_at[("norm", key)] + g)

        def tok_gemm(pe, key, f, kts, blocks, lhsT):
            g = chunk_at[key]
            for tts in blocks:
                for k0 in range(0, kts, 4):
                    w = landed(pe, g)
                    kn, width = w.shape[1], w.shape[2]
                    for n, tt in enumerate(tts):
                        ps = claim(pe, "acc", f + n) if k0 == 0 else bank("acc", f + n)
                        for k in range(kn):
                            x = lhsT(k0 + k, tt)
                            ins = pe.matmul(ps[0:x.shape[1], 0:width], x, w[:, k, :],
                                            start=(k0 + k == 0), stop=(k0 + k == kts - 1))
                        if k0 + kn == kts:
                            ins.then_inc(acc_full, 1)
                    if k0 + kn < kts:
                        ins.then_inc(chunk_read, 1)
                    g += 1
                f += len(tts)

        def feat_gemm(pe, key, f, n, rhs):
            for i in range(n):
                if i % 2 == 0:
                    w = landed(pe, chunk_at[key] + i // 2)
                ps = claim(pe, "acc", f + i)
                for kt in range(KT):
                    x = rhs(kt)
                    ins = pe.matmul(ps[:, 0:x.shape[1]], w[:, kt, (i % 2) * P:(i % 2 + 1) * P], x,
                                    start=(kt == 0), stop=(kt == KT - 1))
                ins.then_inc(acc_full, 1)

        att_max, att_comb, att_sunk = sem("att_max"), sem("att_comb"), sem("att_sunk")
        att_units = [0]
        sunk_units = [0]

        class Attention:

            def __init__(self, key, n, q, k, width, v, y, prob, probT, bias=None, sink=None, neg_lam=None, diff=lambda u: False):
                self.key, self.n, self.q, self.k, self.width, self.v, self.y = key, n, q, k, width, v, y
                self.prob, self.probT, self.bias, self.sink, self.neg_lam, self.diff = prob, probT, bias, sink, neg_lam, diff
                self.base = att_units[0]
                att_units[0] += n
                self.sunk = sunk_units[0]
                if sink:
                    sunk_units[0] += n
                self.neg_max, self.total, self.recip = (stats(2 * n) for _ in range(3))
                self.extra = stats(2 * n) if sink else None
                self.mix = stats(n) if neg_lam is not None else None
                self.tr = [tr_at[key]]
                for u in range(n):
                    blocks = (1 if diff(u) else 2) * (width(u) // P)
                    self.tr.append(self.tr[-1] + -(-blocks // 4))

            def banks_of(self, u):
                return [acc_at[self.key] + 2 * u + m for m in range(2)]

            def blocks(self, u):
                return [(m, kb) for m in range(1 if self.diff(u) else 2) for kb in range(self.width(u) // P)]

            def scores(self, pe, u):
                for m, f in enumerate(self.banks_of(u)):
                    ps = claim(pe, "acc", f)
                    pe.matmul(ps[:, 0:self.width(u)], self.q(u, m), self.k(u, m), start=True, stop=True).then_inc(acc_full, 1)

            def turn(self, pe, u):
                pe.wait_ge(att_comb, self.base + u + 1)
                b = self.blocks(u)
                for i in range(self.tr[u + 1] - self.tr[u]):
                    ps = claim(pe, "tr", self.tr[u] + i)
                    for n, (m, kb) in enumerate(b[4 * i:4 * i + 4]):
                        ins = pe.transpose(ps[:, n * P:(n + 1) * P], self.prob[:, u % 2, m, kb * P:(kb + 1) * P], ident)
                    ins.then_inc(tr_full, 1)

            def values(self, pe, u):
                for f in range(self.tr[u], self.tr[u + 1]):
                    wait_drained(pe, "tr", f)
                ps = claim(pe, "sc", sc_at[self.key] + u)
                b = self.blocks(u)
                for n, (m, kb) in enumerate(b):
                    x = self.v(u, m, kb)
                    e = x.shape[1]
                    ins = pe.matmul(ps[:, m * e:(m + 1) * e], self.probT[:, u % 2, n * P:(n + 1) * P], x,
                                    start=(kb == 0), stop=(kb == self.width(u) // P - 1))
                ins.then_inc(sc_full, 1)

            def tensor(self, pe):
                self.scores(pe, 0)
                for u in range(self.n):
                    if u + 1 < self.n:
                        self.scores(pe, u + 1)
                    if u >= 1:
                        self.values(pe, u - 1)
                    self.turn(pe, u)
                self.values(pe, self.n - 1)

            def maxima(self, dve, u):
                w = self.width(u)
                ps = [filled(dve, "acc", f) for f in self.banks_of(u)]
                if self.bias:
                    for m in range(2):
                        c0, b = self.bias(u, m)
                        ins = dve.tensor_tensor(ps[m][:, c0:w], ps[m][:, c0:w], b, ALU.add)
                    link(dve, ins)
                for m in range(2):
                    ins = dve.tensor_reduce(self.neg_max[:, 2 * u + m:2 * u + m + 1], ps[m][:, 0:w], AX_X, ALU.max, negate=True)
                if self.sink:
                    link(dve, ins)
                    h = self.sink(u)
                    ins = dve.tensor_tensor(self.neg_max[:, 2 * u:2 * u + 2], self.neg_max[:, 2 * u:2 * u + 2],
                                            neg_sink[:, h:h + 2], ALU.min)
                ins.then_inc(att_max, 1)

            def combine(self, dve, u):
                for f in self.banks_of(u):
                    wait_drained(dve, "acc", f)
                total, recip = self.total[:, 2 * u:2 * u + 2], self.recip[:, 2 * u:2 * u + 2]
                if self.sink:
                    dve.wait_ge(att_sunk, 2 * (self.sunk + u) + 2)
                    link(dve, dve.tensor_tensor(total, total, self.extra[:, 2 * u:2 * u + 2], ALU.add))
                ins = dve.reciprocal(recip, total)
                if self.diff(u):
                    link(dve, ins)
                    mix = self.mix[:, u:u + 1]
                    link(dve, dve.scalar_tensor_tensor(mix, total[:, 0:1], recip[:, 1:2], self.neg_lam, ALU.mult, ALU.mult))
                    w = self.width(u)
                    ins = dve.scalar_tensor_tensor(self.prob[:, u % 2, 0, 0:w], self.prob[:, u % 2, 1, 0:w], mix,
                                                   self.prob[:, u % 2, 0, 0:w], ALU.mult, ALU.add)
                ins.then_inc(att_comb, 1)

            def outputs(self, dve, u):
                f = sc_at[self.key] + u
                ps = filled(dve, "sc", f)
                if self.diff(u):
                    ins = dve.tensor_scalar(self.y(u), ps[:, 0:P], self.recip[:, 2 * u:2 * u + 1], None, ALU.mult)
                else:
                    ins = dve.tensor_tensor(self.y(u).rearrange("p (m e) -> p m e", m=2),
                                            ps[:, 0:P].rearrange("p (m e) -> p m e", m=2),
                                            self.recip[:, 2 * u:2 * u + 2].unsqueeze(2).broadcast_to([P, 2, HD]), ALU.mult)
                ins.then_inc(drain("sc", f), 1)

            def vector(self, dve, hook=None):
                for u in range(self.n + 2):
                    if u < self.n:
                        self.maxima(dve, u)
                    if 1 <= u <= self.n:
                        self.combine(dve, u - 1)
                    if u >= 2:
                        self.outputs(dve, u - 2)
                    if hook:
                        hook(u)

            def exps(self, act, u):
                w = self.width(u)
                act.wait_ge(att_max, self.base + u + 1)
                if u >= 2:
                    act.wait_ge(tr_full, self.tr[u - 1])
                for m, f in enumerate(self.banks_of(u)):
                    act.activation(self.prob[:, u % 2, m, 0:w], bank("acc", f)[:, 0:w], ACT.Exp,
                                   bias=self.neg_max[:, 2 * u + m:2 * u + m + 1],
                                   accum_out=self.total[:, 2 * u + m:2 * u + m + 1]).then_inc(drain("acc", f), 1)
                if self.sink:
                    for m in range(2):
                        h = self.sink(u) + m
                        act.activation(self.extra[:, 2 * u + m:2 * u + m + 1], bcast[:, 2 + h:3 + h], ACT.Exp,
                                       bias=self.neg_max[:, 2 * u + m:2 * u + m + 1]).then_inc(att_sunk, 1)

            def keep_turned(self, act, u):
                if u >= 2:
                    act.wait_ge(sc_full, sc_at[self.key] + u - 1)
                n = len(self.blocks(u))
                for i, f in enumerate(range(self.tr[u], self.tr[u + 1])):
                    c0, c1 = 512 * i, min(512 * i + 512, P * n)
                    act.activation(self.probT[:, u % 2, c0:c1], filled(act, "tr", f)[:, 0:c1 - c0], ACT.Copy)\
                       .then_inc(drain("tr", f), 1)

            def scalar(self, act, hook=None):
                for u in range(self.n + 1):
                    if u < self.n:
                        self.exps(act, u)
                    if u >= 1:
                        self.keep_turned(act, u - 1)
                    if hook:
                        hook(u)

        params_cleared, params_landed, first_landed, keep_landed = (
            sem("params_cleared"), sem("params_landed"), sem("first_landed"), sem("keep_landed"))
        rows_landed, x_landed, t5_stored, t5_landed = sem("rows_landed"), sem("x_landed"), sem("t5_stored"), sem("t5_landed")
        half_set, lam_prod, lam_exp, bcast_row, bcast_set, t5_vec_ready = (
            sem("half_set"), sem("lam_prod"), sem("lam_exp"), sem("bcast_row"), sem("bcast_set"), sem("t5_vec_ready"))
        silu_ready = sem("silu_ready")
        masks_set = sem("masks_set")
        row_dmas = [0]

        def setup_act_dma(act):
            act.dma_start(keep[:, :], consts[0]).then_inc(keep_landed, 16)
            act.dma_start(mask_rows[:, :], consts[2]).then_inc(keep_landed, 16)
            act.dma_start(lrow[0:1, 0:2 * 4 * HD], I["diff_lambda"].rearrange("(o l) a b -> o (l a b)", o=1)).then_inc(rows_landed, 16)
            act.dma_start(lrow[0:1, 512:520], I["b_sink_2"]).then_inc(rows_landed, 16)
            act.dma_start(relb[0:REL_BUCKETS, :], I["rel_bias"]).then_inc(rows_landed, 16)
            act.dma_start(first[:, :], consts[1]).then_inc(first_landed, 16)
            act.wait_ge(params_cleared, 1)
            for g, group in enumerate(PARAM_GROUPS):
                r = 0
                for name, n in group:
                    src = I[name]
                    letters = "abcd"[:len(src.shape)]
                    flat = src.rearrange(" ".join(letters) + " -> (" + " ".join(letters) + ")") if len(letters) > 1 else src
                    if name in HALF_ROWS:
                        for hd in range(2):
                            act.dma_start(prow[r:r + n, g, hd * HD:(hd + 1) * HD],
                                          flat.rearrange("(n c) -> n c", c=HD)).then_inc(params_landed, 16)
                            row_dmas[0] += 1
                    else:
                        off = (g - 4) * P if name == "conv_w" else 0
                        act.dma_start(prow[r:r + n, g, :], flat.rearrange("(n c) -> n c", c=P)[off:off + n, :])\
                           .then_inc(params_landed, 16)
                        row_dmas[0] += 1
                    r += n

        n_param_dmas = sum(2 if name in HALF_ROWS else 1 for group in PARAM_GROUPS for name, _ in group)

        def setup_pool(pool):
            pool.memset(prow[:, :, :], 0.0).then_inc(params_cleared, 1)
            pool.memset(half[:, :], -0.5).then_inc(half_set, 1)
            pool.wait_ge(half_set, 1)

        def setup_pe(pe):
            pe.wait_ge(keep_landed, 32)
            pe.wait_ge(params_landed, 16 * n_param_dmas)
            for i in range(2):
                f = tr_at["params"] + i
                ps = claim(pe, "tr", f)
                for n, g in enumerate(range(4 * i, min(4 * i + 4, len(PARAM_GROUPS)))):
                    ins = pe.transpose(ps[:, n * P:(n + 1) * P], prow[:, g, :], ident)
                ins.then_inc(tr_full, 1)
            pe.wait_ge(bcast_row, 2)
            f = acc_at["bcast"]
            pe.matmul(claim(pe, "acc", f)[:, 0:10], ones[0:1, :], lprod[0:1, 0:10], start=True, stop=True).then_inc(acc_full, 1)
            pe.wait_ge(rows_landed, 48)
            pe.wait_ge(first_landed, 16)
            f = acc_at["t5"]
            pe.matmul(claim(pe, "acc", f)[0:N_BIAS, 0:384], relb[0:REL_BUCKETS, :], first_const("bucket_hot")[0:REL_BUCKETS, :],
                      start=True, stop=True).then_inc(acc_full, 1)
            pe.wait_ge(t5_landed, 16)
            for i in range(N_BIAS // 2):
                ps = claim(pe, "acc", f + 1 + i)
                pe.matmul(ps[:, :], first_const("flip"), hankel[:, 2 * i:2 * i + 2, :], start=True, stop=True).then_inc(acc_full, 1)

        def setup_dve(dve):
            dve.wait_ge(keep_landed, 32)
            dve.tensor_copy(masks[:, :], mask_rows[:, :]).then_inc(masks_set, 1)
            for i in range(2):
                f = tr_at["params"] + i
                ps = filled(dve, "tr", f)
                n = min(4, len(PARAM_GROUPS) - 4 * i)
                dve.tensor_copy(pcol[:, 4 * i:4 * i + n, :], ps[:, 0:n * P].rearrange("p (a b) -> p a b", a=n)).then_inc(drain("tr", f), 1)
            dve.wait_ge(rows_landed, 48)
            lam = lrow[0:1, 0:512].rearrange("p (a two c) -> p a two c", a=4, two=2)
            prods = lprod[0:1, 0:256].rearrange("p (a c) -> p a c", a=4)
            link(dve, dve.tensor_tensor(prods, lam[:, :, 0, :], lam[:, :, 1, :], ALU.mult))
            dve.tensor_reduce(lsum[0:1, 0:4], prods, AX_X, ALU.add).then_inc(lam_prod, 1)
            dve.wait_ge(lam_exp, 1)
            for l in range(DEPTH):
                link(dve, dve.tensor_tensor(lprod[0:1, l:l + 1], lsum[0:1, 2 * l + 5:2 * l + 6], lsum[0:1, 2 * l + 4:2 * l + 5], ALU.subtract))
                link(dve, dve.tensor_scalar(lprod[0:1, l:l + 1], lprod[0:1, l:l + 1], -LAMBDA_INIT[l], None, ALU.add))
            dve.tensor_copy(lprod[0:1, 2:10], lrow[0:1, 512:520]).then_inc(bcast_row, 2)
            ps = filled(dve, "acc", acc_at["bcast"])
            dve.tensor_copy(bcast[:, :], ps[:, 0:10]).then_inc(bcast_set, 1)
            dve.wait_ge(bcast_set, 1)
            dve.tensor_scalar(neg_sink[:, :], bcast[:, 2:10], -1.0, None, ALU.mult).then_inc(drain("acc", acc_at["bcast"]), 1)
            f = acc_at["t5"]
            dve.tensor_copy(t5_vec[0:N_BIAS, :], filled(dve, "acc", f)[0:N_BIAS, 0:384]).then_inc(drain("acc", f), 1)
            for i in range(N_BIAS // 2):
                ps = filled(dve, "acc", f + 1 + i)
                dve.tensor_tensor(t5_bias[:, 2 * i:2 * i + 2, :], ps[:, :].rearrange("p (a b) -> p a b", a=2),
                                  first_const("causal").unsqueeze(1).broadcast_to([P, 2, SEQ]), ALU.add)\
                   .then_inc(drain("acc", f + 1 + i), 1)

        def setup_act(act):
            act.wait_ge(lam_prod, 1)
            act.activation(lsum[0:1, 4:8], lsum[0:1, 0:4], ACT.Exp).then_inc(lam_exp, 1)
            wait_drained(act, "tr", tr_at["params"])
            act.activation(silu_c[:, :, 0], col("c_2", 0, KT), ACT.Silu)
            act.activation(silu_c[:, :, 1], col("c_ctx_2", 0, KT), ACT.Silu).then_inc(silu_ready, 1)
            wait_drained(act, "acc", acc_at["t5"])
            act.dma_start(t5_scratch, t5_vec[0:N_BIAS, :]).then_inc(t5_stored, 16)
            act.wait_ge(t5_stored, 16)
            act.dma_start(hankel[:, :, :], bass.AP(tensor=t5_scratch.tensor, offset=0, ap=[[1, P], [384, N_BIAS], [1, SEQ]]))\
               .then_inc(t5_landed, 16)

        mod_ready = sem("mod_ready")

        def ada_pe(pe, l):
            if l == 0:
                pe.wait_ge(silu_ready, 1)

            def turn(c):
                wait_drained(pe, "acc", acc_at[("ada", l)] + c)
                f = tr_at[("ada", l)] + c
                ps = claim(pe, "tr", f)
                for i in range(4):
                    ins = pe.transpose(ps[:, 2 * i:2 * i + 2], mod_row[0:2, c % 2, i * P:(i + 1) * P], ident[0:2, 0:2])
                ins.then_inc(tr_full, 1)

            g = chunk_at[("ada", l)]
            for c in range(12):
                f = acc_at[("ada", l)] + c
                ps = claim(pe, "acc", f)
                for k in range(KT):
                    if k % 4 == 0:
                        w = landed(pe, g)
                        g += 1
                    ins = pe.matmul(ps[0:2, :], silu_c[:, k, :], w[:, k % 4, :], start=(k == 0), stop=(k == KT - 1))
                    if k == 3:
                        ins.then_inc(chunk_read, 1)
                ins.then_inc(acc_full, 1)
                if c >= 1:
                    turn(c - 1)
            turn(11)

        def ada_act(act, l):
            for c in range(12):
                f = acc_at[("ada", l)] + c
                if 12 * l + c >= 2:
                    act.wait_ge(tr_full, tr_at[("ada", (12 * l + c - 2) // 12)] + (12 * l + c - 2) % 12 + 1)
                act.wait_ge(acc_full, f + 1)
                act.activation(mod_row[0:2, c % 2, :], bank("acc", f)[0:2, :], ACT.Copy).then_inc(drain("acc", f), 1)

        def ada_dve(dve, l):
            for c in range(12):
                f = tr_at[("ada", l)] + c
                ps = filled(dve, "tr", f)
                ins = dve.tensor_tensor(mod[:, l, 4 * c:4 * c + 4, :], ps[:, 0:8].rearrange("p (a b) -> p a b", a=4),
                                        col("b_ada_2", 48 * l + 4 * c, 4).unsqueeze(2).broadcast_to([P, 4, 2]), ALU.add)
                ins.then_inc(drain("tr", f), 1)
            wait_drained(dve, "tr", tr_at[("ada", l)] + 11)
            wait_drained(dve, "tr", tr_at[("ada", l)] + 10)
            for w, (pre, post) in enumerate([("g_pre_mix_2", "g_post_mix_2"), ("g_pre_ff_2", "g_post_ff_2")]):
                scale, gate = mod[:, l, (3 * w + 1) * KT:(3 * w + 2) * KT, :], mod[:, l, (3 * w + 2) * KT:(3 * w + 3) * KT, :]
                dve.scalar_tensor_tensor(mod_gain[:, l, w], scale, 1.0, col(pre, KT * l, KT).unsqueeze(2).broadcast_to([P, KT, 2]),
                                         ALU.add, ALU.mult)
                dve.tensor_tensor(mod_gate[:, l, w], gate, col(post, KT * l, KT).unsqueeze(2).broadcast_to([P, KT, 2]),
                                  ALU.mult).then_inc(mod_ready, 1)

        QK = {0: 0, 1: 1, 3: 2, 4: 3}
        PREV = {1: 0, 2: 1, 4: 3, 5: 4}
        qk_squared, qk_mean, qk_rstd = sem("qk_squared"), sem("qk_mean"), sem("qk_rstd")
        qk_ss = qk_ms = qk_rs = stats(8 * 8)

        def qkv_pe(pe, l):
            norm_wait(pe, ("attn", l))
            g = chunk_at[("qkv", l)]
            for cb in range(6):
                f = acc_at[("qkv", l)] + 2 * cb
                for k0 in (0, 4):
                    w = landed(pe, g)
                    g += 1
                    for tt in range(TT):
                        ps = claim(pe, "acc", f + tt) if k0 == 0 else bank("acc", f + tt)
                        for k in range(4):
                            ins = pe.matmul(ps[:, :], hT[:, k0 + k, tt * P:(tt + 1) * P], w[:, k, :],
                                            start=(k0 + k == 0), stop=(k0 + k == KT - 1))
                        if k0:
                            ins.then_inc(acc_full, 1)
                    if k0 == 0:
                        ins.then_inc(chunk_read, 1)
                if cb in PREV:
                    for tt in range(TT):
                        u = 2 * QK[PREV[cb]] + tt
                        wait_drained(pe, "acc", acc_at[("qkv", l)] + 2 * PREV[cb] + tt)
                        t = tr_at[("qkv", l)] + u
                        ps = claim(pe, "tr", t)
                        for j in range(4):
                            ins = pe.transpose(ps[:, j * P:(j + 1) * P], qn[:, tt, j * P:(j + 1) * P], ident)
                        ins.then_inc(tr_full, 1)

        def qk_turned(eng, l, u):
            t = tr_at[("qkv", l)] + u
            ps = filled(eng, "tr", t)
            return t, ps[:, :].rearrange("p (a b) -> p a b", a=4), qkT[:, u // 2, :, (u % 2) * P:(u % 2 + 1) * P]

        def qkv_act(act, l):
            for cb in range(6):
                for tt in range(TT):
                    f = acc_at[("qkv", l)] + 2 * cb + tt
                    ps = filled(act, "acc", f)
                    if cb not in QK:
                        act.activation(vv[:, cb // 3, tt, :], ps[:, :], ACT.Copy).then_inc(drain("acc", f), 1)
                        continue
                    u = 8 * l + 2 * QK[cb] + tt
                    if u >= 2:
                        act.wait_ge(qk_mean, u - 1)
                    act.activation(sq[:, tt, :], ps[:, :], ACT.Square).then_inc(qk_squared, 1)
                if cb in PREV and QK[PREV[cb]] % 2 == 1:
                    for tt in range(TT):
                        t, ps, dst = qk_turned(act, l, 2 * QK[PREV[cb]] + tt)
                        act.activation(dst, ps, ACT.Identity, scale=col("qk_norm_g", 4 * l + QK[PREV[cb]])).then_inc(drain("tr", t), 1)

        def qkv_pool(pool, l):
            for u in range(8 * l, 8 * l + 8):
                c = 8 * (u % 8)
                pool.wait_ge(qk_mean, u + 1)
                pool.tensor_tensor(qk_rs[:, c:c + 8], qk_ms[:, c:c + 8], half[:, 0:8], ALU.pow).then_inc(qk_rstd, 1)

        def qkv_dve(dve, l):
            for cb in range(6):
                if cb in QK:
                    for tt in range(TT):
                        u = 2 * QK[cb] + tt
                        c = 8 * u
                        dve.wait_ge(qk_squared, 8 * l + u + 1)
                        link(dve, dve.tensor_reduce(qk_ss[:, c:c + 8], sq[:, tt, :].rearrange("p (h e) -> p h e", e=HD), AX_X, ALU.add))
                        dve.tensor_scalar(qk_ms[:, c:c + 8], qk_ss[:, c:c + 8], 1.0 / HD, EPS, ALU.mult, ALU.add).then_inc(qk_mean, 1)
                    for tt in range(TT):
                        u = 2 * QK[cb] + tt
                        c = 8 * u
                        f = acc_at[("qkv", l)] + 2 * cb + tt
                        dve.wait_ge(qk_rstd, 8 * l + u + 1)
                        if u >= 2:
                            dve.wait_ge(tr_full, tr_at[("qkv", l)] + u - 1)
                        dve.tensor_tensor(qn[:, tt, :].rearrange("p (h e) -> p h e", e=HD),
                                          bank("acc", f)[:, :].rearrange("p (h e) -> p h e", e=HD),
                                          qk_rs[:, c:c + 8].unsqueeze(2).broadcast_to([P, 8, HD]), ALU.mult).then_inc(drain("acc", f), 1)
                if cb in PREV and QK[PREV[cb]] % 2 == 0:
                    for tt in range(TT):
                        t, ps, dst = qk_turned(dve, l, 2 * QK[PREV[cb]] + tt)
                        dve.tensor_scalar(dst, ps, col("qk_norm_g", 4 * l + QK[PREV[cb]]), SCALE, ALU.mult, ALU.mult).then_inc(drain("tr", t), 1)

        def att1(l):
            def qk(i, u):
                p = u // 2
                return qkT[:, (2 * (p // 4)) + i, p % 4, :]

            def bias(u, m):
                p, qt = u // 2, u % 2
                h = p if p < 4 else 4 + 2 * (p - 4) + m
                return 0, t5_bias[:, h, (1 - qt) * P:SEQ]

            def v(u, m, kb):
                p = u // 2
                return vv[:, 0, kb, p * P:(p + 1) * P] if p < 4 else vv[:, 1, kb, (2 * (p - 4) + m) * HD:(2 * (p - 4) + m + 1) * HD]

            return Attention(("att1", l), 16,
                             lambda u, m: qk(0, u)[m * HD:(m + 1) * HD, (u % 2) * P:(u % 2 + 1) * P],
                             lambda u, m: qk(1, u)[m * HD:(m + 1) * HD, 0:(u % 2 + 1) * P],
                             lambda u: (u % 2 + 1) * P, v, lambda u: y1[:, u % 2, (u // 2) * P:(u // 2 + 1) * P],
                             prob, probT, bias=bias, neg_lam=bcast[:, l:l + 1], diff=lambda u: u < 8)

        sub_ss, sub_ms, sub_rs = stats(8), stats(8), stats(8)
        sub_summed, sub_mean, sub_rstd, sub_scaled = sem("sub_summed"), sem("sub_mean"), sem("sub_rstd"), sem("sub_scaled")

        def subnorm_act(act, l, att):
            def hook(u):
                if u == 11:
                    for n in range(8):
                        wait_drained(act, "sc", sc_at[att.key] + n)
                        act.activation(sq[:, n % 2, 0:P], y1[:, n % 2, (n // 2) * P:(n // 2 + 1) * P], ACT.Square,
                                       accum_out=sub_ss[:, n:n + 1]).then_inc(sub_summed, 1)
                        act.wait_ge(sub_summed, 8 * l + n + 1)
            return hook

        def subnorm_dve(dve, l, att):
            def hook(u):
                if u == 13:
                    dve.wait_ge(sub_summed, 8 * l + 8)
                    dve.tensor_scalar(sub_ms[:, :], sub_ss[:, :], 1.0 / P, EPS, ALU.mult, ALU.add).then_inc(sub_mean, 1)
                if u == 15:
                    dve.wait_ge(sub_rstd, l + 1)
                    for n in (6, 7):
                        wait_drained(dve, "sc", sc_at[att.key] + n)
                    rs = sub_rs[:, :].rearrange("p (h t) -> p t h", t=TT)
                    for qt in range(TT):
                        y = y1[:, qt, 0:512].rearrange("p (h e) -> p h e", e=P)
                        dve.tensor_tensor(y, y, rs[:, qt, :].unsqueeze(2).broadcast_to([P, 4, P]), ALU.mult).then_inc(sub_scaled, 1)
            return hook

        def subnorm_pool(pool, l):
            pool.wait_ge(sub_mean, l + 1)
            pool.tensor_tensor(sub_rs[:, :], sub_ms[:, :], half[:, 0:8], ALU.pow).then_inc(sub_rstd, 1)

        def yT1_pe(pe, l, att):
            pe.wait_ge(sub_scaled, TT * (l + 1))
            for f in (att.n - 2, att.n - 1):
                wait_drained(pe, "sc", sc_at[att.key] + f)
            for g in range(4):
                f = tr_at[("yT1", l)] + g
                ps = claim(pe, "tr", f)
                for i in range(2):
                    for tt in range(TT):
                        kt = 2 * g + i
                        ins = pe.transpose(ps[:, i * SEQ + tt * P:i * SEQ + (tt + 1) * P], y1[:, tt, kt * P:(kt + 1) * P], ident)
                ins.then_inc(tr_full, 1)

        def yT1_dve(dve, l):
            for g in range(4):
                f = tr_at[("yT1", l)] + g
                ps = filled(dve, "tr", f)
                dst = yT1[:, 2 * g:2 * g + 2, :].rearrange("p a b -> p (a b)")
                if g < 2:
                    ins = dve.tensor_scalar(dst, ps[:, :], col("diff_subln_g", l), 1.0 - LAMBDA_INIT[l], ALU.mult, ALU.mult)
                else:
                    ins = dve.tensor_copy(dst, ps[:, :])
                ins.then_inc(drain("tr", f), 1)

        def out1_pe(pe, l):
            for g in (2, 3):
                wait_drained(pe, "tr", tr_at[("yT1", l)] + g)
            tok_gemm(pe, ("out1", l), acc_at[("out1", l)], KT, [LAT] * 2, lambda kt, tt: yT1[:, kt, tt * P:(tt + 1) * P])

        def add_dve(dve, f0):
            for hf in range(2):
                for tt in range(TT):
                    f = f0 + 2 * hf + tt
                    ps = filled(dve, "acc", f)
                    x = h_lat[:, tt, hf * 512:(hf + 1) * 512]
                    dve.tensor_tensor(x, x, ps[:, :], ALU.add).then_inc(drain("acc", f), 1)

        conv_scaled, conv_done, act_done, g_done = sem("conv_scaled"), sem("conv_done"), sem("act_done"), sem("g_done")

        def up1_pe(pe, l):
            norm_wait(pe, ("ffn", l))
            for i in range(FT):
                if i % 2 == 0:
                    w = [landed(pe, chunk_at[("up1", l)] + i + s) for s in range(2)]
                f = acc_at[("up1", l)] + i
                ps = claim(pe, "acc", f)
                for s in range(2):
                    for kt in range(KT):
                        ins = pe.matmul(ps[:, s * SEQ:(s + 1) * SEQ], w[s][:, kt, (i % 2) * P:(i % 2 + 1) * P], hT[:, kt, :],
                                        start=(kt == 0), stop=(kt == KT - 1))
                ins.then_inc(acc_full, 1)

        def conv_col(l, j, i, s):
            return col("conv_w", (l * CONV + j) * 2 * FT + s * FT + i)

        def up1_act(act, l):
            for i in range(FT + 1):
                n = FT * l + i
                if i < FT:
                    ps = filled(act, "acc", acc_at[("up1", l)] + i)
                    if n >= 2:
                        act.wait_ge(g_done, n - 1)
                    for s in range(2):
                        act.activation(conv[:, i % 2, s, :], ps[:, s * SEQ:(s + 1) * SEQ], ACT.Identity,
                                       bias=col("conv_b", l * 2 * FT + s * FT + i), scale=conv_col(l, 2, i, s)).then_inc(conv_scaled, 1)
                if i >= 1:
                    wait_drained(act, "acc", acc_at[("up1", l)] + i - 1)
                    act.activation(act_g[:, (i - 1) % 2, :], conv[:, (i - 1) % 2, 0, :], ACT.Silu).then_inc(act_done, 1)

        def up1_dve(dve, l):
            for i in range(FT):
                f = acc_at[("up1", l)] + i
                dve.wait_ge(conv_scaled, 2 * (FT * l + i) + 2)
                ps = bank("acc", f)
                for j, back in ((1, 1), (0, 2)):
                    for s in range(2):
                        c = conv[:, i % 2, s, back:SEQ]
                        ins = dve.scalar_tensor_tensor(c, ps[:, s * SEQ:(s + 1) * SEQ - back], conv_col(l, j, i, s), c, ALU.mult, ALU.add)
                    if j:
                        link(dve, ins)
                ins.then_inc(drain("acc", f), 1)

        def up1_pool(pool, l):
            for i in range(FT):
                pool.wait_ge(act_done, FT * l + i + 1)
                pool.tensor_tensor(gT[:, i, :], act_g[:, i % 2, :], conv[:, i % 2, 1, :], ALU.mult).then_inc(g_done, 1)

        def down1_pe(pe, l):
            pe.wait_ge(g_done, FT * (l + 1))
            tok_gemm(pe, ("down1", l), acc_at[("down1", l)], FT, [LAT] * 2, lambda kt, tt: gT[:, kt, tt * P:(tt + 1) * P])

        S2 = 2 * SEQ
        r2 = Region(at1)
        uT = r2.take(KT, S2)
        yT = uT
        at2 = r2.at
        pA = r2.take(AT, S2)
        at_rwkv = r2.at
        q_tok = r2.take(4, 512)
        k_tok = r2.take(4, 256)
        v_tok = r2.take(4, P)
        qT = r2.take(4, S2)
        kT = r2.take(2, S2)
        probB = r2.take(2, 2, 512)
        probBT = r2.take(2, 1024)
        yB = r2.take(4, 512)
        rope_t = r2.take(2, 512)
        rr, kf, vf = pA[:, 0:4, :], pA[:, 4:8, :], pA[:, 8:12, :]
        r3 = Region(0)
        kk = r3.take(4, S2)
        kd_sum = r3.take(4, S2)
        l_pe = r3.take(4, CH + 1)
        l_pi = r3.take(4, CH)
        vst = r3.take(4, CH)
        assert r3.at <= at1
        r3 = Region(at_rwkv)
        lc = r3.take(4, S2)
        kka = r3.take(4, S2)
        kd = r3.take(4, S2)
        lora = r3.take(2, 512)
        ar = r3.take(4, 2, CH)
        ar_bd = r3.take(4, 2, P)
        bh_bd = r3.take(4, P)
        kh_bd = r3.take(4, P)
        b_tok = r3.take(4, P)
        k_tk = r3.take(4, P)
        nq = r3.take(4, 4, P)
        xi = r3.take(4, P)
        xiT = r3.take(4, P)
        yi = r3.take(4, P)
        g_sb = r3.take(4, CH)
        u_sb = r3.take(4, CH)
        state = r3.take(2, 4, CH)
        s_tmp = r3.take(4, CH)
        sig = nq[:, 0:2, :, :].rearrange("p a b c -> p a (b c)")
        iclr = nq[:, 2:4, :, :].rearrange("p a b c -> p a (b c)")
        g2 = pA[:, 12, :]
        y_st = yT[:, 0:4, :].rearrange("p j (c v) -> p j c v", c=NCH)
        def tail(at):
            r = Region(at)
            return r.take(4, D), r.take(2, D), r.take(2, KT, P), r.at

        o_mix0, gate_mix0, diag_mix0, _ = tail(at2)
        r4 = Region(at2)
        hid = r4.take(FT2, S2)
        relu_t = r4.take(2, 512)
        gate_ff = r4.take(2, D)
        diag_ff = r4.take(2, KT, P)
        o_ff = uT.rearrange("p a b -> p (a b)").rearrange("p (t d) -> p t d", t=4)

        ctx_landed, lora_landed, g2_landed = sem("ctx_landed"), sem("lora_landed"), sem("g2_landed")
        near_landed = sem("near_landed")

        def mod_shift(l, w, s):
            return lambda kt: mod[:, l, 3 * w * KT + kt, s:s + 1]

        def mod_mul(l, w, s):
            return lambda kt: mod_gain[:, l, w, kt, s:s + 1]

        shift_mid = stats(AT)
        shift_mid_set, shift_scaled, lora_in = sem("shift_mid_set"), sem("shift_scaled"), sem("lora_in")

        def projA_pe(pe):
            for s in (1, 0):
                norm_wait(pe, ("mix", 0, s))
            feat_gemm(pe, "projA", acc_at["projA"], AT, lambda kt: uT[:, kt, :])

        def projA_act(act):
            act.wait_ge(shift_mid_set, 1)
            for i in range(AT):
                f = acc_at["projA"] + i
                act.activation(pA[:, i, :], filled(act, "acc", f)[:, :], ACT.Identity,
                               scale=shift_mid[:, i:i + 1]).then_inc(shift_scaled, 1)
            for i, func in ((12, ACT.Tanh), (14, ACT.Sigmoid)):
                wait_drained(act, "acc", acc_at["projA"] + i)
                act.activation(pA[:, i, :], pA[:, i, :], func).then_inc(lora_in, 1)

        def projA_dve(dve):
            prev, nxt = col("a_mu_prev_2", 0, AT), col("a_mu_next_2", 0, AT)
            link(dve, dve.tensor_tensor(shift_mid[:, :], prev, nxt, ALU.add))
            dve.tensor_scalar(shift_mid[:, :], shift_mid[:, :], -1.0, 1.0, ALU.mult, ALU.add).then_inc(shift_mid_set, 1)
            for i in range(AT):
                f = acc_at["projA"] + i
                dve.wait_ge(shift_scaled, i + 1)
                ps = bank("acc", f)[:, :].rearrange("p (s t) -> p s t", s=2)
                p = pA[:, i, :].rearrange("p (s t) -> p s t", s=2)
                link(dve, dve.scalar_tensor_tensor(p[:, :, 1:], ps[:, :, 0:SEQ - 1], col("a_mu_prev_2", i), p[:, :, 1:], ALU.mult, ALU.add))
                dve.scalar_tensor_tensor(p[:, :, 0:SEQ - 1], ps[:, :, 1:], col("a_mu_next_2", i), p[:, :, 0:SEQ - 1],
                                         ALU.mult, ALU.add).then_inc(drain("acc", f), 1)

        def projA_wait(eng):
            for i in range(AT - 4, AT):
                wait_drained(eng, "acc", acc_at["projA"] + i)

        roped = sem("roped")

        def rope(dve, x, heads, tt, tmp, done, count):
            cos, sin = const("cos")[:, tt * HD:(tt + 1) * HD], const("sin")[:, tt * HD:(tt + 1) * HD]
            t0, t1 = tmp[:, 0, 0:heads * HD], tmp[:, 1, 0:heads * HD]
            cut = lambda v: v.rearrange("p (h a b f) -> p h a b f", h=heads, a=2, b=2)
            xs, ts, ss = cut(x), cut(t1), sin.rearrange("p (a b f) -> p a b f", a=2, b=2)
            dve.tensor_tensor(t0.rearrange("p (h e) -> p h e", h=heads), x.rearrange("p (h e) -> p h e", h=heads),
                              cos.unsqueeze(1).broadcast_to([P, heads, HD]), ALU.mult)
            for b in range(2):
                ins = dve.tensor_tensor(ts[:, :, :, b, :], xs[:, :, :, 1 - b, :],
                                        ss[:, :, b, :].unsqueeze(1).broadcast_to([P, heads, 2, 16]), ALU.mult)
            link(dve, ins)
            dve.tensor_tensor(x, t0, t1, ALU.add).then_inc(done, 1)
            dve.wait_ge(done, count)

        def projB_pe(pe):
            tok_gemm(pe, "projB", acc_at["projB"], KT, [ALL] * 2, lambda kt, tt: uT[:, kt, tt * P:(tt + 1) * P])
            for tt in ALL:
                wait_drained(pe, "acc", acc_at["projB"] + tt)
                wait_drained(pe, "acc", acc_at["projB"] + 4 + tt)
                if tt >= 2:
                    pe.wait_ge(roped, 2 * (tt - 1))
                for x, n, f in ((q_tok, 4, 2 * tt), (k_tok, 2, 2 * tt + 1)):
                    ps = claim(pe, "tr", tr_at["projB"] + f)
                    for j in range(n):
                        ins = pe.transpose(ps[:, j * P:(j + 1) * P], x[:, tt, j * P:(j + 1) * P], ident)
                    ins.then_inc(tr_full, 1)

        def dup_heads(ps, n=2):
            return ps.rearrange("p (k e) -> p k e", k=2).unsqueeze(2).broadcast_to([P, 2, n, HD])

        def projB_act(act):
            for tt in ALL:
                f = acc_at["projB"] + tt
                act.activation(q_tok[:, tt, :], filled(act, "acc", f)[:, :], ACT.Copy).then_inc(drain("acc", f), 1)
            for tt in ALL:
                f = acc_at["projB"] + 4 + tt
                ps = filled(act, "acc", f)
                act.activation(k_tok[:, tt, :].rearrange("p (k n e) -> p k n e", k=2, n=2), dup_heads(ps[:, 0:P]), ACT.Copy)
                act.activation(v_tok[:, tt, :], ps[:, P:2 * P], ACT.Copy).then_inc(drain("acc", f), 1)
            for tt in ALL:
                f = tr_at["projB"] + 2 * tt
                act.activation(qT[:, :, tt * P:(tt + 1) * P], filled(act, "tr", f)[:, :].rearrange("p (a b) -> p a b", a=4),
                               ACT.Copy, scale=SCALE).then_inc(drain("tr", f), 1)
                f += 1
                act.activation(kT[:, :, tt * P:(tt + 1) * P], filled(act, "tr", f)[:, 0:2 * P].rearrange("p (a b) -> p a b", a=2),
                               ACT.Copy).then_inc(drain("tr", f), 1)

        def projB_dve(dve):
            for tt in (0, 1):
                wait_drained(dve, "acc", acc_at["projB"] + 2 + tt)
                wait_drained(dve, "acc", acc_at["projB"] + 6 + tt)
                rope(dve, q_tok[:, 2 + tt, :], 8, tt, rope_t, roped, 2 * tt + 1)
                rope(dve, k_tok[:, 2 + tt, :], 4, tt, rope_t, roped, 2 * tt + 2)

        def projB_wait(pe):
            for f in (6, 7):
                wait_drained(pe, "tr", tr_at["projB"] + f)

        def heads(x, u, m, cols):
            return x[m * HD:(m + 1) * HD, u // 2, cols]

        def kv_of(u):
            return u // 4

        def attBl():
            return Attention("attBl", 8, lambda u, m: heads(qT, u, m, slice(SEQ + (u % 2) * P, SEQ + (u % 2 + 1) * P)),
                             lambda u, m: kT[m * HD:(m + 1) * HD, kv_of(u), :], lambda u: S2,
                             lambda u, m, kb: v_tok[:, kb, kv_of(u) * HD:(kv_of(u) + 1) * HD],
                             lambda u: yB[:, 2 + u % 2, (u // 2) * P:(u // 2 + 1) * P], probB, probBT,
                             bias=lambda u, m: (SEQ, const("band")[:, (u % 2) * SEQ:(u % 2 + 1) * SEQ]), sink=lambda u: 2 * (u // 2))

        def attBc():
            return Attention("attBc", 8, lambda u, m: heads(qT, u, m, slice((u % 2) * P, (u % 2 + 1) * P)),
                             lambda u, m: kT[m * HD:(m + 1) * HD, kv_of(u), 0:SEQ], lambda u: SEQ,
                             lambda u, m, kb: v_tok[:, kb, kv_of(u) * HD:(kv_of(u) + 1) * HD],
                             lambda u: yB[:, u % 2, (u // 2) * P:(u // 2 + 1) * P], probB, probBT, sink=lambda u: 2 * (u // 2))

        def yTB_pe(pe):
            for key in ("attBl", "attBc"):
                for u in (6, 7):
                    wait_drained(pe, "sc", sc_at[key] + u)
            for tt in ALL:
                f = tr_at["yTB"] + tt
                ps = claim(pe, "tr", f)
                for j in range(4):
                    ins = pe.transpose(ps[:, j * P:(j + 1) * P], yB[:, tt, j * P:(j + 1) * P], ident)
                ins.then_inc(tr_full, 1)

        def yTB_act(act):
            for tt in ALL:
                f = tr_at["yTB"] + tt
                act.activation(yT[:, 4:8, tt * P:(tt + 1) * P], filled(act, "tr", f)[:, :].rearrange("p (a b) -> p a b", a=4),
                               ACT.Copy).then_inc(drain("tr", f), 1)

        kk_squared, kk_clear, kk_rn, kk_done = sem("kk_squared"), sem("kk_clear"), sem("kk_rn"), sem("kk_done")
        bd_cleared = sem("bd_cleared")
        cum_done, decay_ready, prep_done = sem("cum_done"), sem("decay_ready"), sem("prep_done")
        l_mid, l_end, l_step, f_step = stats(4 * NCH), stats(4 * NCH), stats(4 * NCH), stats(4 * NCH)
        by_chunk = lambda v: v.rearrange("p (j c) -> p j c", j=4)
        ORDER = [list(range(NCH)), [3, 2, 1, 0, 7, 6, 5, 4]]

        def kk_dve(dve):
            projA_wait(dve)
            for j in range(4):
                dve.tensor_scalar(kk[:, j, :], kf[:, j, :], col("a_k_k_2", j), None, ALU.mult).then_inc(kk_done, 1)
            for j in range(4):
                f = acc_at["kk"] + j
                dve.tensor_scalar(kd_sum[:, j, :], filled(dve, "acc", f)[:, :], 1e-24, None, ALU.max).then_inc(drain("acc", f), 1)
            for j in range(4):
                dve.wait_ge(kk_rn, j + 1)
                if j == 0:
                    dve.wait_ge(kk_done, 4)
                dve.tensor_tensor(kk[:, j, :], kk[:, j, :], kd_sum[:, j, :], ALU.mult).then_inc(kk_done, 1)

        def kk_act(act):
            for j in range(4):
                act.wait_ge(kk_done, j + 1)
                act.activation(lc[:, j, :], kk[:, j, :], ACT.Square).then_inc(kk_squared, 1)

        def kk_pe(pe):
            for j in range(4):
                f = acc_at["kk"] + j
                pe.wait_ge(kk_squared, j + 1)
                ps = claim(pe, "acc", f)
                pe.matmul(ps[:, :], head_ones, lc[:, j, :], start=True, stop=True).then_inc(acc_full, 1)

        def kk_pool(pool):
            pool.wait_ge(tr_full, tr_at["yTB"] + 4)
            pool.memset(kka[:, :, :], -0.5).then_inc(kk_clear, 1)
            for x in (ar_bd[:, :, :, :], bh_bd[:, :, :], kh_bd[:, :, :]):
                pool.memset(x, 0.0).then_inc(bd_cleared, 1)
            pool.wait_ge(kk_clear, 1)
            pool.wait_ge(bd_cleared, 3)
            for j in range(4):
                wait_drained(pool, "acc", acc_at["kk"] + j)
                pool.tensor_tensor(kd_sum[:, j, :], kd_sum[:, j, :], kka[:, j, :], ALU.pow).then_inc(kk_rn, 1)

        def prep_pe(pe, d):
            if d == 0:
                pe.wait_ge(lora_landed, 32)
                pe.wait_ge(lora_in, 1)
            s = slice(d * 64, d * 64 + 64)
            for j in range(4):
                for i, x in enumerate((pA[s, 12, :], pA[s, 13, :])):
                    ps = claim(pe, "acc", acc_at[("prep", d)] + 2 * j + i)
                    pe.matmul(ps[:, :], lora[s, i, j * P:(j + 1) * P], x, start=True, stop=True).then_inc(acc_full, 1)

        def prep_act(act, d):
            if d:
                act.wait_ge(acc_full, acc_at[("chunk", 0, NCH - 1)] + 28)
            for j in range(4):
                if j >= 2:
                    act.wait_ge(prep_done, 4 * d + j - 1)
                for i, (x, b) in enumerate(((sig, "a_w0_2"), (iclr, "a_a0_2"))):
                    f = acc_at[("prep", d)] + 2 * j + i
                    act.activation(x[:, j % 2, :], filled(act, "acc", f)[:, :], ACT.Sigmoid, bias=col(b, 4 * d + j)).then_inc(drain("acc", f), 1)
            if d:
                act.dma_start(g2, I["a_g2_2"][0]).then_inc(g2_landed, 16)
            act.wait_ge(cum_done, d + 1)
            act.activation(f_step[:, :], l_step[:, :], ACT.Exp, scale=-DECAY).then_inc(decay_ready, 1)

        def prep_dve(dve, d):
            edge = const("scan_edge")
            if d:
                dve.wait_ge(bk_done, 4 * NCH)
            if d == 0:
                dve.wait_ge(kk_done, 8)
            for j in range(4):
                for i in range(2):
                    wait_drained(dve, "acc", acc_at[("prep", d)] + 2 * j + i)
                x = lc[:, j, :]
                if d == 0:
                    dve.tensor_tensor_scan(x, edge[:, 0:S2], sig[:, j % 2, :], 0.0, ALU.mult, ALU.add)
                else:
                    dve.tensor_tensor_scan(x[:, ::-1], edge[:, 1:S2 + 1][:, ::-1], sig[:, j % 2, :][:, ::-1], 0.0, ALU.mult, ALU.add)
                dve.tensor_tensor(kka[:, j, :], kk[:, j, :], iclr[:, j % 2, :], ALU.mult)
                link(dve, dve.scalar_tensor_tensor(kd[:, j, :], iclr[:, j % 2, :], -1.0, kf[:, j, :], ALU.add, ALU.mult))
                link(dve, dve.scalar_tensor_tensor(kd[:, j, :], kd[:, j, :], col("a_k_a_2", j), kf[:, j, :], ALU.mult, ALU.add))
                if d == 0:
                    ins = dve.tensor_copy(kd_sum[:, j, :], kd[:, j, :])
                else:
                    ins = dve.tensor_tensor(kd_sum[:, j, :], kd_sum[:, j, :], kd[:, j, :], ALU.add)
                ins.then_inc(prep_done, 1)
            dve.wait_ge(prep_done, 4 * d + 4)
            chunked = lc[:, :, :].rearrange("p j (c t) -> p (j c) t", t=CH)
            link(dve, dve.tensor_copy(l_mid[:, :], chunked[:, :, CH // 2 - 1 + d]))
            link(dve, dve.tensor_tensor(chunked, chunked, l_mid[:, :].unsqueeze(2).broadcast_to([P, 4 * NCH, CH]), ALU.subtract))
            link(dve, dve.tensor_copy(l_end[:, :], chunked[:, :, 0 if d else CH - 1]))
            mid, end, step = by_chunk(l_mid[:, :]), by_chunk(l_end[:, :]), by_chunk(l_step[:, :])
            link(dve, dve.memset(l_step[:, :], 0.0))
            for a, b, n in ([(0, 1, 7)] if d == 0 else [(1, 0, 3), (0, 7, 1), (5, 4, 3)]):
                ins = dve.tensor_tensor(step[:, :, a:a + n], end[:, :, a:a + n], mid[:, :, b:b + n], ALU.add)
            ins.then_inc(cum_done, 1)

        pe_exp, ar_done, bk_done, bd_done = sem("pe_exp"), sem("ar_done"), sem("bk_done"), sem("bd_done")
        xi_set = sem("xi_set")

        def chunk_fills(d, s):
            f = acc_at[("chunk", d, s)]
            return {"nq": f, "lev0": f + 2, "lev": f + 4, "g": f + 24, "u": f + 25, "s": f + 26, "y": f + 27}

        def chunk_act(act, d, s):
            n, ci = NCH * d + s, ORDER[d][s]
            sl = slice(ci * CH, (ci + 1) * CH)
            F, T = chunk_fills(d, s), tr_at[("chunk", d, s)]
            if n:
                act.wait_ge(ar_done, n)
                act.wait_ge(bk_done, 4 * n)
            act.wait_ge(cum_done, d + 1)
            incl = 1 - d
            act.activation(l_pe[:, :, incl:incl + CH], lc[:, :, sl], ACT.Exp, scale=-DECAY)
            act.activation(l_pe[:, :, CH * d:CH * d + 1], by_chunk(l_mid[:, :])[:, :, ci:ci + 1], ACT.Exp, scale=DECAY)
            act.activation(l_pi[:, :, :], lc[:, :, sl], ACT.Exp, scale=DECAY).then_inc(pe_exp, 1)
            act.wait_ge(ar_done, n + 1)
            if n:
                act.wait_ge(acc_full, acc_at[("chunk", (n - 1) // NCH, (n - 1) % NCH)] + 28)
            else:
                act.wait_ge(bd_cleared, 3)
            for hd in range(2):
                h = slice(hd * HD, hd * HD + HD)
                act.activation(ar_bd[h, :, :, h], ar[h, :, :, :], ACT.Copy).then_inc(bd_done, 1)
            ps = filled(act, "tr", T)
            for hd in range(2):
                h = slice(hd * HD, hd * HD + HD)
                ins = act.activation(vst[h, :, :], ps[0:CH, :].rearrange("p (j c) -> p j c", j=4)[:, :, h], ACT.Copy)
            ins.then_inc(drain("tr", T), 1)
            for i, x in ((1, b_tok), (2, k_tk)):
                act.activation(x[:, :, :], filled(act, "tr", T + i)[:, :].rearrange("p (j c) -> p j c", j=4), ACT.Copy).then_inc(drain("tr", T + i), 1)
            for lev in range(1, 6):
                for g in range(2):
                    f = F["lev"] + 4 * (lev - 1) + g
                    act.activation(yi[:, 2 * g:2 * g + 2, :], filled(act, "acc", f)[:, 0:2 * P].rearrange("p (j c) -> p j c", j=2),
                                   ACT.Copy).then_inc(drain("acc", f), 1)
            for f, x in ((F["g"], g_sb), (F["u"], u_sb)):
                act.activation(x[:, :, :], filled(act, "acc", f)[:, 0:4 * CH].rearrange("p (j c) -> p j c", j=4), ACT.Copy).then_inc(drain("acc", f), 1)

        def chunk_pool(pool, d, s):
            n, ci = NCH * d + s, ORDER[d][s]
            sl = slice(ci * CH, (ci + 1) * CH)
            if n:
                pool.wait_ge(acc_full, acc_at[("chunk", (n - 1) // NCH, (n - 1) % NCH)] + 28)
            for j in range(4):
                pool.tensor_copy(xi[:, j, :], ident)
                ins = pool.tensor_copy(xiT[:, j, :], ident)
            ins.then_inc(xi_set, 1)
            pool.wait_ge(xi_set, n + 1)
            pool.wait_ge(pe_exp, n + 1)
            pool.wait_ge(prep_done, 4 * d + 4)
            for hd in range(2):
                h = slice(hd * HD, hd * HD + HD)
                for i, (x, y) in enumerate(((bh_bd, kka), (kh_bd, kd))):
                    pool.tensor_tensor(x[h, :, h], y[h, :, sl], l_pi[h, :, :], ALU.mult).then_inc(bk_done, 1)
                    pool.wait_ge(bk_done, 4 * n + 2 * hd + i + 1)

        def chunk_pe(pe, d, s):
            n, ci = NCH * d + s, ORDER[d][s]
            sl = slice(ci * CH, (ci + 1) * CH)
            F, T = chunk_fills(d, s), tr_at[("chunk", d, s)]
            st = state[:, s % 2]
            ps = claim(pe, "tr", T)
            for j in range(4):
                ins = pe.transpose(ps[0:CH, j * P:(j + 1) * P], vf[:, j, sl], ident)
            ins.then_inc(tr_full, 1)
            pe.wait_ge(bk_done, 4 * n + 4)
            for i, x in ((1, bh_bd), (2, kh_bd)):
                ps = claim(pe, "tr", T + i)
                for j in range(4):
                    ins = pe.transpose(ps[:, j * P:(j + 1) * P], x[:, j, :], ident)
                ins.then_inc(tr_full, 1)
            pe.wait_ge(ar_done, n + 1)
            for g in range(2):
                ps = claim(pe, "acc", F["nq"] + g)
                for i in range(2):
                    for b, x in enumerate((bh_bd, kh_bd)):
                        ins = pe.matmul(ps[:, (2 * i + b) * P:(2 * i + b + 1) * P], x[:, 2 * g + i, :],
                                        ar[:, 2 * g + i, :, :].rearrange("p a t -> p (a t)"), start=True, stop=True)
                ins.then_inc(acc_full, 1)
            for g in range(2):
                wait_drained(pe, "acc", F["nq"] + g)
                ps = claim(pe, "acc", F["lev0"] + g)
                for i in range(2):
                    ins = pe.matmul(ps[:, i * P:(i + 1) * P], nq[:, 2 * g + i, 0, :], ident, start=True, stop=True)
                ins.then_inc(acc_full, 1)
            for lev in range(1, 6):
                for g in range(2):
                    wait_drained(pe, "acc", F["lev0"] + g if lev == 1 else F["lev"] + 4 * (lev - 2) + 2 + g)
                    f = F["lev"] + 4 * (lev - 1) + g
                    ps = claim(pe, "acc", f)
                    for i in range(2):
                        ins = pe.matmul(ps[:, i * P:(i + 1) * P], nq[:, 2 * g + i, 0, :], xi[:, 2 * g + i, :], start=True, stop=True)
                    ins.then_inc(acc_full, 1)
                for g in range(2):
                    wait_drained(pe, "acc", F["lev"] + 4 * (lev - 1) + g)
                    f = F["lev"] + 4 * (lev - 1) + 2 + g
                    ps = claim(pe, "acc", f)
                    for i in range(2):
                        j = 2 * g + i
                        if lev < 5:
                            pe.matmul(ps[:, i * P:(i + 1) * P], xiT[:, j, :], yi[:, j, :], start=True, stop=True)
                        ins = pe.matmul(ps[:, (2 + i) * P:(3 + i) * P], yi[:, j, :], xiT[:, j, :], start=True, stop=True)
                    ins.then_inc(acc_full, 1)
            first_chunk = s == 0
            out4 = lambda ps, j: ps[:, j * CH:(j + 1) * CH]
            wait_drained(pe, "tr", T)
            wait_drained(pe, "tr", T + 1)
            wait_drained(pe, "tr", T + 2)
            pe.wait_ge(bd_done, 2 * n + 2)
            if not first_chunk:
                wait_drained(pe, "acc", chunk_fills(d, s - 1)["s"])
            ps = claim(pe, "acc", F["g"])
            for j in range(4):
                ins = pe.matmul(out4(ps, j), nq[:, j, 2, :], vst[:, j, :], start=True, stop=first_chunk)
                if not first_chunk:
                    ins = pe.matmul(out4(ps, j), ar_bd[:, j, 0, :], st[:, j, :], start=False, stop=True)
            ins.then_inc(acc_full, 1)
            for g in range(2):
                wait_drained(pe, "acc", F["lev"] + 16 + 2 + g)
            wait_drained(pe, "acc", F["g"])
            ps = claim(pe, "acc", F["u"])
            for j in range(4):
                ins = pe.matmul(out4(ps, j), xiT[:, j, :], g_sb[:, j, :], start=True, stop=True)
            ins.then_inc(acc_full, 1)
            wait_drained(pe, "acc", F["u"])
            ps = claim(pe, "acc", F["s"])
            for j in range(4):
                pe.matmul(out4(ps, j), b_tok[:, j, :], u_sb[:, j, :], start=True, stop=False)
                ins = pe.matmul(out4(ps, j), k_tk[:, j, :], vst[:, j, :], start=False, stop=True)
            ins.then_inc(acc_full, 1)
            ps = claim(pe, "acc", F["y"])
            for j in range(4):
                pe.matmul(out4(ps, j), nq[:, j, 1, :], u_sb[:, j, :], start=True, stop=False)
                ins = pe.matmul(out4(ps, j), nq[:, j, 3, :], vst[:, j, :], start=False, stop=first_chunk)
                if not first_chunk:
                    ins = pe.matmul(out4(ps, j), ar_bd[:, j, 1, :], st[:, j, :], start=False, stop=True)
            ins.then_inc(acc_full, 1)

        def chunk_dve(dve, d, s):
            n, ci = NCH * d + s, ORDER[d][s]
            sl = slice(ci * CH, (ci + 1) * CH)
            F = chunk_fills(d, s)
            dve.wait_ge(pe_exp, n + 1)
            incl = 1 - d
            if n:
                dve.wait_ge(bd_done, 2 * n)
            dve.scalar_tensor_tensor(ar[:, :, 0, :], kk[:, :, sl], -1.0, l_pe[:, :, 1 - incl:1 - incl + CH], ALU.mult, ALU.mult)
            dve.tensor_tensor(ar[:, :, 1, :], rr[:, :, sl], l_pe[:, :, incl:incl + CH], ALU.mult).then_inc(ar_done, 1)
            tri = const(f"tri{d}").rearrange("p (a h t) -> p a h t", a=4, h=2)
            for g in range(2):
                ps = filled(dve, "acc", F["nq"] + g)
                for i in range(2):
                    x = ps[:, i * 2 * P:(i + 1) * 2 * P].rearrange("p (a t) -> p a t", a=4).unsqueeze(2).broadcast_to([P, 4, 2, CH])
                    ins = dve.tensor_tensor(nq[:, 2 * g + i, :, :].rearrange("p a (h t) -> p a h t", h=2), x, tri, ALU.mult)
                ins.then_inc(drain("acc", F["nq"] + g), 1)
            names = ("low", "up") if d == 0 else ("up", "low")
            wide = lambda lev, i: mask(f"{names[i]}{lev}").unsqueeze(1).broadcast_to([P, 2, P])
            two = lambda ps, i: ps[:, i * 2 * P:(i + 1) * 2 * P].rearrange("p (j c) -> p j c", j=2)
            dve.wait_ge(xi_set, n + 1)
            if n == 0:
                dve.wait_ge(masks_set, 1)
            for lev in range(6):
                for g in range(2):
                    jj = slice(2 * g, 2 * g + 2)
                    f = F["lev0"] + g if lev == 0 else F["lev"] + 4 * (lev - 1) + 2 + g
                    ps = filled(dve, "acc", f)
                    if lev == 0:
                        dve.copy_predicated(xi[:, jj, :], wide(0, 0), two(ps, 0))
                        wait_drained(dve, "acc", F["nq"] + g)
                        ins = dve.copy_predicated(xiT[:, jj, :], wide(0, 1), nq[:, jj, 0, :])
                    else:
                        if lev < 5:
                            dve.copy_predicated(xi[:, jj, :], wide(lev, 0), two(ps, 0))
                        ins = dve.copy_predicated(xiT[:, jj, :], wide(lev, 1), two(ps, 1))
                    ins.then_inc(drain("acc", f), 1)
            ps = filled(dve, "acc", F["s"])[:, 0:4 * CH].rearrange("p (j c) -> p j c", j=4)
            nxt = state[:, (s + 1) % 2]
            if s == 0:
                dve.wait_ge(decay_ready, d + 1)
                x = ps
            else:
                wait_drained(dve, "acc", chunk_fills(d, s - 1)["s"])
                link(dve, dve.tensor_tensor(s_tmp[:, :, :], ps, state[:, s % 2], ALU.add))
                x = s_tmp[:, :, :]
            dve.tensor_tensor(nxt, x, by_chunk(f_step[:, :])[:, :, ci:ci + 1].broadcast_to([P, 4, CH]), ALU.mult)\
               .then_inc(drain("acc", F["s"]), 1)
            ps = filled(dve, "acc", F["y"])[:, 0:4 * CH].rearrange("p (j c) -> p j c", j=4)
            y = y_st[:, :, ci, :]
            if d == 0:
                ins = dve.tensor_copy(y, ps)
            else:
                ins = dve.tensor_tensor(y, y, ps, ALU.add)
            ins.then_inc(drain("acc", F["y"]), 1)

        gn_sum, gn_mean, gn_sq, gn_var, gn_rs = (stats(4 * NCH) for _ in range(5))
        gn_var_ready, gn_rstd, y_normed, bonus_in = sem("gn_var_ready"), sem("gn_rstd"), sem("y_normed"), sem("bonus_in")
        y_all = y_st.rearrange("p j c v -> p (j c) v")
        half32 = nq[:, 0, 0, 0:32]
        half_cleared = sem("half_cleared")

        def rwkv_out_pool(pool):
            pool.wait_ge(acc_full, acc_at[("chunk", 1, NCH - 1)] + 28)
            pool.memset(half32, -0.5).then_inc(half_cleared, 1)
            pool.wait_ge(half_cleared, 1)
            pool.wait_ge(gn_var_ready, 1)
            pool.tensor_tensor(gn_rs[:, :], gn_var[:, :], half32, ALU.pow).then_inc(gn_rstd, 1)

        def rwkv_out_dve(dve):
            wait_drained(dve, "acc", chunk_fills(1, NCH - 1)["y"])
            wide = lambda v: v.unsqueeze(2).broadcast_to([P, 4 * NCH, CH])
            squares = lc[:, :, :].rearrange("p j (c v) -> p (j c) v", v=CH)
            for j in range(4):
                dve.scalar_tensor_tensor(kd_sum[:, j, :], rr[:, j, :], col("a_r_k_2", j), kd_sum[:, j, :], ALU.mult, ALU.mult).then_inc(bonus_in, 1)
            link(dve, dve.tensor_reduce(gn_sum[:, :], y_all, AX_X, ALU.add))
            link(dve, dve.tensor_scalar(gn_mean[:, :], gn_sum[:, :], 1.0 / HD, None, ALU.mult))
            link(dve, dve.tensor_tensor(y_all, y_all, wide(gn_mean[:, :]), ALU.subtract))
            link(dve, dve.tensor_tensor(squares, y_all, y_all, ALU.mult))
            link(dve, dve.tensor_reduce(gn_sq[:, :], squares, AX_X, ALU.add))
            dve.tensor_scalar(gn_var[:, :], gn_sq[:, :], 1.0 / HD, GN_EPS, ALU.mult, ALU.add).then_inc(gn_var_ready, 1)
            dve.wait_ge(gn_rstd, 1)
            dve.tensor_tensor(y_all, y_all, wide(gn_rs[:, :]), ALU.mult).then_inc(y_normed, 1)
            for j in range(4):
                f = acc_at["rwkv_out"] + 2 * j
                for i in range(2):
                    wait_drained(dve, "tr", tr_at["rwkv_out"] + 2 * j + i)
                a = yT[:, j, :]
                dve.tensor_tensor(lc[:, j, :], filled(dve, "acc", f)[:, :], vf[:, j, :], ALU.mult).then_inc(drain("acc", f), 1)
                link(dve, dve.tensor_scalar(a, a, col("a_gn_w_2", j), col("a_gn_b_2", j), ALU.mult, ALU.add))
                wait_drained(dve, "acc", f)
                link(dve, dve.tensor_tensor(a, a, lc[:, j, :], ALU.add))
                dve.tensor_tensor(a, a, filled(dve, "acc", f + 1)[:, :], ALU.mult).then_inc(drain("acc", f + 1), 1)

        def rwkv_out_pe(pe):
            pe.wait_ge(g2_landed, 16)
            pe.wait_ge(lora_in, 2)
            pe.wait_ge(y_normed, 1)
            for j in range(4):
                for i in range(2):
                    f = tr_at["rwkv_out"] + 2 * j + i
                    ps = claim(pe, "tr", f)
                    for c in range(4):
                        ins = pe.transpose(ps[0:CH, c * P:(c + 1) * P], y_st[:, j, 4 * i + c, :], ident)
                    ins.then_inc(tr_full, 1)
            for j in range(4):
                f = acc_at["rwkv_out"] + 2 * j
                pe.wait_ge(bonus_in, j + 1)
                pe.matmul(claim(pe, "acc", f)[:, :], head_ones, kd_sum[:, j, :], start=True, stop=True).then_inc(acc_full, 1)
                pe.matmul(claim(pe, "acc", f + 1)[:, :], g2[:, j * P:(j + 1) * P], pA[:, 14, :], start=True, stop=True).then_inc(acc_full, 1)

        def rwkv_out_act(act):
            for j in range(4):
                for i in range(2):
                    f = tr_at["rwkv_out"] + 2 * j + i
                    ps = filled(act, "tr", f)[0:CH, :].rearrange("p (c x) -> p c x", c=4)
                    for hd in range(2):
                        h = slice(hd * HD, hd * HD + HD)
                        dst = yT[h, j, i * SEQ:(i + 1) * SEQ].rearrange("p (c t) -> p c t", c=4)
                        ins = act.activation(dst, ps[:, :, h], ACT.Copy)
                    ins.then_inc(drain("tr", f), 1)

        gate_diag, post_squared, post_mean, post_rstd, h_updated = (
            sem("gate_diag"), sem("post_squared"), sem("post_mean"), sem("post_rstd"), sem("h_updated"))
        posts = {}

        class Post:

            def __init__(self, key, l, w, streams, o, gate, diag, free):
                self.key, self.l, self.w, self.streams, self.o, self.gate, self.diag, self.free = key, l, w, streams, o, gate, diag, free
                self.tiles = [(s, (h_ctx if s else h_lat)[:, t, :]) for s in streams for t in range(TT)]
                n = len(self.tiles)
                self.f0 = acc_at[key] + 2 * len(streams)
                self.ss, self.sum, self.ms, self.rs = stats(2 * n), stats(n), stats(n), stats(n)
                self.index = len(posts)
                self.gates_before = sum(len(p.streams) for p in posts.values())
                self.tiles_before = sum(len(p.tiles) for p in posts.values())
                posts[key] = self

            def pool_gate(self, pool):
                self.free(pool)
                for i, s in enumerate(self.streams):
                    for kt in range(KT):
                        ins = pool.tensor_scalar(self.diag[:, i, kt, :], ident, mod_gate[:, self.l, self.w, kt, s:s + 1], None, ALU.mult)
                    ins.then_inc(gate_diag, 1)

            def pool_rstd(self, pool):
                pool.wait_ge(post_mean, self.index + 1)
                pool.tensor_tensor(self.rs[:, :], self.ms[:, :], half[:, 0:len(self.tiles)], ALU.pow).then_inc(post_rstd, 1)

            def tensor_gate(self, pe):
                for i in range(len(self.streams)):
                    pe.wait_ge(gate_diag, self.gates_before + i + 1)
                    for hf in range(2):
                        ps = claim(pe, "acc", acc_at[self.key] + 2 * i + hf)
                        pe.matmul(ps[:, :], ones, self.diag[:, i, 4 * hf:4 * hf + 4, :].rearrange("p a b -> p (a b)"),
                                  start=True, stop=True).then_inc(acc_full, 1)

            def scalar(self, act):
                for i in range(len(self.streams)):
                    for hf in range(2):
                        f = acc_at[self.key] + 2 * i + hf
                        act.activation(self.gate[:, i, hf * 512:(hf + 1) * 512], filled(act, "acc", f)[:, :], ACT.Copy).then_inc(drain("acc", f), 1)
                n = len(self.tiles)
                for hf in range(2):
                    for t in range(n):
                        ps = filled(act, "acc", self.f0 + hf * n + t)
                        act.activation(self.o[:, t, hf * 512:(hf + 1) * 512], ps[:, :], ACT.Square,
                                       accum_out=self.ss[:, hf * n + t:hf * n + t + 1]).then_inc(post_squared, 1)

            def vector(self, dve):
                n = len(self.tiles)
                for hf in range(2):
                    for t in range(n):
                        f = self.f0 + hf * n + t
                        dve.wait_ge(post_squared, 2 * self.tiles_before + hf * n + t + 1)
                        dve.tensor_copy(self.o[:, t, hf * 512:(hf + 1) * 512], bank("acc", f)[:, :]).then_inc(drain("acc", f), 1)
                link(dve, dve.tensor_tensor(self.sum[:, :], self.ss[:, 0:n], self.ss[:, n:2 * n], ALU.add))
                dve.tensor_scalar(self.ms[:, :], self.sum[:, :], 1.0 / D, EPS, ALU.mult, ALU.add).then_inc(post_mean, 1)
                for f in range(self.f0 - 2 * len(self.streams), self.f0):
                    wait_drained(dve, "acc", f)
                for f in range(self.f0 + 2 * n - 4, self.f0 + 2 * n):
                    wait_drained(dve, "acc", f)
                dve.wait_ge(post_rstd, self.index + 1)
                for t, (s, h) in enumerate(self.tiles):
                    link(dve, dve.scalar_tensor_tensor(self.o[:, t, :], self.o[:, t, :], self.rs[:, t:t + 1],
                                                       self.gate[:, self.streams.index(s), :], ALU.mult, ALU.mult))
                    dve.tensor_tensor(h, h, self.o[:, t, :], ALU.add).then_inc(h_updated, 1)

            def updated(self, eng):
                eng.wait_ge(h_updated, self.tiles_before + len(self.tiles))

        relu_ready, hid_ready = sem("relu_ready"), sem("hid_ready")

        def ff1_pe(pe, key, streams, l, w):
            for s in streams:
                norm_wait(pe, ("ff", l, s))
            feat_gemm(pe, key, acc_at[key], FT2, lambda kt: uT[:, kt, 0:SEQ * len(streams)])

        def ff1_act(act, key, n0, width):
            for i in range(FT2):
                f = acc_at[key] + i
                ps = filled(act, "acc", f)
                if n0 + i >= 2:
                    act.wait_ge(hid_ready, n0 + i - 1)
                act.activation(relu_t[:, i % 2, 0:width], ps[:, 0:width], ACT.Relu).then_inc(drain("acc", f), 1)

        def ff1_dve(dve, key, width):
            for i in range(FT2):
                wait_drained(dve, "acc", acc_at[key] + i)
                x = relu_t[:, i % 2, 0:width]
                dve.tensor_tensor(hid[:, i, 0:width], x, x, ALU.mult).then_inc(hid_ready, 1)

        r5 = Region(0)
        dk_tok = r5.take(4, 256)
        dv_tok = r5.take(4, P)
        dq_tok = r5.take(2, 512)
        gain_row = r5.take(2, HD)
        assert r5.at <= N_BIAS * SEQ
        r5 = Region(at2)
        near = r5.take(2, 8, SEQ)
        cv_tok = r5.take(4, 512)
        cqT = r5.take(4, SEQ)
        ckT = r5.take(4, S2)
        dqT = r5.take(4, SEQ)
        dkT = r5.take(2, S2)
        y2 = r5.take(TT, D)
        rope2 = r5.take(2, 512)
        sq2 = r5.take(2, 512)
        prob2 = r5.take(2, 2, 512)
        prob2T = r5.take(2, 1024)
        tail2 = r5.at
        hank2 = prob2.rearrange("p a b c -> p (a b c)")
        hank2b = prob2T.rearrange("p a b -> p (a b)")
        hankels = [v.rearrange("p (h k) -> p h k", h=8) for v in (hank2, hank2b)]
        yT2 = uT.rearrange("p a b -> p (a b)")[:, 0:KT * SEQ].rearrange("p (a b) -> p a b", a=KT)
        o_mix1, gate_mix1, diag_mix1, _ = tail(at2)

        def near_dma(act):
            posts["post_ff0"].updated(act)
            act.dma_start(gain_row[:, 0, :], I["d_q_gain_2"].partition_broadcast(P)).then_inc(gains_landed, 16)
            act.dma_start(gain_row[:, 1, :], I["d_k_gain_2"].partition_broadcast(P)).then_inc(gains_landed, 16)
            rpb = I["c_rpb_2"]
            nd, nc_ = 2 * NA_KH - 1, 2 * NA_KW - 1
            for qt in range(2):
                for i in range(2):
                    r = 2 * qt + i
                    for h in range(8):
                        src = bass.AP(tensor=rpb.tensor, offset=(h * nd + NA_KH - 1 - r) * nc_ + NA_KW - 1 - (GRID_W - 1),
                                      ap=[[1, GRID_W], [nc_, 4], [1, GRID_W]])
                        act.dma_start(hankels[qt][i * GRID_W:(i + 1) * GRID_W, h, :].rearrange("p (t k) -> p t k", t=4), src)\
                          .then_inc(near_landed, 16)

        def near_pe(pe):
            pe.wait_ge(near_landed, 16 * 32)
            for i in range(8):
                ps = claim(pe, "acc", acc_at["near"] + i)
                pe.matmul(ps[:, :], flip64, hankels[i // 4][:, 2 * (i % 4):2 * (i % 4) + 2, :].rearrange("p a b -> p (a b)"),
                          start=True, stop=True).then_inc(acc_full, 1)

        def near_dve(dve):
            for i in range(8):
                f = acc_at["near"] + i
                win = const("near")[:, (i // 4) * SEQ:(i // 4 + 1) * SEQ].unsqueeze(1).broadcast_to([P, 2, SEQ])
                dve.tensor_tensor(near[:, i // 4, 2 * (i % 4):2 * (i % 4) + 2, :],
                                  filled(dve, "acc", f)[:, :].rearrange("p (a b) -> p a b", a=2), win, ALU.add).then_inc(drain("acc", f), 1)

        PQ, PK, PV, PDQ, PDK = (lambda: [acc_at["proj1"] + n for n in (0, 4, 8, 12, 14)])()
        d_mean, d_rstd, d_normed, gains_landed = sem("d_mean"), sem("d_rstd"), sem("d_normed"), sem("gains_landed")
        d_ss, d_ms, d_rs = stats(48), stats(48), stats(48)
        D_UNITS = [(dk_tok[:, tt, :], PDK + tt, 4, 16 + 4 * tt, tt - 2 if tt >= 2 else None) for tt in ALL]
        D_UNITS = [(dq_tok[:, tt, :], PDQ + tt, 8, 8 * tt, tt) for tt in range(TT)] + D_UNITS

        def proj1_pe(pe):
            for s in (1, 0):
                norm_wait(pe, ("mix", 1, s))
            feat_gemm(pe, "proj1", PQ, 4, lambda kt: uT[:, kt, SEQ:S2])
            feat_gemm(pe, "proj1_k", PK, 4, lambda kt: uT[:, kt, :])
            tok_gemm(pe, "proj1_tok", PV, KT, [ALL, LATS, ALL], lambda kt, tt: uT[:, kt, tt * P:(tt + 1) * P])
            for n, (x, f, nh, c, lat) in enumerate(D_UNITS):
                pe.wait_ge(d_normed, n + 1)
                ps = claim(pe, "tr", tr_at["proj1"] + n)
                for j in range(nh // 2):
                    ins = pe.transpose(ps[:, j * P:(j + 1) * P], x[:, j * P:(j + 1) * P], ident)
                ins.then_inc(tr_full, 1)

        def proj1_act(act):
            for i in range(4):
                act.activation(cqT[:, i, :], filled(act, "acc", PQ + i)[:, 0:SEQ], ACT.Copy, scale=SCALE).then_inc(drain("acc", PQ + i), 1)
            for i in range(4):
                act.activation(ckT[:, i, :], filled(act, "acc", PK + i)[:, :], ACT.Copy).then_inc(drain("acc", PK + i), 1)
            for tt in ALL:
                act.activation(cv_tok[:, tt, :], filled(act, "acc", PV + tt)[:, :], ACT.Copy).then_inc(drain("acc", PV + tt), 1)
            for n, (x, f, nh, c, lat) in enumerate(D_UNITS):
                ps = filled(act, "acc", f)
                if n >= 2:
                    act.wait_ge(d_mean, n - 1)
                if nh == 8:
                    act.activation(x, ps[:, :], ACT.Copy)
                    act.activation(sq2[:, n % 2, :], ps[:, :], ACT.Square).then_inc(drain("acc", f), 1)
                else:
                    act.activation(x.rearrange("p (k n e) -> p k n e", k=2, n=2), dup_heads(ps[:, 0:P]), ACT.Copy)
                    act.activation(dv_tok[:, (n - 2), :], ps[:, P:2 * P], ACT.Copy)
                    act.activation(sq2[:, n % 2, 0:4 * HD].rearrange("p (k n e) -> p k n e", k=2, n=2), dup_heads(ps[:, 0:P]),
                                   ACT.Square).then_inc(drain("acc", f), 1)
            for n, (x, f, nh, c, lat) in enumerate(D_UNITS):
                if n >= 2:
                    t = tr_at["proj1"] + n
                    act.activation(dkT[:, :, (n - 2) * P:(n - 1) * P], filled(act, "tr", t)[:, 0:2 * P].rearrange("p (a b) -> p a b", a=2),
                                   ACT.Copy).then_inc(drain("tr", t), 1)
                else:
                    t = tr_at["proj1"] + n
                    act.activation(dqT[:, :, n * P:(n + 1) * P], filled(act, "tr", t)[:, :].rearrange("p (a b) -> p a b", a=4),
                                   ACT.Copy, scale=SCALE).then_inc(drain("tr", t), 1)

        def proj1_pool(pool):
            for n, (x, f, nh, c, lat) in enumerate(D_UNITS):
                pool.wait_ge(d_mean, n + 1)
                pool.tensor_tensor(d_rs[:, c:c + nh], d_ms[:, c:c + nh], half[:, 0:nh], ALU.pow).then_inc(d_rstd, 1)

        def proj1_dve(dve):
            dve.wait_ge(gains_landed, 32)
            for n, (x, f, nh, c, lat) in enumerate(D_UNITS):
                wait_drained(dve, "acc", f)
                link(dve, dve.tensor_reduce(d_ss[:, c:c + nh], sq2[:, n % 2, 0:nh * HD].rearrange("p (h e) -> p h e", e=HD), AX_X, ALU.add))
                dve.tensor_scalar(d_ms[:, c:c + nh], d_ss[:, c:c + nh], 1.0 / HD, EPS, ALU.mult, ALU.add).then_inc(d_mean, 1)
            for n, (x, f, nh, c, lat) in enumerate(D_UNITS):
                dve.wait_ge(d_rstd, n + 1)
                xh = x.rearrange("p (h e) -> p h e", e=HD)
                link(dve, dve.tensor_tensor(xh, xh, d_rs[:, c:c + nh].unsqueeze(2).broadcast_to([P, nh, HD]), ALU.mult))
                ins = dve.tensor_tensor(xh, xh, gain_row[:, 0 if n < 2 else 1, :].unsqueeze(1).broadcast_to([P, nh, HD]), ALU.mult)
                if lat is not None:
                    link(dve, ins)
                    rope(dve, x, nh, lat, rope2, d_normed, n + 1)
                else:
                    ins.then_inc(d_normed, 1)

        def attC():
            return Attention("attC", 8, lambda u, m: heads(cqT, u, m, slice((u % 2) * P, (u % 2 + 1) * P)),
                             lambda u, m: heads(ckT, u, m, slice(0, S2)), lambda u: S2,
                             lambda u, m, kb: cv_tok[:, kb, (2 * (u // 2) + m) * HD:(2 * (u // 2) + m + 1) * HD],
                             lambda u: y2[:, u % 2, (u // 2) * P:(u // 2 + 1) * P], prob2, prob2T,
                             bias=lambda u, m: (SEQ, near[:, u % 2, 2 * (u // 2) + m, :]))

        def attD():
            return Attention("attD", 8, lambda u, m: heads(dqT, u, m, slice((u % 2) * P, (u % 2 + 1) * P)),
                             lambda u, m: dkT[m * HD:(m + 1) * HD, kv_of(u), :], lambda u: S2,
                             lambda u, m, kb: dv_tok[:, kb, kv_of(u) * HD:(kv_of(u) + 1) * HD],
                             lambda u: y2[:, u % 2, 512 + (u // 2) * P:512 + (u // 2 + 1) * P], prob2, prob2T)

        def yT2_pe(pe):
            for key in ("attC", "attD"):
                for u in (6, 7):
                    wait_drained(pe, "sc", sc_at[key] + u)
            for g in range(4):
                f = tr_at["yT1_2"] + g
                ps = claim(pe, "tr", f)
                for i in range(2):
                    for tt in range(TT):
                        kt = 2 * g + i
                        ins = pe.transpose(ps[:, i * SEQ + tt * P:i * SEQ + (tt + 1) * P], y2[:, tt, kt * P:(kt + 1) * P], ident)
                ins.then_inc(tr_full, 1)

        def yT2_act(act):
            for g in range(4):
                f = tr_at["yT1_2"] + g
                act.activation(yT2[:, 2 * g:2 * g + 2, :].rearrange("p a b -> p (a b)"), filled(act, "tr", f)[:, :], ACT.Copy).then_inc(drain("tr", f), 1)


        att = {("att1", l): att1(l) for l in range(DEPTH)}
        att_bl, att_bc, att_c, att_d = attBl(), attBc(), attC(), attD()

        def after_rwkv(pool):
            pool.wait_ge(mod_ready, 2 * DEPTH)
            for i in range(4, 8):
                wait_drained(pool, "acc", acc_at["rwkv_out"] + i)

        mix0 = Post("post_mix0", 0, 0, (1, 0), o_mix0, gate_mix0, diag_mix0, after_rwkv)
        ff0 = Post("post_ff0", 0, 1, (1, 0), o_ff, gate_ff, diag_ff, lambda pool: None)
        mix1 = Post("post_mix1", 1, 0, (0,), o_mix1, gate_mix1, diag_mix1,
                    lambda pool: pool.wait_ge(tr_full, tr_at["yT1_2"] + 4))
        ff1 = Post("post_ff1", 1, 1, (0,), o_ff, gate_ff, diag_ff, lambda pool: None)

        def ctx_ready(eng):
            eng.wait_ge(ctx_landed, 16)

        def mod_norms(l, w):
            out = []
            for s in ((1, 0) if (l, w) != (1, 1) else (0,)):
                if (l, w) == (0, 0):
                    ready = ctx_ready if s else stream_ready(DEPTH, "attn")
                else:
                    ready = {(0, 1): mix0, (1, 0): ff0, (1, 1): mix1}[l, w].updated
                at = SEQ if s == 0 and (l, w) != (1, 1) else 0
                out.append((("ff" if w else "mix", l, s), h_ctx if s else h_lat, ready, mod_mul(l, w, s), mod_shift(l, w, s),
                            uT[:, :, at:at + SEQ]))
            return out
        out_stored = sem("out_stored")

        def stream_ready(l, which):
            def ready(eng):
                if l == 0 and which == "attn":
                    eng.wait_ge(x_landed, 16)
                    return
                f = acc_at[("out1", l)] if which == "ffn" else acc_at[("down1", l - 1)]
                for i in range(4):
                    wait_drained(eng, "acc", f + i)
            return ready

        def mix_lhs(y):
            return lambda kt, tt: y[:, kt, tt * P:(tt + 1) * P]

        block = ctx.enter_context(nc.Block())

        @block.sync
        def _(sp):
            sp.dma_start(h_lat[:, :, :], I["x"][0].rearrange("(t p) d -> p t d", p=P)).then_inc(x_landed, 16)
            sp.dma_start(h_ctx[:, :, :], I["ctx_2"][0].rearrange("(t p) d -> p t d", p=P)).then_inc(ctx_landed, 16)
            for g, src in enumerate(chunks):
                if g >= RING:
                    sp.wait_ge(*release[g - RING])
                sp.dma_start(slot(g), src).then_inc(weights_landed[g % RING], 16)
            ff1.updated(sp)
            sp.dma_start(out.rearrange("(t p) d -> p t d", p=P), h_lat[:, :, :]).then_inc(out_stored, 16)
            sp.wait_ge(out_stored, 16)

        @block.gpsimd
        def _(pool):
            setup_pool(pool)
            for l in range(DEPTH):
                norm_pool(pool, ("attn", l))
                qkv_pool(pool, l)
                subnorm_pool(pool, l)
                norm_pool(pool, ("ffn", l))
                up1_pool(pool, l)
            for key, *_ in mod_norms(0, 0):
                norm_pool(pool, key)
            kk_pool(pool)
            for d in range(2):
                for s in range(NCH):
                    chunk_pool(pool, d, s)
            rwkv_out_pool(pool)
            mix0.pool_gate(pool)
            mix0.pool_rstd(pool)
            ff0.pool_gate(pool)
            for key, *_ in mod_norms(0, 1):
                norm_pool(pool, key)
            ff0.pool_rstd(pool)
            for key, *_ in mod_norms(1, 0):
                norm_pool(pool, key)
            proj1_pool(pool)
            mix1.pool_gate(pool)
            mix1.pool_rstd(pool)
            ff1.pool_gate(pool)
            for key, *_ in mod_norms(1, 1):
                norm_pool(pool, key)
            ff1.pool_rstd(pool)

        @block.scalar
        def _(act):
            setup_act_dma(act)
            setup_act(act)
            for l in range(DEPTH):
                ada_act(act, l)
            for l in range(DEPTH):
                norm_act(act, ("attn", l), h_lat, stream_ready(l, "attn"))
                qkv_act(act, l)
                att[("att1", l)].scalar(act, subnorm_act(act, l, att[("att1", l)]))
                norm_act(act, ("ffn", l), h_lat, stream_ready(l, "ffn"))
                up1_act(act, l)
            for key, src, ready, *_ in mod_norms(0, 0):
                norm_act(act, key, src, ready)
            projA_act(act)
            projB_act(act)
            att_bl.scalar(act)
            att_bc.scalar(act)
            yTB_act(act)
            act.dma_start(lora[:, 0, :], I["a_w2_2"][0].rearrange("d l c -> (d l) c")).then_inc(lora_landed, 16)
            act.dma_start(lora[:, 1, :], I["a_a2_2"][0].rearrange("d l c -> (d l) c")).then_inc(lora_landed, 16)
            kk_act(act)
            for d in range(2):
                prep_act(act, d)
                for s in range(NCH):
                    chunk_act(act, d, s)
            rwkv_out_act(act)
            mix0.scalar(act)
            for key, src, ready, *_ in mod_norms(0, 1):
                norm_act(act, key, src, ready)
            ff1_act(act, "ff1_0", 0, S2)
            ff0.scalar(act)
            near_dma(act)
            for key, src, ready, *_ in mod_norms(1, 0):
                norm_act(act, key, src, ready)
            proj1_act(act)
            att_c.scalar(act)
            att_d.scalar(act)
            yT2_act(act)
            mix1.scalar(act)
            for key, src, ready, *_ in mod_norms(1, 1):
                norm_act(act, key, src, ready)
            ff1_act(act, "ff1_1", FT2, SEQ)
            ff1.scalar(act)

        @block.tensor
        def _(pe):
            setup_pe(pe)
            for l in range(DEPTH):
                ada_pe(pe, l)
            for l in range(DEPTH):
                norm_pe(pe, ("attn", l))
                qkv_pe(pe, l)
                att[("att1", l)].tensor(pe)
                yT1_pe(pe, l, att[("att1", l)])
                out1_pe(pe, l)
                norm_pe(pe, ("ffn", l))
                up1_pe(pe, l)
                down1_pe(pe, l)
            for key, *_ in mod_norms(0, 0):
                norm_pe(pe, key)
            projA_pe(pe)
            projB_pe(pe)
            projB_wait(pe)
            att_bl.tensor(pe)
            att_bc.tensor(pe)
            yTB_pe(pe)
            kk_pe(pe)
            for d in range(2):
                prep_pe(pe, d)
                for s in range(NCH):
                    chunk_pe(pe, d, s)
            rwkv_out_pe(pe)
            mix0.tensor_gate(pe)
            for i in range(4, 8):
                wait_drained(pe, "acc", acc_at["rwkv_out"] + i)
            for tt in (2, 3):
                wait_drained(pe, "tr", tr_at["yTB"] + tt)
            tok_gemm(pe, "out2_0", mix0.f0, KT, [ALL] * 2, mix_lhs(yT))
            for key, *_ in mod_norms(0, 1):
                norm_pe(pe, key)
            ff1_pe(pe, "ff1_0", (1, 0), 0, 1)
            ff0.tensor_gate(pe)
            pe.wait_ge(hid_ready, FT2)
            tok_gemm(pe, "ff2_0", ff0.f0, FT2, [ALL] * 2, mix_lhs(hid))
            for key, *_ in mod_norms(1, 0):
                norm_pe(pe, key)
            near_pe(pe)
            proj1_pe(pe)
            for n in (4, 5):
                wait_drained(pe, "tr", tr_at["proj1"] + n)
            for i in range(4, 8):
                wait_drained(pe, "acc", acc_at["near"] + i)
            att_c.tensor(pe)
            att_d.tensor(pe)
            yT2_pe(pe)
            mix1.tensor_gate(pe)
            for g in (2, 3):
                wait_drained(pe, "tr", tr_at["yT1_2"] + g)
            tok_gemm(pe, "out2_1", mix1.f0, KT, [LAT] * 2, mix_lhs(yT2))
            for key, *_ in mod_norms(1, 1):
                norm_pe(pe, key)
            ff1_pe(pe, "ff1_1", (0,), 1, 1)
            ff1.tensor_gate(pe)
            pe.wait_ge(hid_ready, 2 * FT2)
            tok_gemm(pe, "ff2_1", ff1.f0, FT2, [LAT] * 2, mix_lhs(hid))

        @block.vector
        def _(dve):
            setup_dve(dve)
            for l in range(DEPTH):
                ada_dve(dve, l)
            for l in range(DEPTH):
                norm_dve(dve, ("attn", l), h_lat, stream_ready(l, "attn"), lambda kt: col("ln_attn_g", KT * l + kt), None, hT)
                qkv_dve(dve, l)
                att[("att1", l)].vector(dve, subnorm_dve(dve, l, att[("att1", l)]))
                yT1_dve(dve, l)
                add_dve(dve, acc_at[("out1", l)])
                norm_dve(dve, ("ffn", l), h_lat, stream_ready(l, "ffn"), lambda kt: col("ln_ffn_g", KT * l + kt), None, hT)
                up1_dve(dve, l)
                add_dve(dve, acc_at[("down1", l)])
            dve.wait_ge(mod_ready, 2 * DEPTH)
            for key, src, ready, gain, shift, dst in mod_norms(0, 0):
                norm_dve(dve, key, src, ready, gain, shift, dst)
            projA_dve(dve)
            projB_dve(dve)
            att_bl.vector(dve)
            att_bc.vector(dve)
            kk_dve(dve)
            for d in range(2):
                prep_dve(dve, d)
                for s in range(NCH):
                    chunk_dve(dve, d, s)
            rwkv_out_dve(dve)
            mix0.vector(dve)
            for key, src, ready, gain, shift, dst in mod_norms(0, 1):
                norm_dve(dve, key, src, ready, gain, shift, dst)
            ff1_dve(dve, "ff1_0", S2)
            ff0.vector(dve)
            for key, src, ready, gain, shift, dst in mod_norms(1, 0):
                norm_dve(dve, key, src, ready, gain, shift, dst)
            near_dve(dve)
            proj1_dve(dve)
            att_c.vector(dve)
            att_d.vector(dve)
            mix1.vector(dve)
            for key, src, ready, gain, shift, dst in mod_norms(1, 1):
                norm_dve(dve, key, src, ready, gain, shift, dst)
            ff1_dve(dve, "ff1_1", SEQ)
            ff1.vector(dve)


_INS = ["x", "ln_attn_g", "w_in", "qk_norm_g", "diff_lambda", "diff_subln_g", "w_out", "ln_ffn_g", "w_up", "conv_w",
        "conv_b", "w_down", "rel_bias", "c_2", "ctx_2", "c_ctx_2", "w_ada_2", "b_ada_2", "g_pre_mix_2", "g_post_mix_2",
        "g_pre_ff_2", "g_post_ff_2", "w_in_even_2", "w_in_odd_2", "w_out_2", "w_ff1_2", "w_ff2_2", "a_mu_prev_2",
        "a_mu_next_2", "a_w0_2", "a_w2_2", "a_a0_2", "a_a2_2", "a_g2_2", "a_k_k_2", "a_k_a_2", "a_r_k_2", "a_gn_w_2",
        "a_gn_b_2", "b_sink_2", "c_rpb_2", "d_q_gain_2", "d_k_gain_2"]


def kernel(**inputs):
    import concourse.bacc as _bacc
    from concourse.bass_utils import run_bass_kernel_spmd as _run

    nc = _bacc.Bacc("TRN2", target_bir_lowering=False, num_devices=1)
    arrays, dram = {}, {}
    for name in _INS:
        a = np.ascontiguousarray(inputs[name])
        arrays[f"in_{name}"] = a
        dram[name] = nc.dram_tensor(f"in_{name}", a.shape, mybir.dt.from_np(a.dtype), kind="ExternalInput").ap()
    consts = []
    for name, a in (("const_keep", KEEP), ("const_first", FIRST), ("const_masks", MASKS)):
        arrays[name] = a
        consts.append(nc.dram_tensor(name, a.shape, mybir.dt.from_np(a.dtype), kind="ExternalInput").ap())
    out = nc.dram_tensor("out", (1, SEQ, D), F32, kind="ExternalOutput").ap()
    first_and_second_block(nc, dram, consts, out[0])
    r = _run(nc, [arrays], core_ids=[0])
    return r.results[0]["out"]
```

```python
import math
from contextlib import ExitStack

import numpy as np

import concourse.bass as bass
from concourse import mybir

F32 = mybir.dt.float32
U8 = mybir.dt.uint8
R32 = mybir.dt.float32r
ALU = mybir.AluOpType
ACT = mybir.ActivationFunctionType
AX_X = mybir.AxisListType.X

P = 128
D = 1024
KT = D // P
SEQ = 256
TT = SEQ // P
DEPTH = 2
HD = 64
REL_BUCKETS = 32
N_BIAS = 12
D_FF = 2816
FT = D_FF // P
D_FF2 = 4096
FT2 = D_FF2 // P
CONV = 3
N_ADA = 6 * D // 512
A_IN = 1920
AT = A_IN // P
EPS = 1e-6
GN_EPS = 64e-5
NEG = -1e30
SCALE = HD ** -0.5
LAMBDA_INIT = [0.8 - 0.6 * math.exp(-0.3 * i) for i in range(DEPTH)]
CH = 64
NCH = 2 * SEQ // CH
DECAY = math.exp(-0.5)
RAW = 4
HIGH = 3
SLOT = 4 * 512
GRID_W, NA_KH, NA_KW = 64, 8, 16


def rel_bucket(dist):
    n = np.maximum(dist, 0)
    nf = np.maximum(n, 16).astype(np.float32)
    large = 16 + (np.log(nf / np.float32(16)) / np.float32(math.log(64.0)) * np.float32(16)).astype(np.int32)
    return np.where(n < 16, n, np.minimum(large, 31))


def constants():
    f = np.float32
    keep, first, masks = {}, {}, {}
    eye = np.eye(P, dtype=f)
    keep["ident"] = eye
    keep["flip64"] = np.kron(np.eye(2, dtype=f), np.eye(64, dtype=f)[::-1])
    keep["ones"] = np.ones((P, P), f)
    head = np.arange(P) // 64
    same = (head[:, None] == head[None, :])
    keep["head_ones"] = same.astype(f)
    s, t = np.arange(P)[:, None] % 64, np.arange(P)[None, :] % 64
    for d, (strict, incl) in enumerate([((s < t) & same, (s <= t) & same), ((s > t) & same, (s >= t) & same)]):
        keep[f"tri{d}"] = np.concatenate([strict, incl, strict, incl], 1).astype(f)
    edge = np.ones(2 * SEQ + 2, f)
    edge[::CH] = 0
    keep["scan_edge"] = np.broadcast_to(edge, (P, edge.size))
    tok = np.arange(SEQ)
    inv = (np.float32(10000.0) ** (-np.arange(16, dtype=f) / f(16))).astype(f)
    row, colm = (tok // GRID_W).astype(f)[:, None] * inv, (tok % GRID_W).astype(f)[:, None] * inv
    cos = np.concatenate([np.cos(row), np.cos(row), np.cos(colm), np.cos(colm)], 1).astype(f)
    sin = np.concatenate([-np.sin(row), np.sin(row), -np.sin(colm), np.sin(colm)], 1).astype(f)
    tile = lambda a: a.reshape(TT, P, -1).transpose(1, 0, 2).reshape(P, -1)
    keep["cos"], keep["sin"] = tile(cos), tile(sin)
    q, k = np.arange(SEQ)[:, None], np.arange(SEQ)[None, :]
    keep["band"] = tile(np.where(np.abs(q - k) <= 128, 0, NEG).astype(f))
    qc, kc = q % GRID_W, k % GRID_W
    start = np.clip(qc - NA_KW // 2, 0, GRID_W - NA_KW)
    keep["near"] = tile(np.where((kc >= start) & (kc < start + NA_KW), 0, NEG).astype(f))

    first["flip"] = eye[::-1]
    first["causal"] = np.where(np.arange(SEQ)[None, :] <= P + np.arange(P)[:, None], 0, NEG).astype(f)
    hot = np.zeros((P, 384), f)
    hot[rel_bucket(255 - np.arange(384)), np.arange(384)] = 1
    first["bucket_hot"] = hot

    for lev in range(6):
        m = 1 << lev
        low = (np.arange(P)[:, None] // (2 * m) == np.arange(P)[None, :] // (2 * m)) & (
            (np.arange(P)[:, None] // m) % 2 == 1) & ((np.arange(P)[None, :] // m) % 2 == 0)
        masks[f"low{lev}"] = low.astype(f)
        masks[f"up{lev}"] = low.T.astype(f)
    return keep, first, masks


def packed(parts):
    at, where = 0, {}
    for name, a in parts.items():
        where[name] = (at, a.shape[1])
        at += a.shape[1]
    return np.ascontiguousarray(np.concatenate(list(parts.values()), 1)), where


KEEP, KEEP_AT = packed(constants()[0])
FIRST, FIRST_AT = packed(constants()[1])
MASKS, MASKS_AT = packed(constants()[2])

PARAM_GROUPS = [
    [("ln_attn_g", 16), ("ln_ffn_g", 16), ("diff_subln_g", 2), ("qk_norm_g", 8), ("g_pre_mix_2", 16),
     ("g_post_mix_2", 16), ("g_pre_ff_2", 16), ("g_post_ff_2", 16), ("d_q_gain_2", 1), ("d_k_gain_2", 1),
     ("c_2", 8), ("c_ctx_2", 8)],
    [("a_mu_prev_2", 15), ("a_mu_next_2", 15), ("a_w0_2", 8), ("a_a0_2", 8), ("a_k_k_2", 4), ("a_k_a_2", 4),
     ("a_r_k_2", 4), ("a_gn_w_2", 4), ("a_gn_b_2", 4)],
    [("b_ada_2", 96)],
    [("conv_b", 88)],
    [("conv_w", 128)], [("conv_w", 128)], [("conv_w", 8)],
]
HALF_ROWS = ("qk_norm_g", "d_q_gain_2", "d_k_gain_2")


def first_and_second_block(nc, I, consts, out):
    with ExitStack() as ctx:
        def sb(name, shape, dt=F32):
            return ctx.enter_context(nc.sbuf_tensor(name, shape, dt))

        made = {}

        def sem(name):
            if name not in made:
                made[name] = ctx.enter_context(nc.semaphore(name))
            return made[name]

        h_lat = sb("h_lat", [P, TT, D])
        h_ctx = sb("h_ctx", [P, TT, D])
        pcol = sb("pcol", [P, len(PARAM_GROUPS), P])
        keep = sb("keep", [P, KEEP.shape[1]])
        masks = sb("masks", [P, MASKS.shape[1]], U8)
        mod = sb("mod", [P, DEPTH, 6 * KT, 2])
        mod_gain = sb("mod_gain", [P, DEPTH, 2, KT, 2])
        mod_gate = sb("mod_gate", [P, DEPTH, 2, KT, 2])
        silu_c = sb("silu_c", [P, KT, 2])
        bcast = sb("bcast", [P, 10])
        neg_sink = sb("neg_sink", [P, 8])
        stat = sb("stat", [P, 1320])
        n_arena = 28320
        at_arena = -(-nc.sbuf_base // 32) * 32
        arena = sb("arena", [P, n_arena + (HIGH + RAW) * SLOT])
        edges = [1024 + SLOT * i for i in range(n_arena // SLOT + 1) if 1024 + SLOT * i < n_arena]
        edges += [n_arena + SLOT * i for i in range(HIGH + RAW + 1)]
        windows = [nc.alloc_sbuf_tensor_at(f"rounded{i}", [P, b - a], R32, offset=at_arena + 4 * a)
                   for i, (a, b) in enumerate(zip(edges, edges[1:]))]
        half = sb("half", [P, 4 * NCH])
        banks = [ctx.enter_context(nc.psum_tensor(f"acc{i}", [P, 512], F32)) for i in range(4)]
        trs = [ctx.enter_context(nc.psum_tensor(f"tr{i}", [P, 512], F32)) for i in range(2)]
        scs = [ctx.enter_context(nc.psum_tensor(f"sc{i}", [P, 512], F32)) for i in range(2)]
        t5_scratch = nc.dram_tensor("t5_scratch", [N_BIAS, 384], F32, kind="Internal").ap()

        def const(name):
            at, n = KEEP_AT[name]
            return keep[:, at:at + n]

        def mask(name):
            at, n = MASKS_AT[name]
            return masks[:, at:at + n]

        ident, head_ones, flip64, ones = const("ident"), const("head_ones"), const("flip64"), const("ones")

        stat_at = [0]

        def stats(n):
            at = stat_at[0]
            stat_at[0] += n
            assert stat_at[0] <= 1320
            return stat[:, at:at + n]

        class Region:

            def __init__(self, at=0, slots=0):
                self.at, self.end = at, n_arena + slots * SLOT

            def take(self, *shape):
                n = int(np.prod(shape))
                v = arena[:, self.at:self.at + n]
                self.at += n
                assert self.at <= self.end, self.at
                if len(shape) == 2:
                    v = v.rearrange("p (a b) -> p a b", a=shape[0])
                elif len(shape) == 3:
                    v = v.rearrange("p (a b c) -> p a b c", a=shape[0], b=shape[1])
                elif len(shape) == 4:
                    v = v.rearrange("p (a b c d) -> p a b c d", a=shape[0], b=shape[1], c=shape[2])
                return v

        param_at = {}
        for g, group in enumerate(PARAM_GROUPS):
            r = 0
            for name, n in group:
                if name != "conv_w":
                    param_at[name] = (g, r)
                r += n

        def col(name, i=0, n=1):
            if name == "conv_w":
                return pcol[:, 4 + i // P, i % P:i % P + n]
            g, r = param_at[name]
            return pcol[:, g, r + i:r + i + n]

        acc_at, tr_at, sc_at = {}, {}, {}
        fills = [0, 0, 0]

        def stage(key, acc=0, tr=0, sc=0):
            acc_at[key], tr_at[key], sc_at[key] = fills
            fills[0] += acc
            fills[1] += tr
            fills[2] += sc

        acc_full, tr_full, sc_full = sem("acc_full"), sem("tr_full"), sem("sc_full")
        acc_drained = [sem(f"acc_drained{i}") for i in range(4)]
        tr_drained = [sem(f"tr_drained{i}") for i in range(2)]
        sc_drained = [sem(f"sc_drained{i}") for i in range(2)]
        POOLS = {"acc": (banks, acc_full, acc_drained), "tr": (trs, tr_full, tr_drained), "sc": (scs, sc_full, sc_drained)}

        def bank(pool, f):
            return POOLS[pool][0][f % len(POOLS[pool][0])]

        def claim(pe, pool, f):
            b, _, drained = POOLS[pool]
            if f >= len(b):
                pe.wait_ge(drained[f % len(b)], f // len(b))
            return b[f % len(b)]

        def filled(eng, pool, f):
            b, full, _ = POOLS[pool]
            eng.wait_ge(full, f + 1)
            return b[f % len(b)]

        def drain(pool, f):
            _, _, drained = POOLS[pool]
            return drained[f % len(drained)]

        def wait_drained(eng, pool, f):
            _, _, drained = POOLS[pool]
            eng.wait_ge(drained[f % len(drained)], f // len(drained) + 1)

        chunks = []
        release = []
        chunk_at = {}
        partial = [0]
        chunk_read = sem("chunk_read")
        whole = set()

        def r32(v):
            row = arena.shape[1]
            p0, at = v.offset // row, v.offset % row
            last = at + sum(step * (n - 1) for step, n in list(v.ap)[1:])
            i = max(n for n, a in enumerate(edges) if a <= at)
            assert last < edges[i + 1], (at, last)
            width = edges[i + 1] - edges[i]
            return bass.AP(tensor=windows[i][:, :].tensor, offset=p0 * width + at - edges[i], ap=[[width, v.ap[0][1]]] + list(v.ap)[1:])


        def plan_tok(key, w, kts, f0, blocks):
            chunk_at[key] = len(chunks)
            n = w.shape[1]
            view = w.rearrange("(k p) n -> p k n", p=P)
            for c, tts in enumerate(blocks):
                f0 += len(tts)
                for k0 in range(0, kts, 4):
                    chunks.append(view[:, k0:min(k0 + 4, kts), 512 * c:min(512 * c + 512, n)])
                    if k0 + 4 >= kts:
                        release.append((acc_full, f0))
                    else:
                        partial[0] += 1
                        release.append((chunk_read, partial[0]))

        def plan_feat(key, w, cols, fills_of):
            chunk_at[key] = len(chunks)
            view = w.rearrange("(k p) n -> p k n", p=P)
            for (c0, c1), f in zip(cols, fills_of):
                chunks.append(view[:, :, c0:c1])
                release.append((acc_full, f))

        def plan_up(l):
            key = ("up1", l)
            up = I["w_up"][l].rearrange("(k p) (s n) -> p k s n", p=P, s=2)
            chunk_at[key] = len(chunks)
            for i in range(FT):
                chunks.append(up[:, :, :, i * P:(i + 1) * P])
                release.append((acc_full, acc_at[key] + i + 1))

        ada_chunk = {}

        def plan_ada(blocks, fill_of):
            for n, b in enumerate(blocks):
                view = I["w_ada_2"][b // N_ADA].rearrange("(k p) n -> p k n", p=P)
                c = 512 * (b % N_ADA)
                ada_chunk[b] = len(chunks)
                for k0 in (0, 4):
                    chunks.append(view[:, k0:k0 + 4, c:c + 512])
                    whole.add(len(chunks) - 1)
                partial[0] += 1
                release.extend([(chunk_read, partial[0]), (sc_full, fill_of(n) + 1)])

        def is_up(g):
            return len(chunks[g].shape) == 4

        def shaped(place, g):
            if is_up(g):
                return place.rearrange("p (k s n) -> p k s n", k=KT, s=2)
            k, n = chunks[g].shape[1], chunks[g].shape[2]
            return place[:, 0:k * n].rearrange("p (k n) -> p k n", k=k)

        def raw_slot(g):
            at = n_arena + (HIGH + (g - chunk_at["out2_0"] + RAW - 1) % RAW) * SLOT
            return arena[:, at:at + SLOT]

        def high_slot(g):
            at = n_arena + (split_no[g] % HIGH) * SLOT
            return arena[:, at:at + SLOT]

        weights_landed = [sem(f"weights_landed{i}") for i in range(RAW)]
        high_made, split_made = sem("high_made"), sem("split_made")
        split_no, split_chunks = {}, []

        def wait_landed(eng, g):
            dmas = sum(2 if is_up(c) else 1 for c in range(g % RAW, g + 1, RAW))
            eng.wait_ge(weights_landed[g % RAW], 16 * dmas)

        def load(sp, g):
            dst, src = shaped(raw_slot(g), g), chunks[g]
            for d, s in [(dst[:, :, s, :], src[:, :, s, :]) for s in range(2)] if is_up(g) else [(dst, src)]:
                sp.dma_start(d, s).then_inc(weights_landed[g % RAW], 16)

        splits = {"high": 0, "low": 0}
        held = [True, True]

        def size(g):
            return int(np.prod(chunks[g].shape[1:]))

        def ahead_act(act, g):
            g = min(g, chunk_at["out2_0"] - 1) if held[0] else g
            while splits["high"] < len(split_chunks) and split_chunks[splits["high"]] <= g:
                n = splits["high"]
                c = split_chunks[n]
                wait_landed(act, c)
                if n >= HIGH:
                    act.wait_ge(*release[split_chunks[n - HIGH]])
                act.activation(r32(high_slot(c)[:, 0:size(c)]), raw_slot(c)[:, 0:size(c)], ACT.Copy).then_inc(high_made, 1)
                splits["high"] += 1

        def ahead_dve(dve, g):
            g = min(g, chunk_at["out2_0"] - 1) if held[1] else g
            while splits["low"] < len(split_chunks) and split_chunks[splits["low"]] <= g:
                n = splits["low"]
                c = split_chunks[n]
                dve.wait_ge(high_made, n + 1)
                w = raw_slot(c)[:, 0:size(c)]
                dve.tensor_tensor(r32(w), w, r32(high_slot(c)[:, 0:size(c)]), ALU.subtract).then_inc(split_made, 1)
                splits["low"] += 1

        def parts(pe, g):
            pe.wait_ge(split_made, split_no[g] + 1)
            return shaped(high_slot(g), g), shaped(raw_slot(g), g)

        def both(pair, cut):
            return tuple(r32(cut(x)) for x in pair)

        def mm3(pe, ps, a, b, first, last):
            (ah, al), (bh, bl) = a, b
            pe.matmul(ps, ah, bh, start=first, stop=False)
            pe.matmul(ps, ah, bl, start=False, stop=False)
            return pe.matmul(ps, al, bh, start=False, stop=last)

        LAT = [0, 1]
        ALL = [0, 1, 2, 3]
        LATS = [2, 3]
        stage("params", tr=2)
        norm_n = {}

        def plan_norm(key):
            norm_n[key] = len(norm_n)
            stage(("norm", key), tr=4)

        def pairs(ncols):
            return [(c, min(c + 256, ncols)) for c in range(0, ncols, 256)]

        for l in range(DEPTH):
            plan_norm(("attn", l))
            stage(("qkv", l), acc=12, tr=8)
            plan_tok(("qkv", l), I["w_in"][l], KT, acc_at[("qkv", l)], [LAT] * 6)
            if l == 0:
                stage("bcast", acc=1)
                stage("t5", acc=1 + N_BIAS // 2)
            stage(("att1", l), acc=32, tr=16 + 8, sc=16 + 8)
            plan_ada(range(8 * l, 8 * l + 8), lambda n: sc_at[("att1", l)] + 3 * n)
            stage(("yT1", l), tr=4)
            stage(("out1", l), acc=4)
            plan_tok(("out1", l), I["w_out"][l], KT, acc_at[("out1", l)], [LAT] * 2)
            plan_norm(("ffn", l))
            stage(("up1", l), acc=FT)
            plan_up(l)
            stage(("down1", l), acc=4)
            plan_tok(("down1", l), I["w_down"][l], FT, acc_at[("down1", l)], [LAT] * 2)

        def pair_fills(key, n):
            return [acc_at[key] + min(i + 2, n) for i in range(0, n, 2)]

        plan_norm(("mix", 0, 1))
        plan_norm(("mix", 0, 0))
        stage("projA", acc=AT)
        plan_feat("projA", I["w_in_even_2"][0][:, 0:A_IN], pairs(A_IN), pair_fills("projA", AT))
        stage("projB", acc=8, tr=8)
        plan_tok("projB", I["w_in_even_2"][0][:, A_IN:A_IN + 768], KT, acc_at["projB"], [ALL] * 2)
        stage("attBl", acc=16, tr=16 + 4, sc=8 + 4)
        plan_ada(range(16, 20), lambda n: sc_at["attBl"] + 3 * n)
        stage("attBc", acc=16, tr=8 + 4, sc=8 + 4)
        plan_ada(range(20, 24), lambda n: sc_at["attBc"] + 3 * n)
        stage("yTB", tr=4)
        stage("kk", acc=1, tr=4)
        for d in range(2):
            stage(("prep", d), acc=8)
            for s in range(NCH):
                stage(("chunk", d, s), acc=28, tr=3)
        stage("rwkv_out", acc=8, tr=8)
        stage("post_mix0", acc=4 + 8)
        plan_tok("out2_0", I["w_out_2"][0], KT, acc_at["post_mix0"] + 4, [ALL] * 2)
        plan_norm(("ff", 0, 1))
        plan_norm(("ff", 0, 0))
        EIGHTHS, ET = 8, FT2 // 8

        def plan_ff1(e):
            stage(("ff1", e), acc=ET)
            plan_feat(("ff1", e), I["w_ff1_2"][0][:, e * ET * P:(e + 1) * ET * P], pairs(ET * P), pair_fills(("ff1", e), ET))

        def plan_ff2(e):
            stage(("ff2", e), acc=8)
            plan_tok(("ff2", e), I["w_ff2_2"][0][e * ET * P:(e + 1) * ET * P, :], ET, acc_at[("ff2", e)], [ALL] * 2)

        plan_ff1(0)
        stage("post_ff0", acc=4)
        for e in range(EIGHTHS):
            if e + 1 < EIGHTHS:
                plan_ff1(e + 1)
            plan_ff2(e)
        plan_norm(("mix", 1, 1))
        plan_norm(("mix", 1, 0))
        stage("near", acc=8)
        stage("proj1", acc=4 + 4 + 4 + 2 + 4, tr=6)
        f = acc_at["proj1"]
        plan_feat("proj1", I["w_in_odd_2"][0][:, 0:1024], pairs(1024), [f + 2, f + 4, f + 6, f + 8])
        chunk_at["proj1_k"] = chunk_at["proj1"] + 2
        plan_tok("proj1_tok", I["w_in_odd_2"][0][:, 1024:2304], KT, f + 8, [ALL, LATS, ALL])
        stage("attC", acc=16, tr=16, sc=8)
        stage("attD", acc=16, tr=16, sc=8)
        stage("yT1_2", tr=4)
        stage("post_mix1", acc=2 + 4)
        plan_tok("out2_1", I["w_out_2"][1], KT, acc_at["post_mix1"] + 2, [LAT] * 2)
        plan_norm(("ff", 1, 0))
        stage("ff1_1", acc=FT2)
        plan_feat("ff1_1", I["w_ff1_2"][1], pairs(D_FF2), pair_fills("ff1_1", FT2))
        stage("post_ff1", acc=2 + 4)
        plan_tok("ff2_1", I["w_ff2_2"][1], FT2, acc_at["post_ff1"] + 2, [LAT] * 2)

        split_chunks += [g for g in range(len(chunks)) if g not in whole]
        split_no.update({g: n for n, g in enumerate(split_chunks)})

        r1 = Region()
        t5_bias = r1.take(N_BIAS, SEQ)
        xn = r1.take(TT, D)
        at1 = r1.at
        hT = r1.take(KT, SEQ), r1.take(KT, SEQ)
        yT1 = hT
        at_gate = r1.at
        qkT = r1.take(4, 4, SEQ)
        vv = r1.take(2, TT, 512)
        qn = r1.take(2, 512)
        sq = r1.take(2, 512)
        at_att = r1.at
        prob = r1.take(2, 2, 512)
        probT = r1.take(2, 1024)
        y1 = r1.take(TT, D)
        mod_row = r1.take(512)
        r1b = Region(at_gate)
        gT = r1b.take(FT, SEQ), r1b.take(FT, SEQ)
        conv = r1b.take(2, 2, SEQ)
        act_g = r1b.take(2, SEQ)
        r0 = Region(at_att)
        prow = r0.take(len(PARAM_GROUPS), P)
        first = r0.take(FIRST.shape[1])
        mask_rows = r0.take(MASKS.shape[1])
        lrow = r0.take(520)
        lprod = r0.take(2 * DEPTH * HD)
        lsum = r0.take(8)
        relb = r0.take(N_BIAS)
        t5_vec = r0.take(384)
        hankel = r0.take(N_BIAS, SEQ)

        def first_const(name):
            at, n = FIRST_AT[name]
            return first[:, at:at + n]

        norm_ss = norm_ms = norm_rs = stats(2 * 16)
        norm_summed, norm_mean, norm_rstd, norm_xn = (
            sem("norm_summed"), sem("norm_mean"), sem("norm_rstd"), sem("norm_xn"))
        norm_high_set, norm_done = sem("norm_high_set"), sem("norm_done")
        dve_chain = sem("dve_chain")
        chain = [0]

        def link(dve, ins):
            chain[0] += 1
            ins.then_inc(dve_chain, 1)
            dve.wait_ge(dve_chain, chain[0])

        def norm_act(act, key, src, ready):
            n = norm_n[key]
            ready(act)
            if n:
                act.wait_ge(tr_full, tr_at[("norm", [k for k in norm_n if norm_n[k] == n - 1][0])] + 4)
            for tt in range(TT):
                act.activation(xn[:, tt, :], src[:, tt, :], ACT.Square,
                               accum_out=norm_ss[:, 2 * n + tt:2 * n + tt + 1]).then_inc(norm_summed, 1)

        def norm_pool(pool, key):
            n = norm_n[key]
            pool.wait_ge(norm_mean, n + 1)
            pool.tensor_tensor(norm_rs[:, 2 * n:2 * n + 2], norm_ms[:, 2 * n:2 * n + 2], half[:, 0:2],
                               ALU.pow).then_inc(norm_rstd, 1)

        def norm_high(act, key, gain, shift, dst):
            for g in range(4):
                f = tr_at[("norm", key)] + g
                if shift:
                    wait_drained(act, "tr", f)
                else:
                    ps = filled(act, "tr", f)
                for i in range(2):
                    kt = 2 * g + i
                    hi, lo = r32(dst[0][:, kt, :]), dst[1][:, kt, :]
                    if shift:
                        ins = act.activation(hi, lo, ACT.Copy)
                    else:
                        ins = act.activation(hi, ps[:, i * SEQ:(i + 1) * SEQ], ACT.Identity, scale=gain(kt))
                ins.then_inc(norm_high_set, 1)

        def norm_dve(dve, key, src, ready, gain, shift, dst):
            n = norm_n[key]
            dve.wait_ge(norm_summed, 2 * n + 2)
            dve.tensor_scalar(norm_ms[:, 2 * n:2 * n + 2], norm_ss[:, 2 * n:2 * n + 2], 1.0 / D, EPS,
                              ALU.mult, ALU.add).then_inc(norm_mean, 1)
            ready(dve)
            dve.wait_ge(norm_rstd, n + 1)
            for tt in range(TT):
                dve.tensor_scalar(xn[:, tt, :], src[:, tt, :], norm_rs[:, 2 * n + tt:2 * n + tt + 1], None,
                                  ALU.mult).then_inc(norm_xn, 1)
            for g in range(5 if shift else 4):
                f = tr_at[("norm", key)] + g
                if shift and g < 4:
                    ps = filled(dve, "tr", f)
                    for i in range(2):
                        kt = 2 * g + i
                        ins = dve.tensor_scalar(dst[1][:, kt, :], ps[:, i * SEQ:(i + 1) * SEQ], gain(kt), shift(kt), ALU.mult, ALU.add)
                    ins.then_inc(drain("tr", f), 1)
                if shift and g:
                    dve.wait_ge(norm_high_set, 4 * n + g)
                    for i in range(2):
                        hi, lo = (v[:, 2 * g - 2 + i, :] for v in dst)
                        ins = dve.tensor_tensor(r32(lo), lo, r32(hi), ALU.subtract)
                    ins.then_inc(norm_done, 1)
                if not shift:
                    dve.wait_ge(norm_high_set, 4 * n + g + 1)
                    for i in range(2):
                        kt = 2 * g + i
                        hi, lo = (v[:, kt, :] for v in dst)
                        dve.scalar_tensor_tensor(r32(lo), bank("tr", f)[:, i * SEQ:(i + 1) * SEQ], gain(kt), r32(hi), ALU.mult, ALU.subtract)\
                           .then_inc(drain("tr", f) if i else norm_done, 1)

        def norm_pe(pe, key):
            n = norm_n[key]
            for g in range(4):
                f = tr_at[("norm", key)] + g
                ps = claim(pe, "tr", f)
                for i in range(2):
                    for tt in range(TT):
                        if g == 0 and i == 0:
                            pe.wait_ge(norm_xn, 2 * n + tt + 1)
                        kt = 2 * g + i
                        ins = pe.transpose(ps[:, i * SEQ + tt * P:i * SEQ + (tt + 1) * P],
                                           xn[:, tt, kt * P:(kt + 1) * P], ident)
                ins.then_inc(tr_full, 1)

        def norm_wait(pe, key):
            pe.wait_ge(norm_done, 4 * norm_n[key] + 4)
            wait_drained(pe, "tr", tr_at[("norm", key)] + 3)

        def tok_gemm(pe, key, f, kts, blocks, lhsT, ready=None):
            g = chunk_at[key]
            for tts in blocks:
                for k0 in range(0, kts, 4):
                    w = parts(pe, g)
                    kn, width = chunks[g].shape[1], chunks[g].shape[2]
                    if ready:
                        ready(k0 + kn)
                    for n, tt in enumerate(tts):
                        ps = claim(pe, "acc", f + n) if k0 == 0 else bank("acc", f + n)
                        for k in range(kn):
                            ins = mm3(pe, ps[:, 0:width], lhsT(k0 + k, tt), both(w, lambda v: v[:, k, :]),
                                      k0 + k == 0, k0 + k == kts - 1)
                        if k0 + kn == kts:
                            ins.then_inc(acc_full, 1)
                    if k0 + kn < kts:
                        ins.then_inc(chunk_read, 1)
                    g += 1
                f += len(tts)

        def tok_walk(eng, ahead, key, kts, blocks, evacuate=None):
            g = chunk_at[key]
            for b in range(blocks):
                n = -(-kts // 4)
                for i in range(n - 1):
                    ahead(eng, g + i + HIGH)
                if evacuate:
                    evacuate(b)
                ahead(eng, g + n - 1 + HIGH)
                g += n

        def feat_gemm(pe, key, f, n, rhs):
            for i in range(n):
                if i % 2 == 0:
                    w = parts(pe, chunk_at[key] + i // 2)
                ps = claim(pe, "acc", f + i)
                for kt in range(KT):
                    x = rhs(kt)
                    ins = mm3(pe, ps[:, 0:x[0].shape[1]], both(w, lambda v: v[:, kt, (i % 2) * P:(i % 2 + 1) * P]), x,
                              kt == 0, kt == KT - 1)
                ins.then_inc(acc_full, 1)

        att_max, att_comb, att_sunk = sem("att_max"), sem("att_comb"), sem("att_sunk")
        att_units = [0]
        sunk_units = [0]

        class Attention:

            def __init__(self, key, n, q, k, width, v, y, prob, probT, bias=None, sink=None, neg_lam=None, diff=lambda u: False, ada=None):
                self.key, self.n, self.q, self.k, self.width, self.v, self.y = key, n, q, k, width, v, y
                self.prob, self.probT, self.bias, self.sink, self.neg_lam, self.diff = prob, probT, bias, sink, neg_lam, diff
                self.ada = list(ada) if ada is not None else []
                self.sc = [sc_at[key] + u + (u // 2 + 1 if self.ada else 0) for u in range(n)]
                self.base = att_units[0]
                att_units[0] += n
                self.sunk = sunk_units[0]
                if sink:
                    sunk_units[0] += n
                self.neg_max, self.total, self.recip = (stats(2 * n) for _ in range(3))
                self.extra = stats(2 * n) if sink else None
                self.mix = stats(n) if neg_lam is not None else None
                self.tr, self.ada_tr = [], []
                f = tr_at[key]
                for u in range(n + 1):
                    if self.ada and u % 2 == 0 and u >= 2:
                        self.ada_tr.append(f)
                        f += 1
                    if u < n:
                        blocks = (1 if diff(u) else 2) * (width(u) // P)
                        self.tr.append(range(f, f + -(-blocks // 4)))
                        f += -(-blocks // 4)

            def ada_fill(self, i):
                return sc_at[self.key] + 3 * i

            def banks_of(self, u):
                return [acc_at[self.key] + 2 * u + m for m in range(2)]

            def blocks(self, u):
                return [(m, kb) for m in range(1 if self.diff(u) else 2) for kb in range(self.width(u) // P)]

            def scores(self, pe, u):
                for m, f in enumerate(self.banks_of(u)):
                    ps = claim(pe, "acc", f)
                    pe.matmul(ps[:, 0:self.width(u)], self.q(u, m), self.k(u, m), start=True, stop=True).then_inc(acc_full, 1)

            def turn(self, pe, u):
                pe.wait_ge(att_comb, self.base + u + 1)
                b = self.blocks(u)
                for i, f in enumerate(self.tr[u]):
                    ps = claim(pe, "tr", f)
                    for n, (m, kb) in enumerate(b[4 * i:4 * i + 4]):
                        ins = pe.transpose(ps[:, n * P:(n + 1) * P], self.prob[:, u % 2, m, kb * P:(kb + 1) * P], ident)
                    ins.then_inc(tr_full, 1)

            def values(self, pe, u):
                for f in self.tr[u]:
                    wait_drained(pe, "tr", f)
                ps = claim(pe, "sc", self.sc[u])
                b = self.blocks(u)
                for n, (m, kb) in enumerate(b):
                    x = self.v(u, m, kb)
                    e = x.shape[1]
                    ins = pe.matmul(ps[:, m * e:(m + 1) * e], self.probT[:, u % 2, n * P:(n + 1) * P], x,
                                    start=(kb == 0), stop=(kb == self.width(u) // P - 1))
                ins.then_inc(sc_full, 1)

            def tensor(self, pe):
                self.scores(pe, 0)
                for u in range(self.n):
                    if u + 1 < self.n:
                        self.scores(pe, u + 1)
                    if u >= 1:
                        self.values(pe, u - 1)
                    if self.ada and u % 2 == 0:
                        if u:
                            ada_turn(pe, self, u // 2 - 1)
                        ada_pe(pe, self, u // 2)
                    self.turn(pe, u)
                if self.ada:
                    ada_turn(pe, self, len(self.ada) - 1)
                self.values(pe, self.n - 1)

            def maxima(self, dve, u):
                w = self.width(u)
                ps = [filled(dve, "acc", f) for f in self.banks_of(u)]
                if self.bias:
                    for m in range(2):
                        c0, b = self.bias(u, m)
                        ins = dve.tensor_tensor(ps[m][:, c0:w], ps[m][:, c0:w], b, ALU.add)
                    link(dve, ins)
                for m in range(2):
                    ins = dve.tensor_reduce(self.neg_max[:, 2 * u + m:2 * u + m + 1], ps[m][:, 0:w], AX_X, ALU.max, negate=True)
                if self.sink:
                    link(dve, ins)
                    h = self.sink(u)
                    ins = dve.tensor_tensor(self.neg_max[:, 2 * u:2 * u + 2], self.neg_max[:, 2 * u:2 * u + 2],
                                            neg_sink[:, h:h + 2], ALU.min)
                ins.then_inc(att_max, 1)

            def combine(self, dve, u):
                for f in self.banks_of(u):
                    wait_drained(dve, "acc", f)
                total, recip = self.total[:, 2 * u:2 * u + 2], self.recip[:, 2 * u:2 * u + 2]
                if self.sink:
                    dve.wait_ge(att_sunk, 2 * (self.sunk + u) + 2)
                    link(dve, dve.tensor_tensor(total, total, self.extra[:, 2 * u:2 * u + 2], ALU.add))
                ins = dve.reciprocal(recip, total)
                if self.diff(u):
                    link(dve, ins)
                    mix = self.mix[:, u:u + 1]
                    link(dve, dve.scalar_tensor_tensor(mix, total[:, 0:1], recip[:, 1:2], self.neg_lam, ALU.mult, ALU.mult))
                    w = self.width(u)
                    ins = dve.scalar_tensor_tensor(self.prob[:, u % 2, 0, 0:w], self.prob[:, u % 2, 1, 0:w], mix,
                                                   self.prob[:, u % 2, 0, 0:w], ALU.mult, ALU.add)
                ins.then_inc(att_comb, 1)

            def outputs(self, dve, u):
                f = self.sc[u]
                ps = filled(dve, "sc", f)
                if self.diff(u):
                    ins = dve.tensor_scalar(self.y(u), ps[:, 0:P], self.recip[:, 2 * u:2 * u + 1], None, ALU.mult)
                else:
                    ins = dve.tensor_tensor(self.y(u).rearrange("p (m e) -> p m e", m=2),
                                            ps[:, 0:P].rearrange("p (m e) -> p m e", m=2),
                                            self.recip[:, 2 * u:2 * u + 2].unsqueeze(2).broadcast_to([P, 2, HD]), ALU.mult)
                ins.then_inc(drain("sc", f), 1)

            def vector(self, dve, hook=None):
                for u in range(self.n + 2):
                    if u < self.n:
                        self.maxima(dve, u)
                    if 1 <= u <= self.n:
                        self.combine(dve, u - 1)
                    if u >= 2:
                        self.outputs(dve, u - 2)
                    if self.ada and u % 2 == 1 and u >= 3:
                        ada_dve(dve, self, u // 2 - 1)
                    if hook:
                        hook(u)

            def exps(self, act, u):
                w = self.width(u)
                act.wait_ge(att_max, self.base + u + 1)
                if u >= 2:
                    act.wait_ge(tr_full, self.tr[u - 2][-1] + 1)
                for m, f in enumerate(self.banks_of(u)):
                    act.activation(self.prob[:, u % 2, m, 0:w], bank("acc", f)[:, 0:w], ACT.Exp,
                                   bias=self.neg_max[:, 2 * u + m:2 * u + m + 1],
                                   accum_out=self.total[:, 2 * u + m:2 * u + m + 1]).then_inc(drain("acc", f), 1)
                if self.sink:
                    for m in range(2):
                        h = self.sink(u) + m
                        act.activation(self.extra[:, 2 * u + m:2 * u + m + 1], bcast[:, 2 + h:3 + h], ACT.Exp,
                                       bias=self.neg_max[:, 2 * u + m:2 * u + m + 1]).then_inc(att_sunk, 1)

            def keep_turned(self, act, u):
                if u >= 2:
                    act.wait_ge(sc_full, self.sc[u - 2] + 1)
                n = len(self.blocks(u))
                for i, f in enumerate(self.tr[u]):
                    c0, c1 = 512 * i, min(512 * i + 512, P * n)
                    act.activation(self.probT[:, u % 2, c0:c1], filled(act, "tr", f)[:, 0:c1 - c0], ACT.Copy)\
                       .then_inc(drain("tr", f), 1)

            def scalar(self, act, hook=None):
                for u in range(self.n + 1):
                    if u < self.n:
                        self.exps(act, u)
                    if u >= 1:
                        self.keep_turned(act, u - 1)
                    if self.ada and u % 2 == 1:
                        ada_act(act, self, u // 2)
                    if hook:
                        hook(u)

        params_cleared, params_landed, first_landed, keep_landed = (
            sem("params_cleared"), sem("params_landed"), sem("first_landed"), sem("keep_landed"))
        rows_landed, x_landed, t5_stored, t5_landed = sem("rows_landed"), sem("x_landed"), sem("t5_stored"), sem("t5_landed")
        half_set, lam_prod, lam_exp, bcast_row, bcast_set, t5_vec_ready = (
            sem("half_set"), sem("lam_prod"), sem("lam_exp"), sem("bcast_row"), sem("bcast_set"), sem("t5_vec_ready"))
        silu_ready = sem("silu_ready")
        masks_set, sub_gain_set = sem("masks_set"), sem("sub_gain_set")
        sub_gain = stats(DEPTH)
        row_dmas = [0]

        def setup_act_dma(act):
            act.dma_start(keep[:, :], consts[0]).then_inc(keep_landed, 16)
            act.dma_start(mask_rows[:, :], consts[2]).then_inc(keep_landed, 16)
            act.dma_start(lrow[0:1, 0:2 * 4 * HD], I["diff_lambda"].rearrange("(o l) a b -> o (l a b)", o=1)).then_inc(rows_landed, 16)
            act.dma_start(lrow[0:1, 512:520], I["b_sink_2"]).then_inc(rows_landed, 16)
            act.dma_start(relb[0:REL_BUCKETS, :], I["rel_bias"]).then_inc(rows_landed, 16)
            act.dma_start(first[:, :], consts[1]).then_inc(first_landed, 16)
            act.wait_ge(params_cleared, 1)
            for g, group in enumerate(PARAM_GROUPS):
                r = 0
                for name, n in group:
                    src = I[name]
                    letters = "abcd"[:len(src.shape)]
                    flat = src.rearrange(" ".join(letters) + " -> (" + " ".join(letters) + ")") if len(letters) > 1 else src
                    if name in HALF_ROWS:
                        for hd in range(2):
                            act.dma_start(prow[r:r + n, g, hd * HD:(hd + 1) * HD],
                                          flat.rearrange("(n c) -> n c", c=HD)).then_inc(params_landed, 16)
                            row_dmas[0] += 1
                    else:
                        off = (g - 4) * P if name == "conv_w" else 0
                        act.dma_start(prow[r:r + n, g, :], flat.rearrange("(n c) -> n c", c=P)[off:off + n, :])\
                           .then_inc(params_landed, 16)
                        row_dmas[0] += 1
                    r += n

        n_param_dmas = sum(2 if name in HALF_ROWS else 1 for group in PARAM_GROUPS for name, _ in group)

        def setup_pool(pool):
            pool.memset(prow[:, :, :], 0.0).then_inc(params_cleared, 1)
            pool.memset(half[:, :], -0.5).then_inc(half_set, 1)
            pool.wait_ge(half_set, 1)

        def setup_pe(pe):
            pe.wait_ge(keep_landed, 32)
            pe.wait_ge(params_landed, 16 * n_param_dmas)
            for i in range(2):
                f = tr_at["params"] + i
                ps = claim(pe, "tr", f)
                for n, g in enumerate(range(4 * i, min(4 * i + 4, len(PARAM_GROUPS)))):
                    ins = pe.transpose(ps[:, n * P:(n + 1) * P], prow[:, g, :], ident)
                ins.then_inc(tr_full, 1)

        def setup_bias_pe(pe):
            pe.wait_ge(bcast_row, 2)
            f = acc_at["bcast"]
            pe.matmul(claim(pe, "acc", f)[:, 0:10], ones[0:1, :], lprod[0:1, 0:10], start=True, stop=True).then_inc(acc_full, 1)
            pe.wait_ge(rows_landed, 48)
            pe.wait_ge(first_landed, 16)
            f = acc_at["t5"]
            pe.matmul(claim(pe, "acc", f)[0:N_BIAS, 0:384], relb[0:REL_BUCKETS, :], first_const("bucket_hot")[0:REL_BUCKETS, :],
                      start=True, stop=True).then_inc(acc_full, 1)
            pe.wait_ge(t5_landed, 16)
            for i in range(N_BIAS // 2):
                ps = claim(pe, "acc", f + 1 + i)
                pe.matmul(ps[:, :], first_const("flip"), hankel[:, 2 * i:2 * i + 2, :], start=True, stop=True).then_inc(acc_full, 1)

        def setup_dve(dve):
            dve.wait_ge(keep_landed, 32)
            dve.tensor_copy(masks[:, :], mask_rows[:, :]).then_inc(masks_set, 1)
            for i in range(2):
                f = tr_at["params"] + i
                ps = filled(dve, "tr", f)
                n = min(4, len(PARAM_GROUPS) - 4 * i)
                dve.tensor_copy(pcol[:, 4 * i:4 * i + n, :], ps[:, 0:n * P].rearrange("p (a b) -> p a b", a=n)).then_inc(drain("tr", f), 1)

        def setup_bias_dve(dve):
            dve.wait_ge(rows_landed, 48)
            lam = lrow[0:1, 0:512].rearrange("p (a two c) -> p a two c", a=4, two=2)
            prods = lprod[0:1, 0:256].rearrange("p (a c) -> p a c", a=4)
            link(dve, dve.tensor_tensor(prods, lam[:, :, 0, :], lam[:, :, 1, :], ALU.mult))
            dve.tensor_reduce(lsum[0:1, 0:4], prods, AX_X, ALU.add).then_inc(lam_prod, 1)
            dve.wait_ge(lam_exp, 1)
            for l in range(DEPTH):
                link(dve, dve.tensor_tensor(lprod[0:1, l:l + 1], lsum[0:1, 2 * l + 5:2 * l + 6], lsum[0:1, 2 * l + 4:2 * l + 5], ALU.subtract))
                link(dve, dve.tensor_scalar(lprod[0:1, l:l + 1], lprod[0:1, l:l + 1], -LAMBDA_INIT[l], None, ALU.add))
            dve.tensor_copy(lprod[0:1, 2:10], lrow[0:1, 512:520]).then_inc(bcast_row, 2)
            for l in range(DEPTH):
                ins = dve.tensor_scalar(sub_gain[:, l:l + 1], col("diff_subln_g", l), 1.0 - LAMBDA_INIT[l], None, ALU.mult)
            ins.then_inc(sub_gain_set, 1)
            ps = filled(dve, "acc", acc_at["bcast"])
            dve.tensor_copy(bcast[:, :], ps[:, 0:10]).then_inc(bcast_set, 1)
            dve.wait_ge(bcast_set, 1)
            dve.tensor_scalar(neg_sink[:, :], bcast[:, 2:10], -1.0, None, ALU.mult).then_inc(drain("acc", acc_at["bcast"]), 1)
            f = acc_at["t5"]
            dve.tensor_copy(t5_vec[0:N_BIAS, :], filled(dve, "acc", f)[0:N_BIAS, 0:384]).then_inc(drain("acc", f), 1)
            for i in range(N_BIAS // 2):
                ps = filled(dve, "acc", f + 1 + i)
                dve.tensor_tensor(t5_bias[:, 2 * i:2 * i + 2, :], ps[:, :].rearrange("p (a b) -> p a b", a=2),
                                  first_const("causal").unsqueeze(1).broadcast_to([P, 2, SEQ]), ALU.add)\
                   .then_inc(drain("acc", f + 1 + i), 1)

        def setup_bias_act(act):
            act.wait_ge(lam_prod, 1)
            act.activation(lsum[0:1, 4:8], lsum[0:1, 0:4], ACT.Exp).then_inc(lam_exp, 1)
            act.activation(silu_c[:, :, 0], col("c_2", 0, KT), ACT.Silu)
            act.activation(silu_c[:, :, 1], col("c_ctx_2", 0, KT), ACT.Silu).then_inc(silu_ready, 1)
            wait_drained(act, "acc", acc_at["t5"])
            act.dma_start(t5_scratch, t5_vec[0:N_BIAS, :]).then_inc(t5_stored, 16)
            act.wait_ge(t5_stored, 16)
            act.dma_start(hankel[:, :, :], bass.AP(tensor=t5_scratch.tensor, offset=0, ap=[[1, P], [384, N_BIAS], [1, SEQ]]))\
               .then_inc(t5_landed, 16)

        mod_ready = sem("mod_ready")

        def ada_pe(pe, att, i):
            b = att.ada[i]
            if b == 0:
                pe.wait_ge(silu_ready, 1)
            ps = claim(pe, "sc", att.ada_fill(i))
            for n in range(2):
                g = ada_chunk[b] + n
                wait_landed(pe, g)
                w = shaped(raw_slot(g), g)
                for k in range(4):
                    ins = pe.matmul(ps[0:2, :], silu_c[:, 4 * n + k, :], w[:, k, :], start=(n + k == 0), stop=(4 * n + k == KT - 1))
                ins.then_inc(sc_full if n else chunk_read, 1)

        def ada_act(act, att, i):
            f = att.ada_fill(i)
            ps = filled(act, "sc", f)
            act.activation(mod_row[0:2, :], ps[0:2, :], ACT.Copy).then_inc(drain("sc", f), 1)

        def ada_turn(pe, att, i):
            wait_drained(pe, "sc", att.ada_fill(i))
            ps = claim(pe, "tr", att.ada_tr[i])
            for n in range(4):
                ins = pe.transpose(ps[:, 2 * n:2 * n + 2], mod_row[0:2, n * P:(n + 1) * P], ident[0:2, 0:2])
            ins.then_inc(tr_full, 1)

        def ada_dve(dve, att, i):
            l, c = att.ada[i] // N_ADA, att.ada[i] % N_ADA
            ps = filled(dve, "tr", att.ada_tr[i])
            dve.tensor_tensor(mod[:, l, 4 * c:4 * c + 4, :], ps[:, 0:8].rearrange("p (a b) -> p a b", a=4),
                              col("b_ada_2", 6 * KT * l + 4 * c, 4).unsqueeze(2).broadcast_to([P, 4, 2]), ALU.add)\
               .then_inc(drain("tr", att.ada_tr[i]), 1)

        def ada_gains(dve, att, l):
            wait_drained(dve, "tr", att.ada_tr[att.ada.index(N_ADA * (l + 1) - 1)])
            for w, (pre, post) in enumerate([("g_pre_mix_2", "g_post_mix_2"), ("g_pre_ff_2", "g_post_ff_2")]):
                scale, gate = mod[:, l, (3 * w + 1) * KT:(3 * w + 2) * KT, :], mod[:, l, (3 * w + 2) * KT:(3 * w + 3) * KT, :]
                dve.scalar_tensor_tensor(mod_gain[:, l, w], scale, 1.0, col(pre, KT * l, KT).unsqueeze(2).broadcast_to([P, KT, 2]),
                                         ALU.add, ALU.mult)
                dve.tensor_tensor(mod_gate[:, l, w], gate, col(post, KT * l, KT).unsqueeze(2).broadcast_to([P, KT, 2]),
                                  ALU.mult).then_inc(mod_ready, 1)

        QK = {0: 0, 1: 1, 3: 2, 4: 3}
        PREV = {1: 0, 2: 1, 4: 3, 5: 4}
        qk_squared, qk_mean, qk_rstd = sem("qk_squared"), sem("qk_mean"), sem("qk_rstd")
        qk_ss = qk_ms = qk_rs = stats(8 * 8)

        def qkv_pe(pe, l):
            norm_wait(pe, ("attn", l))
            g = chunk_at[("qkv", l)]
            for cb in range(6):
                f = acc_at[("qkv", l)] + 2 * cb
                for k0 in (0, 4):
                    w = parts(pe, g)
                    g += 1
                    for tt in range(TT):
                        ps = claim(pe, "acc", f + tt) if k0 == 0 else bank("acc", f + tt)
                        for k in range(4):
                            x = both(hT, lambda v: v[:, k0 + k, tt * P:(tt + 1) * P])
                            ins = mm3(pe, ps[:, :], x, both(w, lambda v: v[:, k, :]), k0 + k == 0, k0 + k == KT - 1)
                        if k0:
                            ins.then_inc(acc_full, 1)
                    if k0 == 0:
                        ins.then_inc(chunk_read, 1)
                if cb in PREV:
                    for tt in range(TT):
                        u = 2 * QK[PREV[cb]] + tt
                        wait_drained(pe, "acc", acc_at[("qkv", l)] + 2 * PREV[cb] + tt)
                        t = tr_at[("qkv", l)] + u
                        ps = claim(pe, "tr", t)
                        for j in range(4):
                            ins = pe.transpose(ps[:, j * P:(j + 1) * P], qn[:, tt, j * P:(j + 1) * P], ident)
                        ins.then_inc(tr_full, 1)

        def qk_turned(eng, l, u):
            t = tr_at[("qkv", l)] + u
            ps = filled(eng, "tr", t)
            return t, ps[:, :].rearrange("p (a b) -> p a b", a=4), qkT[:, u // 2, :, (u % 2) * P:(u % 2 + 1) * P]

        def qkv_act(act, l):
            g = chunk_at[("qkv", l)]
            for cb in range(6):
                ahead_act(act, g + 2 * cb + HIGH)
                for tt in range(TT):
                    f = acc_at[("qkv", l)] + 2 * cb + tt
                    ps = filled(act, "acc", f)
                    if cb not in QK:
                        act.activation(vv[:, cb // 3, tt, :], ps[:, :], ACT.Copy).then_inc(drain("acc", f), 1)
                        continue
                    u = 8 * l + 2 * QK[cb] + tt
                    if u >= 2:
                        act.wait_ge(qk_mean, u - 1)
                    act.activation(sq[:, tt, :], ps[:, :], ACT.Square).then_inc(qk_squared, 1)
                ahead_act(act, g + 2 * cb + 1 + HIGH)
                if cb in PREV and QK[PREV[cb]] % 2 == 1:
                    for tt in range(TT):
                        t, ps, dst = qk_turned(act, l, 2 * QK[PREV[cb]] + tt)
                        act.activation(dst, ps, ACT.Identity, scale=col("qk_norm_g", 4 * l + QK[PREV[cb]])).then_inc(drain("tr", t), 1)

        def qkv_pool(pool, l):
            for u in range(8 * l, 8 * l + 8):
                c = 8 * (u % 8)
                pool.wait_ge(qk_mean, u + 1)
                pool.tensor_tensor(qk_rs[:, c:c + 8], qk_ms[:, c:c + 8], half[:, 0:8], ALU.pow).then_inc(qk_rstd, 1)

        def qkv_dve(dve, l):
            g = chunk_at[("qkv", l)]
            for cb in range(6):
                ahead_dve(dve, g + 2 * cb + HIGH)
                if cb in QK:
                    for tt in range(TT):
                        u = 2 * QK[cb] + tt
                        c = 8 * u
                        dve.wait_ge(qk_squared, 8 * l + u + 1)
                        link(dve, dve.tensor_reduce(qk_ss[:, c:c + 8], sq[:, tt, :].rearrange("p (h e) -> p h e", e=HD), AX_X, ALU.add))
                        dve.tensor_scalar(qk_ms[:, c:c + 8], qk_ss[:, c:c + 8], 1.0 / HD, EPS, ALU.mult, ALU.add).then_inc(qk_mean, 1)
                    for tt in range(TT):
                        u = 2 * QK[cb] + tt
                        c = 8 * u
                        f = acc_at[("qkv", l)] + 2 * cb + tt
                        dve.wait_ge(qk_rstd, 8 * l + u + 1)
                        if u >= 2:
                            dve.wait_ge(tr_full, tr_at[("qkv", l)] + u - 1)
                        dve.tensor_tensor(qn[:, tt, :].rearrange("p (h e) -> p h e", e=HD),
                                          bank("acc", f)[:, :].rearrange("p (h e) -> p h e", e=HD),
                                          qk_rs[:, c:c + 8].unsqueeze(2).broadcast_to([P, 8, HD]), ALU.mult).then_inc(drain("acc", f), 1)
                if cb in PREV and QK[PREV[cb]] % 2 == 0:
                    for tt in range(TT):
                        t, ps, dst = qk_turned(dve, l, 2 * QK[PREV[cb]] + tt)
                        dve.tensor_scalar(dst, ps, col("qk_norm_g", 4 * l + QK[PREV[cb]]), SCALE, ALU.mult, ALU.mult).then_inc(drain("tr", t), 1)
                ahead_dve(dve, g + 2 * cb + 1 + HIGH)

        def att1(l):
            def qk(i, u):
                p = u // 2
                return qkT[:, (2 * (p // 4)) + i, p % 4, :]

            def bias(u, m):
                p, qt = u // 2, u % 2
                h = p if p < 4 else 4 + 2 * (p - 4) + m
                return 0, t5_bias[:, h, (1 - qt) * P:SEQ]

            def v(u, m, kb):
                p = u // 2
                return vv[:, 0, kb, p * P:(p + 1) * P] if p < 4 else vv[:, 1, kb, (2 * (p - 4) + m) * HD:(2 * (p - 4) + m + 1) * HD]

            return Attention(("att1", l), 16,
                             lambda u, m: qk(0, u)[m * HD:(m + 1) * HD, (u % 2) * P:(u % 2 + 1) * P],
                             lambda u, m: qk(1, u)[m * HD:(m + 1) * HD, 0:(u % 2 + 1) * P],
                             lambda u: (u % 2 + 1) * P, v, lambda u: y1[:, u % 2, (u // 2) * P:(u // 2 + 1) * P],
                             prob, probT, bias=bias, neg_lam=bcast[:, l:l + 1], diff=lambda u: u < 8,
                             ada=range(8 * l, 8 * l + 8))

        yT1_high = sem("yT1_high")
        sub_ss, sub_ms, sub_rs = stats(8), stats(8), stats(8)
        sub_summed, sub_mean, sub_rstd, sub_scaled = sem("sub_summed"), sem("sub_mean"), sem("sub_rstd"), sem("sub_scaled")

        def subnorm_act(act, l, att):
            def hook(u):
                if u == 11:
                    for n in range(8):
                        wait_drained(act, "sc", att.sc[n])
                        act.activation(sq[:, n % 2, 0:P], y1[:, n % 2, (n // 2) * P:(n // 2 + 1) * P], ACT.Square,
                                       accum_out=sub_ss[:, n:n + 1]).then_inc(sub_summed, 1)
                        act.wait_ge(sub_summed, 8 * l + n + 1)
            return hook

        def subnorm_dve(dve, l, att):
            def hook(u):
                if u == 13:
                    dve.wait_ge(sub_summed, 8 * l + 8)
                    dve.tensor_scalar(sub_ms[:, :], sub_ss[:, :], 1.0 / P, EPS, ALU.mult, ALU.add).then_inc(sub_mean, 1)
                if u == 15:
                    dve.wait_ge(sub_rstd, l + 1)
                    for n in (6, 7):
                        wait_drained(dve, "sc", att.sc[n])
                    rs = sub_rs[:, :].rearrange("p (h t) -> p t h", t=TT)
                    for qt in range(TT):
                        y = y1[:, qt, 0:512].rearrange("p (h e) -> p h e", e=P)
                        dve.tensor_tensor(y, y, rs[:, qt, :].unsqueeze(2).broadcast_to([P, 4, P]), ALU.mult).then_inc(sub_scaled, 1)
            return hook

        def subnorm_pool(pool, l):
            pool.wait_ge(sub_mean, l + 1)
            pool.tensor_tensor(sub_rs[:, :], sub_ms[:, :], half[:, 0:8], ALU.pow).then_inc(sub_rstd, 1)

        def yT1_pe(pe, l, att):
            pe.wait_ge(sub_scaled, TT * (l + 1))
            for f in (att.n - 2, att.n - 1):
                wait_drained(pe, "sc", att.sc[f])
            for g in range(4):
                f = tr_at[("yT1", l)] + g
                ps = claim(pe, "tr", f)
                for i in range(2):
                    for tt in range(TT):
                        kt = 2 * g + i
                        ins = pe.transpose(ps[:, i * SEQ + tt * P:i * SEQ + (tt + 1) * P], y1[:, tt, kt * P:(kt + 1) * P], ident)
                ins.then_inc(tr_full, 1)

        def yT1_gain(l, g):
            return (sub_gain[:, l:l + 1] if g < 2 else 1.0)

        def yT1_act(act, l):
            act.wait_ge(sub_gain_set, 1)
            for g in range(4):
                ps = filled(act, "tr", tr_at[("yT1", l)] + g)
                dst = yT1[0][:, 2 * g:2 * g + 2, :].rearrange("p a b -> p (a b)")
                act.activation(r32(dst), ps[:, :], ACT.Identity, scale=yT1_gain(l, g)).then_inc(yT1_high, 1)

        def yT1_dve(dve, l):
            dve.wait_ge(sub_gain_set, 1)
            for g in range(4):
                f = tr_at[("yT1", l)] + g
                ps = filled(dve, "tr", f)
                hi, lo = (v[:, 2 * g:2 * g + 2, :].rearrange("p a b -> p (a b)") for v in yT1)
                dve.wait_ge(yT1_high, 4 * l + g + 1)
                dve.scalar_tensor_tensor(r32(lo), ps[:, :], yT1_gain(l, g), r32(hi), ALU.mult, ALU.subtract).then_inc(drain("tr", f), 1)

        def out1_pe(pe, l):
            for g in (2, 3):
                wait_drained(pe, "tr", tr_at[("yT1", l)] + g)
            tok_gemm(pe, ("out1", l), acc_at[("out1", l)], KT, [LAT] * 2,
                     lambda kt, tt: both(yT1, lambda v: v[:, kt, tt * P:(tt + 1) * P]))

        def add_dve(dve, key, kts):
            def add(hf):
                for tt in range(TT):
                    f = acc_at[key] + 2 * hf + tt
                    ps = filled(dve, "acc", f)
                    x = h_lat[:, tt, hf * 512:(hf + 1) * 512]
                    dve.tensor_tensor(x, x, ps[:, :], ALU.add).then_inc(drain("acc", f), 1)

            tok_walk(dve, ahead_dve, key, kts, 2, add)

        conv_scaled, act_done, g_full, g_high, g_done = (
            sem("conv_scaled"), sem("act_done"), sem("g_full"), sem("g_high"), sem("g_done"))

        def up1_pe(pe, l):
            norm_wait(pe, ("ffn", l))
            for i in range(FT):
                w = parts(pe, chunk_at[("up1", l)] + i)
                f = acc_at[("up1", l)] + i
                ps = claim(pe, "acc", f)
                for s in range(2):
                    for kt in range(KT):
                        ins = mm3(pe, ps[:, s * SEQ:(s + 1) * SEQ], both(w, lambda v: v[:, kt, s, :]), both(hT, lambda v: v[:, kt, :]),
                                  kt == 0, kt == KT - 1)
                ins.then_inc(acc_full, 1)

        def conv_col(l, j, i, s):
            return col("conv_w", (l * CONV + j) * 2 * FT + s * FT + i)

        def up1_act(act, l):
            for i in range(FT + 2):
                n = FT * l + i
                if i < FT:
                    ps = filled(act, "acc", acc_at[("up1", l)] + i)
                    if n >= 2:
                        act.wait_ge(g_full, n - 1)
                    for s in range(2):
                        act.activation(conv[:, i % 2, s, :], ps[:, s * SEQ:(s + 1) * SEQ], ACT.Identity,
                                       bias=col("conv_b", l * 2 * FT + s * FT + i), scale=conv_col(l, 2, i, s)).then_inc(conv_scaled, 1)
                if 1 <= i <= FT:
                    wait_drained(act, "acc", acc_at[("up1", l)] + i - 1)
                    act.activation(act_g[:, (i - 1) % 2, :], conv[:, (i - 1) % 2, 0, :], ACT.Silu).then_inc(act_done, 1)
                if i >= 2:
                    act.wait_ge(g_full, n - 1)
                    act.activation(r32(gT[0][:, i - 2, :]), gT[1][:, i - 2, :], ACT.Copy).then_inc(g_high, 1)
                if i < FT:
                    ahead_act(act, chunk_at[("up1", l)] + i + HIGH)

        def up1_dve(dve, l):
            for i in range(FT):
                f = acc_at[("up1", l)] + i
                dve.wait_ge(conv_scaled, 2 * (FT * l + i) + 2)
                ps = bank("acc", f)
                for j, back in ((1, 1), (0, 2)):
                    for s in range(2):
                        c = conv[:, i % 2, s, back:SEQ]
                        ins = dve.scalar_tensor_tensor(c, ps[:, s * SEQ:(s + 1) * SEQ - back], conv_col(l, j, i, s), c, ALU.mult, ALU.add)
                    if j:
                        link(dve, ins)
                ins.then_inc(drain("acc", f), 1)
                ahead_dve(dve, chunk_at[("up1", l)] + i + HIGH)

        def up1_pool(pool, l):
            for i in range(FT + 2):
                n = FT * l + i
                if i < FT:
                    pool.wait_ge(act_done, n + 1)
                    pool.tensor_tensor(gT[1][:, i, :], act_g[:, i % 2, :], conv[:, i % 2, 1, :], ALU.mult).then_inc(g_full, 1)
                if i >= 2:
                    pool.wait_ge(g_high, n - 1)
                    lo = gT[1][:, i - 2, :]
                    pool.tensor_tensor(r32(lo), lo, r32(gT[0][:, i - 2, :]), ALU.subtract).then_inc(g_done, 1)

        def down1_pe(pe, l):
            tok_gemm(pe, ("down1", l), acc_at[("down1", l)], FT, [LAT] * 2,
                     lambda kt, tt: both(gT, lambda v: v[:, kt, tt * P:(tt + 1) * P]), lambda n: pe.wait_ge(g_done, FT * l + n))

        S2 = 2 * SEQ
        r2 = Region(at1)
        uT = r2.take(KT, S2), r2.take(KT, S2)
        yT = uT
        at2 = r2.at
        pA = r2.take(AT, S2)
        at_rwkv = r2.at
        q_tok = r2.take(4, 512)
        yB = q_tok
        k_tok = r2.take(4, 256)
        v_tok = r2.take(4, P)
        probBT = r2.take(2, 1024)
        rope_t = r2.take(2, 512)
        mod_row2 = r2.take(512)
        r0 = Region(0)
        qT = r0.take(4, S2)
        kT = r0.take(2, S2)
        probB = r0.take(2, 2, 512)
        assert r0.at <= at1
        rr, kf, vf = pA[:, 0:4, :], pA[:, 4:8, :], pA[:, 8:12, :]
        r3 = Region(0)
        kk = r3.take(4, S2)
        kd_sum = r3.take(4, S2)
        l_pe = r3.take(4, CH + 1)
        l_pi = r3.take(4, CH)
        vst = r3.take(4, CH)
        assert r3.at <= at1
        r3 = Region(at_rwkv, slots=HIGH + RAW - 1)
        lc = r3.take(4, S2)
        kka = r3.take(4, S2)
        kd = r3.take(4, S2)
        lora = r3.take(2, 512)
        ar = r3.take(4, 2, CH)
        ar_bd = r3.take(4, 2, P)
        bh_bd = r3.take(4, P)
        kh_bd = r3.take(4, P)
        b_tok = r3.take(4, P)
        k_tk = r3.take(4, P)
        nq = r3.take(4, 4, P)
        xi = r3.take(4, P)
        xiT = r3.take(4, P)
        yi = r3.take(4, P)
        g_sb = r3.take(4, CH)
        u_sb = r3.take(4, CH)
        state = r3.take(2, 4, CH)
        s_tmp = g_sb
        sig = nq[:, 0:2, :, :].rearrange("p a b c -> p a (b c)")
        iclr = nq[:, 2:4, :, :].rearrange("p a b c -> p a (b c)")
        g2 = pA[:, 12, :]
        y_full = yT[1]
        y_st = y_full[:, 0:4, :].rearrange("p j (c v) -> p j c v", c=NCH)
        def tail(at):
            r = Region(at)
            return r.take(4, D), r.take(2, D), r.take(2, KT, P), r.at

        o_mix0, gate_mix0, diag_mix0, _ = tail(at2)
        r4 = Region(0)
        gate_ff = r4.take(2, D)
        diag_ff = xn.rearrange("p t (k c) -> p t k c", c=P)
        r4 = Region(at2)
        hid = r4.take(2, ET, S2), r4.take(2, ET, S2)
        o_ff0 = r4.take(4, D)
        r4 = Region(at1)
        uT1 = r4.take(KT, SEQ), r4.take(KT, SEQ)
        hid1 = r4.take(FT2, SEQ), r4.take(FT2, SEQ)
        o_ff1 = r4.take(TT, D)

        ctx_landed, lora_landed, g2_landed = sem("ctx_landed"), sem("lora_landed"), sem("g2_landed")
        near_landed = sem("near_landed")

        def mod_shift(l, w, s):
            return lambda kt: mod[:, l, 3 * w * KT + kt, s:s + 1]

        def mod_mul(l, w, s):
            return lambda kt: mod_gain[:, l, w, kt, s:s + 1]

        shift_mid = stats(AT)
        shift_mid_set, shift_scaled, lora_in = sem("shift_mid_set"), sem("shift_scaled"), sem("lora_in")

        def projA_pe(pe):
            for s in (1, 0):
                norm_wait(pe, ("mix", 0, s))
            feat_gemm(pe, "projA", acc_at["projA"], AT, lambda kt: both(uT, lambda v: v[:, kt, :]))

        def projA_act(act):
            act.wait_ge(shift_mid_set, 1)
            for i in range(AT):
                f = acc_at["projA"] + i
                act.activation(pA[:, i, :], filled(act, "acc", f)[:, :], ACT.Identity,
                               scale=shift_mid[:, i:i + 1]).then_inc(shift_scaled, 1)
                if i % 2 == 1 or i == AT - 1:
                    ahead_act(act, chunk_at["projA"] + i // 2 + HIGH)
            for i, func in ((12, ACT.Tanh), (14, ACT.Sigmoid)):
                wait_drained(act, "acc", acc_at["projA"] + i)
                act.activation(pA[:, i, :], pA[:, i, :], func).then_inc(lora_in, 1)

        def projA_dve(dve):
            prev, nxt = col("a_mu_prev_2", 0, AT), col("a_mu_next_2", 0, AT)
            link(dve, dve.tensor_tensor(shift_mid[:, :], prev, nxt, ALU.add))
            dve.tensor_scalar(shift_mid[:, :], shift_mid[:, :], -1.0, 1.0, ALU.mult, ALU.add).then_inc(shift_mid_set, 1)
            for i in range(AT):
                f = acc_at["projA"] + i
                dve.wait_ge(shift_scaled, i + 1)
                ps = bank("acc", f)[:, :].rearrange("p (s t) -> p s t", s=2)
                p = pA[:, i, :].rearrange("p (s t) -> p s t", s=2)
                link(dve, dve.scalar_tensor_tensor(p[:, :, 1:], ps[:, :, 0:SEQ - 1], col("a_mu_prev_2", i), p[:, :, 1:], ALU.mult, ALU.add))
                dve.scalar_tensor_tensor(p[:, :, 0:SEQ - 1], ps[:, :, 1:], col("a_mu_next_2", i), p[:, :, 0:SEQ - 1],
                                         ALU.mult, ALU.add).then_inc(drain("acc", f), 1)
                if i % 2 == 1 or i == AT - 1:
                    ahead_dve(dve, chunk_at["projA"] + i // 2 + HIGH)

        def projA_wait(eng):
            for i in range(AT - 4, AT):
                wait_drained(eng, "acc", acc_at["projA"] + i)

        roped = sem("roped")

        def rope(dve, x, heads, tt, tmp, done, count):
            cos, sin = const("cos")[:, tt * HD:(tt + 1) * HD], const("sin")[:, tt * HD:(tt + 1) * HD]
            t0, t1 = tmp[:, 0, 0:heads * HD], tmp[:, 1, 0:heads * HD]
            cut = lambda v: v.rearrange("p (h a b f) -> p h a b f", h=heads, a=2, b=2)
            xs, ts, ss = cut(x), cut(t1), sin.rearrange("p (a b f) -> p a b f", a=2, b=2)
            dve.tensor_tensor(t0.rearrange("p (h e) -> p h e", h=heads), x.rearrange("p (h e) -> p h e", h=heads),
                              cos.unsqueeze(1).broadcast_to([P, heads, HD]), ALU.mult)
            for b in range(2):
                ins = dve.tensor_tensor(ts[:, :, :, b, :], xs[:, :, :, 1 - b, :],
                                        ss[:, :, b, :].unsqueeze(1).broadcast_to([P, heads, 2, 16]), ALU.mult)
            link(dve, ins)
            dve.tensor_tensor(x, t0, t1, ALU.add).then_inc(done, 1)
            dve.wait_ge(done, count)

        def projB_pe(pe):
            tok_gemm(pe, "projB", acc_at["projB"], KT, [ALL] * 2, lambda kt, tt: both(uT, lambda v: v[:, kt, tt * P:(tt + 1) * P]))
            for tt in ALL:
                wait_drained(pe, "acc", acc_at["projB"] + tt)
                wait_drained(pe, "acc", acc_at["projB"] + 4 + tt)
                if tt >= 2:
                    pe.wait_ge(roped, 2 * (tt - 1))
                for x, n, f in ((q_tok, 4, 2 * tt), (k_tok, 2, 2 * tt + 1)):
                    ps = claim(pe, "tr", tr_at["projB"] + f)
                    for j in range(n):
                        ins = pe.transpose(ps[:, j * P:(j + 1) * P], x[:, tt, j * P:(j + 1) * P], ident)
                    ins.then_inc(tr_full, 1)

        def dup_heads(ps, n=2):
            return ps.rearrange("p (k e) -> p k e", k=2).unsqueeze(2).broadcast_to([P, 2, n, HD])

        def projB_act(act):
            def qkv(block):
                for tt in ALL:
                    f = acc_at["projB"] + 4 * block + tt
                    ps = filled(act, "acc", f)
                    if block == 0:
                        act.activation(q_tok[:, tt, :], ps[:, :], ACT.Copy).then_inc(drain("acc", f), 1)
                    else:
                        act.activation(k_tok[:, tt, :].rearrange("p (k n e) -> p k n e", k=2, n=2), dup_heads(ps[:, 0:P]), ACT.Copy)
                        act.activation(v_tok[:, tt, :], ps[:, P:2 * P], ACT.Copy).then_inc(drain("acc", f), 1)

            tok_walk(act, ahead_act, "projB", KT, 2, qkv)
            for tt in ALL:
                f = tr_at["projB"] + 2 * tt
                act.activation(qT[:, :, tt * P:(tt + 1) * P], filled(act, "tr", f)[:, :].rearrange("p (a b) -> p a b", a=4),
                               ACT.Copy, scale=SCALE).then_inc(drain("tr", f), 1)
                f += 1
                act.activation(kT[:, :, tt * P:(tt + 1) * P], filled(act, "tr", f)[:, 0:2 * P].rearrange("p (a b) -> p a b", a=2),
                               ACT.Copy).then_inc(drain("tr", f), 1)

        def projB_dve(dve):
            tok_walk(dve, ahead_dve, "projB", KT, 2)
            for tt in (0, 1):
                wait_drained(dve, "acc", acc_at["projB"] + 2 + tt)
                wait_drained(dve, "acc", acc_at["projB"] + 6 + tt)
                rope(dve, q_tok[:, 2 + tt, :], 8, tt, rope_t, roped, 2 * tt + 1)
                rope(dve, k_tok[:, 2 + tt, :], 4, tt, rope_t, roped, 2 * tt + 2)

        def projB_wait(pe):
            for f in (6, 7):
                wait_drained(pe, "tr", tr_at["projB"] + f)

        def heads(x, u, m, cols):
            return x[m * HD:(m + 1) * HD, u // 2, cols]

        def kv_of(u):
            return u // 4

        def attBl():
            return Attention("attBl", 8, lambda u, m: heads(qT, u, m, slice(SEQ + (u % 2) * P, SEQ + (u % 2 + 1) * P)),
                             lambda u, m: kT[m * HD:(m + 1) * HD, kv_of(u), :], lambda u: S2,
                             lambda u, m, kb: v_tok[:, kb, kv_of(u) * HD:(kv_of(u) + 1) * HD],
                             lambda u: yB[:, 2 + u % 2, (u // 2) * P:(u // 2 + 1) * P], probB, probBT,
                             bias=lambda u, m: (SEQ, const("band")[:, (u % 2) * SEQ:(u % 2 + 1) * SEQ]), sink=lambda u: 2 * (u // 2), ada=range(16, 20))

        def attBc():
            return Attention("attBc", 8, lambda u, m: heads(qT, u, m, slice((u % 2) * P, (u % 2 + 1) * P)),
                             lambda u, m: kT[m * HD:(m + 1) * HD, kv_of(u), 0:SEQ], lambda u: SEQ,
                             lambda u, m, kb: v_tok[:, kb, kv_of(u) * HD:(kv_of(u) + 1) * HD],
                             lambda u: yB[:, u % 2, (u // 2) * P:(u // 2 + 1) * P], probB, probBT, sink=lambda u: 2 * (u // 2), ada=range(20, 24))

        yTB_high = sem("yTB_high")

        def yTB_pe(pe, atts):
            for att in atts:
                for u in (6, 7):
                    wait_drained(pe, "sc", att.sc[u])
            for tt in ALL:
                f = tr_at["yTB"] + tt
                ps = claim(pe, "tr", f)
                for j in range(4):
                    ins = pe.transpose(ps[:, j * P:(j + 1) * P], yB[:, tt, j * P:(j + 1) * P], ident)
                ins.then_inc(tr_full, 1)

        def yTB_act(act):
            for tt in ALL:
                ps = filled(act, "tr", tr_at["yTB"] + tt)
                act.activation(r32(yT[0][:, 4:8, tt * P:(tt + 1) * P]), ps[:, :].rearrange("p (a b) -> p a b", a=4),
                               ACT.Copy).then_inc(yTB_high, 1)

        def yTB_dve(dve):
            for tt in ALL:
                f = tr_at["yTB"] + tt
                ps = filled(dve, "tr", f)
                dve.wait_ge(yTB_high, tt + 1)
                hi, lo = (v[:, 4:8, tt * P:(tt + 1) * P] for v in yT)
                dve.tensor_tensor(r32(lo), ps[:, :].rearrange("p (a b) -> p a b", a=4), r32(hi), ALU.subtract).then_inc(drain("tr", f), 1)

        kk_squared, kk_rn, kk_wide, kk_done = sem("kk_squared"), sem("kk_rn"), sem("kk_wide"), sem("kk_done")
        bd_cleared = sem("bd_cleared")
        cum_done, decay_ready, prep_done = sem("cum_done"), sem("decay_ready"), sem("prep_done")
        l_mid, l_end, l_step, f_step = stats(4 * NCH), stats(4 * NCH), stats(4 * NCH), stats(4 * NCH)
        kk_ss, kk_rs = stats(4 * 8), stats(4 * 8)
        by_chunk = lambda v: v.rearrange("p (j c) -> p j c", j=4)
        ORDER = [list(range(NCH)), [3, 2, 1, 0, 7, 6, 5, 4]]

        def kk_dve(dve):
            projA_wait(dve)
            for j in range(4):
                dve.tensor_scalar(kk[:, j, :], kf[:, j, :], col("a_k_k_2", j), None, ALU.mult).then_inc(kk_done, 1)
            f = acc_at["kk"]
            dve.tensor_scalar(kk_ss[:, :], filled(dve, "acc", f)[:, 0:32], 1e-24, None, ALU.max).then_inc(drain("acc", f), 1)
            dve.wait_ge(kk_rn, 1)
            dve.tensor_copy(lc[:, :, :].rearrange("p a (b e) -> p (a b) e", e=HD), kk_rs[:, :].unsqueeze(2).broadcast_to([P, 32, HD]))\
               .then_inc(kk_wide, 1)
            for j in range(4):
                f = tr_at["kk"] + j
                ps = filled(dve, "tr", f)
                if j == 0:
                    dve.wait_ge(kk_done, 4)
                dve.tensor_tensor(kk[:, j, :], kk[:, j, :], ps[:, :], ALU.mult).then_inc(drain("tr", f), 1)

        def kk_act(act):
            for j in range(4):
                act.wait_ge(kk_done, j + 1)
                act.activation(lc[:, j, :], kk[:, j, :], ACT.Square).then_inc(kk_squared, 1)

        def kk_pe(pe):
            f = acc_at["kk"]
            ps = claim(pe, "acc", f)
            for j in range(4):
                pe.wait_ge(kk_squared, j + 1)
                for tt in ALL:
                    c = 8 * tt + 2 * j
                    ins = pe.matmul(ps[:, c:c + 2], lc[:, j, tt * P:(tt + 1) * P], head_ones[:, 0:P:HD], start=True, stop=True)
            ins.then_inc(acc_full, 1)
            pe.wait_ge(kk_wide, 1)
            wide = lc[:, :, :].rearrange("p a b -> p (a b)")
            for j in range(4):
                ps = claim(pe, "tr", tr_at["kk"] + j)
                for tt in ALL:
                    c = 8 * tt + 2 * j
                    ins = pe.transpose(ps[:, tt * P:(tt + 1) * P], wide[:, c * HD:(c + 2) * HD], ident)
                ins.then_inc(tr_full, 1)

        def kk_pool(pool):
            wait_drained(pool, "acc", acc_at["kk"])
            pool.tensor_tensor(kk_rs[:, :], kk_ss[:, :], half[:, :], ALU.pow).then_inc(kk_rn, 1)
            for x in (ar_bd[:, :, :, :], bh_bd[:, :, :], kh_bd[:, :, :]):
                pool.memset(x, 0.0).then_inc(bd_cleared, 1)
            pool.wait_ge(bd_cleared, 3)

        def prep_pe(pe, d):
            if d == 0:
                pe.wait_ge(lora_landed, 32)
                pe.wait_ge(lora_in, 1)
            s = slice(d * 64, d * 64 + 64)
            for j in range(4):
                for i, x in enumerate((pA[s, 12, :], pA[s, 13, :])):
                    ps = claim(pe, "acc", acc_at[("prep", d)] + 2 * j + i)
                    pe.matmul(ps[:, :], lora[s, i, j * P:(j + 1) * P], x, start=True, stop=True).then_inc(acc_full, 1)

        def prep_act(act, d):
            if d:
                act.wait_ge(acc_full, acc_at[("chunk", 0, NCH - 1)] + 28)
            for j in range(4):
                if j >= 2:
                    act.wait_ge(prep_done, 4 * d + j - 1)
                for i, (x, b) in enumerate(((sig, "a_w0_2"), (iclr, "a_a0_2"))):
                    f = acc_at[("prep", d)] + 2 * j + i
                    act.activation(x[:, j % 2, :], filled(act, "acc", f)[:, :], ACT.Sigmoid, bias=col(b, 4 * d + j)).then_inc(drain("acc", f), 1)
            if d:
                act.dma_start(g2, I["a_g2_2"][0]).then_inc(g2_landed, 16)
            act.wait_ge(cum_done, d + 1)
            act.activation(f_step[:, :], l_step[:, :], ACT.Exp, scale=-DECAY).then_inc(decay_ready, 1)

        def prep_dve(dve, d):
            edge = const("scan_edge")
            if d:
                dve.wait_ge(bk_done, 4 * NCH)
            if d == 0:
                for j in (2, 3):
                    wait_drained(dve, "tr", tr_at["kk"] + j)
            for j in range(4):
                for i in range(2):
                    wait_drained(dve, "acc", acc_at[("prep", d)] + 2 * j + i)
                x = lc[:, j, :]
                if d == 0:
                    dve.tensor_tensor_scan(x, edge[:, 0:S2], sig[:, j % 2, :], 0.0, ALU.mult, ALU.add)
                else:
                    dve.tensor_tensor_scan(x[:, ::-1], edge[:, 1:S2 + 1][:, ::-1], sig[:, j % 2, :][:, ::-1], 0.0, ALU.mult, ALU.add)
                dve.tensor_tensor(kka[:, j, :], kk[:, j, :], iclr[:, j % 2, :], ALU.mult)
                link(dve, dve.scalar_tensor_tensor(kd[:, j, :], iclr[:, j % 2, :], -1.0, kf[:, j, :], ALU.add, ALU.mult))
                link(dve, dve.scalar_tensor_tensor(kd[:, j, :], kd[:, j, :], col("a_k_a_2", j), kf[:, j, :], ALU.mult, ALU.add))
                if d == 0:
                    ins = dve.tensor_copy(kd_sum[:, j, :], kd[:, j, :])
                else:
                    ins = dve.tensor_tensor(kd_sum[:, j, :], kd_sum[:, j, :], kd[:, j, :], ALU.add)
                ins.then_inc(prep_done, 1)
            dve.wait_ge(prep_done, 4 * d + 4)
            chunked = lc[:, :, :].rearrange("p j (c t) -> p (j c) t", t=CH)
            link(dve, dve.tensor_copy(l_mid[:, :], chunked[:, :, CH // 2 - 1 + d]))
            link(dve, dve.tensor_tensor(chunked, chunked, l_mid[:, :].unsqueeze(2).broadcast_to([P, 4 * NCH, CH]), ALU.subtract))
            link(dve, dve.tensor_copy(l_end[:, :], chunked[:, :, 0 if d else CH - 1]))
            mid, end, step = by_chunk(l_mid[:, :]), by_chunk(l_end[:, :]), by_chunk(l_step[:, :])
            link(dve, dve.memset(l_step[:, :], 0.0))
            for a, b, n in ([(0, 1, 7)] if d == 0 else [(1, 0, 3), (0, 7, 1), (5, 4, 3)]):
                ins = dve.tensor_tensor(step[:, :, a:a + n], end[:, :, a:a + n], mid[:, :, b:b + n], ALU.add)
            ins.then_inc(cum_done, 1)

        pe_exp, ar_done, bk_done, bd_done = sem("pe_exp"), sem("ar_done"), sem("bk_done"), sem("bd_done")
        xi_set = sem("xi_set")

        def chunk_fills(d, s):
            f = acc_at[("chunk", d, s)]
            return {"nq": f, "lev0": f + 2, "lev": f + 4, "g": f + 24, "u": f + 25, "s": f + 26, "y": f + 27}

        def chunk_act(act, d, s):
            n, ci = NCH * d + s, ORDER[d][s]
            sl = slice(ci * CH, (ci + 1) * CH)
            F, T = chunk_fills(d, s), tr_at[("chunk", d, s)]
            if n:
                act.wait_ge(ar_done, n)
                act.wait_ge(bk_done, 4 * n)
            act.wait_ge(cum_done, d + 1)
            incl = 1 - d
            act.activation(l_pe[:, :, incl:incl + CH], lc[:, :, sl], ACT.Exp, scale=-DECAY)
            act.activation(l_pe[:, :, CH * d:CH * d + 1], by_chunk(l_mid[:, :])[:, :, ci:ci + 1], ACT.Exp, scale=DECAY)
            act.activation(l_pi[:, :, :], lc[:, :, sl], ACT.Exp, scale=DECAY).then_inc(pe_exp, 1)
            act.wait_ge(ar_done, n + 1)
            if n:
                act.wait_ge(acc_full, acc_at[("chunk", (n - 1) // NCH, (n - 1) % NCH)] + 28)
            else:
                act.wait_ge(bd_cleared, 3)
            for hd in range(2):
                h = slice(hd * HD, hd * HD + HD)
                act.activation(ar_bd[h, :, :, h], ar[h, :, :, :], ACT.Copy).then_inc(bd_done, 1)
            ps = filled(act, "tr", T)
            for hd in range(2):
                h = slice(hd * HD, hd * HD + HD)
                ins = act.activation(vst[h, :, :], ps[0:CH, :].rearrange("p (j c) -> p j c", j=4)[:, :, h], ACT.Copy)
            ins.then_inc(drain("tr", T), 1)
            for i, x in ((1, b_tok), (2, k_tk)):
                act.activation(x[:, :, :], filled(act, "tr", T + i)[:, :].rearrange("p (j c) -> p j c", j=4), ACT.Copy).then_inc(drain("tr", T + i), 1)
            for lev in range(1, 6):
                for g in range(2):
                    f = F["lev"] + 4 * (lev - 1) + g
                    act.activation(yi[:, 2 * g:2 * g + 2, :], filled(act, "acc", f)[:, 0:2 * P].rearrange("p (j c) -> p j c", j=2),
                                   ACT.Copy).then_inc(drain("acc", f), 1)
            for f, x in ((F["g"], g_sb), (F["u"], u_sb)):
                act.activation(x[:, :, :], filled(act, "acc", f)[:, 0:4 * CH].rearrange("p (j c) -> p j c", j=4), ACT.Copy).then_inc(drain("acc", f), 1)

        def chunk_pool(pool, d, s):
            n, ci = NCH * d + s, ORDER[d][s]
            sl = slice(ci * CH, (ci + 1) * CH)
            if n:
                pool.wait_ge(acc_full, acc_at[("chunk", (n - 1) // NCH, (n - 1) % NCH)] + 28)
            for j in range(4):
                pool.tensor_copy(xi[:, j, :], ident)
                ins = pool.tensor_copy(xiT[:, j, :], ident)
            ins.then_inc(xi_set, 1)
            pool.wait_ge(xi_set, n + 1)
            pool.wait_ge(pe_exp, n + 1)
            pool.wait_ge(prep_done, 4 * d + 4)
            for hd in range(2):
                h = slice(hd * HD, hd * HD + HD)
                for i, (x, y) in enumerate(((bh_bd, kka), (kh_bd, kd))):
                    pool.tensor_tensor(x[h, :, h], y[h, :, sl], l_pi[h, :, :], ALU.mult).then_inc(bk_done, 1)
                    pool.wait_ge(bk_done, 4 * n + 2 * hd + i + 1)

        def chunk_pe(pe, d, s):
            n, ci = NCH * d + s, ORDER[d][s]
            sl = slice(ci * CH, (ci + 1) * CH)
            F, T = chunk_fills(d, s), tr_at[("chunk", d, s)]
            st = state[:, s % 2]
            ps = claim(pe, "tr", T)
            for j in range(4):
                ins = pe.transpose(ps[0:CH, j * P:(j + 1) * P], vf[:, j, sl], ident)
            ins.then_inc(tr_full, 1)
            pe.wait_ge(bk_done, 4 * n + 4)
            for i, x in ((1, bh_bd), (2, kh_bd)):
                ps = claim(pe, "tr", T + i)
                for j in range(4):
                    ins = pe.transpose(ps[:, j * P:(j + 1) * P], x[:, j, :], ident)
                ins.then_inc(tr_full, 1)
            pe.wait_ge(ar_done, n + 1)
            for g in range(2):
                ps = claim(pe, "acc", F["nq"] + g)
                for i in range(2):
                    for b, x in enumerate((bh_bd, kh_bd)):
                        ins = pe.matmul(ps[:, (2 * i + b) * P:(2 * i + b + 1) * P], x[:, 2 * g + i, :],
                                        ar[:, 2 * g + i, :, :].rearrange("p a t -> p (a t)"), start=True, stop=True)
                ins.then_inc(acc_full, 1)
            for g in range(2):
                wait_drained(pe, "acc", F["nq"] + g)
                ps = claim(pe, "acc", F["lev0"] + g)
                for i in range(2):
                    ins = pe.matmul(ps[:, i * P:(i + 1) * P], nq[:, 2 * g + i, 0, :], ident, start=True, stop=True)
                ins.then_inc(acc_full, 1)
            for lev in range(1, 6):
                for g in range(2):
                    wait_drained(pe, "acc", F["lev0"] + g if lev == 1 else F["lev"] + 4 * (lev - 2) + 2 + g)
                    f = F["lev"] + 4 * (lev - 1) + g
                    ps = claim(pe, "acc", f)
                    for i in range(2):
                        ins = pe.matmul(ps[:, i * P:(i + 1) * P], nq[:, 2 * g + i, 0, :], xi[:, 2 * g + i, :], start=True, stop=True)
                    ins.then_inc(acc_full, 1)
                for g in range(2):
                    wait_drained(pe, "acc", F["lev"] + 4 * (lev - 1) + g)
                    f = F["lev"] + 4 * (lev - 1) + 2 + g
                    ps = claim(pe, "acc", f)
                    for i in range(2):
                        j = 2 * g + i
                        if lev < 5:
                            pe.matmul(ps[:, i * P:(i + 1) * P], xiT[:, j, :], yi[:, j, :], start=True, stop=True)
                        ins = pe.matmul(ps[:, (2 + i) * P:(3 + i) * P], yi[:, j, :], xiT[:, j, :], start=True, stop=True)
                    ins.then_inc(acc_full, 1)
            first_chunk = s == 0
            out4 = lambda ps, j: ps[:, j * CH:(j + 1) * CH]
            wait_drained(pe, "tr", T)
            wait_drained(pe, "tr", T + 1)
            wait_drained(pe, "tr", T + 2)
            pe.wait_ge(bd_done, 2 * n + 2)
            if not first_chunk:
                wait_drained(pe, "acc", chunk_fills(d, s - 1)["s"])
            ps = claim(pe, "acc", F["g"])
            for j in range(4):
                ins = pe.matmul(out4(ps, j), nq[:, j, 2, :], vst[:, j, :], start=True, stop=first_chunk)
                if not first_chunk:
                    ins = pe.matmul(out4(ps, j), ar_bd[:, j, 0, :], st[:, j, :], start=False, stop=True)
            ins.then_inc(acc_full, 1)
            for g in range(2):
                wait_drained(pe, "acc", F["lev"] + 16 + 2 + g)
            wait_drained(pe, "acc", F["g"])
            ps = claim(pe, "acc", F["u"])
            for j in range(4):
                ins = pe.matmul(out4(ps, j), xiT[:, j, :], g_sb[:, j, :], start=True, stop=True)
            ins.then_inc(acc_full, 1)
            wait_drained(pe, "acc", F["u"])
            ps = claim(pe, "acc", F["s"])
            for j in range(4):
                pe.matmul(out4(ps, j), b_tok[:, j, :], u_sb[:, j, :], start=True, stop=False)
                ins = pe.matmul(out4(ps, j), k_tk[:, j, :], vst[:, j, :], start=False, stop=True)
            ins.then_inc(acc_full, 1)
            ps = claim(pe, "acc", F["y"])
            for j in range(4):
                pe.matmul(out4(ps, j), nq[:, j, 1, :], u_sb[:, j, :], start=True, stop=False)
                ins = pe.matmul(out4(ps, j), nq[:, j, 3, :], vst[:, j, :], start=False, stop=first_chunk)
                if not first_chunk:
                    ins = pe.matmul(out4(ps, j), ar_bd[:, j, 1, :], st[:, j, :], start=False, stop=True)
            ins.then_inc(acc_full, 1)

        def chunk_dve(dve, d, s):
            n, ci = NCH * d + s, ORDER[d][s]
            sl = slice(ci * CH, (ci + 1) * CH)
            F = chunk_fills(d, s)
            dve.wait_ge(pe_exp, n + 1)
            incl = 1 - d
            if n:
                dve.wait_ge(bd_done, 2 * n)
            dve.scalar_tensor_tensor(ar[:, :, 0, :], kk[:, :, sl], -1.0, l_pe[:, :, 1 - incl:1 - incl + CH], ALU.mult, ALU.mult)
            dve.tensor_tensor(ar[:, :, 1, :], rr[:, :, sl], l_pe[:, :, incl:incl + CH], ALU.mult).then_inc(ar_done, 1)
            tri = const(f"tri{d}").rearrange("p (a h t) -> p a h t", a=4, h=2)
            for g in range(2):
                ps = filled(dve, "acc", F["nq"] + g)
                for i in range(2):
                    x = ps[:, i * 2 * P:(i + 1) * 2 * P].rearrange("p (a t) -> p a t", a=4).unsqueeze(2).broadcast_to([P, 4, 2, CH])
                    ins = dve.tensor_tensor(nq[:, 2 * g + i, :, :].rearrange("p a (h t) -> p a h t", h=2), x, tri, ALU.mult)
                ins.then_inc(drain("acc", F["nq"] + g), 1)
            names = ("low", "up") if d == 0 else ("up", "low")
            wide = lambda lev, i: mask(f"{names[i]}{lev}").unsqueeze(1).broadcast_to([P, 2, P])
            two = lambda ps, i: ps[:, i * 2 * P:(i + 1) * 2 * P].rearrange("p (j c) -> p j c", j=2)
            dve.wait_ge(xi_set, n + 1)
            if n == 0:
                dve.wait_ge(masks_set, 1)
            for lev in range(6):
                for g in range(2):
                    jj = slice(2 * g, 2 * g + 2)
                    f = F["lev0"] + g if lev == 0 else F["lev"] + 4 * (lev - 1) + 2 + g
                    ps = filled(dve, "acc", f)
                    if lev == 0:
                        dve.copy_predicated(xi[:, jj, :], wide(0, 0), two(ps, 0))
                        wait_drained(dve, "acc", F["nq"] + g)
                        ins = dve.copy_predicated(xiT[:, jj, :], wide(0, 1), nq[:, jj, 0, :])
                    else:
                        if lev < 5:
                            dve.copy_predicated(xi[:, jj, :], wide(lev, 0), two(ps, 0))
                        ins = dve.copy_predicated(xiT[:, jj, :], wide(lev, 1), two(ps, 1))
                    ins.then_inc(drain("acc", f), 1)
            ps = filled(dve, "acc", F["s"])[:, 0:4 * CH].rearrange("p (j c) -> p j c", j=4)
            nxt = state[:, (s + 1) % 2]
            if s == 0:
                dve.wait_ge(decay_ready, d + 1)
                x = ps
            else:
                wait_drained(dve, "acc", chunk_fills(d, s - 1)["s"])
                link(dve, dve.tensor_tensor(s_tmp[:, :, :], ps, state[:, s % 2], ALU.add))
                x = s_tmp[:, :, :]
            dve.tensor_tensor(nxt, x, by_chunk(f_step[:, :])[:, :, ci:ci + 1].broadcast_to([P, 4, CH]), ALU.mult)\
               .then_inc(drain("acc", F["s"]), 1)
            ps = filled(dve, "acc", F["y"])[:, 0:4 * CH].rearrange("p (j c) -> p j c", j=4)
            y = y_st[:, :, ci, :]
            if d == 0:
                ins = dve.tensor_copy(y, ps)
            else:
                ins = dve.tensor_tensor(y, y, ps, ALU.add)
            ins.then_inc(drain("acc", F["y"]), 1)

        gn_sum, gn_mean, gn_sq, gn_var, gn_rs = (stats(4 * NCH) for _ in range(5))
        gn_var_ready, gn_rstd, y_normed, bonus_in = sem("gn_var_ready"), sem("gn_rstd"), sem("y_normed"), sem("bonus_in")
        yA_high, yA_low = sem("yA_high"), sem("yA_low")
        y_all = y_st.rearrange("p j c v -> p (j c) v")

        def rwkv_out_pool(pool):
            pool.wait_ge(acc_full, acc_at[("chunk", 1, NCH - 1)] + 28)
            pool.wait_ge(gn_var_ready, 1)
            pool.tensor_tensor(gn_rs[:, :], gn_var[:, :], half[:, :], ALU.pow).then_inc(gn_rstd, 1)

        def scan_over(eng):
            F = chunk_fills(1, NCH - 1)
            eng.wait_ge(acc_full, F["y"] + 1)
            wait_drained(eng, "acc", F["s"])
            wait_drained(eng, "acc", F["y"])

        def rwkv_out_dve(dve):
            wait_drained(dve, "acc", chunk_fills(1, NCH - 1)["y"])
            wide = lambda v: v.unsqueeze(2).broadcast_to([P, 4 * NCH, CH])
            squares = lc[:, :, :].rearrange("p j (c v) -> p (j c) v", v=CH)
            for j in range(4):
                dve.scalar_tensor_tensor(kd_sum[:, j, :], rr[:, j, :], col("a_r_k_2", j), kd_sum[:, j, :], ALU.mult, ALU.mult).then_inc(bonus_in, 1)
            link(dve, dve.tensor_reduce(gn_sum[:, :], y_all, AX_X, ALU.add))
            link(dve, dve.tensor_scalar(gn_mean[:, :], gn_sum[:, :], 1.0 / HD, None, ALU.mult))
            link(dve, dve.tensor_tensor(y_all, y_all, wide(gn_mean[:, :]), ALU.subtract))
            link(dve, dve.tensor_tensor(squares, y_all, y_all, ALU.mult))
            link(dve, dve.tensor_reduce(gn_sq[:, :], squares, AX_X, ALU.add))
            dve.tensor_scalar(gn_var[:, :], gn_sq[:, :], 1.0 / HD, GN_EPS, ALU.mult, ALU.add).then_inc(gn_var_ready, 1)
            dve.wait_ge(gn_rstd, 1)
            dve.tensor_tensor(y_all, y_all, wide(gn_rs[:, :]), ALU.mult).then_inc(y_normed, 1)
            for j in range(4):
                f = acc_at["rwkv_out"] + 2 * j
                for i in range(2):
                    wait_drained(dve, "tr", tr_at["rwkv_out"] + 2 * j + i)
                a = y_full[:, j, :]
                dve.tensor_tensor(lc[:, j, :], filled(dve, "acc", f)[:, :], vf[:, j, :], ALU.mult).then_inc(drain("acc", f), 1)
                link(dve, dve.tensor_scalar(a, a, col("a_gn_w_2", j), col("a_gn_b_2", j), ALU.mult, ALU.add))
                wait_drained(dve, "acc", f)
                link(dve, dve.tensor_tensor(a, a, lc[:, j, :], ALU.add))
                dve.tensor_tensor(a, a, filled(dve, "acc", f + 1)[:, :], ALU.mult).then_inc(drain("acc", f + 1), 1)
            for j in range(4):
                dve.wait_ge(yA_high, j + 1)
                dve.tensor_tensor(r32(y_full[:, j, :]), y_full[:, j, :], r32(yT[0][:, j, :]), ALU.subtract).then_inc(yA_low, 1)

        def rwkv_out_pe(pe):
            pe.wait_ge(g2_landed, 16)
            pe.wait_ge(lora_in, 2)
            pe.wait_ge(y_normed, 1)
            for j in range(4):
                for i in range(2):
                    f = tr_at["rwkv_out"] + 2 * j + i
                    ps = claim(pe, "tr", f)
                    for c in range(4):
                        ins = pe.transpose(ps[0:CH, c * P:(c + 1) * P], y_st[:, j, 4 * i + c, :], ident)
                    ins.then_inc(tr_full, 1)
            for j in range(4):
                f = acc_at["rwkv_out"] + 2 * j
                pe.wait_ge(bonus_in, j + 1)
                pe.matmul(claim(pe, "acc", f)[:, :], head_ones, kd_sum[:, j, :], start=True, stop=True).then_inc(acc_full, 1)
                pe.matmul(claim(pe, "acc", f + 1)[:, :], g2[:, j * P:(j + 1) * P], pA[:, 14, :], start=True, stop=True).then_inc(acc_full, 1)

        def rwkv_out_act(act):
            for j in range(4):
                for i in range(2):
                    f = tr_at["rwkv_out"] + 2 * j + i
                    ps = filled(act, "tr", f)[0:CH, :].rearrange("p (c x) -> p c x", c=4)
                    for hd in range(2):
                        h = slice(hd * HD, hd * HD + HD)
                        dst = y_full[h, j, i * SEQ:(i + 1) * SEQ].rearrange("p (c t) -> p c t", c=4)
                        ins = act.activation(dst, ps[:, :, h], ACT.Copy)
                    ins.then_inc(drain("tr", f), 1)
            for j in range(4):
                wait_drained(act, "acc", acc_at["rwkv_out"] + 2 * j + 1)
                act.activation(r32(yT[0][:, j, :]), y_full[:, j, :], ACT.Copy).then_inc(yA_high, 1)

        gate_diag, post_squared, post_mean, post_rstd, h_updated = (
            sem("gate_diag"), sem("post_squared"), sem("post_mean"), sem("post_rstd"), sem("h_updated"))
        posts = {}

        class Post:

            def __init__(self, key, l, w, streams, o, gate, diag, squares, free, product=None, kts=None):
                self.key, self.l, self.w, self.streams, self.o, self.gate, self.diag = key, l, w, streams, o, gate, diag
                self.squares, self.free, self.product, self.kts = squares, free, product, kts
                self.tiles = [(s, (h_ctx if s else h_lat)[:, t, :]) for s in streams for t in range(TT)]
                n = len(self.tiles)
                self.gate0 = acc_at[key]
                self.f0 = acc_at[key] + 2 * len(streams)
                self.ss, self.sum, self.ms, self.rs = stats(2 * n), stats(n), stats(n), stats(n)
                self.index = len(posts)
                self.gates_before = sum(len(p.streams) for p in posts.values())
                self.tiles_before = sum(len(p.tiles) for p in posts.values())
                posts[key] = self

            def pool_gate(self, pool):
                pool.wait_ge(mod_ready, 2 * DEPTH)
                self.free(pool)
                for i, s in enumerate(self.streams):
                    for kt in range(KT):
                        ins = pool.tensor_scalar(self.diag[:, i, kt, :], ident, mod_gate[:, self.l, self.w, kt, s:s + 1], None, ALU.mult)
                    ins.then_inc(gate_diag, 1)

            def pool_rstd(self, pool):
                pool.wait_ge(post_mean, self.index + 1)
                pool.tensor_tensor(self.rs[:, :], self.ms[:, :], half[:, 0:len(self.tiles)], ALU.pow).then_inc(post_rstd, 1)

            def tensor_gate(self, pe):
                for i in range(len(self.streams)):
                    pe.wait_ge(gate_diag, self.gates_before + i + 1)
                    for hf in range(2):
                        ps = claim(pe, "acc", self.gate0 + 2 * i + hf)
                        pe.matmul(ps[:, :], ones, self.diag[:, i, 4 * hf:4 * hf + 4, :].rearrange("p a b -> p (a b)"),
                                  start=True, stop=True).then_inc(acc_full, 1)

            def scalar_gate(self, act):
                for i in range(len(self.streams)):
                    for hf in range(2):
                        f = self.gate0 + 2 * i + hf
                        act.activation(self.gate[:, i, hf * 512:(hf + 1) * 512], filled(act, "acc", f)[:, :], ACT.Copy).then_inc(drain("acc", f), 1)

            def scalar(self, act):
                n = len(self.tiles)

                def squares(hf):
                    for t in range(n):
                        ps = filled(act, "acc", self.f0 + hf * n + t)
                        act.activation(self.o[:, t, hf * 512:(hf + 1) * 512], ps[:, :], ACT.Square,
                                       accum_out=self.ss[:, hf * n + t:hf * n + t + 1]).then_inc(post_squared, 1)

                tok_walk(act, ahead_act, self.product, self.kts, 2, squares)

            def vector(self, dve):
                n = len(self.tiles)

                def keep_product(hf):
                    for t in range(n):
                        f = self.f0 + hf * n + t
                        dve.wait_ge(post_squared, 2 * self.tiles_before + hf * n + t + 1)
                        dve.tensor_copy(self.o[:, t, hf * 512:(hf + 1) * 512], bank("acc", f)[:, :]).then_inc(drain("acc", f), 1)

                tok_walk(dve, ahead_dve, self.product, self.kts, 2, keep_product)
                for f in range(self.f0 + 2 * n - 4, self.f0 + 2 * n):
                    wait_drained(dve, "acc", f)
                link(dve, dve.tensor_tensor(self.sum[:, :], self.ss[:, 0:n], self.ss[:, n:2 * n], ALU.add))
                self.update(dve)

            def add_round(self, dve, key, first):
                def add(hf):
                    for t in range(len(self.tiles)):
                        f = acc_at[key] + len(self.tiles) * hf + t
                        ps, o = filled(dve, "acc", f), self.o[:, t, hf * 512:(hf + 1) * 512]
                        if first:
                            ins = dve.tensor_copy(o, ps[:, :])
                        else:
                            ins = dve.tensor_tensor(o, o, ps[:, :], ALU.add)
                        ins.then_inc(drain("acc", f), 1)

                tok_walk(dve, ahead_dve, key, ET, 2, add)

            def scalar_rounds(self, act, last):
                n = len(self.tiles)
                for t in range(n):
                    wait_drained(act, "acc", acc_at[last] + n + t)
                    act.activation(self.squares[:, t, :], self.o[:, t, :], ACT.Square, accum_out=self.sum[:, t:t + 1]).then_inc(post_squared, 2)

            def vector_rounds(self, dve, last):
                n = len(self.tiles)
                for t in range(n):
                    wait_drained(dve, "acc", acc_at[last] + n + t)
                dve.wait_ge(post_squared, 2 * self.tiles_before + 2 * n)
                self.update(dve)

            def update(self, dve):
                dve.tensor_scalar(self.ms[:, :], self.sum[:, :], 1.0 / D, EPS, ALU.mult, ALU.add).then_inc(post_mean, 1)
                for f in range(self.gate0, self.gate0 + 2 * len(self.streams)):
                    wait_drained(dve, "acc", f)
                dve.wait_ge(post_rstd, self.index + 1)
                for t, (s, h) in enumerate(self.tiles):
                    link(dve, dve.scalar_tensor_tensor(self.o[:, t, :], self.o[:, t, :], self.rs[:, t:t + 1],
                                                       self.gate[:, self.streams.index(s), :], ALU.mult, ALU.mult))
                    dve.tensor_tensor(h, h, self.o[:, t, :], ALU.add).then_inc(h_updated, 1)

            def updated(self, eng):
                eng.wait_ge(h_updated, self.tiles_before + len(self.tiles))

        hid_squared, hid_high, hid_ready = sem("hid_squared"), sem("hid_high"), sem("hid_ready")

        def hidden_act(act, key, n0, n, place):
            for i in range(n + 1):
                if i < n:
                    f = acc_at[key] + i
                    lo = place(i)[1]
                    ps = filled(act, "acc", f)
                    act.activation(lo, ps[:, 0:lo.shape[1]], ACT.Relu).then_inc(drain("acc", f), 1)
                if i:
                    hi, lo = place(i - 1)
                    act.wait_ge(hid_squared, n0 + i)
                    act.activation(r32(hi), lo, ACT.Copy).then_inc(hid_high, 1)
                if i < n and i % 2:
                    ahead_act(act, chunk_at[key] + i // 2 + HIGH)

        def hidden_dve(dve, key, n0, n, place):
            for i in range(n + 1):
                if i < n:
                    lo = place(i)[1]
                    wait_drained(dve, "acc", acc_at[key] + i)
                    dve.tensor_tensor(lo, lo, lo, ALU.mult).then_inc(hid_squared, 1)
                if i:
                    hi, lo = place(i - 1)
                    dve.wait_ge(hid_high, n0 + i)
                    dve.tensor_tensor(r32(lo), lo, r32(hi), ALU.subtract).then_inc(hid_ready, 1)
                if i < n and i % 2:
                    ahead_dve(dve, chunk_at[key] + i // 2 + HIGH)

        def eighth(e):
            return ("ff1", e), e * ET, ET, lambda i: tuple(v[:, e % 2, i, :] for v in hid)

        def ff0_tensor(pe, post):
            for s in (1, 0):
                norm_wait(pe, ("ff", 0, s))
            for e in range(EIGHTHS + 1):
                if e < EIGHTHS:
                    feat_gemm(pe, ("ff1", e), acc_at[("ff1", e)], ET, lambda kt: both(uT, lambda v: v[:, kt, :]))
                if e == 0:
                    post.tensor_gate(pe)
                else:
                    pe.wait_ge(hid_ready, e * ET)
                    tok_gemm(pe, ("ff2", e - 1), acc_at[("ff2", e - 1)], ET, [ALL] * 2,
                             lambda kt, tt: both(hid, lambda v: v[:, (e - 1) % 2, kt, tt * P:(tt + 1) * P]))

        def ff0_scalar(act, post):
            for e in range(EIGHTHS + 1):
                if e < EIGHTHS:
                    hidden_act(act, *eighth(e))
                if e == 0:
                    post.scalar_gate(act)
                else:
                    tok_walk(act, ahead_act, ("ff2", e - 1), ET, 2)
            post.scalar_rounds(act, ("ff2", EIGHTHS - 1))

        def ff0_vector(dve, post):
            for e in range(EIGHTHS + 1):
                if e < EIGHTHS:
                    hidden_dve(dve, *eighth(e))
                if e:
                    post.add_round(dve, ("ff2", e - 1), e == 1)
            post.vector_rounds(dve, ("ff2", EIGHTHS - 1))

        ff1_tiles = ("ff1_1", FT2, FT2, lambda i: tuple(v[:, i, :] for v in hid1))

        def ff1_tensor(pe, post):
            norm_wait(pe, ("ff", 1, 0))
            feat_gemm(pe, "ff1_1", acc_at["ff1_1"], FT2, lambda kt: both(uT1, lambda v: v[:, kt, :]))
            post.tensor_gate(pe)
            tok_gemm(pe, "ff2_1", post.f0, FT2, [LAT] * 2, lambda kt, tt: both(hid1, lambda v: v[:, kt, tt * P:(tt + 1) * P]),
                     lambda n: pe.wait_ge(hid_ready, FT2 + n))

        r5 = Region(0)
        dk_tok = r5.take(4, 256)
        dv_tok = r5.take(4, P)
        dq_tok = r5.take(2, 512)
        gain_row = r5.take(2, HD)
        assert r5.at <= N_BIAS * SEQ
        r5 = Region(at2)
        near = r5.take(2, 8, SEQ)
        cv_tok = r5.take(4, 512)
        cqT = r5.take(4, SEQ)
        ckT = r5.take(4, S2)
        dqT = r5.take(4, SEQ)
        dkT = r5.take(2, S2)
        at_y2 = r5.at
        y2 = r5.take(TT, D)
        r5 = Region(at_y2)
        rope2 = r5.take(2, 512)
        sq2 = r5.take(2, 512)
        yT2 = uT1
        r5 = Region(at1 + 2 * KT * SEQ)
        prob2 = r5.take(2, 2, 512)
        prob2T = r5.take(2, 1024)
        assert r5.at <= at2
        hankels = [v.rearrange("p a b -> p (a b)").rearrange("p (h k) -> p h k", h=8) for v in (cv_tok, ckT)]
        o_mix1, gate_mix1, diag_mix1, _ = tail(at2)

        def near_dma(act):
            posts["post_ff0"].updated(act)
            act.dma_start(gain_row[:, 0, :], I["d_q_gain_2"].partition_broadcast(P)).then_inc(gains_landed, 16)
            act.dma_start(gain_row[:, 1, :], I["d_k_gain_2"].partition_broadcast(P)).then_inc(gains_landed, 16)
            rpb = I["c_rpb_2"]
            nd, nc_ = 2 * NA_KH - 1, 2 * NA_KW - 1
            for qt in range(2):
                for i in range(2):
                    r = 2 * qt + i
                    for h in range(8):
                        src = bass.AP(tensor=rpb.tensor, offset=(h * nd + NA_KH - 1 - r) * nc_ + NA_KW - 1 - (GRID_W - 1),
                                      ap=[[1, GRID_W], [nc_, 4], [1, GRID_W]])
                        act.dma_start(hankels[qt][i * GRID_W:(i + 1) * GRID_W, h, :].rearrange("p (t k) -> p t k", t=4), src)\
                          .then_inc(near_landed, 16)

        def near_pe(pe):
            pe.wait_ge(near_landed, 16 * 32)
            for i in range(8):
                ps = claim(pe, "acc", acc_at["near"] + i)
                pe.matmul(ps[:, :], flip64, hankels[i // 4][:, 2 * (i % 4):2 * (i % 4) + 2, :].rearrange("p a b -> p (a b)"),
                          start=True, stop=True).then_inc(acc_full, 1)

        def near_dve(dve):
            for i in range(8):
                f = acc_at["near"] + i
                win = const("near")[:, (i // 4) * SEQ:(i // 4 + 1) * SEQ].unsqueeze(1).broadcast_to([P, 2, SEQ])
                dve.tensor_tensor(near[:, i // 4, 2 * (i % 4):2 * (i % 4) + 2, :],
                                  filled(dve, "acc", f)[:, :].rearrange("p (a b) -> p a b", a=2), win, ALU.add).then_inc(drain("acc", f), 1)

        PQ, PK, PV, PDQ, PDK = (lambda: [acc_at["proj1"] + n for n in (0, 4, 8, 12, 14)])()
        d_mean, d_rstd, d_normed, gains_landed = sem("d_mean"), sem("d_rstd"), sem("d_normed"), sem("gains_landed")
        d_ss, d_ms, d_rs = stats(48), stats(48), stats(48)
        D_UNITS = [(dk_tok[:, tt, :], PDK + tt, 4, 16 + 4 * tt, tt - 2 if tt >= 2 else None) for tt in ALL]
        D_UNITS = [(dq_tok[:, tt, :], PDQ + tt, 8, 8 * tt, tt) for tt in range(TT)] + D_UNITS

        def proj1_pe(pe):
            for s in (1, 0):
                norm_wait(pe, ("mix", 1, s))
            feat_gemm(pe, "proj1", PQ, 4, lambda kt: both(uT, lambda v: v[:, kt, SEQ:S2]))
            feat_gemm(pe, "proj1_k", PK, 4, lambda kt: both(uT, lambda v: v[:, kt, :]))
            tok_gemm(pe, "proj1_tok", PV, KT, [ALL, LATS, ALL], lambda kt, tt: both(uT, lambda v: v[:, kt, tt * P:(tt + 1) * P]))
            for n, (x, f, nh, c, lat) in enumerate(D_UNITS):
                pe.wait_ge(d_normed, n + 1)
                ps = claim(pe, "tr", tr_at["proj1"] + n)
                for j in range(nh // 2):
                    ins = pe.transpose(ps[:, j * P:(j + 1) * P], x[:, j * P:(j + 1) * P], ident)
                ins.then_inc(tr_full, 1)

        def proj1_act(act):
            for i in range(4):
                act.activation(cqT[:, i, :], filled(act, "acc", PQ + i)[:, 0:SEQ], ACT.Copy, scale=SCALE).then_inc(drain("acc", PQ + i), 1)
                if i % 2:
                    ahead_act(act, chunk_at["proj1"] + i // 2 + HIGH)
            for i in range(4):
                act.activation(ckT[:, i, :], filled(act, "acc", PK + i)[:, :], ACT.Copy).then_inc(drain("acc", PK + i), 1)
                if i % 2:
                    ahead_act(act, chunk_at["proj1_k"] + i // 2 + HIGH)

            def c_values():
                for tt in ALL:
                    act.activation(cv_tok[:, tt, :], filled(act, "acc", PV + tt)[:, :], ACT.Copy).then_inc(drain("acc", PV + tt), 1)

            def d_units(units):
                for n in units:
                    x, f, nh, c, lat = D_UNITS[n]
                    ps = filled(act, "acc", f)
                    if n >= 2:
                        act.wait_ge(d_mean, n - 1)
                    if nh == 8:
                        act.activation(x, ps[:, :], ACT.Copy)
                        act.activation(sq2[:, n % 2, :], ps[:, :], ACT.Square).then_inc(drain("acc", f), 1)
                    else:
                        act.activation(x.rearrange("p (k n e) -> p k n e", k=2, n=2), dup_heads(ps[:, 0:P]), ACT.Copy)
                        act.activation(dv_tok[:, (n - 2), :], ps[:, P:2 * P], ACT.Copy)
                        act.activation(sq2[:, n % 2, 0:4 * HD].rearrange("p (k n e) -> p k n e", k=2, n=2), dup_heads(ps[:, 0:P]),
                                       ACT.Square).then_inc(drain("acc", f), 1)

            tok_walk(act, ahead_act, "proj1_tok", KT, 3, lambda b: c_values() if b == 0 else d_units(range(2) if b == 1 else range(2, 6)))
            for n, (x, f, nh, c, lat) in enumerate(D_UNITS):
                if n >= 2:
                    t = tr_at["proj1"] + n
                    act.activation(dkT[:, :, (n - 2) * P:(n - 1) * P], filled(act, "tr", t)[:, 0:2 * P].rearrange("p (a b) -> p a b", a=2),
                                   ACT.Copy).then_inc(drain("tr", t), 1)
                else:
                    t = tr_at["proj1"] + n
                    act.activation(dqT[:, :, n * P:(n + 1) * P], filled(act, "tr", t)[:, :].rearrange("p (a b) -> p a b", a=4),
                                   ACT.Copy, scale=SCALE).then_inc(drain("tr", t), 1)

        def proj1_pool(pool):
            for n, (x, f, nh, c, lat) in enumerate(D_UNITS):
                pool.wait_ge(d_mean, n + 1)
                pool.tensor_tensor(d_rs[:, c:c + nh], d_ms[:, c:c + nh], half[:, 0:nh], ALU.pow).then_inc(d_rstd, 1)

        def proj1_dve(dve):
            dve.wait_ge(gains_landed, 32)
            for key in ("proj1", "proj1_k"):
                for i in range(2):
                    wait_drained(dve, "acc", (PQ if key == "proj1" else PK) + 2 * i + 1)
                    ahead_dve(dve, chunk_at[key] + i + HIGH)

            def means(units):
                for n in units:
                    mean(n, *D_UNITS[n])

            def mean(n, x, f, nh, c, lat):
                wait_drained(dve, "acc", f)
                link(dve, dve.tensor_reduce(d_ss[:, c:c + nh], sq2[:, n % 2, 0:nh * HD].rearrange("p (h e) -> p h e", e=HD), AX_X, ALU.add))
                dve.tensor_scalar(d_ms[:, c:c + nh], d_ss[:, c:c + nh], 1.0 / HD, EPS, ALU.mult, ALU.add).then_inc(d_mean, 1)

            tok_walk(dve, ahead_dve, "proj1_tok", KT, 3, lambda b: means(range(2) if b == 1 else range(2, 6)) if b else None)
            for n, (x, f, nh, c, lat) in enumerate(D_UNITS):
                dve.wait_ge(d_rstd, n + 1)
                xh = x.rearrange("p (h e) -> p h e", e=HD)
                link(dve, dve.tensor_tensor(xh, xh, d_rs[:, c:c + nh].unsqueeze(2).broadcast_to([P, nh, HD]), ALU.mult))
                ins = dve.tensor_tensor(xh, xh, gain_row[:, 0 if n < 2 else 1, :].unsqueeze(1).broadcast_to([P, nh, HD]), ALU.mult)
                if lat is not None:
                    link(dve, ins)
                    rope(dve, x, nh, lat, rope2, d_normed, n + 1)
                else:
                    ins.then_inc(d_normed, 1)

        def attC():
            return Attention("attC", 8, lambda u, m: heads(cqT, u, m, slice((u % 2) * P, (u % 2 + 1) * P)),
                             lambda u, m: heads(ckT, u, m, slice(0, S2)), lambda u: S2,
                             lambda u, m, kb: cv_tok[:, kb, (2 * (u // 2) + m) * HD:(2 * (u // 2) + m + 1) * HD],
                             lambda u: y2[:, u % 2, (u // 2) * P:(u // 2 + 1) * P], prob2, prob2T,
                             bias=lambda u, m: (SEQ, near[:, u % 2, 2 * (u // 2) + m, :]))

        def attD():
            return Attention("attD", 8, lambda u, m: heads(dqT, u, m, slice((u % 2) * P, (u % 2 + 1) * P)),
                             lambda u, m: dkT[m * HD:(m + 1) * HD, kv_of(u), :], lambda u: S2,
                             lambda u, m, kb: dv_tok[:, kb, kv_of(u) * HD:(kv_of(u) + 1) * HD],
                             lambda u: y2[:, u % 2, 512 + (u // 2) * P:512 + (u // 2 + 1) * P], prob2, prob2T)

        yT2_high = sem("yT2_high")

        def yT2_pe(pe, atts):
            for att in atts:
                for u in (6, 7):
                    wait_drained(pe, "sc", att.sc[u])
            for g in range(4):
                f = tr_at["yT1_2"] + g
                ps = claim(pe, "tr", f)
                for i in range(2):
                    for tt in range(TT):
                        kt = 2 * g + i
                        ins = pe.transpose(ps[:, i * SEQ + tt * P:i * SEQ + (tt + 1) * P], y2[:, tt, kt * P:(kt + 1) * P], ident)
                ins.then_inc(tr_full, 1)

        def yT2_act(act):
            for g in range(4):
                act.activation(r32(yT2[0][:, 2 * g:2 * g + 2, :].rearrange("p a b -> p (a b)")),
                               filled(act, "tr", tr_at["yT1_2"] + g)[:, :], ACT.Copy).then_inc(yT2_high, 1)

        def yT2_dve(dve):
            for g in range(4):
                f = tr_at["yT1_2"] + g
                hi, lo = (v[:, 2 * g:2 * g + 2, :].rearrange("p a b -> p (a b)") for v in yT2)
                ps = filled(dve, "tr", f)
                dve.wait_ge(yT2_high, g + 1)
                dve.tensor_tensor(r32(lo), ps[:, :], r32(hi), ALU.subtract).then_inc(drain("tr", f), 1)


        att = {("att1", l): att1(l) for l in range(DEPTH)}
        att_bl, att_bc, att_c, att_d = attBl(), attBc(), attC(), attD()

        def after_rwkv(pool):
            for i in range(4, 8):
                wait_drained(pool, "acc", acc_at["rwkv_out"] + i)

        def after_norm(key):
            return lambda pool: pool.wait_ge(tr_full, tr_at[("norm", key)] + 4)

        mix0 = Post("post_mix0", 0, 0, (1, 0), o_mix0, gate_mix0, diag_mix0, None, after_rwkv, "out2_0", KT)
        ff0 = Post("post_ff0", 0, 1, (1, 0), o_ff0, gate_ff, diag_ff,
                   hid[0].rearrange("p a b c -> p (a b c)").rearrange("p (t d) -> p t d", d=D), after_norm(("ff", 0, 0)))
        mix1 = Post("post_mix1", 1, 0, (0,), o_mix1, gate_mix1, diag_mix1, None,
                    lambda pool: pool.wait_ge(tr_full, tr_at["yT1_2"] + 4), "out2_1", KT)
        ff1 = Post("post_ff1", 1, 1, (0,), o_ff1, gate_ff, diag_ff, None, after_norm(("ff", 1, 0)), "ff2_1", FT2)

        def ctx_ready(eng):
            eng.wait_ge(ctx_landed, 16)

        def mod_norms(l, w):
            out = []
            for s in ((1, 0) if (l, w) != (1, 1) else (0,)):
                if (l, w) == (0, 0):
                    ready = ctx_ready if s else stream_ready(DEPTH, "attn")
                else:
                    ready = {(0, 1): mix0, (1, 0): ff0, (1, 1): mix1}[l, w].updated
                dst = uT1 if (l, w) == (1, 1) else tuple(v[:, :, SEQ:] if s == 0 else v[:, :, 0:SEQ] for v in uT)
                out.append((("ff" if w else "mix", l, s), h_ctx if s else h_lat, ready, mod_mul(l, w, s), mod_shift(l, w, s), dst))
            return out
        out_stored = sem("out_stored")

        def stream_ready(l, which):
            def ready(eng):
                if l == 0 and which == "attn":
                    eng.wait_ge(x_landed, 16)
                    return
                f = acc_at[("out1", l)] if which == "ffn" else acc_at[("down1", l - 1)]
                for i in range(4):
                    wait_drained(eng, "acc", f + i)
            return ready

        def mix_lhs(y):
            return lambda kt, tt: both(y, lambda v: v[:, kt, tt * P:(tt + 1) * P])

        block = ctx.enter_context(nc.Block())

        def norm_scalar(act, key, src, ready, gain, shift, dst):
            norm_act(act, key, src, ready)
            norm_high(act, key, gain, shift, dst)

        def first_norm(l, which):
            gain = lambda kt: col("ln_attn_g" if which == "attn" else "ln_ffn_g", KT * l + kt)
            return (which, l), h_lat, stream_ready(l, which), gain, None, hT

        @block.sync
        def _(sp):
            sp.dma_start(h_lat[:, :, :], I["x"][0].rearrange("(t p) d -> p t d", p=P)).then_inc(x_landed, 16)
            sp.dma_start(h_ctx[:, :, :], I["ctx_2"][0].rearrange("(t p) d -> p t d", p=P)).then_inc(ctx_landed, 16)
            for g in range(len(chunks)):
                if g == chunk_at["out2_0"] + 1:
                    scan_over(sp)
                if g >= RAW:
                    sp.wait_ge(*release[g - RAW])
                load(sp, g)
            ff1.updated(sp)
            sp.dma_start(out.rearrange("(t p) d -> p t d", p=P), h_lat[:, :, :]).then_inc(out_stored, 16)
            sp.wait_ge(out_stored, 16)

        @block.gpsimd
        def _(pool):
            setup_pool(pool)
            for l in range(DEPTH):
                norm_pool(pool, ("attn", l))
                qkv_pool(pool, l)
                subnorm_pool(pool, l)
                norm_pool(pool, ("ffn", l))
                up1_pool(pool, l)
            for key, *_ in mod_norms(0, 0):
                norm_pool(pool, key)
            kk_pool(pool)
            for d in range(2):
                for s in range(NCH):
                    chunk_pool(pool, d, s)
            rwkv_out_pool(pool)
            mix0.pool_gate(pool)
            mix0.pool_rstd(pool)
            for key, *_ in mod_norms(0, 1):
                norm_pool(pool, key)
            ff0.pool_gate(pool)
            ff0.pool_rstd(pool)
            for key, *_ in mod_norms(1, 0):
                norm_pool(pool, key)
            proj1_pool(pool)
            mix1.pool_gate(pool)
            mix1.pool_rstd(pool)
            for key, *_ in mod_norms(1, 1):
                norm_pool(pool, key)
            ff1.pool_gate(pool)
            ff1.pool_rstd(pool)

        @block.scalar
        def _(act):
            setup_act_dma(act)
            ahead_act(act, HIGH - 1)
            for l in range(DEPTH):
                norm_scalar(act, *first_norm(l, "attn"))
                qkv_act(act, l)
                if l == 0:
                    setup_bias_act(act)
                att[("att1", l)].scalar(act, subnorm_act(act, l, att[("att1", l)]))
                ahead_act(act, chunk_at[("out1", l)] + HIGH - 1)
                yT1_act(act, l)
                tok_walk(act, ahead_act, ("out1", l), KT, 2)
                norm_scalar(act, *first_norm(l, "ffn"))
                up1_act(act, l)
                tok_walk(act, ahead_act, ("down1", l), FT, 2)
            for norm in mod_norms(0, 0):
                norm_scalar(act, *norm)
            projA_act(act)
            projB_act(act)
            att_bl.scalar(act)
            att_bc.scalar(act)
            yTB_act(act)
            act.dma_start(lora[:, 0, :], I["a_w2_2"][0].rearrange("d l c -> (d l) c")).then_inc(lora_landed, 16)
            act.dma_start(lora[:, 1, :], I["a_a2_2"][0].rearrange("d l c -> (d l) c")).then_inc(lora_landed, 16)
            kk_act(act)
            for d in range(2):
                prep_act(act, d)
                for s in range(NCH):
                    chunk_act(act, d, s)
            scan_over(act)
            held[0] = False
            rwkv_out_act(act)
            ahead_act(act, chunk_at["out2_0"] + HIGH - 1)
            mix0.scalar_gate(act)
            mix0.scalar(act)
            for norm in mod_norms(0, 1):
                norm_scalar(act, *norm)
            ff0_scalar(act, ff0)
            near_dma(act)
            for norm in mod_norms(1, 0):
                norm_scalar(act, *norm)
            proj1_act(act)
            att_c.scalar(act)
            att_d.scalar(act)
            yT2_act(act)
            mix1.scalar_gate(act)
            mix1.scalar(act)
            for norm in mod_norms(1, 1):
                norm_scalar(act, *norm)
            hidden_act(act, *ff1_tiles)
            ff1.scalar_gate(act)
            ff1.scalar(act)

        @block.tensor
        def _(pe):
            setup_pe(pe)
            for l in range(DEPTH):
                norm_pe(pe, ("attn", l))
                qkv_pe(pe, l)
                if l == 0:
                    setup_bias_pe(pe)
                att[("att1", l)].tensor(pe)
                yT1_pe(pe, l, att[("att1", l)])
                out1_pe(pe, l)
                norm_pe(pe, ("ffn", l))
                up1_pe(pe, l)
                down1_pe(pe, l)
            for key, *_ in mod_norms(0, 0):
                norm_pe(pe, key)
            projA_pe(pe)
            projB_pe(pe)
            projB_wait(pe)
            att_bl.tensor(pe)
            att_bc.tensor(pe)
            yTB_pe(pe, (att_bl, att_bc))
            kk_pe(pe)
            for d in range(2):
                prep_pe(pe, d)
                for s in range(NCH):
                    chunk_pe(pe, d, s)
            rwkv_out_pe(pe)
            mix0.tensor_gate(pe)
            pe.wait_ge(yA_low, 4)
            for tt in (2, 3):
                wait_drained(pe, "tr", tr_at["yTB"] + tt)
            tok_gemm(pe, "out2_0", mix0.f0, KT, [ALL] * 2, mix_lhs(yT))
            for key, *_ in mod_norms(0, 1):
                norm_pe(pe, key)
            ff0_tensor(pe, ff0)
            for key, *_ in mod_norms(1, 0):
                norm_pe(pe, key)
            near_pe(pe)
            proj1_pe(pe)
            for n in (4, 5):
                wait_drained(pe, "tr", tr_at["proj1"] + n)
            for i in range(4, 8):
                wait_drained(pe, "acc", acc_at["near"] + i)
            att_c.tensor(pe)
            att_d.tensor(pe)
            yT2_pe(pe, (att_c, att_d))
            mix1.tensor_gate(pe)
            for g in (2, 3):
                wait_drained(pe, "tr", tr_at["yT1_2"] + g)
            tok_gemm(pe, "out2_1", mix1.f0, KT, [LAT] * 2, mix_lhs(yT2))
            for key, *_ in mod_norms(1, 1):
                norm_pe(pe, key)
            ff1_tensor(pe, ff1)

        @block.vector
        def _(dve):
            setup_dve(dve)
            ahead_dve(dve, HIGH - 1)
            for l in range(DEPTH):
                norm_dve(dve, *first_norm(l, "attn"))
                qkv_dve(dve, l)
                if l == 0:
                    setup_bias_dve(dve)
                att[("att1", l)].vector(dve, subnorm_dve(dve, l, att[("att1", l)]))
                if l == 1:
                    ada_gains(dve, att[("att1", l)], 0)
                ahead_dve(dve, chunk_at[("out1", l)] + HIGH - 1)
                yT1_dve(dve, l)
                add_dve(dve, ("out1", l), KT)
                norm_dve(dve, *first_norm(l, "ffn"))
                up1_dve(dve, l)
                add_dve(dve, ("down1", l), FT)
            dve.wait_ge(mod_ready, 2)
            for norm in mod_norms(0, 0):
                norm_dve(dve, *norm)
            projA_dve(dve)
            projB_dve(dve)
            att_bl.vector(dve)
            att_bc.vector(dve)
            ada_gains(dve, att_bc, 1)
            yTB_dve(dve)
            kk_dve(dve)
            for d in range(2):
                prep_dve(dve, d)
                for s in range(NCH):
                    chunk_dve(dve, d, s)
            scan_over(dve)
            held[1] = False
            rwkv_out_dve(dve)
            ahead_dve(dve, chunk_at["out2_0"] + HIGH - 1)
            mix0.vector(dve)
            for norm in mod_norms(0, 1):
                norm_dve(dve, *norm)
            ff0_vector(dve, ff0)
            for norm in mod_norms(1, 0):
                norm_dve(dve, *norm)
            near_dve(dve)
            proj1_dve(dve)
            att_c.vector(dve)
            att_d.vector(dve)
            yT2_dve(dve)
            mix1.vector(dve)
            for norm in mod_norms(1, 1):
                norm_dve(dve, *norm)
            hidden_dve(dve, *ff1_tiles)
            ff1.vector(dve)


_INS = ["x", "ln_attn_g", "w_in", "qk_norm_g", "diff_lambda", "diff_subln_g", "w_out", "ln_ffn_g", "w_up", "conv_w",
        "conv_b", "w_down", "rel_bias", "c_2", "ctx_2", "c_ctx_2", "w_ada_2", "b_ada_2", "g_pre_mix_2", "g_post_mix_2",
        "g_pre_ff_2", "g_post_ff_2", "w_in_even_2", "w_in_odd_2", "w_out_2", "w_ff1_2", "w_ff2_2", "a_mu_prev_2",
        "a_mu_next_2", "a_w0_2", "a_w2_2", "a_a0_2", "a_a2_2", "a_g2_2", "a_k_k_2", "a_k_a_2", "a_r_k_2", "a_gn_w_2",
        "a_gn_b_2", "b_sink_2", "c_rpb_2", "d_q_gain_2", "d_k_gain_2"]


def kernel(**inputs):
    import concourse.bacc as _bacc
    from concourse.bass_utils import run_bass_kernel_spmd as _run

    nc = _bacc.Bacc("TRN2", target_bir_lowering=False, num_devices=1)
    arrays, dram = {}, {}
    for name in _INS:
        a = np.ascontiguousarray(inputs[name])
        arrays[f"in_{name}"] = a
        dram[name] = nc.dram_tensor(f"in_{name}", a.shape, mybir.dt.from_np(a.dtype), kind="ExternalInput").ap()
    consts = []
    for name, a in (("const_keep", KEEP), ("const_first", FIRST), ("const_masks", MASKS)):
        arrays[name] = a
        consts.append(nc.dram_tensor(name, a.shape, mybir.dt.from_np(a.dtype), kind="ExternalInput").ap())
    out = nc.dram_tensor("out", (1, SEQ, D), F32, kind="ExternalOutput").ap()
    first_and_second_block(nc, dram, consts, out[0])
    r = _run(nc, [arrays], core_ids=[0])
    return r.results[0]["out"]
```

```python
import math
from contextlib import ExitStack

import numpy as np

import concourse.bass as bass
from concourse import mybir

F32 = mybir.dt.float32
U8 = mybir.dt.uint8
R32 = mybir.dt.float32r
ALU = mybir.AluOpType
ACT = mybir.ActivationFunctionType
AX_X = mybir.AxisListType.X

P = 128
D = 1024
KT = D // P
SEQ = 256
TT = SEQ // P
DEPTH = 2
HD = 64
REL_BUCKETS = 32
N_BIAS = 12
D_FF = 2816
FT = D_FF // P
D_FF2 = 4096
FT2 = D_FF2 // P
CONV = 3
N_ADA = 6 * D // 512
A_IN = 1920
AT = A_IN // P
EPS = 1e-6
GN_EPS = 64e-5
NEG = -1e30
SCALE = HD ** -0.5
LAMBDA_INIT = [0.8 - 0.6 * math.exp(-0.3 * i) for i in range(DEPTH)]
CH = 64
NCH = 2 * SEQ // CH
LEVELS = 6
DECAY = math.exp(-0.5)
RAW = 4
HIGH = 3
SLOT = 4 * 512
GRID_W, NA_KH, NA_KW = 64, 8, 16


def rel_bucket(dist):
    n = np.maximum(dist, 0)
    nf = np.maximum(n, 16).astype(np.float32)
    large = 16 + (np.log(nf / np.float32(16)) / np.float32(math.log(64.0)) * np.float32(16)).astype(np.int32)
    return np.where(n < 16, n, np.minimum(large, 31))


def constants():
    f = np.float32
    keep, first = {}, {}
    eye = np.eye(P, dtype=f)
    keep["ident"] = eye
    keep["flip64"] = np.kron(np.eye(2, dtype=f), np.eye(64, dtype=f)[::-1])
    keep["ones"] = np.ones((P, P), f)
    head = np.arange(P) // 64
    same = (head[:, None] == head[None, :])
    keep["head_ones"] = same.astype(f)
    s, t = np.arange(P)[:, None] % 64, np.arange(P)[None, :] % 64
    for d, (strict, incl) in enumerate([(s < t, s <= t), (s > t, s >= t)]):
        keep[f"tri{d}"] = np.concatenate([incl & same, strict & same, incl & same], 1).astype(f)
    keep["pairs"] = np.concatenate([np.arange(P)[:, None] % HD // (1 << lev) == 2 * np.arange(HD >> lev + 1) + i
                                    for i in range(2) for lev in range(LEVELS)], 1).astype(f)
    edge = np.ones(2 * SEQ + 2, f)
    edge[::CH] = 0
    keep["scan_edge"] = np.broadcast_to(edge, (P, edge.size))
    tok = np.arange(SEQ)
    inv = (np.float32(10000.0) ** (-np.arange(16, dtype=f) / f(16))).astype(f)
    row, colm = (tok // GRID_W).astype(f)[:, None] * inv, (tok % GRID_W).astype(f)[:, None] * inv
    cos = np.concatenate([np.cos(row), np.cos(row), np.cos(colm), np.cos(colm)], 1).astype(f)
    sin = np.concatenate([-np.sin(row), np.sin(row), -np.sin(colm), np.sin(colm)], 1).astype(f)
    tile = lambda a: a.reshape(TT, P, -1).transpose(1, 0, 2).reshape(P, -1)
    keep["cos"], keep["sin"] = tile(cos), tile(sin)
    q, k = np.arange(SEQ)[:, None], np.arange(SEQ)[None, :]
    keep["band"] = tile(np.where(np.abs(q - k) <= 128, 0, NEG).astype(f))
    qc, kc = q % GRID_W, k % GRID_W
    start = np.clip(qc - NA_KW // 2, 0, GRID_W - NA_KW)
    keep["near"] = tile(np.where((kc >= start) & (kc < start + NA_KW), 0, NEG).astype(f))

    first["flip"] = eye[::-1]
    first["causal"] = np.where(np.arange(SEQ)[None, :] <= P + np.arange(P)[:, None], 0, NEG).astype(f)
    hot = np.zeros((P, 384), f)
    hot[rel_bucket(255 - np.arange(384)), np.arange(384)] = 1
    first["bucket_hot"] = hot
    return keep, first


def packed(parts):
    at, where = 0, {}
    for name, a in parts.items():
        where[name] = (at, a.shape[1])
        at += a.shape[1]
    return np.ascontiguousarray(np.concatenate(list(parts.values()), 1)), where


KEEP, KEEP_AT = packed(constants()[0])
FIRST, FIRST_AT = packed(constants()[1])

PARAM_GROUPS = [
    [("ln_attn_g", 16), ("ln_ffn_g", 16), ("diff_subln_g", 2), ("qk_norm_g", 8), ("g_pre_mix_2", 16),
     ("g_post_mix_2", 16), ("g_pre_ff_2", 16), ("g_post_ff_2", 16), ("d_q_gain_2", 1), ("d_k_gain_2", 1),
     ("c_2", 8), ("c_ctx_2", 8)],
    [("a_mu_prev_2", 15), ("a_mu_next_2", 15), ("a_w0_2", 8), ("a_a0_2", 8), ("a_k_k_2", 4), ("a_k_a_2", 4),
     ("a_r_k_2", 4), ("a_gn_w_2", 4), ("a_gn_b_2", 4)],
    [("b_ada_2", 96)],
    [("conv_b", 88)],
    [("conv_w", 128)], [("conv_w", 128)], [("conv_w", 8)],
]
HALF_ROWS = ("qk_norm_g", "d_q_gain_2", "d_k_gain_2")


def first_and_second_block(nc, I, consts, out):
    with ExitStack() as ctx:
        def sb(name, shape, dt=F32):
            return ctx.enter_context(nc.sbuf_tensor(name, shape, dt))

        made = {}

        def sem(name):
            if name not in made:
                made[name] = ctx.enter_context(nc.semaphore(name))
            return made[name]

        h_lat = sb("h_lat", [P, TT, D])
        h_ctx = sb("h_ctx", [P, TT, D])
        pcol = sb("pcol", [P, len(PARAM_GROUPS), P])
        keep = sb("keep", [P, KEEP.shape[1]])
        pairs8 = sb("pairs8", [P, 2, HD - 1], U8)
        mod = sb("mod", [P, DEPTH, 6 * KT, 2])
        mod_gain = sb("mod_gain", [P, DEPTH, 2, KT, 2])
        mod_gate = sb("mod_gate", [P, DEPTH, 2, KT, 2])
        silu_c = sb("silu_c", [P, KT, 2])
        bcast = sb("bcast", [P, 10])
        neg_sink = sb("neg_sink", [P, 8])
        stat = sb("stat", [P, 1460])
        n_arena = 28424
        at_arena = -(-nc.sbuf_base // 32) * 32
        arena = sb("arena", [P, n_arena + (HIGH + RAW) * SLOT])
        edges = [1024 + SLOT * i for i in range(n_arena // SLOT + 1) if 1024 + SLOT * i < n_arena]
        edges += [n_arena + SLOT * i for i in range(HIGH + RAW + 1)]
        windows = [nc.alloc_sbuf_tensor_at(f"rounded{i}", [P, b - a], R32, offset=at_arena + 4 * a)
                   for i, (a, b) in enumerate(zip(edges, edges[1:]))]
        half = sb("half", [P, 4 * NCH])
        banks = [ctx.enter_context(nc.psum_tensor(f"acc{i}", [P, 512], F32)) for i in range(4)]
        trs = [ctx.enter_context(nc.psum_tensor(f"tr{i}", [P, 512], F32)) for i in range(2)]
        scs = [ctx.enter_context(nc.psum_tensor(f"sc{i}", [P, 512], F32)) for i in range(2)]
        t5_scratch = nc.dram_tensor("t5_scratch", [N_BIAS, 384], F32, kind="Internal").ap()

        def const(name):
            at, n = KEEP_AT[name]
            return keep[:, at:at + n]

        ident, head_ones, flip64, ones = const("ident"), const("head_ones"), const("flip64"), const("ones")

        stat_at = [0]

        def stats(n):
            at = stat_at[0]
            stat_at[0] += n
            assert stat_at[0] <= 1460
            return stat[:, at:at + n]

        class Region:

            def __init__(self, at=0, slots=0):
                self.at, self.end = at, n_arena + slots * SLOT

            def take(self, *shape):
                n = int(np.prod(shape))
                v = arena[:, self.at:self.at + n]
                self.at += n
                assert self.at <= self.end, self.at
                if len(shape) == 2:
                    v = v.rearrange("p (a b) -> p a b", a=shape[0])
                elif len(shape) == 3:
                    v = v.rearrange("p (a b c) -> p a b c", a=shape[0], b=shape[1])
                elif len(shape) == 4:
                    v = v.rearrange("p (a b c d) -> p a b c d", a=shape[0], b=shape[1], c=shape[2])
                return v

        param_at = {}
        for g, group in enumerate(PARAM_GROUPS):
            r = 0
            for name, n in group:
                if name != "conv_w":
                    param_at[name] = (g, r)
                r += n

        def col(name, i=0, n=1):
            if name == "conv_w":
                return pcol[:, 4 + i // P, i % P:i % P + n]
            g, r = param_at[name]
            return pcol[:, g, r + i:r + i + n]

        acc_at, tr_at, sc_at = {}, {}, {}
        fills = [0, 0, 0]

        def stage(key, acc=0, tr=0, sc=0):
            acc_at[key], tr_at[key], sc_at[key] = fills
            fills[0] += acc
            fills[1] += tr
            fills[2] += sc

        acc_full, tr_full, sc_full = sem("acc_full"), sem("tr_full"), sem("sc_full")
        acc_drained = [sem(f"acc_drained{i}") for i in range(4)]
        tr_drained = [sem(f"tr_drained{i}") for i in range(2)]
        sc_drained = [sem(f"sc_drained{i}") for i in range(2)]
        POOLS = {"acc": (banks, acc_full, acc_drained), "tr": (trs, tr_full, tr_drained), "sc": (scs, sc_full, sc_drained)}

        def bank(pool, f):
            return POOLS[pool][0][f % len(POOLS[pool][0])]

        def claim(pe, pool, f):
            b, _, drained = POOLS[pool]
            if f >= len(b):
                pe.wait_ge(drained[f % len(b)], f // len(b))
            return b[f % len(b)]

        def filled(eng, pool, f):
            b, full, _ = POOLS[pool]
            eng.wait_ge(full, f + 1)
            return b[f % len(b)]

        def drain(pool, f):
            _, _, drained = POOLS[pool]
            return drained[f % len(drained)]

        def wait_drained(eng, pool, f):
            _, _, drained = POOLS[pool]
            eng.wait_ge(drained[f % len(drained)], f // len(drained) + 1)

        chunks = []
        release = []
        chunk_at = {}
        partial = [0]
        chunk_read = sem("chunk_read")
        whole = set()

        def r32(v):
            row = arena.shape[1]
            p0, at = v.offset // row, v.offset % row
            last = at + sum(step * (n - 1) for step, n in list(v.ap)[1:])
            i = max(n for n, a in enumerate(edges) if a <= at)
            assert last < edges[i + 1], (at, last)
            width = edges[i + 1] - edges[i]
            return bass.AP(tensor=windows[i][:, :].tensor, offset=p0 * width + at - edges[i], ap=[[width, v.ap[0][1]]] + list(v.ap)[1:])


        def plan_tok(key, w, kts, f0, blocks):
            chunk_at[key] = len(chunks)
            n = w.shape[1]
            view = w.rearrange("(k p) n -> p k n", p=P)
            for c, tts in enumerate(blocks):
                f0 += len(tts)
                for k0 in range(0, kts, 4):
                    chunks.append(view[:, k0:min(k0 + 4, kts), 512 * c:min(512 * c + 512, n)])
                    if k0 + 4 >= kts:
                        release.append((acc_full, f0))
                    else:
                        partial[0] += 1
                        release.append((chunk_read, partial[0]))

        def plan_feat(key, w, cols, fills_of):
            chunk_at[key] = len(chunks)
            view = w.rearrange("(k p) n -> p k n", p=P)
            for (c0, c1), f in zip(cols, fills_of):
                chunks.append(view[:, :, c0:c1])
                release.append((acc_full, f))

        def plan_up(l):
            key = ("up1", l)
            up = I["w_up"][l].rearrange("(k p) (s n) -> p k s n", p=P, s=2)
            chunk_at[key] = len(chunks)
            for i in range(FT):
                chunks.append(up[:, :, :, i * P:(i + 1) * P])
                release.append((acc_full, acc_at[key] + i + 1))

        ada_chunk = {}

        def plan_ada(blocks, fill_of):
            for n, b in enumerate(blocks):
                view = I["w_ada_2"][b // N_ADA].rearrange("(k p) n -> p k n", p=P)
                c = 512 * (b % N_ADA)
                ada_chunk[b] = len(chunks)
                for k0 in (0, 4):
                    chunks.append(view[:, k0:k0 + 4, c:c + 512])
                    whole.add(len(chunks) - 1)
                partial[0] += 1
                release.extend([(chunk_read, partial[0]), (sc_full, fill_of(n) + 1)])

        def is_up(g):
            return len(chunks[g].shape) == 4

        def shaped(place, g):
            if is_up(g):
                return place.rearrange("p (k s n) -> p k s n", k=KT, s=2)
            k, n = chunks[g].shape[1], chunks[g].shape[2]
            return place[:, 0:k * n].rearrange("p (k n) -> p k n", k=k)

        def raw_slot(g):
            at = n_arena + (HIGH + (g - chunk_at["out2_0"] + RAW - 1) % RAW) * SLOT
            return arena[:, at:at + SLOT]

        def high_slot(g):
            at = n_arena + (split_no[g] % HIGH) * SLOT
            return arena[:, at:at + SLOT]

        weights_landed = [sem(f"weights_landed{i}") for i in range(RAW)]
        high_made, split_made = sem("high_made"), sem("split_made")
        split_no, split_chunks = {}, []

        def wait_landed(eng, g):
            dmas = sum(2 if is_up(c) else 1 for c in range(g % RAW, g + 1, RAW))
            eng.wait_ge(weights_landed[g % RAW], 16 * dmas)

        def load(sp, g):
            dst, src = shaped(raw_slot(g), g), chunks[g]
            for d, s in [(dst[:, :, s, :], src[:, :, s, :]) for s in range(2)] if is_up(g) else [(dst, src)]:
                sp.dma_start(d, s).then_inc(weights_landed[g % RAW], 16)

        splits = {"high": 0, "low": 0}
        held = [True, True]

        def size(g):
            return int(np.prod(chunks[g].shape[1:]))

        def ahead_act(act, g):
            g = min(g, chunk_at["out2_0"] - 1) if held[0] else g
            while splits["high"] < len(split_chunks) and split_chunks[splits["high"]] <= g:
                n = splits["high"]
                c = split_chunks[n]
                wait_landed(act, c)
                if n >= HIGH:
                    act.wait_ge(*release[split_chunks[n - HIGH]])
                act.activation(r32(high_slot(c)[:, 0:size(c)]), raw_slot(c)[:, 0:size(c)], ACT.Copy).then_inc(high_made, 1)
                splits["high"] += 1

        def ahead_dve(dve, g):
            g = min(g, chunk_at["out2_0"] - 1) if held[1] else g
            while splits["low"] < len(split_chunks) and split_chunks[splits["low"]] <= g:
                n = splits["low"]
                c = split_chunks[n]
                dve.wait_ge(high_made, n + 1)
                w = raw_slot(c)[:, 0:size(c)]
                dve.tensor_tensor(r32(w), w, r32(high_slot(c)[:, 0:size(c)]), ALU.subtract).then_inc(split_made, 1)
                splits["low"] += 1

        def parts(pe, g):
            pe.wait_ge(split_made, split_no[g] + 1)
            return shaped(high_slot(g), g), shaped(raw_slot(g), g)

        def both(pair, cut):
            return tuple(r32(cut(x)) for x in pair)

        def mm3(pe, ps, a, b, first, last):
            (ah, al), (bh, bl) = a, b
            pe.matmul(ps, ah, bh, start=first, stop=False)
            pe.matmul(ps, ah, bl, start=False, stop=False)
            return pe.matmul(ps, al, bh, start=False, stop=last)

        LAT = [0, 1]
        ALL = [0, 1, 2, 3]
        LATS = [2, 3]
        stage("params", tr=1)
        norm_n = {}

        def plan_norm(key):
            norm_n[key] = len(norm_n)
            stage(("norm", key), tr=4)

        def pairs(ncols):
            return [(c, min(c + 256, ncols)) for c in range(0, ncols, 256)]

        for l in range(DEPTH):
            plan_norm(("attn", l))
            if l == 0:
                stage("bcast", acc=1)
                stage("t5", acc=1)
            stage(("qkv", l), acc=12, tr=8)
            plan_tok(("qkv", l), I["w_in"][l], KT, acc_at[("qkv", l)], [LAT] * 6)
            if l == 0:
                stage("t5_rows", acc=N_BIAS // 2)
                stage("later_params", tr=2)
            stage(("att1", l), acc=32, tr=16 + 8, sc=16 + 8)
            plan_ada(range(8 * l, 8 * l + 8), lambda n: sc_at[("att1", l)] + 3 * n)
            stage(("yT1", l), tr=4)
            stage(("out1", l), acc=4)
            plan_tok(("out1", l), I["w_out"][l], KT, acc_at[("out1", l)], [LAT] * 2)
            plan_norm(("ffn", l))
            stage(("up1", l), acc=FT)
            plan_up(l)
            stage(("down1", l), acc=4)
            plan_tok(("down1", l), I["w_down"][l], FT, acc_at[("down1", l)], [LAT] * 2)

        def pair_fills(key, n):
            return [acc_at[key] + min(i + 2, n) for i in range(0, n, 2)]

        plan_norm(("mix", 0, 1))
        plan_norm(("mix", 0, 0))
        stage("projA", acc=AT)
        plan_feat("projA", I["w_in_even_2"][0][:, 0:A_IN], pairs(A_IN), pair_fills("projA", AT))
        stage("projB", acc=8, tr=8)
        plan_tok("projB", I["w_in_even_2"][0][:, A_IN:A_IN + 768], KT, acc_at["projB"], [ALL] * 2)
        stage("attBl", acc=16, tr=16 + 4, sc=8 + 4)
        plan_ada(range(16, 20), lambda n: sc_at["attBl"] + 3 * n)
        stage("attBc", acc=16, tr=8 + 4, sc=8 + 4)
        plan_ada(range(20, 24), lambda n: sc_at["attBc"] + 3 * n)
        stage("yTB", tr=4)
        stage("kk", acc=1, tr=4)
        stage("prep", acc=16)
        for s in range(NCH):
            stage(("step", s), acc=12, tr=6, sc=2 + 4 * (LEVELS - 1))
        stage("gate_mix0", acc=4)
        stage("rwkv_out", acc=8, tr=8)
        stage("post_mix0", acc=8)
        plan_tok("out2_0", I["w_out_2"][0], KT, acc_at["post_mix0"], [ALL] * 2)
        plan_norm(("ff", 0, 1))
        plan_norm(("ff", 0, 0))
        EIGHTHS, ET = 8, FT2 // 8

        def plan_ff1(e):
            stage(("ff1", e), acc=ET)
            plan_feat(("ff1", e), I["w_ff1_2"][0][:, e * ET * P:(e + 1) * ET * P], pairs(ET * P), pair_fills(("ff1", e), ET))

        def plan_ff2(e):
            stage(("ff2", e), acc=8)
            plan_tok(("ff2", e), I["w_ff2_2"][0][e * ET * P:(e + 1) * ET * P, :], ET, acc_at[("ff2", e)], [ALL] * 2)

        plan_ff1(0)
        stage("gate_ff0", acc=4)
        for e in range(EIGHTHS):
            if e + 1 < EIGHTHS:
                plan_ff1(e + 1)
            plan_ff2(e)
        plan_norm(("mix", 1, 1))
        plan_norm(("mix", 1, 0))
        stage("near", acc=8)
        stage("proj1", acc=4 + 4 + 4 + 2 + 4, tr=6)
        f = acc_at["proj1"]
        plan_feat("proj1", I["w_in_odd_2"][0][:, 0:1024], pairs(1024), [f + 2, f + 4, f + 6, f + 8])
        chunk_at["proj1_k"] = chunk_at["proj1"] + 2
        plan_tok("proj1_tok", I["w_in_odd_2"][0][:, 1024:2304], KT, f + 8, [ALL, LATS, ALL])
        stage("gate_mix1", acc=2)
        stage("attC", acc=16, tr=16, sc=8)
        stage("attD", acc=16, tr=16, sc=8)
        stage("yT1_2", tr=4)
        stage("post_mix1", acc=4)
        plan_tok("out2_1", I["w_out_2"][1], KT, acc_at["post_mix1"], [LAT] * 2)
        plan_norm(("ff", 1, 0))
        stage("ff1_1", acc=FT2)
        plan_feat("ff1_1", I["w_ff1_2"][1], pairs(D_FF2), pair_fills("ff1_1", FT2))
        stage("gate_ff1", acc=2)
        stage("post_ff1", acc=4)
        plan_tok("ff2_1", I["w_ff2_2"][1], FT2, acc_at["post_ff1"], [LAT] * 2)

        split_chunks += [g for g in range(len(chunks)) if g not in whole]
        split_no.update({g: n for n, g in enumerate(split_chunks)})

        r1 = Region()
        t5_bias = r1.take(N_BIAS, SEQ)
        xn = r1.take(TT, D)
        at1 = r1.at
        hT = r1.take(KT, SEQ), r1.take(KT, SEQ)
        yT1 = hT
        at_gate = r1.at
        qkT = r1.take(4, 4, SEQ)
        vv = r1.take(2, TT, 512)
        qn = r1.take(2, 512)
        sq = r1.take(2, 512)
        at_att = r1.at
        prob = r1.take(2, 2, 512)
        probT = r1.take(2, 1024)
        y1 = r1.take(TT, D)
        mod_row = r1.take(512)
        r1b = Region(at_gate)
        gT = r1b.take(FT, SEQ), r1b.take(FT, SEQ)
        conv = r1b.take(2, 2, SEQ)
        act_g = r1b.take(2, SEQ)
        r0 = Region(at_att)
        prow = r0.take(len(PARAM_GROUPS), P)
        first = r0.take(FIRST.shape[1])
        lrow = r0.take(520)
        lprod = r0.take(2 * DEPTH * HD)
        lsum = r0.take(8)
        relb = r0.take(N_BIAS)
        t5_vec = r0.take(384)
        hankel = r0.take(N_BIAS, SEQ)

        def first_const(name):
            at, n = FIRST_AT[name]
            return first[:, at:at + n]

        norm_ss = norm_ms = norm_rs = stats(2 * 16)
        norm_summed, norm_mean, norm_rstd, norm_xn = (
            sem("norm_summed"), sem("norm_mean"), sem("norm_rstd"), sem("norm_xn"))
        norm_high_set, norm_done = sem("norm_high_set"), sem("norm_done")
        norm_highs = [0]
        dve_chain = sem("dve_chain")
        chain = [0]

        def link(dve, ins):
            chain[0] += 1
            ins.then_inc(dve_chain, 1)
            dve.wait_ge(dve_chain, chain[0])

        def norm_act(act, key, src, ready, gain, shift, dst):
            n = norm_n[key]
            for tt in range(TT):
                ready(act, tt)
                act.activation(dst[0][:, 4 * tt:4 * tt + 4, :], src[:, tt, :].rearrange("p (a b) -> p a b", b=SEQ), ACT.Square,
                               accum_out=norm_ss[:, 2 * n + tt:2 * n + tt + 1]).then_inc(norm_summed, 1)

        def norm_pool(pool, key):
            n = norm_n[key]
            pool.wait_ge(norm_mean, n + 1)
            pool.tensor_tensor(norm_rs[:, 2 * n:2 * n + 2], norm_ms[:, 2 * n:2 * n + 2], half[:, 0:2],
                               ALU.pow).then_inc(norm_rstd, 1)

        def norm_high(act, key, src, ready, gain, shift, dst):
            for g in range(4):
                f = tr_at[("norm", key)] + g
                if shift and g % 2 == 0:
                    wait_drained(act, "tr", f)
                else:
                    ps = filled(act, "tr", f)
                for i in range(2):
                    kt = 2 * g + i
                    hi, lo = r32(dst[0][:, kt, :]), dst[1][:, kt, :]
                    if shift and g % 2 == 0:
                        ins = act.activation(hi, lo, ACT.Copy)
                    elif shift:
                        x = ps[:, i * SEQ:(i + 1) * SEQ]
                        act.activation(lo, x, ACT.Identity, bias=shift(kt), scale=gain(kt))
                        ins = act.activation(hi, x, ACT.Identity, bias=shift(kt), scale=gain(kt))
                    else:
                        ins = act.activation(hi, ps[:, i * SEQ:(i + 1) * SEQ], ACT.Identity, scale=gain(kt))
                ins.then_inc(norm_high_set if not shift or g % 2 == 0 else drain("tr", f), 1)

        def norm_dve(dve, key, src, ready, gain, shift, dst):
            n = norm_n[key]
            dve.wait_ge(norm_summed, 2 * n + 2)
            dve.tensor_scalar(norm_ms[:, 2 * n:2 * n + 2], norm_ss[:, 2 * n:2 * n + 2], 1.0 / D, EPS,
                              ALU.mult, ALU.add).then_inc(norm_mean, 1)
            ready(dve)
            if n:
                dve.wait_ge(tr_full, tr_at[("norm", [k for k in norm_n if norm_n[k] == n - 1][0])] + 4)
            dve.wait_ge(norm_rstd, n + 1)
            for tt in range(TT):
                dve.tensor_scalar(xn[:, tt, :], src[:, tt, :], norm_rs[:, 2 * n + tt:2 * n + tt + 1], None,
                                  ALU.mult).then_inc(norm_xn, 1)
            for g in range(5 if shift else 4):
                f = tr_at[("norm", key)] + g
                if shift and g in (0, 2):
                    ps = filled(dve, "tr", f)
                    for i in range(2):
                        kt = 2 * g + i
                        ins = dve.tensor_scalar(dst[1][:, kt, :], ps[:, i * SEQ:(i + 1) * SEQ], gain(kt), shift(kt), ALU.mult, ALU.add)
                    ins.then_inc(drain("tr", f), 1)
                if shift and g:
                    if g % 2:
                        norm_highs[0] += 1
                        dve.wait_ge(norm_high_set, norm_highs[0])
                    else:
                        wait_drained(dve, "tr", f - 1)
                    for i in range(2):
                        hi, lo = (v[:, 2 * g - 2 + i, :] for v in dst)
                        ins = dve.tensor_tensor(r32(lo), lo, r32(hi), ALU.subtract)
                    ins.then_inc(norm_done, 1)
                if not shift:
                    norm_highs[0] += 1
                    dve.wait_ge(norm_high_set, norm_highs[0])
                    for i in range(2):
                        kt = 2 * g + i
                        hi, lo = (v[:, kt, :] for v in dst)
                        dve.scalar_tensor_tensor(r32(lo), bank("tr", f)[:, i * SEQ:(i + 1) * SEQ], gain(kt), r32(hi), ALU.mult, ALU.subtract)\
                           .then_inc(drain("tr", f) if i else norm_done, 1)

        def norm_pe(pe, key):
            n = norm_n[key]
            for g in range(4):
                f = tr_at[("norm", key)] + g
                ps = claim(pe, "tr", f)
                for i in range(2):
                    for tt in range(TT):
                        if g == 0 and i == 0:
                            pe.wait_ge(norm_xn, 2 * n + tt + 1)
                        kt = 2 * g + i
                        ins = pe.transpose(ps[:, i * SEQ + tt * P:i * SEQ + (tt + 1) * P],
                                           xn[:, tt, kt * P:(kt + 1) * P], ident)
                ins.then_inc(tr_full, 1)

        def norm_wait(pe, key):
            pe.wait_ge(norm_done, 4 * norm_n[key] + 4)
            wait_drained(pe, "tr", tr_at[("norm", key)] + 3)

        def tok_gemm(pe, key, f, kts, blocks, lhsT, ready=None):
            g = chunk_at[key]
            for tts in blocks:
                for k0 in range(0, kts, 4):
                    w = parts(pe, g)
                    kn, width = chunks[g].shape[1], chunks[g].shape[2]
                    if ready:
                        ready(k0 + kn)
                    for n, tt in enumerate(tts):
                        ps = claim(pe, "acc", f + n) if k0 == 0 else bank("acc", f + n)
                        for k in range(kn):
                            ins = mm3(pe, ps[:, 0:width], lhsT(k0 + k, tt), both(w, lambda v: v[:, k, :]),
                                      k0 + k == 0, k0 + k == kts - 1)
                        if k0 + kn == kts:
                            ins.then_inc(acc_full, 1)
                    if k0 + kn < kts:
                        ins.then_inc(chunk_read, 1)
                    g += 1
                f += len(tts)

        def tok_walk(eng, ahead, key, kts, blocks, evacuate=None, last=True):
            g = chunk_at[key]
            for b in range(blocks):
                n = -(-kts // 4)
                for i in range(n - 1):
                    ahead(eng, g + i + HIGH)
                if evacuate:
                    evacuate(b)
                if last or b + 1 < blocks:
                    ahead(eng, g + n - 1 + HIGH)
                g += n

        def feat_gemm(pe, key, f, n, rhs):
            for i in range(n):
                if i % 2 == 0:
                    w = parts(pe, chunk_at[key] + i // 2)
                ps = claim(pe, "acc", f + i)
                for kt in range(KT):
                    x = rhs(kt)
                    ins = mm3(pe, ps[:, 0:x[0].shape[1]], both(w, lambda v: v[:, kt, (i % 2) * P:(i % 2 + 1) * P]), x,
                              kt == 0, kt == KT - 1)
                ins.then_inc(acc_full, 1)

        att_max, att_comb, att_sunk = sem("att_max"), sem("att_comb"), sem("att_sunk")
        att_units = [0]
        sunk_units = [0]

        class Attention:

            def __init__(self, key, n, q, k, width, v, y, prob, probT, bias=None, sink=None, neg_lam=None, diff=lambda u: False, ada=None, following=None):
                self.key, self.n, self.q, self.k, self.width, self.v, self.y = key, n, q, k, width, v, y
                self.prob, self.probT, self.bias, self.sink, self.neg_lam, self.diff = prob, probT, bias, sink, neg_lam, diff
                self.following = following
                self.ada = list(ada) if ada is not None else []
                self.sc = [sc_at[key] + u + (u // 2 + 1 if self.ada else 0) for u in range(n)]
                self.base = att_units[0]
                att_units[0] += n
                self.sunk = sunk_units[0]
                if sink:
                    sunk_units[0] += n
                self.neg_max, self.total, self.recip = (stats(2 * n) for _ in range(3))
                self.extra = stats(2 * n) if sink else None
                self.mix = stats(n) if neg_lam is not None else None
                self.tr, self.ada_tr = [], []
                f = tr_at[key]
                for u in range(n + 1):
                    if self.ada and u % 2 == 0 and u >= 2:
                        self.ada_tr.append(f)
                        f += 1
                    if u < n:
                        blocks = (1 if diff(u) else 2) * (width(u) // P)
                        self.tr.append(range(f, f + -(-blocks // 4)))
                        f += -(-blocks // 4)

            def ada_fill(self, i):
                return sc_at[self.key] + 3 * i

            def banks_of(self, u):
                return [acc_at[self.key] + 2 * u + m for m in range(2)]

            def blocks(self, u):
                return [(m, kb) for m in range(1 if self.diff(u) else 2) for kb in range(self.width(u) // P)]

            def scores(self, pe, u):
                for m, f in enumerate(self.banks_of(u)):
                    ps = claim(pe, "acc", f)
                    pe.matmul(ps[:, 0:self.width(u)], self.q(u, m), self.k(u, m), start=True, stop=True).then_inc(acc_full, 1)

            def turn(self, pe, u):
                pe.wait_ge(att_comb, self.base + u + 1)
                b = self.blocks(u)
                for i, f in enumerate(self.tr[u]):
                    ps = claim(pe, "tr", f)
                    for n, (m, kb) in enumerate(b[4 * i:4 * i + 4]):
                        ins = pe.transpose(ps[:, n * P:(n + 1) * P], self.prob[:, u % 2, m, kb * P:(kb + 1) * P], ident)
                    ins.then_inc(tr_full, 1)

            def values(self, pe, u):
                for f in self.tr[u]:
                    wait_drained(pe, "tr", f)
                ps = claim(pe, "sc", self.sc[u])
                b = self.blocks(u)
                for n, (m, kb) in enumerate(b):
                    x = self.v(u, m, kb)
                    e = x.shape[1]
                    ins = pe.matmul(ps[:, m * e:(m + 1) * e], self.probT[:, u % 2, n * P:(n + 1) * P], x,
                                    start=(kb == 0), stop=(kb == self.width(u) // P - 1))
                ins.then_inc(sc_full, 1)

            def tensor(self, pe):
                self.scores(pe, 0)
                for u in range(self.n):
                    if u + 1 < self.n:
                        self.scores(pe, u + 1)
                    if u >= 1:
                        self.values(pe, u - 1)
                    if self.ada and u % 2 == 0:
                        if u:
                            ada_turn(pe, self, u // 2 - 1)
                        ada_pe(pe, self, u // 2)
                    self.turn(pe, u)
                if self.ada:
                    ada_turn(pe, self, len(self.ada) - 1)
                self.values(pe, self.n - 1)

            def maxima(self, dve, u):
                w = self.width(u)
                ps = [filled(dve, "acc", f) for f in self.banks_of(u)]
                if self.bias:
                    for m in range(2):
                        c0, b = self.bias(u, m)
                        ins = dve.tensor_tensor(ps[m][:, c0:w], ps[m][:, c0:w], b, ALU.add)
                    link(dve, ins)
                for m in range(2):
                    ins = dve.tensor_reduce(self.neg_max[:, 2 * u + m:2 * u + m + 1], ps[m][:, 0:w], AX_X, ALU.max, negate=True)
                if self.sink:
                    link(dve, ins)
                    h = self.sink(u)
                    ins = dve.tensor_tensor(self.neg_max[:, 2 * u:2 * u + 2], self.neg_max[:, 2 * u:2 * u + 2],
                                            neg_sink[:, h:h + 2], ALU.min)
                ins.then_inc(att_max, 1)

            def combine(self, dve, u):
                for f in self.banks_of(u):
                    wait_drained(dve, "acc", f)
                total, recip = self.total[:, 2 * u:2 * u + 2], self.recip[:, 2 * u:2 * u + 2]
                if self.sink:
                    dve.wait_ge(att_sunk, 2 * (self.sunk + u) + 2)
                    link(dve, dve.tensor_tensor(total, total, self.extra[:, 2 * u:2 * u + 2], ALU.add))
                ins = dve.reciprocal(recip, total)
                if self.diff(u):
                    link(dve, ins)
                    mix = self.mix[:, u:u + 1]
                    link(dve, dve.scalar_tensor_tensor(mix, total[:, 0:1], recip[:, 1:2], self.neg_lam, ALU.mult, ALU.mult))
                    w = self.width(u)
                    ins = dve.scalar_tensor_tensor(self.prob[:, u % 2, 0, 0:w], self.prob[:, u % 2, 1, 0:w], mix,
                                                   self.prob[:, u % 2, 0, 0:w], ALU.mult, ALU.add)
                ins.then_inc(att_comb, 1)

            def outputs(self, dve, u):
                f = self.sc[u]
                ps = filled(dve, "sc", f)
                if self.diff(u):
                    ins = dve.tensor_scalar(self.y(u), ps[:, 0:P], self.recip[:, 2 * u:2 * u + 1], None, ALU.mult)
                else:
                    ins = dve.tensor_tensor(self.y(u).rearrange("p (m e) -> p m e", m=2),
                                            ps[:, 0:P].rearrange("p (m e) -> p m e", m=2),
                                            self.recip[:, 2 * u:2 * u + 2].unsqueeze(2).broadcast_to([P, 2, HD]), ALU.mult)
                ins.then_inc(drain("sc", f), 1)

            def vector(self, dve, hook=None):
                for u in range(self.n + 2):
                    if 1 <= u <= self.n:
                        self.combine(dve, u - 1)
                    if u < self.n:
                        self.maxima(dve, u)
                    if u == self.n and self.following is not None:
                        ahead_dve(dve, self.following)
                    if u >= 2:
                        self.outputs(dve, u - 2)
                    if self.ada and u % 2 == 1 and u >= 3:
                        ada_dve(dve, self, u // 2 - 1)
                    if hook:
                        hook(u)

            def exps(self, act, u):
                w = self.width(u)
                act.wait_ge(att_max, self.base + u + 1)
                if u >= 2:
                    act.wait_ge(tr_full, self.tr[u - 2][-1] + 1)
                for m, f in enumerate(self.banks_of(u)):
                    act.activation(self.prob[:, u % 2, m, 0:w], bank("acc", f)[:, 0:w], ACT.Exp,
                                   bias=self.neg_max[:, 2 * u + m:2 * u + m + 1],
                                   accum_out=self.total[:, 2 * u + m:2 * u + m + 1]).then_inc(drain("acc", f), 1)
                if self.sink:
                    for m in range(2):
                        h = self.sink(u) + m
                        act.activation(self.extra[:, 2 * u + m:2 * u + m + 1], bcast[:, 2 + h:3 + h], ACT.Exp,
                                       bias=self.neg_max[:, 2 * u + m:2 * u + m + 1]).then_inc(att_sunk, 1)

            def keep_turned(self, act, u):
                if u >= 2:
                    act.wait_ge(sc_full, self.sc[u - 2] + 1)
                n = len(self.blocks(u))
                for i, f in enumerate(self.tr[u]):
                    c0, c1 = 512 * i, min(512 * i + 512, P * n)
                    act.activation(self.probT[:, u % 2, c0:c1], filled(act, "tr", f)[:, 0:c1 - c0], ACT.Copy)\
                       .then_inc(drain("tr", f), 1)

            def scalar(self, act, hook=None):
                for u in range(self.n + 1):
                    if u < self.n:
                        self.exps(act, u)
                    if u >= 1:
                        self.keep_turned(act, u - 1)
                    if self.ada and u % 2 == 1:
                        ada_act(act, self, u // 2)
                    if u >= self.n - 1 and self.following is not None:
                        ahead_act(act, self.following + u - self.n + 1)
                    if hook:
                        hook(u)

        ident_landed, later_params_landed = sem("ident_landed"), sem("later_params_landed")
        params_cleared, params_landed, first_landed, keep_landed = (
            sem("params_cleared"), sem("params_landed"), sem("first_landed"), sem("keep_landed"))
        rows_landed, x_landed, t5_stored, t5_landed = sem("rows_landed"), sem("x_landed"), sem("t5_stored"), sem("t5_landed")
        half_set, lam_prod, lam_exp, bcast_row, bcast_set, t5_vec_ready = (
            sem("half_set"), sem("lam_prod"), sem("lam_exp"), sem("bcast_row"), sem("bcast_set"), sem("t5_vec_ready"))
        silu_ready = sem("silu_ready")
        pairs8_set, sub_gain_set = sem("pairs8_set"), sem("sub_gain_set")
        sub_gain = stats(DEPTH)

        def param_dmas(eng, groups, landed):
            eng.wait_ge(params_cleared, 2 if groups[-1] else 1)
            for g in groups:
                r = 0
                for name, n in PARAM_GROUPS[g]:
                    src = I[name]
                    letters = "abcd"[:len(src.shape)]
                    flat = src.rearrange(" ".join(letters) + " -> (" + " ".join(letters) + ")") if len(letters) > 1 else src
                    if name in HALF_ROWS:
                        eng.dma_start(prow[r:r + n, g, :].rearrange("n (two c) -> n two c", two=2),
                                      flat.rearrange("(n c) -> n c", c=HD).unsqueeze(1).broadcast_to([n, 2, HD])).then_inc(landed, 16)
                    else:
                        off = (g - 4) * P if name == "conv_w" else 0
                        eng.dma_start(prow[r:r + n, g, :], flat.rearrange("(n c) -> n c", c=P)[off:off + n, :]).then_inc(landed, 16)
                    r += n

        def first_sync_dma(sp):
            sp.dma_start(h_lat[:, :, :], I["x"][0].rearrange("(t p) d -> p t d", p=P)).then_inc(x_landed, 16)
            sp.dma_start(keep[:, 0:P], consts[0][:, 0:P]).then_inc(ident_landed, 16)
            param_dmas(sp, [0], params_landed)
            sp.dma_start(lrow[0:1, 0:2 * 4 * HD], I["diff_lambda"].rearrange("(o l) a b -> o (l a b)", o=1)).then_inc(rows_landed, 16)
            sp.dma_start(lrow[0:1, 512:520], I["b_sink_2"]).then_inc(rows_landed, 16)

        def setup_sync_dma(sp):
            sp.dma_start(relb[0:REL_BUCKETS, :], I["rel_bias"]).then_inc(first_landed, 16)
            sp.dma_start(first[:, :], consts[1]).then_inc(first_landed, 16)
            sp.dma_start(keep[:, P:], consts[0][:, P:]).then_inc(keep_landed, 16)

        def later_sync_dma(sp):
            param_dmas(sp, range(1, len(PARAM_GROUPS)), later_params_landed)
            sp.dma_start(h_ctx[:, :, :], I["ctx_2"][0].rearrange("(t p) d -> p t d", p=P)).then_inc(ctx_landed, 16)

        def t5_sync_dma(sp):
            wait_drained(sp, "acc", acc_at["t5"])
            sp.dma_start(t5_scratch, t5_vec[0:N_BIAS, :]).then_inc(t5_stored, 16)
            sp.wait_ge(t5_stored, 16)
            sp.dma_start(hankel[:, :, :], bass.AP(tensor=t5_scratch.tensor, offset=0, ap=[[1, P], [384, N_BIAS], [1, SEQ]]))\
              .then_inc(t5_landed, 16)


        def setup_pool(pool):
            pool.memset(prow[:, 0, :], 0.0).then_inc(params_cleared, 1)
            pool.memset(prow[:, 1:, :], 0.0).then_inc(params_cleared, 1)
            pool.memset(half[:, :], -0.5).then_inc(half_set, 1)
            pool.wait_ge(half_set, 1)

        def setup_pe(pe):
            pe.wait_ge(ident_landed, 16)
            pe.wait_ge(params_landed, 16 * len(PARAM_GROUPS[0]))
            pe.transpose(claim(pe, "tr", tr_at["params"])[:, 0:P], prow[:, 0, :], ident).then_inc(tr_full, 1)

        LATER_FILLS = [range(1, 4), range(4, len(PARAM_GROUPS))]

        def later_params_pe(pe):
            pe.wait_ge(later_params_landed, 16 * sum(len(group) for group in PARAM_GROUPS[1:]))
            for i, groups in enumerate(LATER_FILLS):
                ps = claim(pe, "tr", tr_at["later_params"] + i)
                for n, g in enumerate(groups):
                    ins = pe.transpose(ps[:, n * P:(n + 1) * P], prow[:, g, :], ident)
                ins.then_inc(tr_full, 1)

        def setup_bias_pe(pe):
            pe.wait_ge(keep_landed, 16)
            pe.wait_ge(bcast_row, 2)
            f = acc_at["bcast"]
            pe.matmul(claim(pe, "acc", f)[:, 0:10], ones[0:1, :], lprod[0:1, 0:10], start=True, stop=True).then_inc(acc_full, 1)
            pe.wait_ge(first_landed, 32)
            f = acc_at["t5"]
            pe.matmul(claim(pe, "acc", f)[0:N_BIAS, 0:384], relb[0:REL_BUCKETS, :], first_const("bucket_hot")[0:REL_BUCKETS, :],
                      start=True, stop=True).then_inc(acc_full, 1)

        def t5_pe(pe):
            pe.wait_ge(t5_landed, 16)
            for i in range(N_BIAS // 2):
                ps = claim(pe, "acc", acc_at["t5_rows"] + i)
                pe.matmul(ps[:, :], first_const("flip"), hankel[:, 2 * i:2 * i + 2, :], start=True, stop=True).then_inc(acc_full, 1)

        def setup_dve(dve):
            f = tr_at["params"]
            dve.tensor_copy(pcol[:, 0, :], filled(dve, "tr", f)[:, 0:P]).then_inc(drain("tr", f), 1)

        def later_params_dve(dve):
            for i, groups in enumerate(LATER_FILLS):
                f, n = tr_at["later_params"] + i, len(groups)
                dve.tensor_copy(pcol[:, groups[0]:groups[-1] + 1, :], filled(dve, "tr", f)[:, 0:n * P].rearrange("p (a b) -> p a b", a=n))\
                   .then_inc(drain("tr", f), 1)

        def lambda_dve(dve):
            dve.wait_ge(rows_landed, 32)
            lam = lrow[0:1, 0:512].rearrange("p (a two c) -> p a two c", a=4, two=2)
            prods = lprod[0:1, 0:256].rearrange("p (a c) -> p a c", a=4)
            link(dve, dve.tensor_tensor(prods, lam[:, :, 0, :], lam[:, :, 1, :], ALU.mult))
            dve.tensor_reduce(lsum[0:1, 0:4], prods, AX_X, ALU.add).then_inc(lam_prod, 1)

        def setup_bias_dve(dve):
            dve.wait_ge(lam_exp, 1)
            for l in range(DEPTH):
                link(dve, dve.tensor_tensor(lprod[0:1, l:l + 1], lsum[0:1, 2 * l + 5:2 * l + 6], lsum[0:1, 2 * l + 4:2 * l + 5], ALU.subtract))
                link(dve, dve.tensor_scalar(lprod[0:1, l:l + 1], lprod[0:1, l:l + 1], -LAMBDA_INIT[l], None, ALU.add))
            dve.tensor_copy(lprod[0:1, 2:10], lrow[0:1, 512:520]).then_inc(bcast_row, 2)
            for l in range(DEPTH):
                ins = dve.tensor_scalar(sub_gain[:, l:l + 1], col("diff_subln_g", l), 1.0 - LAMBDA_INIT[l], None, ALU.mult)
            ins.then_inc(sub_gain_set, 1)
            ps = filled(dve, "acc", acc_at["bcast"])
            dve.tensor_copy(bcast[:, :], ps[:, 0:10]).then_inc(bcast_set, 1)
            dve.wait_ge(bcast_set, 1)
            dve.tensor_scalar(neg_sink[:, :], bcast[:, 2:10], -1.0, None, ALU.mult).then_inc(drain("acc", acc_at["bcast"]), 1)
            f = acc_at["t5"]
            dve.tensor_copy(t5_vec[0:N_BIAS, :], filled(dve, "acc", f)[0:N_BIAS, 0:384]).then_inc(drain("acc", f), 1)

        def t5_dve(dve):
            dve.wait_ge(keep_landed, 16)
            dve.tensor_copy(pairs8[:, :, :].rearrange("p a b -> p (a b)"), const("pairs")).then_inc(pairs8_set, 1)
            f = acc_at["t5_rows"]
            for i in range(N_BIAS // 2):
                ps = filled(dve, "acc", f + i)
                dve.tensor_tensor(t5_bias[:, 2 * i:2 * i + 2, :], ps[:, :].rearrange("p (a b) -> p a b", a=2),
                                  first_const("causal").unsqueeze(1).broadcast_to([P, 2, SEQ]), ALU.add)\
                   .then_inc(drain("acc", f + i), 1)

        def setup_bias_act(act):
            act.wait_ge(lam_prod, 1)
            wait_drained(act, "tr", tr_at["params"])
            act.activation(lsum[0:1, 4:8], lsum[0:1, 0:4], ACT.Exp).then_inc(lam_exp, 1)
            act.activation(silu_c[:, :, 0], col("c_2", 0, KT), ACT.Silu)
            act.activation(silu_c[:, :, 1], col("c_ctx_2", 0, KT), ACT.Silu).then_inc(silu_ready, 1)

        mod_ready = sem("mod_ready")

        def ada_pe(pe, att, i):
            b = att.ada[i]
            if b == 0:
                pe.wait_ge(silu_ready, 1)
            ps = claim(pe, "sc", att.ada_fill(i))
            for n in range(2):
                g = ada_chunk[b] + n
                wait_landed(pe, g)
                w = shaped(raw_slot(g), g)
                for k in range(4):
                    ins = pe.matmul(ps[0:2, :], silu_c[:, 4 * n + k, :], w[:, k, :], start=(n + k == 0), stop=(4 * n + k == KT - 1))
                ins.then_inc(sc_full if n else chunk_read, 1)

        def ada_act(act, att, i):
            f = att.ada_fill(i)
            ps = filled(act, "sc", f)
            act.activation(mod_row[0:2, :], ps[0:2, :], ACT.Copy).then_inc(drain("sc", f), 1)

        def ada_turn(pe, att, i):
            wait_drained(pe, "sc", att.ada_fill(i))
            ps = claim(pe, "tr", att.ada_tr[i])
            for n in range(4):
                ins = pe.transpose(ps[:, 2 * n:2 * n + 2], mod_row[0:2, n * P:(n + 1) * P], ident[0:2, 0:2])
            ins.then_inc(tr_full, 1)

        def ada_dve(dve, att, i):
            l, c = att.ada[i] // N_ADA, att.ada[i] % N_ADA
            ps = filled(dve, "tr", att.ada_tr[i])
            dve.tensor_tensor(mod[:, l, 4 * c:4 * c + 4, :], ps[:, 0:8].rearrange("p (a b) -> p a b", a=4),
                              col("b_ada_2", 6 * KT * l + 4 * c, 4).unsqueeze(2).broadcast_to([P, 4, 2]), ALU.add)\
               .then_inc(drain("tr", att.ada_tr[i]), 1)

        def ada_gains(dve, att, l):
            wait_drained(dve, "tr", att.ada_tr[att.ada.index(N_ADA * (l + 1) - 1)])
            for w, (pre, post) in enumerate([("g_pre_mix_2", "g_post_mix_2"), ("g_pre_ff_2", "g_post_ff_2")]):
                scale, gate = mod[:, l, (3 * w + 1) * KT:(3 * w + 2) * KT, :], mod[:, l, (3 * w + 2) * KT:(3 * w + 3) * KT, :]
                dve.scalar_tensor_tensor(mod_gain[:, l, w], scale, 1.0, col(pre, KT * l, KT).unsqueeze(2).broadcast_to([P, KT, 2]),
                                         ALU.add, ALU.mult)
                dve.tensor_tensor(mod_gate[:, l, w], gate, col(post, KT * l, KT).unsqueeze(2).broadcast_to([P, KT, 2]),
                                  ALU.mult).then_inc(mod_ready, 1)

        QK = {0: 0, 1: 1, 3: 2, 4: 3}
        PREV = {1: 0, 2: 1, 4: 3, 5: 4}
        qk_squared, qk_mean, qk_rstd = sem("qk_squared"), sem("qk_mean"), sem("qk_rstd")
        qk_ss = qk_ms = qk_rs = stats(8 * 8)

        def qkv_pe(pe, l):
            norm_wait(pe, ("attn", l))
            g = chunk_at[("qkv", l)]
            for cb in range(6):
                f = acc_at[("qkv", l)] + 2 * cb
                for k0 in (0, 4):
                    w = parts(pe, g)
                    g += 1
                    for tt in range(TT):
                        ps = claim(pe, "acc", f + tt) if k0 == 0 else bank("acc", f + tt)
                        for k in range(4):
                            x = both(hT, lambda v: v[:, k0 + k, tt * P:(tt + 1) * P])
                            ins = mm3(pe, ps[:, :], x, both(w, lambda v: v[:, k, :]), k0 + k == 0, k0 + k == KT - 1)
                        if k0:
                            ins.then_inc(acc_full, 1)
                    if k0 == 0:
                        ins.then_inc(chunk_read, 1)
                if cb in PREV:
                    for tt in range(TT):
                        u = 2 * QK[PREV[cb]] + tt
                        wait_drained(pe, "acc", acc_at[("qkv", l)] + 2 * PREV[cb] + tt)
                        t = tr_at[("qkv", l)] + u
                        ps = claim(pe, "tr", t)
                        for j in range(4):
                            ins = pe.transpose(ps[:, j * P:(j + 1) * P], qn[:, tt, j * P:(j + 1) * P], ident)
                        ins.then_inc(tr_full, 1)

        def qk_turned(eng, l, u):
            t = tr_at[("qkv", l)] + u
            ps = filled(eng, "tr", t)
            return t, ps[:, :].rearrange("p (a b) -> p a b", a=4), qkT[:, u // 2, :, (u % 2) * P:(u % 2 + 1) * P]

        def qkv_act(act, l):
            g = chunk_at[("qkv", l)]
            for cb in range(6):
                ahead_act(act, g + 2 * cb + HIGH)
                for tt in range(TT):
                    f = acc_at[("qkv", l)] + 2 * cb + tt
                    ps = filled(act, "acc", f)
                    if cb not in QK:
                        act.activation(vv[:, cb // 3, tt, :], ps[:, :], ACT.Copy).then_inc(drain("acc", f), 1)
                        continue
                    u = 8 * l + 2 * QK[cb] + tt
                    if u >= 2:
                        act.wait_ge(qk_mean, u - 1)
                    act.activation(sq[:, tt, :], ps[:, :], ACT.Square).then_inc(qk_squared, 1)
                ahead_act(act, g + 2 * cb + 1 + HIGH)
                if cb in PREV and QK[PREV[cb]] % 2 == 1:
                    for tt in range(TT):
                        t, ps, dst = qk_turned(act, l, 2 * QK[PREV[cb]] + tt)
                        act.activation(dst, ps, ACT.Identity, scale=col("qk_norm_g", 4 * l + QK[PREV[cb]])).then_inc(drain("tr", t), 1)

        def qkv_pool(pool, l):
            for u in range(8 * l, 8 * l + 8):
                c = 8 * (u % 8)
                pool.wait_ge(qk_mean, u + 1)
                pool.tensor_tensor(qk_rs[:, c:c + 8], qk_ms[:, c:c + 8], half[:, 0:8], ALU.pow).then_inc(qk_rstd, 1)

        def qkv_dve(dve, l):
            g = chunk_at[("qkv", l)]
            for cb in range(6):
                ahead_dve(dve, g + 2 * cb + HIGH)
                if cb in QK:
                    for tt in range(TT):
                        u = 2 * QK[cb] + tt
                        c = 8 * u
                        dve.wait_ge(qk_squared, 8 * l + u + 1)
                        link(dve, dve.tensor_reduce(qk_ss[:, c:c + 8], sq[:, tt, :].rearrange("p (h e) -> p h e", e=HD), AX_X, ALU.add))
                        dve.tensor_scalar(qk_ms[:, c:c + 8], qk_ss[:, c:c + 8], 1.0 / HD, EPS, ALU.mult, ALU.add).then_inc(qk_mean, 1)
                    for tt in range(TT):
                        u = 2 * QK[cb] + tt
                        c = 8 * u
                        f = acc_at[("qkv", l)] + 2 * cb + tt
                        dve.wait_ge(qk_rstd, 8 * l + u + 1)
                        if u >= 2:
                            dve.wait_ge(tr_full, tr_at[("qkv", l)] + u - 1)
                        dve.tensor_tensor(qn[:, tt, :].rearrange("p (h e) -> p h e", e=HD),
                                          bank("acc", f)[:, :].rearrange("p (h e) -> p h e", e=HD),
                                          qk_rs[:, c:c + 8].unsqueeze(2).broadcast_to([P, 8, HD]), ALU.mult).then_inc(drain("acc", f), 1)
                if cb in PREV and QK[PREV[cb]] % 2 == 0:
                    for tt in range(TT):
                        t, ps, dst = qk_turned(dve, l, 2 * QK[PREV[cb]] + tt)
                        dve.tensor_scalar(dst, ps, col("qk_norm_g", 4 * l + QK[PREV[cb]]), SCALE, ALU.mult, ALU.mult).then_inc(drain("tr", t), 1)
                ahead_dve(dve, g + 2 * cb + 1 + HIGH)

        def att1(l):
            def qk(i, u):
                p = u // 2
                return qkT[:, (2 * (p // 4)) + i, p % 4, :]

            def bias(u, m):
                p, qt = u // 2, u % 2
                h = p if p < 4 else 4 + 2 * (p - 4) + m
                return 0, t5_bias[:, h, (1 - qt) * P:SEQ]

            def v(u, m, kb):
                p = u // 2
                return vv[:, 0, kb, p * P:(p + 1) * P] if p < 4 else vv[:, 1, kb, (2 * (p - 4) + m) * HD:(2 * (p - 4) + m + 1) * HD]

            return Attention(("att1", l), 16,
                             lambda u, m: qk(0, u)[m * HD:(m + 1) * HD, (u % 2) * P:(u % 2 + 1) * P],
                             lambda u, m: qk(1, u)[m * HD:(m + 1) * HD, 0:(u % 2 + 1) * P],
                             lambda u: (u % 2 + 1) * P, v, lambda u: y1[:, u % 2, (u // 2) * P:(u // 2 + 1) * P],
                             prob, probT, bias=bias, neg_lam=bcast[:, l:l + 1], diff=lambda u: u < 8,
                             ada=range(8 * l, 8 * l + 8), following=chunk_at[("out1", l)])

        yT1_high = sem("yT1_high")
        sub_ss, sub_ms, sub_rs = stats(8), stats(8), stats(8)
        sub_summed, sub_mean, sub_rstd, sub_scaled = sem("sub_summed"), sem("sub_mean"), sem("sub_rstd"), sem("sub_scaled")

        def subnorm_act(act, l, att):
            def hook(u):
                if u == 11:
                    for n in range(8):
                        wait_drained(act, "sc", att.sc[n])
                        act.activation(sq[:, n % 2, 0:P], y1[:, n % 2, (n // 2) * P:(n // 2 + 1) * P], ACT.Square,
                                       accum_out=sub_ss[:, n:n + 1]).then_inc(sub_summed, 1)
                        act.wait_ge(sub_summed, 8 * l + n + 1)
            return hook

        def subnorm_dve(dve, l, att):
            def hook(u):
                if u == 13:
                    dve.wait_ge(sub_summed, 8 * l + 8)
                    dve.tensor_scalar(sub_ms[:, :], sub_ss[:, :], 1.0 / P, EPS, ALU.mult, ALU.add).then_inc(sub_mean, 1)
                if u == 15:
                    dve.wait_ge(sub_rstd, l + 1)
                    for n in (6, 7):
                        wait_drained(dve, "sc", att.sc[n])
                    rs = sub_rs[:, :].rearrange("p (h t) -> p t h", t=TT)
                    for qt in range(TT):
                        y = y1[:, qt, 0:512].rearrange("p (h e) -> p h e", e=P)
                        dve.tensor_tensor(y, y, rs[:, qt, :].unsqueeze(2).broadcast_to([P, 4, P]), ALU.mult).then_inc(sub_scaled, 1)
            return hook

        def subnorm_pool(pool, l):
            pool.wait_ge(sub_mean, l + 1)
            pool.tensor_tensor(sub_rs[:, :], sub_ms[:, :], half[:, 0:8], ALU.pow).then_inc(sub_rstd, 1)

        def yT1_pe(pe, l, att):
            pe.wait_ge(sub_scaled, TT * (l + 1))
            for f in (att.n - 2, att.n - 1):
                wait_drained(pe, "sc", att.sc[f])
            for g in range(4):
                f = tr_at[("yT1", l)] + g
                ps = claim(pe, "tr", f)
                for i in range(2):
                    for tt in range(TT):
                        kt = 2 * g + i
                        ins = pe.transpose(ps[:, i * SEQ + tt * P:i * SEQ + (tt + 1) * P], y1[:, tt, kt * P:(kt + 1) * P], ident)
                ins.then_inc(tr_full, 1)

        def yT1_gain(l, g):
            return (sub_gain[:, l:l + 1] if g < 2 else 1.0)

        def yT1_act(act, l):
            act.wait_ge(sub_gain_set, 1)
            for g in range(4):
                ps = filled(act, "tr", tr_at[("yT1", l)] + g)
                dst = yT1[0][:, 2 * g:2 * g + 2, :].rearrange("p a b -> p (a b)")
                act.activation(r32(dst), ps[:, :], ACT.Identity, scale=yT1_gain(l, g)).then_inc(yT1_high, 1)

        def yT1_dve(dve, l):
            dve.wait_ge(sub_gain_set, 1)
            for g in range(4):
                f = tr_at[("yT1", l)] + g
                ps = filled(dve, "tr", f)
                hi, lo = (v[:, 2 * g:2 * g + 2, :].rearrange("p a b -> p (a b)") for v in yT1)
                dve.wait_ge(yT1_high, 4 * l + g + 1)
                dve.scalar_tensor_tensor(r32(lo), ps[:, :], yT1_gain(l, g), r32(hi), ALU.mult, ALU.subtract).then_inc(drain("tr", f), 1)

        def out1_pe(pe, l):
            for g in (2, 3):
                wait_drained(pe, "tr", tr_at[("yT1", l)] + g)
            tok_gemm(pe, ("out1", l), acc_at[("out1", l)], KT, [LAT] * 2,
                     lambda kt, tt: both(yT1, lambda v: v[:, kt, tt * P:(tt + 1) * P]))

        def add_dve(dve, key, kts):
            def add(hf):
                for tt in range(TT):
                    f = acc_at[key] + 2 * hf + tt
                    ps = filled(dve, "acc", f)
                    x = h_lat[:, tt, hf * 512:(hf + 1) * 512]
                    dve.tensor_tensor(x, x, ps[:, :], ALU.add).then_inc(drain("acc", f), 1)

            tok_walk(dve, ahead_dve, key, kts, 2, add, last=False)

        conv_scaled, act_done, g_full, g_high, g_done = (
            sem("conv_scaled"), sem("act_done"), sem("g_full"), sem("g_high"), sem("g_done"))

        def up1_pe(pe, l):
            norm_wait(pe, ("ffn", l))
            for i in range(FT):
                w = parts(pe, chunk_at[("up1", l)] + i)
                f = acc_at[("up1", l)] + i
                ps = claim(pe, "acc", f)
                for s in range(2):
                    for kt in range(KT):
                        ins = mm3(pe, ps[:, s * SEQ:(s + 1) * SEQ], both(w, lambda v: v[:, kt, s, :]), both(hT, lambda v: v[:, kt, :]),
                                  kt == 0, kt == KT - 1)
                ins.then_inc(acc_full, 1)

        def conv_col(l, j, i, s):
            return col("conv_w", (l * CONV + j) * 2 * FT + s * FT + i)

        def up1_act(act, l):
            for i in range(FT + 2):
                n = FT * l + i
                if i < FT:
                    ps = filled(act, "acc", acc_at[("up1", l)] + i)
                    if n >= 2:
                        act.wait_ge(g_full, n - 1)
                    for s in range(2):
                        act.activation(conv[:, i % 2, s, :], ps[:, s * SEQ:(s + 1) * SEQ], ACT.Identity,
                                       bias=col("conv_b", l * 2 * FT + s * FT + i), scale=conv_col(l, 2, i, s)).then_inc(conv_scaled, 1)
                if 1 <= i <= FT:
                    wait_drained(act, "acc", acc_at[("up1", l)] + i - 1)
                    act.activation(act_g[:, (i - 1) % 2, :], conv[:, (i - 1) % 2, 0, :], ACT.Silu).then_inc(act_done, 1)
                if i >= 2:
                    act.wait_ge(g_full, n - 1)
                    act.activation(r32(gT[0][:, i - 2, :]), gT[1][:, i - 2, :], ACT.Copy).then_inc(g_high, 1)
                if i < FT:
                    ahead_act(act, chunk_at[("up1", l)] + i + HIGH)

        def up1_dve(dve, l):
            for i in range(FT):
                f = acc_at[("up1", l)] + i
                dve.wait_ge(conv_scaled, 2 * (FT * l + i) + 2)
                ps = bank("acc", f)
                for j, back in ((1, 1), (0, 2)):
                    for s in range(2):
                        c = conv[:, i % 2, s, back:SEQ]
                        ins = dve.scalar_tensor_tensor(c, ps[:, s * SEQ:(s + 1) * SEQ - back], conv_col(l, j, i, s), c, ALU.mult, ALU.add)
                    if j:
                        link(dve, ins)
                ins.then_inc(drain("acc", f), 1)
                ahead_dve(dve, chunk_at[("up1", l)] + i + HIGH)

        def up1_pool(pool, l):
            for i in range(FT + 2):
                n = FT * l + i
                if i < FT:
                    pool.wait_ge(act_done, n + 1)
                    pool.tensor_tensor(gT[1][:, i, :], act_g[:, i % 2, :], conv[:, i % 2, 1, :], ALU.mult).then_inc(g_full, 1)
                if i >= 2:
                    pool.wait_ge(g_high, n - 1)
                    lo = gT[1][:, i - 2, :]
                    pool.tensor_tensor(r32(lo), lo, r32(gT[0][:, i - 2, :]), ALU.subtract).then_inc(g_done, 1)

        def down1_pe(pe, l):
            tok_gemm(pe, ("down1", l), acc_at[("down1", l)], FT, [LAT] * 2,
                     lambda kt, tt: both(gT, lambda v: v[:, kt, tt * P:(tt + 1) * P]), lambda n: pe.wait_ge(g_done, FT * l + n))

        S2 = 2 * SEQ
        r2 = Region(at1)
        uT = r2.take(KT, S2), r2.take(KT, S2)
        yT = uT
        at2 = r2.at
        pA = r2.take(AT, S2)
        at_rwkv = r2.at
        q_tok = r2.take(4, 512)
        yB = q_tok
        k_tok = r2.take(4, 256)
        v_tok = r2.take(4, P)
        probBT = r2.take(2, 1024)
        rope_t = r2.take(2, 512)
        mod_row2 = r2.take(512)
        r0 = Region(0)
        qT = r0.take(4, S2)
        kT = r0.take(2, S2)
        probB = r0.take(2, 2, 512)
        assert r0.at <= at1
        rr, kf, vf = pA[:, 0:4, :], pA[:, 4:8, :], pA[:, 8:12, :]
        r3 = Region(0)
        kk = r3.take(4, S2)
        at_small = r3.at
        lc, kka, kd = [None] * 2, [None] * 2, [None] * 2
        r3 = Region(at_rwkv, slots=HIGH + RAW)
        lc[0] = r3.take(4, S2)
        kd[0] = r3.take(4, S2)
        lc[1] = r3.take(4, S2)
        kka[1] = r3.take(4, S2)
        kka[0] = yT[0][:, 0:4, :]
        kd[1] = kf

        class Scan:
            pass

        scans = [Scan(), Scan()]
        for d, sc_ in enumerate(scans):
            r = Region(at_small) if d == 0 else r3
            sc_.l_pe = r.take(4, CH + 1)
            sc_.l_pi = r.take(4, CH)
            sc_.ar = r.take(4, 2, CH)
            sc_.ar_bd = r.take(4, 2, P)
            sc_.xt = r.take(4, P)
            sc_.vst = r.take(4, CH)
            assert d or r.at <= at1
            r = r3
            sc_.x = r.take(4, P) if d else pA[:, 13, :].rearrange("p (j c) -> p j c", j=4)
            sc_.y = r.take(4, P)
            sc_.bh_bd = r.take(4, P)
            sc_.kh_bd = r.take(4, P)
            sc_.state = r.take(2, 4, CH)
            at_made = r.at
            sc_.b_tok = r.take(4, P)
            sc_.k_tk = r.take(4, P)
            sc_.nq = r.take(4, 4, P)
            at_x = sc_.x.offset % arena.shape[1]
            sc_.g, sc_.u = (arena[:, at:at + 4 * CH].rearrange("p (j c) -> p j c", j=4) for at in (at_x, at_x + 4 * CH))
            sc_.s_tmp = sc_.g
        r3 = Region(at_made, slots=HIGH + RAW)
        lora = r3.take(2, 512)
        sig = r3.take(2, S2)
        iclr = r3.take(2, S2)
        g2 = pA[:, 12, :]
        y_full = yT[1]
        y_st = y_full[:, 0:4, :].rearrange("p j (c v) -> p j c v", c=NCH)
        r4 = Region(0)
        gate_mix0 = r4.take(2, D)
        diag_mix0 = r4.take(2, KT, P)
        assert r4.at <= at1
        r4 = Region(at2)
        o_mix0 = r4.take(4, D)
        r4 = Region(0)
        gate_ff = r4.take(2, D)
        diag_ff = xn.rearrange("p t (k c) -> p t k c", c=P)
        r4 = Region(at2)
        hid = r4.take(2, ET, S2), r4.take(2, ET, S2)
        o_ff0 = r4.take(4, D)
        at_ff0_end = r4.at
        r4 = Region(at1)
        uT1 = r4.take(KT, SEQ), r4.take(KT, SEQ)
        hid1 = r4.take(FT2, SEQ), r4.take(FT2, SEQ)
        o_ff1 = r4.take(TT, D)

        ctx_landed, lora_landed, g2_landed = sem("ctx_landed"), sem("lora_landed"), sem("g2_landed")
        near_landed = sem("near_landed")

        def mod_shift(l, w, s):
            return lambda kt: mod[:, l, 3 * w * KT + kt, s:s + 1]

        def mod_mul(l, w, s):
            return lambda kt: mod_gain[:, l, w, kt, s:s + 1]

        shift_mid = stats(AT)
        shift_mid_set, shift_scaled, lora_in = sem("shift_mid_set"), sem("shift_scaled"), sem("lora_in")

        def projA_pe(pe):
            for s in (1, 0):
                norm_wait(pe, ("mix", 0, s))
            feat_gemm(pe, "projA", acc_at["projA"], AT, lambda kt: both(uT, lambda v: v[:, kt, :]))

        def projA_act(act):
            act.wait_ge(shift_mid_set, 1)
            for i in range(AT):
                f = acc_at["projA"] + i
                act.activation(pA[:, i, :], filled(act, "acc", f)[:, :], ACT.Identity,
                               scale=shift_mid[:, i:i + 1]).then_inc(shift_scaled, 1)
                if i % 2 == 1 or i == AT - 1:
                    ahead_act(act, chunk_at["projA"] + i // 2 + HIGH)
            for i, func in ((12, ACT.Tanh), (14, ACT.Sigmoid)):
                wait_drained(act, "acc", acc_at["projA"] + i)
                act.activation(pA[:, i, :], pA[:, i, :], func).then_inc(lora_in, 1)

        def projA_dve(dve):
            prev, nxt = col("a_mu_prev_2", 0, AT), col("a_mu_next_2", 0, AT)
            link(dve, dve.tensor_tensor(shift_mid[:, :], prev, nxt, ALU.add))
            dve.tensor_scalar(shift_mid[:, :], shift_mid[:, :], -1.0, 1.0, ALU.mult, ALU.add).then_inc(shift_mid_set, 1)
            for i in range(AT):
                f = acc_at["projA"] + i
                dve.wait_ge(shift_scaled, i + 1)
                ps = bank("acc", f)[:, :].rearrange("p (s t) -> p s t", s=2)
                p = pA[:, i, :].rearrange("p (s t) -> p s t", s=2)
                link(dve, dve.scalar_tensor_tensor(p[:, :, 1:], ps[:, :, 0:SEQ - 1], col("a_mu_prev_2", i), p[:, :, 1:], ALU.mult, ALU.add))
                dve.scalar_tensor_tensor(p[:, :, 0:SEQ - 1], ps[:, :, 1:], col("a_mu_next_2", i), p[:, :, 0:SEQ - 1],
                                         ALU.mult, ALU.add).then_inc(drain("acc", f), 1)
                if i % 2 == 1 or i == AT - 1:
                    ahead_dve(dve, chunk_at["projA"] + i // 2 + HIGH)

        def projA_wait(eng):
            for i in range(AT - 4, AT):
                wait_drained(eng, "acc", acc_at["projA"] + i)

        roped = sem("roped")

        def rope(dve, x, heads, tt, tmp, done, count):
            cos, sin = const("cos")[:, tt * HD:(tt + 1) * HD], const("sin")[:, tt * HD:(tt + 1) * HD]
            t0, t1 = tmp[:, 0, 0:heads * HD], tmp[:, 1, 0:heads * HD]
            cut = lambda v: v.rearrange("p (h a b f) -> p h a b f", h=heads, a=2, b=2)
            xs, ts, ss = cut(x), cut(t1), sin.rearrange("p (a b f) -> p a b f", a=2, b=2)
            dve.tensor_tensor(t0.rearrange("p (h e) -> p h e", h=heads), x.rearrange("p (h e) -> p h e", h=heads),
                              cos.unsqueeze(1).broadcast_to([P, heads, HD]), ALU.mult)
            for b in range(2):
                ins = dve.tensor_tensor(ts[:, :, :, b, :], xs[:, :, :, 1 - b, :],
                                        ss[:, :, b, :].unsqueeze(1).broadcast_to([P, heads, 2, 16]), ALU.mult)
            link(dve, ins)
            dve.tensor_tensor(x, t0, t1, ALU.add).then_inc(done, 1)
            dve.wait_ge(done, count)

        def projB_pe(pe):
            tok_gemm(pe, "projB", acc_at["projB"], KT, [ALL] * 2, lambda kt, tt: both(uT, lambda v: v[:, kt, tt * P:(tt + 1) * P]))
            for tt in ALL:
                wait_drained(pe, "acc", acc_at["projB"] + tt)
                wait_drained(pe, "acc", acc_at["projB"] + 4 + tt)
                if tt >= 2:
                    pe.wait_ge(roped, 2 * (tt - 1))
                for x, n, f in ((q_tok, 4, 2 * tt), (k_tok, 2, 2 * tt + 1)):
                    ps = claim(pe, "tr", tr_at["projB"] + f)
                    for j in range(n):
                        ins = pe.transpose(ps[:, j * P:(j + 1) * P], x[:, tt, j * P:(j + 1) * P], ident)
                    ins.then_inc(tr_full, 1)

        def dup_heads(ps, n=2):
            return ps.rearrange("p (k e) -> p k e", k=2).unsqueeze(2).broadcast_to([P, 2, n, HD])

        def projB_act(act):
            def qkv(block):
                for tt in ALL:
                    f = acc_at["projB"] + 4 * block + tt
                    ps = filled(act, "acc", f)
                    if block == 0:
                        act.activation(q_tok[:, tt, :], ps[:, :], ACT.Copy).then_inc(drain("acc", f), 1)
                    else:
                        act.activation(k_tok[:, tt, :].rearrange("p (k n e) -> p k n e", k=2, n=2), dup_heads(ps[:, 0:P]), ACT.Copy)
                        act.activation(v_tok[:, tt, :], ps[:, P:2 * P], ACT.Copy).then_inc(drain("acc", f), 1)

            tok_walk(act, ahead_act, "projB", KT, 2, qkv)
            for tt in ALL:
                f = tr_at["projB"] + 2 * tt
                act.activation(qT[:, :, tt * P:(tt + 1) * P], filled(act, "tr", f)[:, :].rearrange("p (a b) -> p a b", a=4),
                               ACT.Copy, scale=SCALE).then_inc(drain("tr", f), 1)
                f += 1
                act.activation(kT[:, :, tt * P:(tt + 1) * P], filled(act, "tr", f)[:, 0:2 * P].rearrange("p (a b) -> p a b", a=2),
                               ACT.Copy).then_inc(drain("tr", f), 1)

        def projB_dve(dve):
            tok_walk(dve, ahead_dve, "projB", KT, 2)
            for tt in (0, 1):
                wait_drained(dve, "acc", acc_at["projB"] + 2 + tt)
                wait_drained(dve, "acc", acc_at["projB"] + 6 + tt)
                rope(dve, q_tok[:, 2 + tt, :], 8, tt, rope_t, roped, 2 * tt + 1)
                rope(dve, k_tok[:, 2 + tt, :], 4, tt, rope_t, roped, 2 * tt + 2)

        def projB_wait(pe):
            for f in (6, 7):
                wait_drained(pe, "tr", tr_at["projB"] + f)

        def heads(x, u, m, cols):
            return x[m * HD:(m + 1) * HD, u // 2, cols]

        def kv_of(u):
            return u // 4

        def attBl():
            return Attention("attBl", 8, lambda u, m: heads(qT, u, m, slice(SEQ + (u % 2) * P, SEQ + (u % 2 + 1) * P)),
                             lambda u, m: kT[m * HD:(m + 1) * HD, kv_of(u), :], lambda u: S2,
                             lambda u, m, kb: v_tok[:, kb, kv_of(u) * HD:(kv_of(u) + 1) * HD],
                             lambda u: yB[:, 2 + u % 2, (u // 2) * P:(u // 2 + 1) * P], probB, probBT,
                             bias=lambda u, m: (SEQ, const("band")[:, (u % 2) * SEQ:(u % 2 + 1) * SEQ]), sink=lambda u: 2 * (u // 2), ada=range(16, 20))

        def attBc():
            return Attention("attBc", 8, lambda u, m: heads(qT, u, m, slice((u % 2) * P, (u % 2 + 1) * P)),
                             lambda u, m: kT[m * HD:(m + 1) * HD, kv_of(u), 0:SEQ], lambda u: SEQ,
                             lambda u, m, kb: v_tok[:, kb, kv_of(u) * HD:(kv_of(u) + 1) * HD],
                             lambda u: yB[:, u % 2, (u // 2) * P:(u // 2 + 1) * P], probB, probBT, sink=lambda u: 2 * (u // 2), ada=range(20, 24))

        yTB_high = sem("yTB_high")

        def yTB_pe(pe, atts):
            for att in atts:
                for u in (6, 7):
                    wait_drained(pe, "sc", att.sc[u])
            for tt in ALL:
                f = tr_at["yTB"] + tt
                ps = claim(pe, "tr", f)
                for j in range(4):
                    ins = pe.transpose(ps[:, j * P:(j + 1) * P], yB[:, tt, j * P:(j + 1) * P], ident)
                ins.then_inc(tr_full, 1)

        def yTB_act(act):
            for tt in ALL:
                ps = filled(act, "tr", tr_at["yTB"] + tt)
                act.activation(r32(yT[0][:, 4:8, tt * P:(tt + 1) * P]), ps[:, :].rearrange("p (a b) -> p a b", a=4),
                               ACT.Copy).then_inc(yTB_high, 1)

        def yTB_dve(dve):
            for tt in ALL:
                f = tr_at["yTB"] + tt
                ps = filled(dve, "tr", f)
                dve.wait_ge(yTB_high, tt + 1)
                hi, lo = (v[:, 4:8, tt * P:(tt + 1) * P] for v in yT)
                dve.tensor_tensor(r32(lo), ps[:, :].rearrange("p (a b) -> p a b", a=4), r32(hi), ALU.subtract).then_inc(drain("tr", f), 1)

        kk_squared, kk_rn, kk_wide, kk_done = sem("kk_squared"), sem("kk_rn"), sem("kk_wide"), sem("kk_done")
        bd_cleared = sem("bd_cleared")
        cum_done, decay_ready, prep_done = sem("cum_done"), sem("decay_ready"), sem("prep_done")
        l_mid, l_end, l_step, f_step = ([stats(4 * NCH) for _ in range(2)] for _ in range(4))
        kk_ss, kk_rs = stats(4 * 8), stats(4 * 8)
        by_chunk = lambda v: v.rearrange("p (j c) -> p j c", j=4)
        ORDER = [list(range(NCH)), [3, 2, 1, 0, 7, 6, 5, 4]]

        def kk_dve(dve):
            projA_wait(dve)
            for j in range(4):
                dve.tensor_scalar(kk[:, j, :], kf[:, j, :], col("a_k_k_2", j), None, ALU.mult).then_inc(kk_done, 1)
            f = acc_at["kk"]
            dve.tensor_scalar(kk_ss[:, :], filled(dve, "acc", f)[:, 0:32], 1e-24, None, ALU.max).then_inc(drain("acc", f), 1)
            prep_dve(dve, range(1))
            dve.wait_ge(kk_rn, 1)
            dve.tensor_copy(lc[1][:, :, :].rearrange("p a (b e) -> p (a b) e", e=HD), kk_rs[:, :].unsqueeze(2).broadcast_to([P, 32, HD]))\
               .then_inc(kk_wide, 1)
            for j in range(4):
                f = tr_at["kk"] + j
                ps = filled(dve, "tr", f)
                if j == 0:
                    dve.wait_ge(kk_done, 4)
                dve.tensor_tensor(kk[:, j, :], kk[:, j, :], ps[:, :], ALU.mult).then_inc(drain("tr", f), 1)

        def kk_act(act):
            for j in range(4):
                act.wait_ge(kk_done, j + 1)
                act.activation(lc[0][:, j, :], kk[:, j, :], ACT.Square).then_inc(kk_squared, 1)

        def kk_pe(pe):
            f = acc_at["kk"]
            ps = claim(pe, "acc", f)
            for j in range(4):
                pe.wait_ge(kk_squared, j + 1)
                for tt in ALL:
                    c = 8 * tt + 2 * j
                    ins = pe.matmul(ps[:, c:c + 2], lc[0][:, j, tt * P:(tt + 1) * P], head_ones[:, 0:P:HD], start=True, stop=True)
            ins.then_inc(acc_full, 1)
            prep_pe(pe, range(2))
            pe.wait_ge(kk_wide, 1)
            wide = lc[1][:, :, :].rearrange("p a b -> p (a b)")
            for j in range(4):
                ps = claim(pe, "tr", tr_at["kk"] + j)
                for tt in ALL:
                    c = 8 * tt + 2 * j
                    ins = pe.transpose(ps[:, tt * P:(tt + 1) * P], wide[:, c * HD:(c + 2) * HD], ident)
                ins.then_inc(tr_full, 1)

        def kk_pool(pool):
            wait_drained(pool, "acc", acc_at["kk"])
            pool.tensor_tensor(kk_rs[:, :], kk_ss[:, :], half[:, :], ALU.pow).then_inc(kk_rn, 1)
            for q in scans:
                for x in (q.ar_bd[:, :, :, :], q.bh_bd[:, :, :], q.kh_bd[:, :, :], q.y[:, :, :]):
                    pool.memset(x, 0.0).then_inc(bd_cleared, 1)
            pool.wait_ge(bd_cleared, 8)

        kka_done = sem("kka_done")

        def prep_fill(d, j, i):
            return acc_at["prep"] + 8 * d + 2 * j + i

        def prep_pe(pe, units):
            pe.wait_ge(lora_landed, 32)
            pe.wait_ge(lora_in, 1)
            for m in units:
                d, j = divmod(m, 4)
                s = slice(d * 64, d * 64 + 64)
                for i, x in enumerate((pA[s, 12, :], pA[s, 13, :])):
                    ps = claim(pe, "acc", prep_fill(d, j, i))
                    pe.matmul(ps[:, :], lora[s, i, j * P:(j + 1) * P], x, start=True, stop=True).then_inc(acc_full, 1)

        def prep_act(act):
            for m in range(8):
                d, j = divmod(m, 4)
                if m >= 2:
                    act.wait_ge(prep_done, m - 1)
                    act.wait_ge(kka_done, m - 1)
                for i, (x, b) in enumerate(((sig, "a_w0_2"), (iclr, "a_a0_2"))):
                    f = prep_fill(d, j, i)
                    act.activation(x[:, j % 2, :], filled(act, "acc", f)[:, :], ACT.Sigmoid, bias=col(b, m)).then_inc(drain("acc", f), 1)
            act.dma_start(g2, I["a_g2_2"][0]).then_inc(g2_landed, 16)
            for d in range(2):
                step_exps(act, d, 0)
                act.activation(f_step[d], l_step[d], ACT.Exp, scale=-DECAY).then_inc(decay_ready, 1)

        def prep_pool(pool):
            for j in (2, 3):
                wait_drained(pool, "tr", tr_at["kk"] + j)
            for m in range(8):
                d, j = divmod(m, 4)
                wait_drained(pool, "acc", prep_fill(d, j, 1))
                pool.tensor_tensor(kka[d][:, j, :], kk[:, j, :], iclr[:, j % 2, :], ALU.mult).then_inc(kka_done, 1)
            for d in range(2):
                step_bk(pool, d, 0)
            for d in range(2):
                step_identity(pool, d, 0)

        def prep_dve(dve, units):
            edge = const("scan_edge")
            for m in units:
                d, j = divmod(m, 4)
                for i in range(2):
                    wait_drained(dve, "acc", prep_fill(d, j, i))
                x, t = lc[d][:, j, :], sig[:, j % 2, :]
                if d == 0:
                    ins = dve.tensor_tensor_scan(x, edge[:, 0:S2], t, 0.0, ALU.mult, ALU.add)
                else:
                    ins = dve.tensor_tensor_scan(x[:, ::-1], edge[:, 1:S2 + 1][:, ::-1], t[:, ::-1], 0.0, ALU.mult, ALU.add)
                link(dve, ins)
                link(dve, dve.scalar_tensor_tensor(t, iclr[:, j % 2, :], -1.0, kf[:, j, :], ALU.add, ALU.mult))
                dve.scalar_tensor_tensor(kd[d][:, j, :], t, col("a_k_a_2", j), kf[:, j, :], ALU.mult, ALU.add).then_inc(prep_done, 1)
                if j < 3:
                    continue
                chunked = lc[d].rearrange("p j (c t) -> p (j c) t", t=CH)
                link(dve, dve.tensor_copy(l_mid[d], chunked[:, :, CH // 2 - 1 + d]))
                link(dve, dve.tensor_tensor(chunked, chunked, l_mid[d].unsqueeze(2).broadcast_to([P, 4 * NCH, CH]), ALU.subtract))
                link(dve, dve.tensor_copy(l_end[d], chunked[:, :, 0 if d else CH - 1]))
                mid, end, step = by_chunk(l_mid[d]), by_chunk(l_end[d]), by_chunk(l_step[d])
                link(dve, dve.memset(l_step[d], 0.0))
                for a, b, n in ([(0, 1, 7)] if d == 0 else [(1, 0, 3), (0, 7, 1), (5, 4, 3)]):
                    ins = dve.tensor_tensor(step[:, :, a:a + n], end[:, :, a:a + n], mid[:, :, b:b + n], ALU.add)
                ins.then_inc(cum_done, 1)

        pe_exp, ar_done, bk_done, bd_done, n_set, x_set, xt_set = (
            [sem(f"{name}{d}") for d in range(2)] for name in ("pe_exp", "ar_done", "bk_done", "bd_done", "n_set", "x_set", "xt_set"))
        HEADS = [slice(0, HD), slice(HD, P)]

        def cols_of(x, lev, i):
            if len(x.shape) == 3:
                x = x.rearrange("p j c -> p (j c)")
            n = x.shape[1] // HD
            return x.rearrange("p (h b two m) -> p h b two m", h=n, two=2, m=1 << lev)[:, :, :, i, :]

        def in_pairs(x, lev):
            return x.rearrange("p (h b m) -> p h b m", h=8, m=1 << lev)

        def rows_of(lev, i):
            at, n = HD - (HD >> lev), HD >> lev + 1
            return pairs8[:, i, at:at + n].unsqueeze(1).unsqueeze(3).broadcast_to([P, 8, n, 1 << lev])

        def nq_fill(s, d, g):
            return acc_at[("step", s)] + 2 * d + g

        def chain_fill(s, d, what):
            return acc_at[("step", s)] + 4 + 2 * "gusy".index(what) + d

        def lev_fill(s, d, lev, what=1):
            return sc_at[("step", s)] + (d if lev == 0 else 2 + 4 * (lev - 1) + 2 * what + d)

        TURNS = [(0, 1), (0, 2), (1, 1), (1, 2), (0, 0), (1, 0)]

        def turned_fill(s, d, i):
            return tr_at[("step", s)] + TURNS.index((d, i))

        def chunk_cols(d, s):
            return slice(ORDER[d][s] * CH, (ORDER[d][s] + 1) * CH)

        def step_exps(act, d, s):
            q, sl, ci = scans[d], chunk_cols(d, s), ORDER[d][s]
            if s:
                act.wait_ge(ar_done[d], s)
                act.wait_ge(bk_done[d], 4 * s)
            else:
                act.wait_ge(cum_done, d + 1)
            incl = 1 - d
            act.activation(q.l_pe[:, :, incl:incl + CH], lc[d][:, :, sl], ACT.Exp, scale=-DECAY)
            act.activation(q.l_pe[:, :, CH * d:CH * d + 1], by_chunk(l_mid[d])[:, :, ci:ci + 1], ACT.Exp, scale=DECAY)
            act.activation(q.l_pi[:, :, :], lc[d][:, :, sl], ACT.Exp, scale=DECAY).then_inc(pe_exp[d], 1)

        def step_ar(dve, d, s):
            q, sl, incl = scans[d], chunk_cols(d, s), 1 - d
            dve.wait_ge(pe_exp[d], s + 1)
            if s:
                dve.wait_ge(bd_done[d], 2 * s)
            dve.scalar_tensor_tensor(q.ar[:, :, 0, :], kk[:, :, sl], -1.0, q.l_pe[:, :, 1 - incl:1 - incl + CH], ALU.mult, ALU.mult)
            dve.tensor_tensor(q.ar[:, :, 1, :], rr[:, :, sl], q.l_pe[:, :, incl:incl + CH], ALU.mult).then_inc(ar_done[d], 1)

        def step_bk(pool, d, s):
            q, sl = scans[d], chunk_cols(d, s)
            if s:
                pool.wait_ge(tr_full, turned_fill(s - 1, d, 2) + 1)
            else:
                pool.wait_ge(kka_done, 8)
                pool.wait_ge(prep_done, 8)
            pool.wait_ge(pe_exp[d], s + 1)
            for hd, h in enumerate(HEADS):
                for i, (x, y) in enumerate(((q.bh_bd, kka[d]), (q.kh_bd, kd[d]))):
                    pool.tensor_tensor(x[h, :, h], y[h, :, sl], q.l_pi[h, :, :], ALU.mult).then_inc(bk_done[d], 1)
                    pool.wait_ge(bk_done[d], 4 * s + 2 * hd + i + 1)

        def step_identity(pool, d, s):
            q, one = scans[d], ident.unsqueeze(1).broadcast_to([P, 4, P])
            if s:
                pool.wait_ge(acc_full, chain_fill(s - 1, d, "y") + 1)
                wait_drained(pool, "acc", chain_fill(s - 1, d, "s"))
            pool.tensor_copy(q.x[:, :, :], one).then_inc(x_set[d], 1)
            pool.wait_ge(x_set[d], s + 1)

        def step_pool(pool, s):
            if s + 1 < NCH:
                for d in range(2):
                    step_bk(pool, d, s + 1)
                for d in range(2):
                    step_identity(pool, d, s + 1)

        def step_pe(pe, s):
            out4 = lambda ps, j: ps[:, j * CH:(j + 1) * CH]
            first_step = s == 0

            def blocks(ps, at, lhsT, rhs):
                for j in range(4):
                    ins = pe.matmul(ps[:, at + j * HD:at + (j + 1) * HD], lhsT(j), rhs(j), start=True, stop=True)
                return ins

            def turn(d, i):
                x = (vf[:, :, chunk_cols(d, s)], scans[d].bh_bd, scans[d].kh_bd)[i]
                ps = claim(pe, "tr", turned_fill(s, d, i))
                for j in range(4):
                    ins = pe.transpose(ps[0:CH if i == 0 else P, j * P:(j + 1) * P], x[:, j, :], ident)
                ins.then_inc(tr_full, 1)

            for d, q in enumerate(scans):
                pe.wait_ge(bk_done[d], 4 * s + 4)
                pe.wait_ge(ar_done[d], s + 1)
                for g in range(2):
                    ps = claim(pe, "acc", nq_fill(s, d, g))
                    for i in range(2):
                        for b, x in enumerate((q.bh_bd, q.kh_bd)):
                            ins = pe.matmul(ps[:, (2 * i + b) * P:(2 * i + b + 1) * P], x[:, 2 * g + i, :],
                                            q.ar[:, 2 * g + i, :, :].rearrange("p a t -> p (a t)"), start=True, stop=True)
                    ins.then_inc(acc_full, 1)
            for lev in range(LEVELS):
                if lev:
                    for d, q in enumerate(scans):
                        ps = claim(pe, "sc", lev_fill(s, d, lev, 0))
                        blocks(ps, 0, lambda j: q.nq[:, j, 0, :], lambda j: cols_of(q.x[:, j, :], lev, d)).then_inc(sc_full, 1)
                turn(*TURNS[lev])
                for d, q in enumerate(scans):
                    if lev == 0:
                        pe.wait_ge(n_set[d], 2 * s + 2)
                    ps = claim(pe, "sc", lev_fill(s, d, lev))
                    if lev == 0:
                        ins = blocks(ps, 0, lambda j: q.nq[:, j, 0, :], lambda j: cols_of(ident, lev, d))
                    else:
                        pe.wait_ge(xt_set[d], (LEVELS - 1) * s + lev)
                        if lev < LEVELS - 1:
                            ins = blocks(ps, 0, lambda j: q.xt[:, j, :], lambda j: cols_of(q.y[:, j, :], lev, d))
                        else:
                            ins = blocks(ps, 0, lambda j: q.y[:, j, :], lambda j: cols_of(q.xt[:, j, :], lev, 1 - d))
                    ins.then_inc(sc_full, 1)
            for d, q in enumerate(scans):
                wait_drained(pe, "tr", turned_fill(s, d, 0))
                pe.wait_ge(bd_done[d], 2 * s + 2)
                for g in range(2):
                    wait_drained(pe, "acc", nq_fill(s, d, g))
                if not first_step:
                    wait_drained(pe, "acc", chain_fill(s - 1, d, "s"))
                ps = claim(pe, "acc", chain_fill(s, d, "g"))
                for j in range(4):
                    ins = pe.matmul(out4(ps, j), q.nq[:, j, 2, :], q.vst[:, j, :], start=True, stop=first_step)
                    if not first_step:
                        ins = pe.matmul(out4(ps, j), q.ar_bd[:, j, 0, :], q.state[:, s % 2, j, :], start=False, stop=True)
                ins.then_inc(acc_full, 1)
            for d, q in enumerate(scans):
                wait_drained(pe, "sc", lev_fill(s, d, LEVELS - 1))
                wait_drained(pe, "acc", chain_fill(s, d, "g"))
                ps = claim(pe, "acc", chain_fill(s, d, "u"))
                blocks(ps, 0, lambda j: q.xt[:, j, :], lambda j: q.g[:, j, :]).then_inc(acc_full, 1)
            for d, q in enumerate(scans):
                for i in (1, 2):
                    wait_drained(pe, "tr", turned_fill(s, d, i))
                wait_drained(pe, "acc", chain_fill(s, d, "u"))
                ps = claim(pe, "acc", chain_fill(s, d, "s"))
                for j in range(4):
                    pe.matmul(out4(ps, j), q.b_tok[:, j, :], q.u[:, j, :], start=True, stop=False)
                    ins = pe.matmul(out4(ps, j), q.k_tk[:, j, :], q.vst[:, j, :], start=False, stop=True)
                ins.then_inc(acc_full, 1)
            for d, q in enumerate(scans):
                ps = claim(pe, "acc", chain_fill(s, d, "y"))
                for j in range(4):
                    pe.matmul(out4(ps, j), q.nq[:, j, 1, :], q.u[:, j, :], start=True, stop=False)
                    ins = pe.matmul(out4(ps, j), q.nq[:, j, 3, :], q.vst[:, j, :], start=False, stop=first_step)
                    if not first_step:
                        ins = pe.matmul(out4(ps, j), q.ar_bd[:, j, 1, :], q.state[:, s % 2, j, :], start=False, stop=True)
                ins.then_inc(acc_full, 1)

        def step_act(act, s):
            def keep_turned(d, i):
                q, f = scans[d], turned_fill(s, d, i)
                ps = filled(act, "tr", f)
                if i:
                    ins = act.activation((q.b_tok, q.k_tk)[i - 1], ps[:, :].rearrange("p (j c) -> p j c", j=4), ACT.Copy)
                else:
                    for h in HEADS:
                        ins = act.activation(q.vst[h, :, :], ps[0:CH, :].rearrange("p (j c) -> p j c", j=4)[:, :, h], ACT.Copy)
                ins.then_inc(drain("tr", f), 1)

            for d, q in enumerate(scans):
                act.wait_ge(ar_done[d], s + 1)
                if s:
                    act.wait_ge(acc_full, chain_fill(s - 1, d, "y") + 1)
                else:
                    act.wait_ge(bd_cleared, 8)
                for h in HEADS:
                    act.activation(q.ar_bd[h, :, :, h], q.ar[h, :, :, :], ACT.Copy).then_inc(bd_done[d], 1)
            for lev in range(LEVELS):
                if lev:
                    for d, q in enumerate(scans):
                        f = lev_fill(s, d, lev, 0)
                        ps = filled(act, "sc", f)
                        act.activation(cols_of(q.y, lev, d), in_pairs(ps[:, 0:2 * P], lev), ACT.Copy).then_inc(drain("sc", f), 1)
                keep_turned(*TURNS[lev])
                if lev == 2 and s + 1 < NCH:
                    for d in range(2):
                        step_exps(act, d, s + 1)
            for what in "gu":
                for d, q in enumerate(scans):
                    f = chain_fill(s, d, what)
                    act.activation((q.g if what == "g" else q.u)[:, :, :], filled(act, "acc", f)[:, 0:4 * CH].rearrange("p (j c) -> p j c", j=4),
                                   ACT.Copy).then_inc(drain("acc", f), 1)

        y_steps = [[(s, d) for s in range(NCH) for d in range(2) if ORDER[d][s] == ci] for ci in range(NCH)]

        def step_dve(dve, s):
            def matrices(d, g):
                q, f = scans[d], nq_fill(s, d, g)
                tri = const(f"tri{d}").rearrange("p (a h t) -> p a h t", a=3, h=2)
                for i in range(2):
                    x = bank("acc", f)[:, i * 2 * P + CH:(i + 1) * 2 * P].rearrange("p (a t) -> p a t", a=3).unsqueeze(2).broadcast_to([P, 3, 2, CH])
                    ins = dve.tensor_tensor(q.nq[:, 2 * g + i, 1:4, :].rearrange("p a (h t) -> p a h t", h=2), x, tri, ALU.mult)
                ins.then_inc(drain("acc", f), 1)

            for d, q in enumerate(scans):
                for g in range(2):
                    ps = filled(dve, "acc", nq_fill(s, d, g))
                    n_t = ps[:, :].rearrange("p (i a t) -> p i a t", i=2, a=4)[:, :, 0, :].unsqueeze(2).broadcast_to([P, 2, 2, CH])
                    strict = const(f"tri{d}")[:, P:2 * P].rearrange("p (h t) -> p h t", h=2).unsqueeze(1).broadcast_to([P, 2, 2, CH])
                    dve.tensor_tensor(q.nq[:, 2 * g:2 * g + 2, 0, :].rearrange("p i (h t) -> p i h t", h=2), n_t, strict, ALU.mult)\
                       .then_inc(n_set[d], 1)
            matrices(0, 0)
            for lev in range(LEVELS):
                for d, q in enumerate(scans):
                    f = lev_fill(s, d, lev)
                    if lev == 0:
                        dve.wait_ge(x_set[d], s + 1)
                    ps = filled(dve, "sc", f)
                    if lev < LEVELS - 1:
                        dve.copy_predicated(cols_of(q.x, lev, d), rows_of(lev, 1 - d), in_pairs(ps[:, 0:2 * P], lev)).then_inc(drain("sc", f), 1)
                        wait_drained(dve, "sc", f)
                        dve.transpose(q.xt.rearrange("p j c -> p (j c)"), q.x.rearrange("p j c -> p (j c)")).then_inc(xt_set[d], 1)
                    else:
                        dve.wait_ge(xt_set[d], (LEVELS - 1) * (s + 1))
                        dve.copy_predicated(cols_of(q.xt, lev, 1 - d), rows_of(lev, d), in_pairs(ps[:, 0:2 * P], lev)).then_inc(drain("sc", f), 1)
                if lev < 3:
                    matrices((lev + 1) // 2, (lev + 1) % 2)
                if lev == 4 and s + 1 < NCH:
                    for d in range(2):
                        step_ar(dve, d, s + 1)
            for d, q in enumerate(scans):
                f, ci = chain_fill(s, d, "s"), ORDER[d][s]
                x = filled(dve, "acc", f)[:, 0:4 * CH].rearrange("p (j c) -> p j c", j=4)
                if s == 0:
                    dve.wait_ge(decay_ready, d + 1)
                else:
                    wait_drained(dve, "acc", chain_fill(s - 1, d, "s"))
                    link(dve, dve.tensor_tensor(q.s_tmp[:, :, :], x, q.state[:, s % 2], ALU.add))
                    x = q.s_tmp[:, :, :]
                dve.tensor_tensor(q.state[:, (s + 1) % 2], x, by_chunk(f_step[d])[:, :, ci:ci + 1].broadcast_to([P, 4, CH]), ALU.mult)\
                   .then_inc(drain("acc", f), 1)
            for d in range(2):
                f, ci = chain_fill(s, d, "y"), ORDER[d][s]
                ps = filled(dve, "acc", f)[:, 0:4 * CH].rearrange("p (j c) -> p j c", j=4)
                y = y_st[:, :, ci, :]
                if y_steps[ci][0] == (s, d):
                    ins = dve.tensor_copy(y, ps)
                else:
                    wait_drained(dve, "acc", chain_fill(*y_steps[ci][0], "y"))
                    ins = dve.tensor_tensor(y, y, ps, ALU.add)
                ins.then_inc(drain("acc", f), 1)

        gn_sum, gn_mean, gn_sq, gn_var, gn_rs = (stats(4 * NCH) for _ in range(5))
        gn_var_ready, gn_rstd, y_normed, bonus_in = sem("gn_var_ready"), sem("gn_rstd"), sem("y_normed"), sem("bonus_in")
        yA_high, yA_low = sem("yA_high"), sem("yA_low")
        y_all = y_st.rearrange("p j c v -> p (j c) v")

        def rwkv_out_pool(pool):
            pool.wait_ge(gn_var_ready, 1)
            pool.tensor_tensor(gn_rs[:, :], gn_var[:, :], half[:, :], ALU.pow).then_inc(gn_rstd, 1)

        def scan_over(eng):
            for what in "sy":
                for d in range(2):
                    wait_drained(eng, "acc", chain_fill(NCH - 1, d, what))

        def rwkv_out_dve(dve):
            for d in range(2):
                wait_drained(dve, "acc", chain_fill(NCH - 1, d, "y"))
            wide = lambda v: v.unsqueeze(2).broadcast_to([P, 4 * NCH, CH])
            squares = lc[0].rearrange("p j (c v) -> p (j c) v", v=CH)
            link(dve, dve.tensor_reduce(gn_sum[:, :], y_all, AX_X, ALU.add))
            link(dve, dve.tensor_scalar(gn_mean[:, :], gn_sum[:, :], 1.0 / HD, None, ALU.mult))
            link(dve, dve.tensor_tensor(y_all, y_all, wide(gn_mean[:, :]), ALU.subtract))
            link(dve, dve.tensor_tensor(squares, y_all, y_all, ALU.mult))
            link(dve, dve.tensor_reduce(gn_sq[:, :], squares, AX_X, ALU.add))
            dve.tensor_scalar(gn_var[:, :], gn_sq[:, :], 1.0 / HD, GN_EPS, ALU.mult, ALU.add).then_inc(gn_var_ready, 1)
            for j in range(4):
                x = kd[0][:, j, :]
                link(dve, dve.tensor_tensor(x, x, kd[1][:, j, :], ALU.add))
                dve.scalar_tensor_tensor(x, rr[:, j, :], col("a_r_k_2", j), x, ALU.mult, ALU.mult).then_inc(bonus_in, 1)
            dve.wait_ge(gn_rstd, 1)
            dve.tensor_tensor(y_all, y_all, wide(gn_rs[:, :]), ALU.mult).then_inc(y_normed, 1)
            ahead_dve(dve, chunk_at["out2_0"] + HIGH - 1)
            for j in range(4):
                f = acc_at["rwkv_out"] + 2 * j
                for i in range(2):
                    wait_drained(dve, "tr", tr_at["rwkv_out"] + 2 * j + i)
                a = y_full[:, j, :]
                dve.tensor_tensor(lc[0][:, j, :], filled(dve, "acc", f)[:, :], vf[:, j, :], ALU.mult).then_inc(drain("acc", f), 1)
                link(dve, dve.tensor_scalar(a, a, col("a_gn_w_2", j), col("a_gn_b_2", j), ALU.mult, ALU.add))
                wait_drained(dve, "acc", f)
                link(dve, dve.tensor_tensor(a, a, lc[0][:, j, :], ALU.add))
                dve.tensor_tensor(a, a, filled(dve, "acc", f + 1)[:, :], ALU.mult).then_inc(drain("acc", f + 1), 1)
            for j in range(4):
                dve.wait_ge(yA_high, j + 1)
                dve.tensor_tensor(r32(y_full[:, j, :]), y_full[:, j, :], r32(yT[0][:, j, :]), ALU.subtract).then_inc(yA_low, 1)

        def rwkv_out_pe(pe):
            pe.wait_ge(g2_landed, 16)
            pe.wait_ge(lora_in, 2)
            pe.wait_ge(y_normed, 1)
            for j in range(4):
                for i in range(2):
                    f = tr_at["rwkv_out"] + 2 * j + i
                    ps = claim(pe, "tr", f)
                    for c in range(4):
                        ins = pe.transpose(ps[0:CH, c * P:(c + 1) * P], y_st[:, j, 4 * i + c, :], ident)
                    ins.then_inc(tr_full, 1)
            for j in range(4):
                f = acc_at["rwkv_out"] + 2 * j
                pe.wait_ge(bonus_in, j + 1)
                pe.matmul(claim(pe, "acc", f)[:, :], head_ones, kd[0][:, j, :], start=True, stop=True).then_inc(acc_full, 1)
                pe.matmul(claim(pe, "acc", f + 1)[:, :], g2[:, j * P:(j + 1) * P], pA[:, 14, :], start=True, stop=True).then_inc(acc_full, 1)

        def rwkv_out_act(act):
            for j in range(4):
                for i in range(2):
                    f = tr_at["rwkv_out"] + 2 * j + i
                    ps = filled(act, "tr", f)[0:CH, :].rearrange("p (c x) -> p c x", c=4)
                    for hd in range(2):
                        h = slice(hd * HD, hd * HD + HD)
                        dst = y_full[h, j, i * SEQ:(i + 1) * SEQ].rearrange("p (c t) -> p c t", c=4)
                        ins = act.activation(dst, ps[:, :, h], ACT.Copy)
                    ins.then_inc(drain("tr", f), 1)
            for j in range(4):
                wait_drained(act, "acc", acc_at["rwkv_out"] + 2 * j + 1)
                act.activation(r32(yT[0][:, j, :]), y_full[:, j, :], ACT.Copy).then_inc(yA_high, 1)

        gate_diag, post_squared, post_mean, post_rstd, h_updated = (
            sem("gate_diag"), sem("post_squared"), sem("post_mean"), sem("post_rstd"), sem("h_updated"))
        post_gated = sem("post_gated")
        posts = {}

        class Post:

            def __init__(self, key, l, w, streams, o, gate, diag, squares, free, product=None, kts=None):
                self.key, self.l, self.w, self.streams, self.o, self.gate, self.diag = key, l, w, streams, o, gate, diag
                self.squares, self.free, self.product, self.kts = squares, free, product, kts
                self.tiles = [(s, (h_ctx if s else h_lat)[:, t, :]) for s in streams for t in range(TT)]
                n = len(self.tiles)
                self.gate0 = acc_at["gate_" + key]
                self.f0 = acc_at.get("post_" + key)
                self.ss, self.sum, self.ms, self.rs = stats(2 * n), stats(n), stats(n), stats(n)
                self.index = len(posts)
                self.gates_before = sum(len(p.streams) for p in posts.values())
                self.tiles_before = sum(len(p.tiles) for p in posts.values())
                posts[key] = self

            def pool_gate(self, pool):
                pool.wait_ge(mod_ready, 2 * DEPTH)
                self.free(pool)
                for i, s in enumerate(self.streams):
                    for kt in range(KT):
                        ins = pool.tensor_scalar(self.diag[:, i, kt, :], ident, mod_gate[:, self.l, self.w, kt, s:s + 1], None, ALU.mult)
                    ins.then_inc(gate_diag, 1)

            def pool_rstd(self, pool):
                pool.wait_ge(post_mean, self.index + 1)
                pool.tensor_tensor(self.rs[:, :], self.ms[:, :], half[:, 0:len(self.tiles)], ALU.pow).then_inc(post_rstd, 1)

            def tensor_gate(self, pe):
                for i in range(len(self.streams)):
                    pe.wait_ge(gate_diag, self.gates_before + i + 1)
                    for hf in range(2):
                        ps = claim(pe, "acc", self.gate0 + 2 * i + hf)
                        pe.matmul(ps[:, :], ones, self.diag[:, i, 4 * hf:4 * hf + 4, :].rearrange("p a b -> p (a b)"),
                                  start=True, stop=True).then_inc(acc_full, 1)

            def scalar_gate(self, act):
                for i in range(len(self.streams)):
                    for hf in range(2):
                        f = self.gate0 + 2 * i + hf
                        act.activation(self.gate[:, i, hf * 512:(hf + 1) * 512], filled(act, "acc", f)[:, :], ACT.Copy).then_inc(drain("acc", f), 1)

            def scalar(self, act):
                n = len(self.tiles)

                def squares(hf):
                    for t in range(n):
                        ps = filled(act, "acc", self.f0 + hf * n + t)
                        act.activation(self.o[:, t, hf * 512:(hf + 1) * 512], ps[:, :], ACT.Square,
                                       accum_out=self.ss[:, hf * n + t:hf * n + t + 1]).then_inc(post_squared, 1)

                tok_walk(act, ahead_act, self.product, self.kts, 2, squares, last=False)

            def vector(self, dve):
                n = len(self.tiles)

                def keep_product(hf):
                    self.gate_wait(dve)
                    for t in range(n):
                        f = self.f0 + hf * n + t
                        dve.wait_ge(post_squared, 2 * self.tiles_before + hf * n + t + 1)
                        cols = slice(hf * 512, (hf + 1) * 512)
                        dve.tensor_tensor(self.o[:, t, cols], bank("acc", f)[:, :], self.gate_of(t)[:, cols], ALU.mult).then_inc(drain("acc", f), 1)

                tok_walk(dve, ahead_dve, self.product, self.kts, 2, keep_product, last=False)
                for f in range(self.f0 + 2 * n - 4, self.f0 + 2 * n):
                    wait_drained(dve, "acc", f)
                link(dve, dve.tensor_tensor(self.sum[:, :], self.ss[:, 0:n], self.ss[:, n:2 * n], ALU.add))
                self.mean(dve)
                self.update(dve)

            def add_round(self, dve, key, first):
                def add(hf):
                    for t in range(len(self.tiles)):
                        f = acc_at[key] + len(self.tiles) * hf + t
                        ps, o = filled(dve, "acc", f), self.o[:, t, hf * 512:(hf + 1) * 512]
                        if first:
                            ins = dve.tensor_copy(o, ps[:, :])
                        else:
                            ins = dve.tensor_tensor(o, o, ps[:, :], ALU.add)
                        ins.then_inc(drain("acc", f), 1)

                tok_walk(dve, ahead_dve, key, ET, 2, add, last=key != ("ff2", EIGHTHS - 1))

            def gate_of(self, t):
                return self.gate[:, self.streams.index(self.tiles[t][0]), :]

            def gate_wait(self, eng):
                for f in range(self.gate0, self.gate0 + 2 * len(self.streams)):
                    wait_drained(eng, "acc", f)

            def scalar_rounds(self, act, last):
                n = len(self.tiles)
                for t in range(n):
                    wait_drained(act, "acc", acc_at[last] + n + t)
                    act.activation(self.squares[:, t, :], self.o[:, t, :], ACT.Square, accum_out=self.sum[:, t:t + 1]).then_inc(post_squared, 2)

            def vector_rounds(self, dve, last):
                n = len(self.tiles)
                self.gate_wait(dve)
                for t in range(n):
                    wait_drained(dve, "acc", acc_at[last] + n + t)
                    dve.wait_ge(post_squared, 2 * self.tiles_before + 2 * t + 2)
                    if t == n - 1:
                        self.mean(dve)
                    dve.tensor_tensor(self.o[:, t, :], self.o[:, t, :], self.gate_of(t), ALU.mult).then_inc(post_gated, 1)
                dve.wait_ge(post_gated, n)
                self.update(dve)

            def mean(self, dve):
                dve.tensor_scalar(self.ms[:, :], self.sum[:, :], 1.0 / D, EPS, ALU.mult, ALU.add).then_inc(post_mean, 1)

            def update(self, dve):
                dve.wait_ge(post_rstd, self.index + 1)
                for t, (s, h) in enumerate(self.tiles):
                    dve.scalar_tensor_tensor(h, self.o[:, t, :], self.rs[:, t:t + 1], h, ALU.mult, ALU.add).then_inc(h_updated, 1)

            def updated(self, eng, stream=0, tt=TT - 1):
                eng.wait_ge(h_updated, self.tiles_before + len(self.tiles) - (TT if stream else 0) - (TT - 1 - tt))

        hid_squared, hid_high, hid_ready = sem("hid_squared"), sem("hid_high"), sem("hid_ready")

        def hidden_act(act, key, n0, n, place):
            for i in range(n + 1):
                if i < n:
                    f = acc_at[key] + i
                    lo = place(i)[1]
                    ps = filled(act, "acc", f)
                    act.activation(lo, ps[:, 0:lo.shape[1]], ACT.Relu).then_inc(drain("acc", f), 1)
                if i:
                    hi, lo = place(i - 1)
                    act.wait_ge(hid_squared, n0 + i)
                    act.activation(r32(hi), lo, ACT.Copy).then_inc(hid_high, 1)
                if i < n and i % 2:
                    ahead_act(act, chunk_at[key] + i // 2 + HIGH)

        def hidden_dve(dve, key, n0, n, place):
            for i in range(n + 1):
                if i < n:
                    lo = place(i)[1]
                    wait_drained(dve, "acc", acc_at[key] + i)
                    dve.tensor_tensor(lo, lo, lo, ALU.mult).then_inc(hid_squared, 1)
                if i:
                    hi, lo = place(i - 1)
                    dve.wait_ge(hid_high, n0 + i)
                    dve.tensor_tensor(r32(lo), lo, r32(hi), ALU.subtract).then_inc(hid_ready, 1)
                if i < n and i % 2:
                    ahead_dve(dve, chunk_at[key] + i // 2 + HIGH)

        def eighth(e):
            return ("ff1", e), e * ET, ET, lambda i: tuple(v[:, e % 2, i, :] for v in hid)

        def ff0_tensor(pe, post):
            for s in (1, 0):
                norm_wait(pe, ("ff", 0, s))
            for e in range(EIGHTHS + 1):
                if e < EIGHTHS:
                    feat_gemm(pe, ("ff1", e), acc_at[("ff1", e)], ET, lambda kt: both(uT, lambda v: v[:, kt, :]))
                if e == 0:
                    post.tensor_gate(pe)
                else:
                    pe.wait_ge(hid_ready, e * ET)
                    tok_gemm(pe, ("ff2", e - 1), acc_at[("ff2", e - 1)], ET, [ALL] * 2,
                             lambda kt, tt: both(hid, lambda v: v[:, (e - 1) % 2, kt, tt * P:(tt + 1) * P]))

        def ff0_scalar(act, post):
            for e in range(EIGHTHS + 1):
                if e < EIGHTHS:
                    hidden_act(act, *eighth(e))
                if e == 0:
                    post.scalar_gate(act)
                    near_dma(act)
                else:
                    tok_walk(act, ahead_act, ("ff2", e - 1), ET, 2, last=e < EIGHTHS)
            post.scalar_rounds(act, ("ff2", EIGHTHS - 1))

        def ff0_vector(dve, post):
            for e in range(EIGHTHS + 1):
                if e < EIGHTHS:
                    hidden_dve(dve, *eighth(e))
                if e:
                    post.add_round(dve, ("ff2", e - 1), e == 1)
            near_dve(dve, range(4))
            post.vector_rounds(dve, ("ff2", EIGHTHS - 1))
            near_dve(dve, range(4, 8))

        ff1_tiles = ("ff1_1", FT2, FT2, lambda i: tuple(v[:, i, :] for v in hid1))

        def ff1_tensor(pe, post):
            norm_wait(pe, ("ff", 1, 0))
            feat_gemm(pe, "ff1_1", acc_at["ff1_1"], FT2, lambda kt: both(uT1, lambda v: v[:, kt, :]))
            post.tensor_gate(pe)
            tok_gemm(pe, "ff2_1", post.f0, FT2, [LAT] * 2, lambda kt, tt: both(hid1, lambda v: v[:, kt, tt * P:(tt + 1) * P]),
                     lambda n: pe.wait_ge(hid_ready, FT2 + n))

        r5 = Region(0)
        dk_tok = r5.take(4, 256)
        dv_tok = r5.take(4, P)
        dq_tok = r5.take(2, 512)
        gain_row = r5.take(2, HD)
        assert r5.at <= N_BIAS * SEQ
        r5 = Region(at2)
        near = r5.take(2, 8, SEQ)
        cv_tok = r5.take(4, 512)
        cqT = r5.take(4, SEQ)
        ckT = r5.take(4, S2)
        dqT = r5.take(4, SEQ)
        dkT = r5.take(2, S2)
        at_y2 = r5.at
        y2 = r5.take(TT, D)
        r5 = Region(at_y2)
        rope2 = r5.take(2, 512)
        sq2 = r5.take(2, 512)
        yT2 = uT1
        r5 = Region(at1 + 2 * KT * SEQ)
        prob2 = r5.take(2, 2, 512)
        prob2T = r5.take(2, 1024)
        assert r5.at <= at2
        r5 = Region(at_ff0_end)
        hankels = [v.rearrange("p (h k) -> p h k", h=8) for v in (xn.rearrange("p t d -> p (t d)"), r5.take(8 * SEQ))]
        r5 = Region(at2)
        o_mix1 = r5.take(TT, D)
        gate_mix1 = xn[:, 1:2, :]
        diag_mix1 = xn[:, 0:1, :].rearrange("p t (k c) -> p t k c", c=P)

        def near_dma(act):
            for f in range(4):
                wait_drained(act, "acc", acc_at["gate_ff0"] + f)
            act.dma_start(gain_row[:, 0, :], I["d_q_gain_2"].partition_broadcast(P)).then_inc(gains_landed, 16)
            act.dma_start(gain_row[:, 1, :], I["d_k_gain_2"].partition_broadcast(P)).then_inc(gains_landed, 16)
            rpb = I["c_rpb_2"]
            nd, nc_ = 2 * NA_KH - 1, 2 * NA_KW - 1
            for qt in range(2):
                for i in range(2):
                    r = 2 * qt + i
                    for h in range(8):
                        src = bass.AP(tensor=rpb.tensor, offset=(h * nd + NA_KH - 1 - r) * nc_ + NA_KW - 1 - (GRID_W - 1),
                                      ap=[[1, GRID_W], [nc_, 4], [1, GRID_W]])
                        act.dma_start(hankels[qt][i * GRID_W:(i + 1) * GRID_W, h, :].rearrange("p (t k) -> p t k", t=4), src)\
                          .then_inc(near_landed, 16)

        def near_pe(pe):
            pe.wait_ge(near_landed, 16 * 32)
            for i in range(8):
                ps = claim(pe, "acc", acc_at["near"] + i)
                pe.matmul(ps[:, :], flip64, hankels[i // 4][:, 2 * (i % 4):2 * (i % 4) + 2, :].rearrange("p a b -> p (a b)"),
                          start=True, stop=True).then_inc(acc_full, 1)

        def near_used(eng):
            eng.wait_ge(acc_full, acc_at["near"] + 4)

        def near_dve(dve, banks):
            for i in banks:
                f = acc_at["near"] + i
                win = const("near")[:, (i // 4) * SEQ:(i // 4 + 1) * SEQ].unsqueeze(1).broadcast_to([P, 2, SEQ])
                dve.tensor_tensor(near[:, i // 4, 2 * (i % 4):2 * (i % 4) + 2, :],
                                  filled(dve, "acc", f)[:, :].rearrange("p (a b) -> p a b", a=2), win, ALU.add).then_inc(drain("acc", f), 1)

        PQ, PK, PV, PDQ, PDK = (lambda: [acc_at["proj1"] + n for n in (0, 4, 8, 12, 14)])()
        d_mean, d_rstd, d_normed, gains_landed = sem("d_mean"), sem("d_rstd"), sem("d_normed"), sem("gains_landed")
        d_ss, d_ms, d_rs = stats(48), stats(48), stats(48)
        D_UNITS = [(dk_tok[:, tt, :], PDK + tt, 4, 16 + 4 * tt, tt - 2 if tt >= 2 else None) for tt in ALL]
        D_UNITS = [(dq_tok[:, tt, :], PDQ + tt, 8, 8 * tt, tt) for tt in range(TT)] + D_UNITS

        def proj1_pe(pe):
            for s in (1, 0):
                norm_wait(pe, ("mix", 1, s))
            feat_gemm(pe, "proj1", PQ, 4, lambda kt: both(uT, lambda v: v[:, kt, SEQ:S2]))
            feat_gemm(pe, "proj1_k", PK, 4, lambda kt: both(uT, lambda v: v[:, kt, :]))
            tok_gemm(pe, "proj1_tok", PV, KT, [ALL, LATS, ALL], lambda kt, tt: both(uT, lambda v: v[:, kt, tt * P:(tt + 1) * P]))
            for n, (x, f, nh, c, lat) in enumerate(D_UNITS):
                pe.wait_ge(d_normed, n + 1)
                ps = claim(pe, "tr", tr_at["proj1"] + n)
                for j in range(nh // 2):
                    ins = pe.transpose(ps[:, j * P:(j + 1) * P], x[:, j * P:(j + 1) * P], ident)
                ins.then_inc(tr_full, 1)

        def proj1_act(act):
            for i in range(4):
                act.activation(cqT[:, i, :], filled(act, "acc", PQ + i)[:, 0:SEQ], ACT.Copy, scale=SCALE).then_inc(drain("acc", PQ + i), 1)
                if i % 2:
                    ahead_act(act, chunk_at["proj1"] + i // 2 + HIGH)
            for i in range(4):
                act.activation(ckT[:, i, :], filled(act, "acc", PK + i)[:, :], ACT.Copy).then_inc(drain("acc", PK + i), 1)
                if i % 2:
                    ahead_act(act, chunk_at["proj1_k"] + i // 2 + HIGH)

            def c_values():
                for tt in ALL:
                    act.activation(cv_tok[:, tt, :], filled(act, "acc", PV + tt)[:, :], ACT.Copy).then_inc(drain("acc", PV + tt), 1)

            def d_units(units):
                for n in units:
                    x, f, nh, c, lat = D_UNITS[n]
                    ps = filled(act, "acc", f)
                    if n >= 2:
                        act.wait_ge(d_mean, n - 1)
                    if nh == 8:
                        act.activation(x, ps[:, :], ACT.Copy)
                        act.activation(sq2[:, n % 2, :], ps[:, :], ACT.Square).then_inc(drain("acc", f), 1)
                    else:
                        act.activation(x.rearrange("p (k n e) -> p k n e", k=2, n=2), dup_heads(ps[:, 0:P]), ACT.Copy)
                        act.activation(dv_tok[:, (n - 2), :], ps[:, P:2 * P], ACT.Copy)
                        act.activation(sq2[:, n % 2, 0:4 * HD].rearrange("p (k n e) -> p k n e", k=2, n=2), dup_heads(ps[:, 0:P]),
                                       ACT.Square).then_inc(drain("acc", f), 1)

            tok_walk(act, ahead_act, "proj1_tok", KT, 3, lambda b: c_values() if b == 0 else d_units(range(2) if b == 1 else range(2, 6)))
            for n, (x, f, nh, c, lat) in enumerate(D_UNITS):
                if n >= 2:
                    t = tr_at["proj1"] + n
                    act.activation(dkT[:, :, (n - 2) * P:(n - 1) * P], filled(act, "tr", t)[:, 0:2 * P].rearrange("p (a b) -> p a b", a=2),
                                   ACT.Copy).then_inc(drain("tr", t), 1)
                else:
                    t = tr_at["proj1"] + n
                    act.activation(dqT[:, :, n * P:(n + 1) * P], filled(act, "tr", t)[:, :].rearrange("p (a b) -> p a b", a=4),
                                   ACT.Copy, scale=SCALE).then_inc(drain("tr", t), 1)

        def proj1_pool(pool):
            for n, (x, f, nh, c, lat) in enumerate(D_UNITS):
                pool.wait_ge(d_mean, n + 1)
                pool.tensor_tensor(d_rs[:, c:c + nh], d_ms[:, c:c + nh], half[:, 0:nh], ALU.pow).then_inc(d_rstd, 1)

        def proj1_dve(dve):
            dve.wait_ge(gains_landed, 32)
            for key in ("proj1", "proj1_k"):
                for i in range(2):
                    wait_drained(dve, "acc", (PQ if key == "proj1" else PK) + 2 * i + 1)
                    ahead_dve(dve, chunk_at[key] + i + HIGH)

            def means(units):
                for n in units:
                    mean(n, *D_UNITS[n])

            def mean(n, x, f, nh, c, lat):
                wait_drained(dve, "acc", f)
                link(dve, dve.tensor_reduce(d_ss[:, c:c + nh], sq2[:, n % 2, 0:nh * HD].rearrange("p (h e) -> p h e", e=HD), AX_X, ALU.add))
                dve.tensor_scalar(d_ms[:, c:c + nh], d_ss[:, c:c + nh], 1.0 / HD, EPS, ALU.mult, ALU.add).then_inc(d_mean, 1)

            tok_walk(dve, ahead_dve, "proj1_tok", KT, 3, lambda b: means(range(2) if b == 1 else range(2, 6)) if b else None)
            for n, (x, f, nh, c, lat) in enumerate(D_UNITS):
                dve.wait_ge(d_rstd, n + 1)
                xh = x.rearrange("p (h e) -> p h e", e=HD)
                link(dve, dve.tensor_tensor(xh, xh, d_rs[:, c:c + nh].unsqueeze(2).broadcast_to([P, nh, HD]), ALU.mult))
                ins = dve.tensor_tensor(xh, xh, gain_row[:, 0 if n < 2 else 1, :].unsqueeze(1).broadcast_to([P, nh, HD]), ALU.mult)
                if lat is not None:
                    link(dve, ins)
                    rope(dve, x, nh, lat, rope2, d_normed, n + 1)
                else:
                    ins.then_inc(d_normed, 1)

        def attC():
            return Attention("attC", 8, lambda u, m: heads(cqT, u, m, slice((u % 2) * P, (u % 2 + 1) * P)),
                             lambda u, m: heads(ckT, u, m, slice(0, S2)), lambda u: S2,
                             lambda u, m, kb: cv_tok[:, kb, (2 * (u // 2) + m) * HD:(2 * (u // 2) + m + 1) * HD],
                             lambda u: y2[:, u % 2, (u // 2) * P:(u // 2 + 1) * P], prob2, prob2T,
                             bias=lambda u, m: (SEQ, near[:, u % 2, 2 * (u // 2) + m, :]))

        def attD():
            return Attention("attD", 8, lambda u, m: heads(dqT, u, m, slice((u % 2) * P, (u % 2 + 1) * P)),
                             lambda u, m: dkT[m * HD:(m + 1) * HD, kv_of(u), :], lambda u: S2,
                             lambda u, m, kb: dv_tok[:, kb, kv_of(u) * HD:(kv_of(u) + 1) * HD],
                             lambda u: y2[:, u % 2, 512 + (u // 2) * P:512 + (u // 2 + 1) * P], prob2, prob2T)

        yT2_high = sem("yT2_high")

        def yT2_pe(pe, atts):
            for att in atts:
                for u in (6, 7):
                    wait_drained(pe, "sc", att.sc[u])
            for g in range(4):
                f = tr_at["yT1_2"] + g
                ps = claim(pe, "tr", f)
                for i in range(2):
                    for tt in range(TT):
                        kt = 2 * g + i
                        ins = pe.transpose(ps[:, i * SEQ + tt * P:i * SEQ + (tt + 1) * P], y2[:, tt, kt * P:(kt + 1) * P], ident)
                ins.then_inc(tr_full, 1)

        def yT2_act(act):
            for g in range(4):
                act.activation(r32(yT2[0][:, 2 * g:2 * g + 2, :].rearrange("p a b -> p (a b)")),
                               filled(act, "tr", tr_at["yT1_2"] + g)[:, :], ACT.Copy).then_inc(yT2_high, 1)

        def yT2_dve(dve):
            for g in range(4):
                f = tr_at["yT1_2"] + g
                hi, lo = (v[:, 2 * g:2 * g + 2, :].rearrange("p a b -> p (a b)") for v in yT2)
                ps = filled(dve, "tr", f)
                dve.wait_ge(yT2_high, g + 1)
                dve.tensor_tensor(r32(lo), ps[:, :], r32(hi), ALU.subtract).then_inc(drain("tr", f), 1)


        att = {("att1", l): att1(l) for l in range(DEPTH)}
        att_bl, att_bc, att_c, att_d = attBl(), attBc(), attC(), attD()

        def after_norm(key):
            return lambda pool: pool.wait_ge(tr_full, tr_at[("norm", key)] + 4)

        mix0 = Post("mix0", 0, 0, (1, 0), o_mix0, gate_mix0, diag_mix0, None, scan_over, "out2_0", KT)
        ff0 = Post("ff0", 0, 1, (1, 0), o_ff0, gate_ff, diag_ff,
                   uT[0].rearrange("p a b -> p (a b)").rearrange("p (t d) -> p t d", d=D), after_norm(("ff", 0, 0)))
        mix1 = Post("mix1", 1, 0, (0,), o_mix1, gate_mix1, diag_mix1, None, after_norm(("mix", 1, 0)), "out2_1", KT)
        ff1 = Post("ff1", 1, 1, (0,), o_ff1, gate_ff, diag_ff, None, after_norm(("ff", 1, 0)), "ff2_1", FT2)

        def ctx_ready(eng, tt=TT - 1):
            eng.wait_ge(ctx_landed, 16)

        def mod_norms(l, w):
            out = []
            for s in ((1, 0) if (l, w) != (1, 1) else (0,)):
                if (l, w) == (0, 0):
                    ready = ctx_ready if s else stream_ready(DEPTH, "attn")
                else:
                    post = {(0, 1): mix0, (1, 0): ff0, (1, 1): mix1}[l, w]
                    ready = lambda eng, tt=TT - 1, post=post, s=s: post.updated(eng, s, tt)
                dst = uT1 if (l, w) == (1, 1) else tuple(v[:, :, SEQ:] if s == 0 else v[:, :, 0:SEQ] for v in uT)
                out.append((("ff" if w else "mix", l, s), h_ctx if s else h_lat, ready, mod_mul(l, w, s), mod_shift(l, w, s), dst))
            return out
        out_stored = sem("out_stored")

        def stream_ready(l, which):
            def ready(eng, tt=TT - 1):
                if l == 0 and which == "attn":
                    eng.wait_ge(x_landed, 16)
                    return
                f = acc_at[("out1", l)] if which == "ffn" else acc_at[("down1", l - 1)]
                for i in range(3 + tt):
                    wait_drained(eng, "acc", f + i)
            return ready

        def mix_lhs(y):
            return lambda kt, tt: both(y, lambda v: v[:, kt, tt * P:(tt + 1) * P])

        block = ctx.enter_context(nc.Block())

        def norm_scalar(act, following, *norms):
            for norm in norms:
                norm_act(act, *norm)
            ahead_act(act, chunk_at[following] + HIGH - 1)
            for norm in norms:
                norm_high(act, *norm)

        def first_norm(l, which):
            gain = lambda kt: col("ln_attn_g" if which == "attn" else "ln_ffn_g", KT * l + kt)
            return (which, l), h_lat, stream_ready(l, which), gain, None, hT

        @block.sync
        def _(sp):
            first_sync_dma(sp)
            for g in range(len(chunks)):
                if g == 1:
                    setup_sync_dma(sp)
                if g == RAW:
                    later_sync_dma(sp)
                    t5_sync_dma(sp)
                if g == chunk_at["out2_0"]:
                    scan_over(sp)
                if g >= RAW:
                    sp.wait_ge(*release[g - RAW])
                load(sp, g)
            ff1.updated(sp)
            sp.dma_start(out.rearrange("(t p) d -> p t d", p=P), h_lat[:, :, :]).then_inc(out_stored, 16)
            sp.wait_ge(out_stored, 16)

        @block.gpsimd
        def _(pool):
            setup_pool(pool)
            for l in range(DEPTH):
                norm_pool(pool, ("attn", l))
                qkv_pool(pool, l)
                subnorm_pool(pool, l)
                norm_pool(pool, ("ffn", l))
                up1_pool(pool, l)
            for key, *_ in mod_norms(0, 0):
                norm_pool(pool, key)
            kk_pool(pool)
            prep_pool(pool)
            for s in range(NCH):
                step_pool(pool, s)
            mix0.pool_gate(pool)
            rwkv_out_pool(pool)
            mix0.pool_rstd(pool)
            for key, *_ in mod_norms(0, 1):
                norm_pool(pool, key)
            ff0.pool_gate(pool)
            ff0.pool_rstd(pool)
            for key, *_ in mod_norms(1, 0):
                norm_pool(pool, key)
            mix1.pool_gate(pool)
            proj1_pool(pool)
            mix1.pool_rstd(pool)
            for key, *_ in mod_norms(1, 1):
                norm_pool(pool, key)
            ff1.pool_gate(pool)
            ff1.pool_rstd(pool)

        @block.scalar
        def _(act):
            norm_act(act, *first_norm(0, "attn"))
            ahead_act(act, 0)
            setup_bias_act(act)
            norm_high(act, *first_norm(0, "attn"))
            ahead_act(act, HIGH - 1)
            for l in range(DEPTH):
                if l:
                    norm_scalar(act, ("qkv", l), first_norm(l, "attn"))
                qkv_act(act, l)
                att[("att1", l)].scalar(act, subnorm_act(act, l, att[("att1", l)]))
                yT1_act(act, l)
                ahead_act(act, chunk_at[("out1", l)] + HIGH - 1)
                tok_walk(act, ahead_act, ("out1", l), KT, 2, last=False)
                norm_scalar(act, ("up1", l), first_norm(l, "ffn"))
                up1_act(act, l)
                tok_walk(act, ahead_act, ("down1", l), FT, 2, last=False)
            norm_scalar(act, "projA", *mod_norms(0, 0))
            projA_act(act)
            projB_act(act)
            att_bl.scalar(act)
            att_bc.scalar(act)
            yTB_act(act)
            act.dma_start(lora[:, 0, :], I["a_w2_2"][0].rearrange("d l c -> (d l) c")).then_inc(lora_landed, 16)
            act.dma_start(lora[:, 1, :], I["a_a2_2"][0].rearrange("d l c -> (d l) c")).then_inc(lora_landed, 16)
            kk_act(act)
            prep_act(act)
            for s in range(NCH):
                step_act(act, s)
            scan_over(act)
            held[0] = False
            mix0.scalar_gate(act)
            ahead_act(act, chunk_at["out2_0"] + HIGH - 1)
            rwkv_out_act(act)
            mix0.scalar(act)
            norm_scalar(act, ("ff1", 0), *mod_norms(0, 1))
            ff0_scalar(act, ff0)
            norm_scalar(act, "proj1", *mod_norms(1, 0))
            proj1_act(act)
            mix1.scalar_gate(act)
            att_c.scalar(act)
            att_d.scalar(act)
            yT2_act(act)
            mix1.scalar(act)
            norm_scalar(act, "ff1_1", *mod_norms(1, 1))
            hidden_act(act, *ff1_tiles)
            ff1.scalar_gate(act)
            ff1.scalar(act)

        @block.tensor
        def _(pe):
            setup_pe(pe)
            for l in range(DEPTH):
                norm_pe(pe, ("attn", l))
                if l == 0:
                    setup_bias_pe(pe)
                qkv_pe(pe, l)
                if l == 0:
                    t5_pe(pe)
                    later_params_pe(pe)
                att[("att1", l)].tensor(pe)
                yT1_pe(pe, l, att[("att1", l)])
                out1_pe(pe, l)
                norm_pe(pe, ("ffn", l))
                up1_pe(pe, l)
                down1_pe(pe, l)
            for key, *_ in mod_norms(0, 0):
                norm_pe(pe, key)
            projA_pe(pe)
            projB_pe(pe)
            projB_wait(pe)
            att_bl.tensor(pe)
            att_bc.tensor(pe)
            yTB_pe(pe, (att_bl, att_bc))
            kk_pe(pe)
            prep_pe(pe, range(2, 8))
            for s in range(NCH):
                step_pe(pe, s)
            mix0.tensor_gate(pe)
            rwkv_out_pe(pe)
            pe.wait_ge(yA_low, 4)
            for tt in (2, 3):
                wait_drained(pe, "tr", tr_at["yTB"] + tt)
            tok_gemm(pe, "out2_0", mix0.f0, KT, [ALL] * 2, mix_lhs(yT))
            for key, *_ in mod_norms(0, 1):
                norm_pe(pe, key)
            ff0_tensor(pe, ff0)
            near_pe(pe)
            for key, *_ in mod_norms(1, 0):
                norm_pe(pe, key)
            proj1_pe(pe)
            mix1.tensor_gate(pe)
            for n in (4, 5):
                wait_drained(pe, "tr", tr_at["proj1"] + n)
            for i in range(4, 8):
                wait_drained(pe, "acc", acc_at["near"] + i)
            att_c.tensor(pe)
            att_d.tensor(pe)
            yT2_pe(pe, (att_c, att_d))
            for g in (2, 3):
                wait_drained(pe, "tr", tr_at["yT1_2"] + g)
            tok_gemm(pe, "out2_1", mix1.f0, KT, [LAT] * 2, mix_lhs(yT2))
            for key, *_ in mod_norms(1, 1):
                norm_pe(pe, key)
            ff1_tensor(pe, ff1)

        @block.vector
        def _(dve):
            lambda_dve(dve)
            setup_dve(dve)
            for l in range(DEPTH):
                norm_dve(dve, *first_norm(l, "attn"))
                if l == 0:
                    ahead_dve(dve, 0)
                    setup_bias_dve(dve)
                ahead_dve(dve, chunk_at[("qkv", l)] + HIGH - 1)
                qkv_dve(dve, l)
                if l == 0:
                    t5_dve(dve)
                    later_params_dve(dve)
                att[("att1", l)].vector(dve, subnorm_dve(dve, l, att[("att1", l)]))
                if l == 1:
                    ada_gains(dve, att[("att1", l)], 0)
                yT1_dve(dve, l)
                ahead_dve(dve, chunk_at[("out1", l)] + HIGH - 1)
                add_dve(dve, ("out1", l), KT)
                norm_dve(dve, *first_norm(l, "ffn"))
                ahead_dve(dve, chunk_at[("up1", l)] + HIGH - 1)
                up1_dve(dve, l)
                add_dve(dve, ("down1", l), FT)
            dve.wait_ge(mod_ready, 2)
            for norm in mod_norms(0, 0):
                norm_dve(dve, *norm)
            ahead_dve(dve, chunk_at["projA"] + HIGH - 1)
            projA_dve(dve)
            projB_dve(dve)
            att_bl.vector(dve)
            att_bc.vector(dve)
            ada_gains(dve, att_bc, 1)
            yTB_dve(dve)
            kk_dve(dve)
            prep_dve(dve, range(1, 8))
            for d in range(2):
                step_ar(dve, d, 0)
            for s in range(NCH):
                step_dve(dve, s)
            scan_over(dve)
            held[1] = False
            rwkv_out_dve(dve)
            mix0.vector(dve)
            for norm in mod_norms(0, 1):
                norm_dve(dve, *norm)
            ahead_dve(dve, chunk_at[("ff1", 0)] + HIGH - 1)
            ff0_vector(dve, ff0)
            near_used(dve)
            for norm in mod_norms(1, 0):
                norm_dve(dve, *norm)
            ahead_dve(dve, chunk_at["proj1"] + HIGH - 1)
            proj1_dve(dve)
            att_c.vector(dve)
            att_d.vector(dve)
            yT2_dve(dve)
            mix1.vector(dve)
            for norm in mod_norms(1, 1):
                norm_dve(dve, *norm)
            ahead_dve(dve, chunk_at["ff1_1"] + HIGH - 1)
            hidden_dve(dve, *ff1_tiles)
            ff1.vector(dve)


_INS = ["x", "ln_attn_g", "w_in", "qk_norm_g", "diff_lambda", "diff_subln_g", "w_out", "ln_ffn_g", "w_up", "conv_w",
        "conv_b", "w_down", "rel_bias", "c_2", "ctx_2", "c_ctx_2", "w_ada_2", "b_ada_2", "g_pre_mix_2", "g_post_mix_2",
        "g_pre_ff_2", "g_post_ff_2", "w_in_even_2", "w_in_odd_2", "w_out_2", "w_ff1_2", "w_ff2_2", "a_mu_prev_2",
        "a_mu_next_2", "a_w0_2", "a_w2_2", "a_a0_2", "a_a2_2", "a_g2_2", "a_k_k_2", "a_k_a_2", "a_r_k_2", "a_gn_w_2",
        "a_gn_b_2", "b_sink_2", "c_rpb_2", "d_q_gain_2", "d_k_gain_2"]


def kernel(**inputs):
    import concourse.bacc as _bacc
    from concourse.bass_utils import run_bass_kernel_spmd as _run

    nc = _bacc.Bacc("TRN2", target_bir_lowering=False, num_devices=1)
    arrays, dram = {}, {}
    for name in _INS:
        a = np.ascontiguousarray(inputs[name])
        arrays[f"in_{name}"] = a
        dram[name] = nc.dram_tensor(f"in_{name}", a.shape, mybir.dt.from_np(a.dtype), kind="ExternalInput").ap()
    consts = []
    for name, a in (("const_keep", KEEP), ("const_first", FIRST)):
        arrays[name] = a
        consts.append(nc.dram_tensor(name, a.shape, mybir.dt.from_np(a.dtype), kind="ExternalInput").ap())
    out = nc.dram_tensor("out", (1, SEQ, D), F32, kind="ExternalOutput").ap()
    first_and_second_block(nc, dram, consts, out[0])
    r = _run(nc, [arrays], core_ids=[0])
    return r.results[0]["out"]
```
